# Optimizing a Trainium2 kernel written in Bass

```python
import math
import jax, jax.numpy as jnp
from jax import lax
import numpy as np

D_MODEL = 1024
BATCH = 1
SEQ = 512
DEPTH = 1

GRID_W = 64
CTX_LEN = 256
N_ADA = 6
DIFF_HEADS = 8
DIFF_DH = 64
Q_W = 2 * DIFF_HEADS * DIFF_DH
K_W = 2 * DIFF_HEADS * DIFF_DH
V_W = DIFF_HEADS * 2 * DIFF_DH
ATTN_OUT = V_W
Q_BLK = 128
ROPE_BASE = 10000.0
SGU_CHUNK = 128
SGU_GROUPS = 8
SGU_W = 1024
SGU_GROUP_W = SGU_W // SGU_GROUPS
Z_W = 2 * SGU_W
GATE_W = 2 * D_MODEL
IN_W = Q_W + K_W + V_W + Z_W + GATE_W
PEER_HEADS = 8
PEER_N_KEYS = 128
PEER_N_EXPERTS = PEER_N_KEYS * PEER_N_KEYS
PEER_TOPK = 16
PEER_PK_DIM = 128
PEER_Q_DIM = 2 * PEER_PK_DIM
PEER_BLK = 128
RMS_EPS = 1e-6


def rmsnorm(x, g=None, eps=RMS_EPS):
    xf = x.astype(jnp.float32)
    y = xf * lax.rsqrt(jnp.mean(xf * xf, axis=-1, keepdims=True) + eps)
    if g is not None:
        y = y * g.astype(jnp.float32)
    return y.astype(x.dtype)

def layernorm(x, g, b, eps=1e-5):
    xf = x.astype(jnp.float32)
    mu = jnp.mean(xf, axis=-1, keepdims=True)
    xc = xf - mu
    y = xc * lax.rsqrt(jnp.mean(xc * xc, axis=-1, keepdims=True) + eps)
    return (y * g.astype(jnp.float32) + b.astype(jnp.float32)).astype(x.dtype)

def modulate(h, shift, scale):
    return h * (1.0 + scale) + shift

def _rotate(xp, pos):
    nfreq = xp.shape[-1] // 2
    inv = ROPE_BASE ** (-jnp.arange(nfreq, dtype=jnp.float32) / nfreq)
    ang = pos.astype(jnp.float32)[:, None] * inv[None, :]
    cos = jnp.cos(ang)[None, :, None, :]
    sin = jnp.sin(ang)[None, :, None, :]
    x1 = xp[..., :nfreq].astype(jnp.float32)
    x2 = xp[..., nfreq:].astype(jnp.float32)
    return jnp.concatenate([x1 * cos - x2 * sin, x1 * sin + x2 * cos], axis=-1)

def axial_rope(x, rows, cols):
    half = x.shape[-1] // 2
    return jnp.concatenate([_rotate(x[..., :half], rows), _rotate(x[..., half:], cols)], axis=-1).astype(x.dtype)

def diff_attention(q, k, v, lam):
    B, L = q.shape[0], q.shape[1]
    Lk = k.shape[1]
    nb = L // Q_BLK
    qb = q.reshape(B, nb, Q_BLK, 2 * DIFF_HEADS, DIFF_DH).transpose(1, 0, 2, 3, 4)

    def one(qblk):
        s = jnp.einsum('bqhd,bkhd->bhqk', qblk, k).astype(jnp.float32) * (DIFF_DH ** -0.5)
        a = jax.nn.softmax(s, axis=-1).reshape(B, DIFF_HEADS, 2, Q_BLK, Lk)
        a = a[:, :, 0] - lam * a[:, :, 1]
        return jnp.einsum('bhqk,bkhe->bqhe', a.astype(v.dtype), v)

    o = lax.map(one, qb)
    return o.transpose(1, 0, 2, 3, 4).reshape(B, L, DIFF_HEADS, 2 * DIFF_DH)

def spatial_gating(z, ln_g, ln_b, w_s, b_s):
    u, v = jnp.split(z, 2, axis=-1)
    v = layernorm(v, ln_g, ln_b)
    B, L = v.shape[0], v.shape[1]
    vb = v.reshape(B, L // SGU_CHUNK, SGU_CHUNK, SGU_GROUPS, SGU_GROUP_W)
    mixed = jnp.einsum('gpq,bnqgc->bnpgc', w_s, vb) + jnp.transpose(b_s)[None, None, :, :, None]
    return u * mixed.reshape(B, L, SGU_W)

def split_proj(p):
    B, L = p.shape[0], p.shape[1]
    q, k, v, z, gl = jnp.split(p, [Q_W, Q_W + K_W, Q_W + K_W + V_W, Q_W + K_W + V_W + Z_W], axis=-1)
    q = q.reshape(B, L, 2 * DIFF_HEADS, DIFF_DH)
    k = k.reshape(B, L, 2 * DIFF_HEADS, DIFF_DH)
    v = v.reshape(B, L, DIFF_HEADS, 2 * DIFF_DH)
    return q, k, v, z, gl

def mix_branches(q, k_all, v_all, z, gate_logits, lam, lam_init, subln_g,
                 sgu_ln_g, sgu_ln_b, sgu_w, sgu_b, w_branch_attn, w_branch_sgu, w_out):
    B, L = q.shape[0], q.shape[1]
    o = diff_attention(q, k_all, v_all, lam)
    o = rmsnorm(o, subln_g) * (1.0 - lam_init)
    y_attn = o.reshape(B, L, ATTN_OUT) @ w_branch_attn
    y_sgu = spatial_gating(jax.nn.gelu(z, approximate=False), sgu_ln_g, sgu_ln_b, sgu_w, sgu_b) @ w_branch_sgu
    g_attn, g_sgu = jnp.split(jax.nn.sigmoid(gate_logits), 2, axis=-1)
    return (g_attn * y_attn + g_sgu * y_sgu) @ w_out

def peer(h, w_query, sub_keys, u_tab, v_tab):
    B, L, D = h.shape
    T = B * L
    xt = h.reshape(T, D)
    q = rmsnorm((xt @ w_query).reshape(T, PEER_HEADS, 2, PEER_PK_DIM))
    s = jnp.einsum('thpd,pnd->thpn', q, sub_keys).astype(jnp.float32)
    s1, i1 = lax.top_k(s[:, :, 0], PEER_TOPK)
    s2, i2 = lax.top_k(s[:, :, 1], PEER_TOPK)
    n_cand = PEER_TOPK * PEER_TOPK
    cand = (s1[..., :, None] + s2[..., None, :]).reshape(T, PEER_HEADS, n_cand)
    cidx = (i1[..., :, None] * PEER_N_KEYS + i2[..., None, :]).reshape(T, PEER_HEADS, n_cand)
    best, pos = lax.top_k(cand, PEER_TOPK)
    eidx = jnp.take_along_axis(cidx, pos, axis=-1)
    gate = jax.nn.softmax(best, axis=-1)
    nb = T // PEER_BLK

    def one(args):
        xb, ib, gb = args
        act = jax.nn.gelu(jnp.einsum('td,thkd->thk', xb, u_tab[ib]), approximate=False) * gb.astype(xb.dtype)
        return jnp.einsum('thk,thkd->td', act, v_tab[ib])

    out = lax.map(one, (xt.reshape(nb, PEER_BLK, D),
                        eidx.reshape(nb, PEER_BLK, PEER_HEADS, PEER_TOPK),
                        gate.reshape(nb, PEER_BLK, PEER_HEADS, PEER_TOPK)))
    return out.reshape(B, L, D)

def first_inputs(seed: int = 0) -> dict:
    key = jax.random.key(seed)
    ks = jax.random.split(key, 28)
    D = D_MODEL

    def nrm(k, shape, scale):
        return jax.random.normal(k, shape, jnp.float32) * scale

    return {
        'x': nrm(ks[0], (BATCH, SEQ, D), 1.0),
        'c': nrm(ks[1], (BATCH, D), 1.0),
        'ctx': nrm(ks[2], (BATCH, CTX_LEN, D), 1.0),
        'c_ctx': nrm(ks[3], (D,), 1.0),
        'w_ada': nrm(ks[4], (DEPTH, D, N_ADA * D), 0.2 * D ** -0.5),
        'b_ada': nrm(ks[5], (DEPTH, N_ADA * D), 0.02),
        'g_pre_mix': 1.0 + nrm(ks[6], (DEPTH, D), 0.02),
        'g_post_mix': 1.0 + nrm(ks[7], (DEPTH, D), 0.02),
        'g_pre_ffn': 1.0 + nrm(ks[8], (DEPTH, D), 0.02),
        'g_post_ffn': 1.0 + nrm(ks[9], (DEPTH, D), 0.02),
        'w_in': nrm(ks[10], (DEPTH, D, IN_W), D ** -0.5),
        'b_gate': nrm(ks[11], (DEPTH, GATE_W), 0.02),
        'lambda_q1': nrm(ks[12], (DEPTH, DIFF_DH), 0.1),
        'lambda_k1': nrm(ks[13], (DEPTH, DIFF_DH), 0.1),
        'lambda_q2': nrm(ks[14], (DEPTH, DIFF_DH), 0.1),
        'lambda_k2': nrm(ks[15], (DEPTH, DIFF_DH), 0.1),
        'subln_g': 1.0 + nrm(ks[16], (DEPTH, 2 * DIFF_DH), 0.02),
        'sgu_ln_g': 1.0 + nrm(ks[17], (DEPTH, SGU_W), 0.02),
        'sgu_ln_b': nrm(ks[18], (DEPTH, SGU_W), 0.02),
        'sgu_w': nrm(ks[19], (DEPTH, SGU_GROUPS, SGU_CHUNK, SGU_CHUNK), SGU_CHUNK ** -0.5),
        'sgu_b': 1.0 + nrm(ks[20], (DEPTH, SGU_GROUPS, SGU_CHUNK), 0.02),
        'w_branch_attn': nrm(ks[21], (DEPTH, ATTN_OUT, D), ATTN_OUT ** -0.5),
        'w_branch_sgu': nrm(ks[22], (DEPTH, SGU_W, D), SGU_W ** -0.5),
        'w_out': nrm(ks[23], (DEPTH, D, D), D ** -0.5),
        'peer_w_query': nrm(ks[24], (DEPTH, D, PEER_HEADS * PEER_Q_DIM), D ** -0.5),
        'peer_sub_keys': nrm(ks[25], (DEPTH, 2, PEER_N_KEYS, PEER_PK_DIM), PEER_PK_DIM ** -0.5),
        'peer_u': nrm(ks[26], (DEPTH, PEER_N_EXPERTS, D), D ** -0.5),
        'peer_v': nrm(ks[27], (DEPTH, PEER_N_EXPERTS, D), D ** -0.5),
    }

def first_block(x, c, ctx, c_ctx, w_ada, b_ada, g_pre_mix, g_post_mix, g_pre_ffn, g_post_ffn,
              w_in, b_gate, lambda_q1, lambda_k1, lambda_q2, lambda_k2, subln_g,
              sgu_ln_g, sgu_ln_b, sgu_w, sgu_b, w_branch_attn, w_branch_sgu, w_out,
              peer_w_query, peer_sub_keys, peer_u, peer_v):
    B, L, _ = x.shape
    Lc = ctx.shape[1]
    n_rows = L // GRID_W
    rows = jnp.repeat(jnp.arange(n_rows, dtype=jnp.int32), GRID_W)
    cols = jnp.tile(jnp.arange(GRID_W, dtype=jnp.int32), n_rows)

    for l in range(DEPTH):
        last = l == DEPTH - 1
        lam_init = 0.8 - 0.6 * math.exp(-0.3 * l)
        lam = (jnp.exp(jnp.dot(lambda_q1[l].astype(jnp.float32), lambda_k1[l].astype(jnp.float32)))
               - jnp.exp(jnp.dot(lambda_q2[l].astype(jnp.float32), lambda_k2[l].astype(jnp.float32)))
               + lam_init)
        mod = jax.nn.silu(c) @ w_ada[l] + b_ada[l]
        sh1, sc1, gt1, sh2, sc2, gt2 = [m[:, None, :] for m in jnp.split(mod, N_ADA, axis=-1)]
        mod_c = jax.nn.silu(c_ctx) @ w_ada[l] + b_ada[l]
        sh1c, sc1c, gt1c, sh2c, sc2c, gt2c = jnp.split(mod_c, N_ADA, axis=-1)

        h = modulate(rmsnorm(x, g_pre_mix[l]), sh1, sc1)
        hc = modulate(rmsnorm(ctx, g_pre_mix[l]), sh1c, sc1c)
        q, k, v, z, gl = split_proj(h @ w_in[l])
        q = axial_rope(q, rows, cols)
        k = axial_rope(k, rows, cols)
        if last:
            kv_c = hc @ w_in[l][:, Q_W:Q_W + K_W + V_W]
            kc = kv_c[..., :K_W].reshape(B, Lc, 2 * DIFF_HEADS, DIFF_DH)
            vc = kv_c[..., K_W:].reshape(B, Lc, DIFF_HEADS, 2 * DIFF_DH)
        else:
            qc, kc, vc, zc, glc = split_proj(hc @ w_in[l])
        k_all = jnp.concatenate([kc, k], axis=1)
        v_all = jnp.concatenate([vc, v], axis=1)
        y = mix_branches(q, k_all, v_all, z, gl + b_gate[l], lam, lam_init, subln_g[l],
                         sgu_ln_g[l], sgu_ln_b[l], sgu_w[l], sgu_b[l],
                         w_branch_attn[l], w_branch_sgu[l], w_out[l])
        x_new = x + gt1 * rmsnorm(y, g_post_mix[l])

        if not last:
            yc = mix_branches(qc, kc, vc, zc, glc + b_gate[l], lam, lam_init, subln_g[l],
                              sgu_ln_g[l], sgu_ln_b[l], sgu_w[l], sgu_b[l],
                              w_branch_attn[l], w_branch_sgu[l], w_out[l])
            ctx_new = ctx + gt1c * rmsnorm(yc, g_post_mix[l])
            h2c = modulate(rmsnorm(ctx_new, g_pre_ffn[l]), sh2c, sc2c)
            ctx = ctx_new + gt2c * rmsnorm(peer(h2c, peer_w_query[l], peer_sub_keys[l], peer_u[l], peer_v[l]), g_post_ffn[l])

        h2 = modulate(rmsnorm(x_new, g_pre_ffn[l]), sh2, sc2)
        x = x_new + gt2 * rmsnorm(peer(h2, peer_w_query[l], peer_sub_keys[l], peer_u[l], peer_v[l]), g_post_ffn[l])
    return x


DEPTH_2 = 2

N_MIXERS = 2
RWKV_HEAD = 64
RWKV_HEADS = D_MODEL // RWKV_HEAD
DECAY_LORA = 64
AAA_LORA = 64
MV_LORA = 32
GATE_LORA = 160
GN_EPS = 64e-5
N_RWKV_BRANCHES = 6
ATT_HEADS = 16
QK_HEAD = 64
V_HEAD = 64
Q_LORA = 256
KV_LORA = 128
IDX_HEADS = 8
IDX_DIM = 64
TOPK_MAX = 256
Q_BLOCK = 128
DSA_IN = Q_LORA + KV_LORA + IDX_DIM + IDX_HEADS
REL_BUCKETS = 32
REL_MAX_DIST = 128
D_FF = 2816
CONV_W = 3
DN_ALPHA = (2 * DEPTH_2) ** 0.25
DN_BETA = (8 * DEPTH_2) ** -0.25
LN_EPS = 1e-5


def layer_norm(x, g, b, eps=LN_EPS):
    xf = x.astype(jnp.float32)
    mu = xf.mean(-1, keepdims=True)
    var = jnp.square(xf - mu).mean(-1, keepdims=True)
    return ((xf - mu) * lax.rsqrt(var + eps) * g + b).astype(x.dtype)

def rms_norm(x, g, eps=1e-6):
    xf = x.astype(jnp.float32)
    return (xf * lax.rsqrt(jnp.square(xf).mean(-1, keepdims=True) + eps) * g).astype(x.dtype)

def token_shift(x):
    return jnp.pad(x, ((0, 0), (1, 0), (0, 0)))[:, :-1]

def t5_bucket(dist):
    n = jnp.maximum(dist, 0)
    max_exact = REL_BUCKETS // 2
    nf = jnp.maximum(n, 1).astype(jnp.float32)
    large = max_exact + (jnp.log(nf / max_exact) / math.log(REL_MAX_DIST / max_exact)
                         * (REL_BUCKETS - max_exact)).astype(jnp.int32)
    large = jnp.minimum(large, REL_BUCKETS - 1)
    return jnp.where(n < max_exact, n, large)

def _wkv7_step(state, inp):
    r_t, w_t, k_t, v_t, a_t, b_t = inp
    sa = jnp.einsum('bhvk,bhk->bhv', state, a_t)
    state = (state * w_t[:, :, None, :] + sa[..., None] * b_t[:, :, None, :]
             + v_t[..., None] * k_t[:, :, None, :])
    y = jnp.einsum('bhvk,bhk->bhv', state, r_t)
    return state, y

def rwkv7_time_mix(x, v_first, vres, mix, w_rkv, w0, w1, w2, a0, a1, a2, g1, g2,
                   k_k, k_a, r_k, lnx_g, lnx_b, w_o):
    B, S, D = x.shape
    H, N = RWKV_HEADS, RWKV_HEAD
    f32 = jnp.float32
    xx = token_shift(x) - x
    xm = x[None] + xx[None] * mix[:, None, None, :]
    r, k, v = jnp.einsum('nbsd,nde->nbse', xm[:3], w_rkv)
    xv, xw, xa, xg = xm[2], xm[3], xm[4], xm[5]
    w_log = -jax.nn.softplus(-(w0 + jnp.tanh(xw @ w1) @ w2)) - 0.5
    decay = jnp.exp(-jnp.exp(w_log.astype(f32)))
    if vres is None:
        v_first = v
    else:
        v0, v1, v2 = vres
        v = v + (v_first - v) * jax.nn.sigmoid(v0 + (xv @ v1) @ v2)
    a = jax.nn.sigmoid(a0 + (xa @ a1) @ a2)
    g = jax.nn.sigmoid(xg @ g1) @ g2
    heads = lambda t: t.reshape(B, S, H, N)
    kk = heads(k * k_k).astype(f32)
    kk = kk / jnp.maximum(jnp.sqrt(jnp.sum(kk * kk, -1, keepdims=True)), 1e-12)
    k = k * (1 + (a - 1) * k_a)
    rh, kh, vh, ah = heads(r), heads(k), heads(v), heads(a)
    tm = lambda t: jnp.moveaxis(t.astype(f32), 1, 0)
    xs = (tm(rh), tm(heads(decay)), tm(kh), tm(vh), tm(-kk), tm(kk * ah.astype(f32)))
    state0 = jnp.zeros((B, H, N, N), f32)
    _, y = lax.scan(_wkv7_step, state0, xs)
    y = jnp.moveaxis(y, 0, 1)
    mu = y.mean(-1, keepdims=True)
    var = jnp.square(y - mu).mean(-1, keepdims=True)
    y = ((y - mu) * lax.rsqrt(var + GN_EPS)).reshape(B, S, D) * lnx_g + lnx_b
    bonus = jnp.sum(rh * kh * r_k, -1, keepdims=True) * vh
    y = (y.astype(x.dtype) + bonus.reshape(B, S, D)) * g
    return y @ w_o, v_first

def dsa_attention(x, w_in, q_norm_g, kv_norm_g, w_uq, w_uk, w_uv, w_qidx, kidx_g, kidx_b,
                  rel_bias, w_o):
    B, S, D = x.shape
    H = ATT_HEADS
    topk = min(TOPK_MAX, S // 4)
    h = x @ w_in
    c_q, c_kv, k_idx, w_idx = jnp.split(
        h, [Q_LORA, Q_LORA + KV_LORA, Q_LORA + KV_LORA + IDX_DIM], axis=-1)
    c_q = rms_norm(c_q, q_norm_g)
    c_kv = rms_norm(c_kv, kv_norm_g)
    q = (c_q @ w_uq).reshape(B, S, H, QK_HEAD)
    q_idx = (c_q @ w_qidx).reshape(B, S, IDX_HEADS, IDX_DIM)
    k_idx = layer_norm(k_idx, kidx_g, kidx_b)
    w_idx = w_idx * (IDX_HEADS ** -0.5 * IDX_DIM ** -0.5)
    nb = S // Q_BLOCK
    blk = lambda t: jnp.swapaxes(t.reshape((B, nb, Q_BLOCK) + t.shape[2:]), 0, 1)
    starts = jnp.arange(nb, dtype=jnp.int32) * Q_BLOCK
    key_pos = jnp.arange(S, dtype=jnp.int32)
    qk_scale = QK_HEAD ** -0.5

    def block(args):
        q_b, qi_b, wi_b, t0 = args
        t_pos = t0 + jnp.arange(Q_BLOCK, dtype=jnp.int32)
        s_idx = jnp.einsum('bthd,bsd->bths', qi_b, k_idx)
        score = jnp.einsum('bths,bth->bts', jax.nn.relu(s_idx), wi_b).astype(jnp.float32)
        causal = key_pos[None, :] <= t_pos[:, None]
        score = jnp.where(causal[None], score, -jnp.inf)
        _, sel = lax.top_k(score, topk)
        kv_sel = jax.vmap(lambda c, i: c[i])(c_kv, sel)
        q_abs = jnp.einsum('bthd,hdc->bthc', q_b, w_uk)
        logits = jnp.einsum('bthc,btkc->bhtk', q_abs, kv_sel).astype(jnp.float32) * qk_scale
        dist = t_pos[None, :, None] - sel
        bias = rel_bias[t5_bucket(dist)].astype(jnp.float32)
        logits = logits + jnp.moveaxis(bias, -1, 1)
        logits = jnp.where((dist >= 0)[:, None], logits, -jnp.inf)
        p = jax.nn.softmax(logits, axis=-1).astype(x.dtype)
        o_lat = jnp.einsum('bhtk,btkc->bthc', p, kv_sel)
        o = jnp.einsum('bthc,hcv->bthv', o_lat, w_uv)
        return o.reshape(B, Q_BLOCK, H * V_HEAD)

    o = lax.map(block, (blk(q), blk(q_idx), blk(w_idx), starts))
    o = jnp.swapaxes(o, 0, 1).reshape(B, S, H * V_HEAD)
    return o @ w_o

def conv_ffn(x, w_up, conv_w, conv_b, w_down):
    S = x.shape[1]
    u = x @ w_up
    up = jnp.pad(u, ((0, 0), (CONV_W - 1, 0), (0, 0)))
    u = sum(up[:, j:j + S] * conv_w[j] for j in range(CONV_W)) + conv_b
    gate, val = jnp.split(u, 2, axis=-1)
    return (jax.nn.silu(gate) * val) @ w_down

def second_inputs(seed: int = 0) -> dict:
    key = jax.random.key(seed)
    ks = iter(jax.random.split(key, 64))
    f32 = jnp.float32
    n = lambda shape, scale: scale * jax.random.normal(next(ks), shape, f32)
    D, H, N = D_MODEL, RWKV_HEADS, RWKV_HEAD
    n_rwkv = (DEPTH_2 + 1) // 2
    n_dsa = DEPTH_2 // 2
    n_vres = max(n_rwkv - 1, 0)
    return {
        "x": n((BATCH, SEQ, D), 1.0),
        "ln_g": 1.0 + n((DEPTH_2, 2, D), 0.02),
        "ln_b": n((DEPTH_2, 2, D), 0.02),
        "rwkv_mix": jax.random.uniform(next(ks), (n_rwkv, N_RWKV_BRANCHES, D), f32),
        "rwkv_w_rkv": n((n_rwkv, 3, D, D), D ** -0.5),
        "rwkv_w0": -1.5 + n((n_rwkv, D), 1.0),
        "rwkv_w1": n((n_rwkv, D, DECAY_LORA), D ** -0.5),
        "rwkv_w2": n((n_rwkv, DECAY_LORA, D), 0.5 * DECAY_LORA ** -0.5),
        "rwkv_a0": n((n_rwkv, D), 0.1),
        "rwkv_a1": n((n_rwkv, D, AAA_LORA), D ** -0.5),
        "rwkv_a2": n((n_rwkv, AAA_LORA, D), 0.5 * AAA_LORA ** -0.5),
        "rwkv_v0": n((n_vres, D), 0.1),
        "rwkv_v1": n((n_vres, D, MV_LORA), D ** -0.5),
        "rwkv_v2": n((n_vres, MV_LORA, D), 0.5 * MV_LORA ** -0.5),
        "rwkv_g1": n((n_rwkv, D, GATE_LORA), D ** -0.5),
        "rwkv_g2": n((n_rwkv, GATE_LORA, D), GATE_LORA ** -0.5),
        "rwkv_k_k": 0.85 + n((n_rwkv, D), 0.05),
        "rwkv_k_a": 1.0 + n((n_rwkv, D), 0.05),
        "rwkv_r_k": n((n_rwkv, H, N), 0.1),
        "rwkv_lnx_g": 1.0 + n((n_rwkv, D), 0.02),
        "rwkv_lnx_b": n((n_rwkv, D), 0.02),
        "rwkv_w_o": n((n_rwkv, D, D), DN_BETA * D ** -0.5),
        "dsa_w_in": n((n_dsa, D, DSA_IN), D ** -0.5),
        "dsa_q_norm_g": 1.0 + n((n_dsa, Q_LORA), 0.02),
        "dsa_kv_norm_g": 1.0 + n((n_dsa, KV_LORA), 0.02),
        "dsa_w_uq": n((n_dsa, Q_LORA, ATT_HEADS * QK_HEAD), Q_LORA ** -0.5),
        "dsa_w_uk": n((n_dsa, ATT_HEADS, QK_HEAD, KV_LORA), KV_LORA ** -0.5),
        "dsa_w_uv": n((n_dsa, ATT_HEADS, KV_LORA, V_HEAD), KV_LORA ** -0.5),
        "dsa_w_qidx": n((n_dsa, Q_LORA, IDX_HEADS * IDX_DIM), Q_LORA ** -0.5),
        "dsa_kidx_g": 1.0 + n((n_dsa, IDX_DIM), 0.02),
        "dsa_kidx_b": n((n_dsa, IDX_DIM), 0.02),
        "dsa_w_o": n((n_dsa, ATT_HEADS * V_HEAD, D), DN_BETA * (ATT_HEADS * V_HEAD) ** -0.5),
        "rel_bias": n((REL_BUCKETS, ATT_HEADS), 0.5),
        "ffn_w_up": n((DEPTH_2, D, 2 * D_FF), D ** -0.5),
        "ffn_conv_w": n((DEPTH_2, CONV_W, 2 * D_FF), CONV_W ** -0.5),
        "ffn_conv_b": n((DEPTH_2, 2 * D_FF), 0.02),
        "ffn_w_down": n((DEPTH_2, D_FF, D), DN_BETA * D_FF ** -0.5),
    }

def second_block(x, ln_g, ln_b, rwkv_mix, rwkv_w_rkv, rwkv_w0, rwkv_w1, rwkv_w2, rwkv_a0, rwkv_a1,
              rwkv_a2, rwkv_v0, rwkv_v1, rwkv_v2, rwkv_g1, rwkv_g2, rwkv_k_k, rwkv_k_a, rwkv_r_k,
              rwkv_lnx_g, rwkv_lnx_b, rwkv_w_o, dsa_w_in, dsa_q_norm_g, dsa_kv_norm_g, dsa_w_uq,
              dsa_w_uk, dsa_w_uv, dsa_w_qidx, dsa_kidx_g, dsa_kidx_b, dsa_w_o, rel_bias,
              ffn_w_up, ffn_conv_w, ffn_conv_b, ffn_w_down):
    v_first = None
    for i in range(DEPTH_2):
        j = i // N_MIXERS
        if i % N_MIXERS == 0:
            vres = None if j == 0 else (rwkv_v0[j - 1], rwkv_v1[j - 1], rwkv_v2[j - 1])
            h, v_first = rwkv7_time_mix(
                x, v_first, vres, rwkv_mix[j], rwkv_w_rkv[j], rwkv_w0[j], rwkv_w1[j], rwkv_w2[j],
                rwkv_a0[j], rwkv_a1[j], rwkv_a2[j], rwkv_g1[j], rwkv_g2[j], rwkv_k_k[j],
                rwkv_k_a[j], rwkv_r_k[j], rwkv_lnx_g[j], rwkv_lnx_b[j], rwkv_w_o[j])
        else:
            h = dsa_attention(
                x, dsa_w_in[j], dsa_q_norm_g[j], dsa_kv_norm_g[j], dsa_w_uq[j], dsa_w_uk[j],
                dsa_w_uv[j], dsa_w_qidx[j], dsa_kidx_g[j], dsa_kidx_b[j], rel_bias, dsa_w_o[j])
        x = layer_norm(DN_ALPHA * x + h, ln_g[i, 0], ln_b[i, 0])
        f = conv_ffn(x, ffn_w_up[i], ffn_conv_w[i], ffn_conv_b[i], ffn_w_down[i])
        x = layer_norm(DN_ALPHA * x + f, ln_g[i, 1], ln_b[i, 1])
    return x


def setup_inputs(seed=0):
    out = dict(first_inputs(seed))
    for name, value in second_inputs(seed + 1).items():
        if name != "x":
            out[name + "_2"] = value
    return out


def reference(
    x, c, ctx, c_ctx, w_ada, b_ada, g_pre_mix, g_post_mix, g_pre_ffn, g_post_ffn, w_in, b_gate,
    lambda_q1, lambda_k1, lambda_q2, lambda_k2, subln_g, sgu_ln_g, sgu_ln_b, sgu_w, sgu_b,
    w_branch_attn, w_branch_sgu, w_out, peer_w_query, peer_sub_keys, peer_u, peer_v, ln_g_2,
    ln_b_2, rwkv_mix_2, rwkv_w_rkv_2, rwkv_w0_2, rwkv_w1_2, rwkv_w2_2, rwkv_a0_2, rwkv_a1_2,
    rwkv_a2_2, rwkv_v0_2, rwkv_v1_2, rwkv_v2_2, rwkv_g1_2, rwkv_g2_2, rwkv_k_k_2, rwkv_k_a_2,
    rwkv_r_k_2, rwkv_lnx_g_2, rwkv_lnx_b_2, rwkv_w_o_2, dsa_w_in_2, dsa_q_norm_g_2,
    dsa_kv_norm_g_2, dsa_w_uq_2, dsa_w_uk_2, dsa_w_uv_2, dsa_w_qidx_2, dsa_kidx_g_2,
    dsa_kidx_b_2, dsa_w_o_2, rel_bias_2, ffn_w_up_2, ffn_conv_w_2, ffn_conv_b_2, ffn_w_down_2,
):
    x = first_block(
        x, c, ctx, c_ctx, w_ada, b_ada, g_pre_mix, g_post_mix, g_pre_ffn, g_post_ffn, w_in,
        b_gate, lambda_q1, lambda_k1, lambda_q2, lambda_k2, subln_g, sgu_ln_g, sgu_ln_b, sgu_w,
        sgu_b, w_branch_attn, w_branch_sgu, w_out, peer_w_query, peer_sub_keys, peer_u, peer_v,
    )
    return second_block(
        x, ln_g_2, ln_b_2, rwkv_mix_2, rwkv_w_rkv_2, rwkv_w0_2, rwkv_w1_2, rwkv_w2_2, rwkv_a0_2,
        rwkv_a1_2, rwkv_a2_2, rwkv_v0_2, rwkv_v1_2, rwkv_v2_2, rwkv_g1_2, rwkv_g2_2, rwkv_k_k_2,
        rwkv_k_a_2, rwkv_r_k_2, rwkv_lnx_g_2, rwkv_lnx_b_2, rwkv_w_o_2, dsa_w_in_2,
        dsa_q_norm_g_2, dsa_kv_norm_g_2, dsa_w_uq_2, dsa_w_uk_2, dsa_w_uv_2, dsa_w_qidx_2,
        dsa_kidx_g_2, dsa_kidx_b_2, dsa_w_o_2, rel_bias_2, ffn_w_up_2, ffn_conv_w_2,
        ffn_conv_b_2, ffn_w_down_2,
    )


_drawn_inputs = setup_inputs


def setup_inputs(seed=0):
    import zlib

    import numpy as np

    out = dict(_drawn_inputs(seed))
    spreads = {}
    factors = {'g_pre_mix': 4.968,
     'g_post_mix': 6.045,
     'g_post_ffn': 8.0,
     'b_gate': 8.0,
     'lambda_q1': 4.087,
     'lambda_q2': 8.0,
     'lambda_k2': 3.921,
     'subln_g': 7.364,
     'sgu_ln_g': 7.849,
     'sgu_ln_b': 7.892,
     'sgu_b': 7.763,
     'rwkv_w1_2': 5.348,
     'rwkv_w2_2': 5.242,
     'rwkv_a0_2': 5.475,
     'rwkv_k_k_2': 8.0,
     'rwkv_k_a_2': 5.014,
     'rwkv_lnx_g_2': 8.0,
     'rwkv_lnx_b_2': 8.0,
     'dsa_q_norm_g_2': 8.0,
     'dsa_kv_norm_g_2': 8.0,
     'dsa_kidx_g_2': 8.0,
     'dsa_kidx_b_2': 8.0,
     'ffn_conv_b_2': 5.959}
    for name, (base, spread) in spreads.items():
        noise = np.random.default_rng([zlib.crc32(name.encode()), seed]).standard_normal(out[name].shape)
        drawn = base * np.exp(spread * noise) if base else spread * noise
        out[name] = __import__('jax').numpy.asarray(drawn.astype(out[name].dtype))
    for name, factor in factors.items():
        out[name] = (out[name] * factor).astype(out[name].dtype)
    return out
```

```python
from contextlib import ExitStack, contextmanager

import numpy as np

import concourse.bass as bass
from concourse import mybir

F32 = mybir.dt.float32
F32R = mybir.dt.float32r
U32 = mybir.dt.uint32
ALU = mybir.AluOpType
ACT = mybir.ActivationFunctionType
AX = mybir.AxisListType

P = 128
D = 1024
T = 512
CTX = 256
KD = D // P
TT = T // P
W = 512
HEADS = 16
DH = 64
LK = T + CTX
SEM_BASE = 110


@contextmanager
def phase(nc, *names):
    with ExitStack() as ctx:
        sems = [ctx.enter_context(nc.semaphore(n, num=SEM_BASE + i)) for i, n in enumerate(names)]
        yield sems
        nc.all_engine_barrier(sems_to_clear=range(SEM_BASE, SEM_BASE + len(names)))


class Steps:

    def __init__(self, eng, sem):
        self.eng, self.sem, self.n = eng, sem, 0

    def __call__(self, ins, wait=True):
        ins.then_inc(self.sem, 1)
        self.n += 1
        if wait:
            self.eng.wait_ge(self.sem, self.n)

    def wait(self):
        self.eng.wait_ge(self.sem, self.n)


def tensors(nc, ctx):
    def sb(name, shape, dt=F32):
        return ctx.enter_context(nc.sbuf_tensor(name, shape, dt, allow_name_mangling=True))

    def ps(name, shape, dt=F32):
        return ctx.enter_context(nc.psum_tensor(name, shape, dt, allow_name_mangling=True))

    return sb, ps


def root_reciprocal(pool, steps, out, src, eps, mhalf):
    steps(pool.tensor_scalar(out, src, eps, None, ALU.add))
    return pool.tensor_tensor(out, out, mhalf, ALU.pow)


def over_partitions(row):
    return row.to_broadcast([P, row.shape[1]])


def modulation(nc, d):
    NB, BW = 6, 1024
    w = d["w_ada"].rearrange("(k p) n -> p k n", p=P)
    with phase(nc, "c_loaded", "silu_done", "w0_loaded", "w1_loaded", "w_used", "bank_done", "added", "stored") as (
            c_loaded, silu_done, w0_loaded, w1_loaded, w_used, bank_done, added, stored), ExitStack() as ctx:
        sb, ps = tensors(nc, ctx)
        cc = sb("ada_c", [P, KD, 2])
        cs = sb("ada_silu", [P, KD, 2])
        wt = sb("ada_w", [P, 2, KD, BW])
        b2 = sb("ada_b", [2, NB * BW])
        rows = sb("ada_rows", [2, NB * BW])
        acc = ps("ada_acc", [P, 2, 2, W])
        w_loaded = (w0_loaded, w1_loaded)
        with nc.Block() as block:
            @block.sync
            def _(sp):
                sp.dma_start(cc[:], d["c_cols"]).then_inc(c_loaded, 16)
                sp.dma_start(b2[:], d["b_ada"].to_broadcast([2, NB * BW])).then_inc(c_loaded, 16)
                with sp.Fori(0, NB // 2) as i:
                    for u in range(2):
                        sp.wait_ge(w_used, i * 2 + u + 1)
                        sp.dma_start(wt[:, u], w[:, :, bass.ds(i * (2 * BW) + u * BW, BW)]).then_inc(w_loaded[u], 16)
                sp.wait_ge(added, NB * 2 + 4)
                sp.dma_start(d["mod"][0:1, 0:6 * D], rows[0:1, :]).then_inc(stored, 16)
                sp.dma_start(d["mod"][0:1, 6 * D:8 * D], rows[1:2, 0:2 * D]).then_inc(stored, 16)
                sp.wait_ge(stored, 32)

            @block.scalar
            def _(act):
                act.wait_ge(c_loaded, 32)
                act.activation(cs[:], cc[:], ACT.Silu).then_inc(silu_done, 1)

            @block.tensor
            def _(pe):
                pe.sem_inc(w_used, 2)
                pe.wait_ge(silu_done, 1)
                with pe.Fori(0, NB // 2) as i:
                    for u in range(2):
                        pe.wait_ge(w_loaded[u], i * 16 + 16)
                        for s in range(2):
                            pe.wait_ge(added, i * 4 + 2 * u + s + 1)
                            for k in range(KD):
                                mm = pe.matmul(acc[0:2, u, s, :], cs[:, k, :], wt[:, u, k, s * W:(s + 1) * W],
                                               start=(k == 0), stop=(k == KD - 1))
                            mm.then_inc(bank_done, 1)
                        pe.wait_ge(bank_done, i * 4 + 2 * u + 2)
                        pe.sem_inc(w_used, 1)

            @block.vector
            def _(dve):
                dve.sem_inc(added, 4)
                dve.wait_ge(c_loaded, 32)
                with dve.Fori(0, NB // 2) as i:
                    for u in range(2):
                        for s in range(2):
                            dve.wait_ge(bank_done, i * 4 + 2 * u + s + 1)
                            col = bass.ds(i * (2 * BW) + u * BW + s * W, W)
                            dve.tensor_tensor(rows[:, col], acc[0:2, u, s, :], b2[:, col], ALU.add).then_inc(added, 1)


def product3(pe, out, left, right, start, stop):
    pe.matmul(out, left[0], right[0], start=start, stop=False)
    pe.matmul(out, left[0], right[1], start=False, stop=False)
    return pe.matmul(out, left[1], right[0], start=False, stop=stop)


def project(nc, xT, w, out):
    K, tokens = xT.shape
    KC, NB = K // P, w.shape[1] // W
    tiles = tokens // P
    sets = 2 if 2 * tiles <= 8 else 1
    wv = w.rearrange("(k p) n -> p k n", p=P)
    assert NB % 2 == 0
    with phase(nc, "x_loaded", "w0_loaded", "w1_loaded", "x_hi", "x_lo", "w_hi", "w_lo", "block_done", "bank_done",
               "copied", "stored0", "stored1") as (x_loaded, w0_loaded, w1_loaded, x_hi, x_lo, w_hi, w_lo, block_done,
                                                   bank_done, copied, stored0, stored1), ExitStack() as ctx:
        sb, ps = tensors(nc, ctx)
        xh = sb("pr_xh", [P, KC, tokens], F32R)
        xl = sb("pr_xl", [P, KC, tokens], F32R)
        raw = sb("pr_raw", [P, 2, KC, W])
        wh = sb("pr_wh", [P, 2, KC, W], F32R)
        wl = sb("pr_wl", [P, 2, KC, W], F32R)
        stage = sb("pr_stage", [P, 2, tiles, W])
        acc = ps("pr_acc", [P, sets, tiles, W])
        x = stage[:].rearrange("p u t n -> p (u t n)").rearrange("p (k t) -> p k t", k=KC)
        w_loaded, stored = (w0_loaded, w1_loaded), (stored0, stored1)
        with nc.Block() as block:
            @block.sync
            def _(sp):
                sp.dma_start(x, xT.rearrange("(k p) t -> p k t", p=P)).then_inc(x_loaded, 16)
                with sp.Fori(0, NB // 2) as i:
                    for u in range(2):
                        sp.wait_ge(w_lo, i * 2 + u + 1)
                        sp.dma_start(raw[:, u], wv[:, :, bass.ds(i * (2 * W) + u * W, W)]).then_inc(w_loaded[u], 16)

            @block.scalar
            def _(act):
                rows = out.rearrange("(t p) n -> p t n", p=P)

                def hi(i, u):
                    act.wait_ge(w_loaded[u], i * 16 + 16)
                    act.wait_ge(block_done, i * 2 + u + 1)
                    act.activation(wh[:, u], raw[:, u], ACT.Copy).then_inc(w_hi, 1)

                def store(i, u):
                    act.wait_ge(copied, i * (2 * tiles) + (u + 1) * tiles + sets * tiles)
                    act.dma_start(rows[:, :, bass.ds(i * (2 * W) + u * W, W)], stage[:, u]).then_inc(stored[u], 16)

                act.sem_inc(stored0, 16)
                act.sem_inc(stored1, 16)
                act.wait_ge(x_loaded, 16)
                act.activation(xh[:], x, ACT.Copy).then_inc(x_hi, 1)
                hi(0, 0)
                if NB > 2:
                    with act.Fori(0, NB // 2 - 1) as i:
                        hi(i, 1)
                        store(i, 0)
                        hi(i + 1, 0)
                        store(i, 1)
                last = NB // 2 - 1
                hi(last, 1)
                store(last, 0)
                store(last, 1)
                act.wait_ge(stored0, 16 * (NB // 2) + 16)
                act.wait_ge(stored1, 16 * (NB // 2) + 16)

            @block.gpsimd
            def _(pool):
                pool.sem_inc(w_lo, 2)
                with pool.Fori(0, NB // 2) as i:
                    for u in range(2):
                        pool.wait_ge(w_hi, i * 2 + u + 1)
                        pool.tensor_tensor(wl[:, u], raw[:, u], wh[:, u].bitcast(F32), ALU.subtract).then_inc(w_lo, 1)

            @block.tensor
            def _(pe):
                pe.sem_inc(block_done, 2)
                pe.wait_ge(x_lo, 1)
                with pe.Fori(0, NB // 2) as i:
                    for u in range(2):
                        pe.wait_ge(w_lo, i * 2 + u + 3)
                        for t in range(tiles):
                            pe.wait_ge(copied, i * (2 * tiles) + u * tiles + t + 1)
                            tok = slice(t * P, (t + 1) * P)
                            for k in range(KC):
                                mm = product3(pe, acc[:, u % sets, t, :], (xh[:, k, tok], xl[:, k, tok]),
                                              (wh[:, u, k, :], wl[:, u, k, :]), k == 0, k == KC - 1)
                            mm.then_inc(bank_done, 1)
                        pe.wait_ge(bank_done, i * (2 * tiles) + (u + 1) * tiles)
                        pe.sem_inc(block_done, 1)

            @block.vector
            def _(dve):
                dve.sem_inc(copied, sets * tiles)
                dve.wait_ge(x_hi, 1)
                dve.tensor_tensor(xl[:], x, xh[:].bitcast(F32), ALU.subtract).then_inc(x_lo, 1)
                dve.wait_ge(x_lo, 1)
                with dve.Fori(0, NB // 2) as i:
                    for u in range(2):
                        dve.wait_ge(stored[u], i * 16 + 16)
                        for t in range(tiles):
                            dve.wait_ge(bank_done, i * (2 * tiles) + u * tiles + t + 1)
                            dve.tensor_copy(stage[:, u, t, :], acc[:, u % sets, t, :]).then_inc(copied, 1)


def transpose_out(pe, tiles, src, ready, ident, acc, copied, done):
    for i in range(tiles):
        pe.wait_ge(ready, i + 1)
        if i >= 2:
            pe.wait_ge(copied, i - 1)
        rows = src(i)
        for k in range(KD):
            mm = pe.transpose(acc[:, i % 2, k, :], rows[:, k * P:(k + 1) * P], ident[:])
        mm.then_inc(done, 1)


def premix(nc, d):
    CT = CTX // P
    tiles = CT + TT
    with phase(nc, "vec_loaded", "rows_loaded", "gain_done", "squared", "rows_done", "turned", "copied", "stored0", "stored1",
               "rooted", "pool_steps", "dve_steps") as (vec_loaded, rows_loaded, gain_done, squared, rows_done, turned, copied,
                                          stored0, stored1, rooted, pool_steps, dve_steps), ExitStack() as ctx:
        sb, ps = tensors(nc, ctx)
        x = sb("pm_x", [P, tiles, D])
        junk = sb("pm_junk", [P, D])
        ss = sb("pm_ss", [P, tiles])
        rstd = sb("pm_rstd", [P, tiles])
        mhalf = sb("pm_mhalf", [P, tiles])
        g = sb("pm_g", [P, D])
        gain = sb("pm_gain", [P, 2, D])
        shift = sb("pm_shift", [P, 2, D])
        ident = sb("pm_ident", [P, P])
        h = sb("pm_h", [P, tiles, D])
        hT = sb("pm_hT", [P, 2, KD, P])
        acc = ps("pm_acc", [P, 2, KD, P])
        with nc.Block() as block:
            @block.sync
            def _(sp):
                sp.dma_start(x[:, 0:CT], d["ctx"].rearrange("(t p) n -> p t n", p=P)).then_inc(rows_loaded, 16)
                sp.dma_start(x[:, CT:tiles], d["x"].rearrange("(t p) n -> p t n", p=P)).then_inc(rows_loaded, 16)
                sp.dma_start(ident[:], d["ident"]).then_inc(rows_loaded, 16)
                sp.dma_start(g[:], over_partitions(d["g_pre_mix"])).then_inc(vec_loaded, 16)
                for s, at in enumerate((6, 0)):
                    sp.dma_start(shift[:, s], over_partitions(d["mod"][:, at * D:(at + 1) * D])).then_inc(vec_loaded, 16)
                    sp.dma_start(gain[:, s], over_partitions(d["mod"][:, (at + 1) * D:(at + 2) * D])).then_inc(vec_loaded, 16)
                hT_out = d["hT"].rearrange("(k p) t -> p k t", p=P)
                for i in range(tiles):
                    sp.wait_ge(copied, i + 1)
                    sp.dma_start(hT_out[:, :, i * P:(i + 1) * P], hT[:, i % 2]).then_inc((stored0, stored1)[i % 2], 16)
                sp.wait_ge(stored0, 16 * tiles // 2)
                sp.wait_ge(stored1, 16 * tiles // 2)

            @block.scalar
            def _(act):
                act.wait_ge(rows_loaded, 48)
                for i in range(tiles):
                    if i:
                        act.wait_ge(squared, i)
                    act.activation(junk[:], x[:, i], ACT.Square, scale=D ** -0.5, accum_out=ss[:, i:i + 1]).then_inc(squared, 1)
                for i in range(tiles):
                    act.wait_ge(turned, i + 1)
                    if i >= 2:
                        act.wait_ge((stored0, stored1)[i % 2], 16 * (i // 2))
                    act.activation(hT[:, i % 2], acc[:, i % 2], ACT.Copy).then_inc(copied, 1)

            @block.vector
            def _(dve):
                step = Steps(dve, dve_steps)
                dve.wait_ge(vec_loaded, 80)
                for s in range(2):
                    step(dve.scalar_tensor_tensor(gain[:, s], gain[:, s], 1.0, g[:], ALU.add, ALU.mult))
                dve.wait_ge(rooted, 1)
                for i in range(tiles):
                    s = int(i >= CT)
                    step(dve.scalar_tensor_tensor(h[:, i], x[:, i], rstd[:, i:i + 1], gain[:, s], ALU.mult, ALU.mult))
                    dve.tensor_tensor(h[:, i], h[:, i], shift[:, s], ALU.add).then_inc(rows_done, 1)

            @block.gpsimd
            def _(pool):
                steps = Steps(pool, pool_steps)
                steps(pool.memset(mhalf[:], -0.5))
                pool.wait_ge(squared, tiles)
                root_reciprocal(pool, steps, rstd[:], ss[:], 1e-6, mhalf[:]).then_inc(rooted, 1)

            @block.tensor
            def _(pe):
                pe.wait_ge(rows_loaded, 48)
                transpose_out(pe, tiles, lambda i: h[:, i], rows_done, ident, acc, copied, turned)


def join_rms(nc, d, x_in, y_in, g_post, gate_at, x_out, hT_out, g_pre=None, shift_at=None):
    with phase(nc, "vec_loaded", "rows_loaded", "rows_done", "x_done", "turned", "copied", "stored0", "stored1", "x_stored",
               "summed", "rooted", "pool_steps", "dve_steps") as (vec_loaded, rows_loaded, rows_done, x_done, turned, copied, stored0, stored1,
                                                    x_stored, summed, rooted, pool_steps, dve_steps), ExitStack() as ctx:
        sb, ps = tensors(nc, ctx)
        x = sb("jr_x", [P, TT, D])
        y = sb("jr_y", [P, TT, D])
        h = sb("jr_h", [P, TT, D])
        junk = sb("jr_junk", [P, D])
        st = sb("jr_st", [P, TT, 4])
        mhalf = sb("jr_mhalf", [P, 1])
        gp = sb("jr_gp", [P, D])
        gt = sb("jr_gt", [P, D])
        gain = sb("jr_gain", [P, D])
        shift = sb("jr_shift", [P, D])
        g2 = sb("jr_g2", [P, D])
        ident = sb("jr_ident", [P, P])
        hT = sb("jr_hT", [P, 2, KD, P])
        acc = ps("jr_acc", [P, 2, KD, P])

        roots = 2 if g_pre else 1

        def vec(at):
            return over_partitions(d["mod"][:, at * D:(at + 1) * D])

        with nc.Block() as block:
            @block.sync
            def _(sp):
                sp.dma_start(x[:], d[x_in].rearrange("(t p) n -> p t n", p=P)).then_inc(rows_loaded, 16)
                sp.dma_start(y[:], d[y_in].rearrange("(t p) n -> p t n", p=P)).then_inc(rows_loaded, 16)
                sp.dma_start(ident[:], d["ident"]).then_inc(rows_loaded, 16)
                sp.dma_start(gp[:], over_partitions(d[g_post])).then_inc(vec_loaded, 16)
                sp.dma_start(gt[:], vec(gate_at)).then_inc(vec_loaded, 16)
                if g_pre:
                    sp.dma_start(g2[:], over_partitions(d[g_pre])).then_inc(vec_loaded, 16)
                    sp.dma_start(shift[:], vec(shift_at)).then_inc(vec_loaded, 16)
                    sp.dma_start(gain[:], vec(shift_at + 1)).then_inc(vec_loaded, 16)
                turned_out = d[hT_out].rearrange("(k p) t -> p k t", p=P)
                for i in range(TT):
                    sp.wait_ge(x_done, i + 1)
                    sp.dma_start(d[x_out][i * P:(i + 1) * P, :], x[:, i]).then_inc(x_stored, 16)
                    sp.wait_ge(copied, i + 1)
                    sp.dma_start(turned_out[:, :, i * P:(i + 1) * P], hT[:, i % 2]).then_inc((stored0, stored1)[i % 2], 16)
                sp.wait_ge(x_stored, 16 * TT)
                sp.wait_ge(stored0, 16 * TT // 2)
                sp.wait_ge(stored1, 16 * TT // 2)

            @block.scalar
            def _(act):
                for i in range(TT):
                    act.wait_ge(turned, i + 1)
                    if i >= 2:
                        act.wait_ge((stored0, stored1)[i % 2], 16 * (i // 2))
                    act.activation(hT[:, i % 2], acc[:, i % 2], ACT.Copy).then_inc(copied, 1)

            @block.vector
            def _(dve):
                step = Steps(dve, dve_steps)

                def rstd_of(rows, n, i):
                    dve.tensor_tensor_reduce(junk[:], rows, rows, 1.0 / D, 0.0, ALU.mult, ALU.add,
                                             st[:, i, 2 * n:2 * n + 1]).then_inc(summed, 1)
                    dve.wait_ge(rooted, roots * i + n + 1)

                dve.wait_ge(rows_loaded, 48)
                dve.wait_ge(vec_loaded, 80 if g_pre else 32)
                step(dve.tensor_tensor(gt[:], gt[:], gp[:], ALU.mult))
                if g_pre:
                    step(dve.scalar_tensor_tensor(gain[:], gain[:], 1.0, g2[:], ALU.add, ALU.mult))
                for i in range(TT):
                    rstd_of(y[:, i], 0, i)
                    step(dve.scalar_tensor_tensor(y[:, i], y[:, i], st[:, i, 1:2], gt[:], ALU.mult, ALU.mult))
                    dve.tensor_tensor(x[:, i], x[:, i], y[:, i], ALU.add).then_inc(x_done, 1)
                    if g_pre:
                        dve.wait_ge(x_done, i + 1)
                        rstd_of(x[:, i], 1, i)
                        step(dve.scalar_tensor_tensor(h[:, i], x[:, i], st[:, i, 3:4], gain[:], ALU.mult, ALU.mult))
                        dve.tensor_tensor(h[:, i], h[:, i], shift[:], ALU.add).then_inc(rows_done, 1)

            @block.gpsimd
            def _(pool):
                steps = Steps(pool, pool_steps)
                steps(pool.memset(mhalf[:], -0.5))
                for i in range(TT):
                    for n in range(roots):
                        pool.wait_ge(summed, roots * i + n + 1)
                        root_reciprocal(pool, steps, st[:, i, 2 * n + 1:2 * n + 2], st[:, i, 2 * n:2 * n + 1], 1e-6,
                                        mhalf[:]).then_inc(rooted, 1)

            @block.tensor
            def _(pe):
                pe.wait_ge(rows_loaded, 48)
                if g_pre:
                    transpose_out(pe, TT, lambda i: h[:, i], rows_done, ident, acc, copied, turned)
                else:
                    transpose_out(pe, TT, lambda i: x[:, i], x_done, ident, acc, copied, turned)


def join_ln(nc, d, x_in, y_in, g, b, x_out, xT_out=None):
    ALPHA = 4.0 ** 0.25
    with phase(nc, "vec_loaded", "rows_loaded", "x_done", "turned", "copied", "stored0", "stored1", "x_stored",
               "averaged", "rooted", "pool_steps", "dve_steps") as (vec_loaded, rows_loaded, x_done, turned, copied, stored0, stored1, x_stored,
                                                      averaged, rooted, pool_steps, dve_steps), ExitStack() as ctx:
        sb, ps = tensors(nc, ctx)
        x = sb("jl_x", [P, TT, D])
        y = sb("jl_y", [P, TT, D])
        st = sb("jl_st", [P, TT, 2, 6])
        mv = sb("jl_mv", [P, TT, 2])
        rs = sb("jl_rs", [P, TT])
        mhalf = sb("jl_mhalf", [P, 1])
        gv = sb("jl_g", [P, D])
        bv = sb("jl_b", [P, D])
        ident = sb("jl_ident", [P, P])
        xT = sb("jl_xT", [P, 2, KD, P])
        acc = ps("jl_acc", [P, 2, KD, P])
        with nc.Block() as block:
            @block.sync
            def _(sp):
                sp.dma_start(x[:], d[x_in].rearrange("(t p) n -> p t n", p=P)).then_inc(rows_loaded, 16)
                sp.dma_start(y[:], d[y_in].rearrange("(t p) n -> p t n", p=P)).then_inc(rows_loaded, 16)
                sp.dma_start(ident[:], d["ident"]).then_inc(rows_loaded, 16)
                sp.dma_start(gv[:], over_partitions(g)).then_inc(vec_loaded, 16)
                sp.dma_start(bv[:], over_partitions(b)).then_inc(vec_loaded, 16)
                for i in range(TT):
                    sp.wait_ge(x_done, i + 1)
                    sp.dma_start(d[x_out][i * P:(i + 1) * P, :], x[:, i]).then_inc(x_stored, 16)
                    if xT_out:
                        sp.wait_ge(copied, i + 1)
                        sp.dma_start(d[xT_out].rearrange("(k p) t -> p k t", p=P)[:, :, i * P:(i + 1) * P],
                                     xT[:, i % 2]).then_inc((stored0, stored1)[i % 2], 16)
                sp.wait_ge(x_stored, 16 * TT)
                if xT_out:
                    sp.wait_ge(stored0, 16 * TT // 2)
                    sp.wait_ge(stored1, 16 * TT // 2)

            @block.vector
            def _(dve):
                step = Steps(dve, dve_steps)
                dve.wait_ge(rows_loaded, 48)
                dve.wait_ge(vec_loaded, 32)
                for i in range(TT):
                    step(dve.scalar_tensor_tensor(y[:, i], x[:, i], ALPHA, y[:, i], ALU.mult, ALU.add))
                    for s in range(2):
                        step(dve.bn_stats(st[:, i, s, :], y[:, i, s * W:(s + 1) * W]), wait=False)
                    step.wait()
                    dve.bn_aggr(mv[:, i, :], st[:, i].rearrange("p s c -> p (s c)")).then_inc(averaged, 1)
                    dve.wait_ge(rooted, i + 1)
                    step(dve.tensor_scalar(y[:, i], y[:, i], mv[:, i, 0:1], rs[:, i:i + 1], ALU.subtract, ALU.mult))
                    step(dve.tensor_tensor(y[:, i], y[:, i], gv[:], ALU.mult))
                    dve.tensor_tensor(x[:, i], y[:, i], bv[:], ALU.add).then_inc(x_done, 1)

            @block.gpsimd
            def _(pool):
                steps = Steps(pool, pool_steps)
                steps(pool.memset(mhalf[:], -0.5))
                for i in range(TT):
                    pool.wait_ge(averaged, i + 1)
                    root_reciprocal(pool, steps, rs[:, i:i + 1], mv[:, i, 1:2], 1e-5, mhalf[:]).then_inc(rooted, 1)

            if xT_out:
                @block.tensor
                def _(pe):
                    pe.wait_ge(rows_loaded, 48)
                    transpose_out(pe, TT, lambda i: x[:, i], x_done, ident, acc, copied, turned)

                @block.scalar
                def _(act):
                    for i in range(TT):
                        act.wait_ge(turned, i + 1)
                        if i >= 2:
                            act.wait_ge((stored0, stored1)[i % 2], 16 * (i // 2))
                        act.activation(xT[:, i % 2], acc[:, i % 2], ACT.Copy).then_inc(copied, 1)
def diff_attention(nc, d):
    VH = 8
    KT = LK // P
    SCALE = DH ** -0.5
    N = VH * TT
    with phase(nc, "ctx_loaded", "kv_loaded", "q_loaded", "small_loaded", "turn_ready", "turned", "turn_copied",
               "lam_summed", "lam_exp", "lam_done", "k_rotated", "q_rotated", "scores_done", "max_done", "exp_done",
               "probs_done", "probs_turned", "probs_copied", "o_done", "o_copied", "squared", "rooted", "rows_done",
               "o_turned", "o_out", "stored0", "stored1", "pool_steps", "dve_steps") as (
            ctx_loaded, kv_loaded, q_loaded, small_loaded, turn_ready, turned, turn_copied, lam_summed, lam_exp,
            lam_done, k_rotated, q_rotated, scores_done, max_done, exp_done, probs_done, probs_turned, probs_copied,
            o_done, o_copied, squared, rooted, rows_done, o_turned, o_out, stored0, stored1, pool_steps,
            dve_steps), ExitStack() as ctx:
        sb, ps = tensors(nc, ctx)
        q = sb("at_q", [P, TT, D])
        k = sb("at_k", [P, KT, D])
        v = sb("at_v", [P, KT, D])
        qT = sb("at_qT", [P, KD, T])
        kT = sb("at_kT", [P, KD, LK])
        cs = sb("at_cos", [P, 2, TT, 32])
        lam4 = sb("at_lam4", [P, 4, DH])
        lam = sb("at_lam", [P, 8])
        ident = sb("at_ident", [P, P])
        gs = sb("at_gs", [P, P])
        tmp = sb("at_tmp", [P, 2, 2, W])
        e = sb("at_e", [P, 2, 2, LK])
        a = sb("at_a", [P, 2, LK])
        aT = sb("at_aT", [P, 2, LK])
        st = sb("at_st", [P, N, 4])
        rs = sb("at_rs", [P, 2, N])
        mhalf = sb("at_mhalf", [P, VH])
        o = sb("at_o", [P, TT, D])
        ss = sb("at_ss", [P, TT, VH])
        sc = ps("at_sc", [P, 2, 1024])
        tr = [ps("at_tr", [P, 1024]), ps("at_ops", [P, 1024])]
        oT = e[:].rearrange("p a b c -> p (a b c)")[:, 0:2 * D].rearrange("p (a k t) -> p a k t", a=2, k=KD)
        ctx_rows = d["kv"][0:CTX, :].rearrange("(t p) n -> p t n", p=P)
        own_rows = d["kv"][CTX:LK, :].rearrange("(t p) n -> p t n", p=P)
        order = [("k", 0), ("k", 1)] + [(x, i) for i in range(TT) for x in ("k", "q")]

        def rotate(eng, steps, rows, i, n, done):
            x = rows.rearrange("p (h a s f) -> p h a s f", h=HEADS, a=2, s=2)
            x1, x2 = x[:, :, :, 0, :], x[:, :, :, 1, :]
            cos, sin = (cs[:, n2, i, :].rearrange("p (a f) -> p a f", a=2).unsqueeze(1).to_broadcast([P, HEADS, 2, 16])
                        for n2 in range(2))
            t1, t2 = (tmp[:, n, n2, :].rearrange("p (h a f) -> p h a f", h=HEADS, a=2) for n2 in range(2))
            steps(eng.tensor_tensor(t1, x1, sin, ALU.mult), wait=False)
            steps(eng.tensor_tensor(t2, x2, sin, ALU.mult), wait=False)
            steps.wait()
            steps(eng.tensor_tensor(x1, x1, cos, ALU.mult), wait=False)
            steps(eng.tensor_tensor(x2, x2, cos, ALU.mult), wait=False)
            steps.wait()
            steps(eng.tensor_tensor(x1, x1, t2, ALU.subtract), wait=False)
            steps(eng.tensor_tensor(x2, x2, t1, ALU.add), wait=False)
            steps.wait()
            eng.sem_inc(done, 1)

        with nc.Block() as block:
            @block.sync
            def _(sp):
                sp.dma_start(k[:, 0:2], ctx_rows[:, :, 0:D]).then_inc(ctx_loaded, 16)
                sp.dma_start(ident[:], d["ident"]).then_inc(ctx_loaded, 16)
                sp.dma_start(cs[:], d["rope"]).then_inc(small_loaded, 16)
                sp.dma_start(lam4[:], d["lambda4"].to_broadcast([P, 4 * DH])).then_inc(small_loaded, 16)
                sp.dma_start(gs[:], over_partitions(d["subln_g"])).then_inc(small_loaded, 16)
                sp.dma_start(q[:], d["q"].rearrange("(t p) n -> p t n", p=P)).then_inc(q_loaded, 16)
                sp.dma_start(k[:, 2:KT], own_rows[:, :, 0:D]).then_inc(kv_loaded, 16)
                sp.dma_start(v[:, 0:2], ctx_rows[:, :, D:2 * D]).then_inc(kv_loaded, 16)
                sp.dma_start(v[:, 2:KT], own_rows[:, :, D:2 * D]).then_inc(kv_loaded, 16)
                out = d["oT"].rearrange("(k p) t -> p k t", p=P)
                for i in range(TT):
                    sp.wait_ge(o_out, i + 1)
                    sp.dma_start(out[:, :, i * P:(i + 1) * P], oT[:, i % 2]).then_inc((stored0, stored1)[i % 2], 16)
                sp.wait_ge(stored0, 32)
                sp.wait_ge(stored1, 32)

            @block.gpsimd
            def _(pool):
                steps = Steps(pool, pool_steps)
                steps(pool.memset(mhalf[:], -0.5))
                pool.wait_ge(small_loaded, 48)
                pool.wait_ge(kv_loaded, 48)
                for i in range(TT):
                    rotate(pool, steps, k[:, 2 + i], i, 1, k_rotated)
                for i in range(TT):
                    pool.wait_ge(squared, i + 1)
                    root_reciprocal(pool, steps, ss[:, i], ss[:, i], 1e-6, mhalf[:]).then_inc(rooted, 1)

            @block.tensor
            def _(pe):
                pe.wait_ge(ctx_loaded, 32)
                for n, (what, i) in enumerate(order):
                    if what == "q":
                        pe.wait_ge(q_rotated, i + 1)
                    elif i >= 2 or n >= 2:
                        pe.wait_ge(k_rotated, i + 1)
                    if n >= 2:
                        pe.wait_ge(turn_copied, n - 1)
                    rows = q[:, i] if what == "q" else k[:, i if n < 2 else 2 + i]
                    for c in range(KD):
                        mm = pe.transpose(tr[n % 2][:, c * P:(c + 1) * P], rows[:, c * P:(c + 1) * P], ident[:])
                    mm.then_inc(turned, 1)
                pe.wait_ge(turn_copied, len(order))
                pe.wait_ge(kv_loaded, 48)
                for n in range(N + 2):
                    if n < N:
                        h, i = divmod(n, TT)
                        for c in range(2):
                            if n:
                                pe.wait_ge(exp_done, 2 * (n - 1) + c + 1)
                            rows = slice(DH * c, DH * c + DH)
                            lhs = qT[rows, h, i * P:(i + 1) * P]
                            pe.matmul(sc[:, c, 0:W], lhs, kT[rows, h, 0:W], start=True, stop=True)
                            pe.matmul(sc[:, c, W:LK], lhs, kT[rows, h, W:LK], start=True,
                                      stop=True).then_inc(scores_done, 1)
                    if 1 <= n <= N:
                        m = n - 1
                        pe.wait_ge(probs_done, m + 1)
                        if m:
                            pe.wait_ge(probs_copied, m)
                        for c in range(KT):
                            mm = pe.transpose(tr[0][:, c * P:(c + 1) * P], a[:, m % 2, c * P:(c + 1) * P], ident[:])
                        mm.then_inc(probs_turned, 1)
                    if n >= 2:
                        m = n - 2
                        h = m // TT
                        pe.wait_ge(probs_copied, m + 1)
                        if m >= 2:
                            pe.wait_ge(o_copied, m - 1)
                        for c in range(KT):
                            mm = pe.matmul(tr[1][:, (m % 2) * W:(m % 2) * W + P], aT[:, m % 2, c * P:(c + 1) * P],
                                           v[:, c, h * P:(h + 1) * P], start=(c == 0), stop=(c == KT - 1))
                        mm.then_inc(o_done, 1)
                pe.wait_ge(o_copied, N)
                for i in range(TT):
                    pe.wait_ge(rows_done, i + 1)
                    if i >= 2:
                        pe.wait_ge(o_out, i - 1)
                    for c in range(KD):
                        mm = pe.transpose(tr[i % 2][:, c * P:(c + 1) * P], o[:, i, c * P:(c + 1) * P], ident[:])
                    mm.then_inc(o_turned, 1)

            @block.scalar
            def _(act):
                act.wait_ge(lam_summed, 1)
                act.activation(lam[:, 2:4], lam[:, 0:2], ACT.Exp).then_inc(lam_exp, 1)
                for n, (what, i) in enumerate(order):
                    act.wait_ge(turned, n + 1)
                    to = qT[:, :, i * P:(i + 1) * P] if what == "q" else kT[:, :, (i if n < 2 else 2 + i) * P:
                                                                            (i + 1 if n < 2 else 3 + i) * P]
                    act.activation(to, tr[n % 2][:].rearrange("p (k t) -> p k t", k=KD), ACT.Copy).then_inc(turn_copied, 1)
                for n in range(N + 1):
                    if n < N:
                        if n >= 2:
                            act.wait_ge(probs_done, n - 1)
                        for c in range(2):
                            act.wait_ge(max_done, 2 * n + c + 1)
                            act.activation(e[:, n % 2, c], sc[:, c, 0:LK], ACT.Exp, bias=st[:, n, c:c + 1], scale=SCALE,
                                           accum_out=st[:, n, 2 + c:3 + c]).then_inc(exp_done, 1)
                    if n:
                        m = n - 1
                        act.wait_ge(probs_turned, m + 1)
                        if m >= 2:
                            act.wait_ge(o_done, m - 1)
                        act.activation(aT[:, m % 2], tr[0][:, 0:LK], ACT.Copy).then_inc(probs_copied, 1)
                for i in range(TT):
                    act.wait_ge(o_turned, i + 1)
                    if i >= 2:
                        act.wait_ge((stored0, stored1)[i % 2], 16)
                    act.activation(oT[:, i % 2].rearrange("p k t -> p (k t)"), tr[i % 2][:], ACT.Copy).then_inc(o_out, 1)

            @block.vector
            def _(dve):
                step = Steps(dve, dve_steps)
                dve.wait_ge(small_loaded, 48)
                for c in range(2):
                    step(dve.tensor_tensor_reduce(tmp[:, 0, c, 0:DH], lam4[:, 2 * c], lam4[:, 2 * c + 1], 1.0, 0.0,
                                                  ALU.mult, ALU.add, lam[:, c:c + 1]), wait=False)
                step.wait()
                dve.sem_inc(lam_summed, 1)
                dve.wait_ge(lam_exp, 1)
                step(dve.tensor_tensor(lam[:, 4:5], lam[:, 3:4], lam[:, 2:3], ALU.subtract))
                step(dve.tensor_scalar(lam[:, 5:6], lam[:, 4:5], -0.2, None, ALU.add))
                step(dve.tensor_scalar(gs[:], gs[:], 0.8, None, ALU.mult))
                dve.wait_ge(q_loaded, 16)
                for i in range(TT):
                    rotate(dve, step, q[:, i], i, 0, q_rotated)

                def combine(m):
                    dve.wait_ge(exp_done, 2 * m + 2)
                    step(dve.reciprocal(rs[:, :, m], st[:, m, 2:4]))
                    step(dve.tensor_tensor(rs[:, 1, m:m + 1], rs[:, 1, m:m + 1], lam[:, 5:6], ALU.mult))
                    if m >= 2:
                        dve.wait_ge(probs_turned, m - 1)
                    step(dve.tensor_scalar(a[:, m % 2], e[:, m % 2, 0], rs[:, 0, m:m + 1], None, ALU.mult))
                    dve.scalar_tensor_tensor(a[:, m % 2], e[:, m % 2, 1], rs[:, 1, m:m + 1], a[:, m % 2], ALU.mult,
                                             ALU.add).then_inc(probs_done, 1)

                def copy_o(m):
                    h, i = divmod(m, TT)
                    dve.wait_ge(o_done, m + 1)
                    dve.tensor_copy(o[:, i, h * P:(h + 1) * P], tr[1][:, (m % 2) * W:(m % 2) * W + P]).then_inc(o_copied, 1)

                for n in range(N):
                    for c in range(2):
                        dve.wait_ge(scores_done, 2 * n + c + 1)
                        step(dve.tensor_reduce(st[:, n, c:c + 1], sc[:, c, 0:LK], AX.X, ALU.max))
                        dve.tensor_scalar(st[:, n, c:c + 1], st[:, n, c:c + 1], -SCALE, None, ALU.mult).then_inc(max_done, 1)
                    if n:
                        combine(n - 1)
                    if n >= 3:
                        copy_o(n - 3)
                combine(N - 1)
                for m in range(N - 3, N):
                    copy_o(m)
                dve.wait_ge(o_copied, N)
                for i in range(TT):
                    rows = o[:, i].rearrange("p (h c) -> p h c", h=VH)
                    sq = q[:, i]
                    step(dve.tensor_tensor(sq, o[:, i], o[:, i], ALU.mult))
                    step(dve.tensor_reduce(ss[:, i], sq.rearrange("p (h c) -> p h c", h=VH), AX.X, ALU.add))
                    dve.tensor_scalar(ss[:, i], ss[:, i], 1.0 / P, None, ALU.mult).then_inc(squared, 1)
                    dve.wait_ge(rooted, i + 1)
                    step(dve.tensor_tensor(rows, rows, ss[:, i].unsqueeze(2).to_broadcast([P, VH, P]), ALU.mult))
                    dve.tensor_tensor(rows, rows, gs[:].unsqueeze(1).to_broadcast([P, VH, P]), ALU.mult).then_inc(rows_done, 1)


def spatial_gating(nc, d):
    G = 8
    with phase(nc, "z_loaded", "small_loaded", "gelu_done", "averaged", "rooted", "v_done", "mixed", "bank_free",
               "turned", "copied", "stored0", "stored1", "pool_steps", "dve_steps") as (
            z_loaded, small_loaded, gelu_done, averaged, rooted, v_done, mixed, bank_free, turned, copied, stored0,
            stored1, pool_steps, dve_steps), ExitStack() as ctx:
        sb, ps = tensors(nc, ctx)
        z = sb("sg_z", [P, TT, 2 * D])
        ws = sb("sg_ws", [P, G, P])
        bs = sb("sg_bs", [P, G])
        gv = sb("sg_g", [P, D])
        bv = sb("sg_b", [P, D])
        s = sb("sg_s", [P, TT, D])
        st = sb("sg_st", [P, TT, 2, 6])
        mv = sb("sg_mv", [P, TT, 2])
        rs = sb("sg_rs", [P, TT])
        mhalf = sb("sg_mhalf", [P, 1])
        ident = sb("sg_ident", [P, P])
        sT = sb("sg_sT", [P, 2, KD, P])
        mix = ps("sg_mix", [P, 4, TT, P])
        acc = ps("sg_acc", [P, 2, KD, P])
        with nc.Block() as block:
            @block.sync
            def _(sp):
                sp.dma_start(z[:], d["zg"].rearrange("(t p) n -> p t n", p=P)[:, :, 0:2 * D]).then_inc(z_loaded, 16)
                sp.dma_start(ws[:], d["sgu_wT"]).then_inc(small_loaded, 16)
                sp.dma_start(bs[:], d["sgu_bT"]).then_inc(small_loaded, 16)
                sp.dma_start(gv[:], over_partitions(d["sgu_ln_g"])).then_inc(small_loaded, 16)
                sp.dma_start(bv[:], over_partitions(d["sgu_ln_b"])).then_inc(small_loaded, 16)
                sp.dma_start(ident[:], d["ident"]).then_inc(small_loaded, 16)
                out = d["sT"].rearrange("(k p) t -> p k t", p=P)
                for i in range(TT):
                    sp.wait_ge(copied, i + 1)
                    sp.dma_start(out[:, :, i * P:(i + 1) * P], sT[:, i % 2]).then_inc((stored0, stored1)[i % 2], 16)
                sp.wait_ge(stored0, 32)
                sp.wait_ge(stored1, 32)

            @block.scalar
            def _(act):
                act.wait_ge(z_loaded, 16)
                for i in range(TT):
                    act.activation(z[:, i], z[:, i], ACT.Gelu).then_inc(gelu_done, 1)
                for i in range(TT):
                    act.wait_ge(turned, i + 1)
                    if i >= 2:
                        act.wait_ge((stored0, stored1)[i % 2], 16)
                    act.activation(sT[:, i % 2], acc[:, i % 2], ACT.Copy).then_inc(copied, 1)

            @block.gpsimd
            def _(pool):
                steps = Steps(pool, pool_steps)
                steps(pool.memset(mhalf[:], -0.5))
                for i in range(TT):
                    pool.wait_ge(averaged, i + 1)
                    root_reciprocal(pool, steps, rs[:, i:i + 1], mv[:, i, 1:2], 1e-5, mhalf[:]).then_inc(rooted, 1)

            @block.vector
            def _(dve):
                step = Steps(dve, dve_steps)
                dve.wait_ge(small_loaded, 80)
                for i in range(TT):
                    dve.wait_ge(gelu_done, i + 1)
                    v = z[:, i, D:2 * D]
                    for h in range(2):
                        step(dve.bn_stats(st[:, i, h, :], v[:, h * W:(h + 1) * W]), wait=False)
                    step.wait()
                    dve.bn_aggr(mv[:, i, :], st[:, i].rearrange("p s c -> p (s c)")).then_inc(averaged, 1)
                    dve.wait_ge(rooted, i + 1)
                    step(dve.tensor_scalar(v, v, mv[:, i, 0:1], rs[:, i:i + 1], ALU.subtract, ALU.mult))
                    step(dve.tensor_tensor(v, v, gv[:], ALU.mult))
                    dve.tensor_tensor(v, v, bv[:], ALU.add).then_inc(v_done, 1)
                for g in range(G):
                    cols = slice(g * P, (g + 1) * P)
                    dve.wait_ge(mixed, g + 1)
                    dve.scalar_tensor_tensor(s[:, :, cols], mix[:, g % 4], bs[:, g:g + 1], z[:, :, cols], ALU.add,
                                             ALU.mult).then_inc(bank_free, 1)

            @block.tensor
            def _(pe):
                pe.wait_ge(small_loaded, 80)
                pe.wait_ge(v_done, TT)
                for g in range(G):
                    if g >= 4:
                        pe.wait_ge(bank_free, g - 3)
                    pe.matmul(mix[:, g % 4], ws[:, g, :], z[:, :, D + g * P:D + (g + 1) * P], start=True,
                              stop=True).then_inc(mixed, 1)
                pe.wait_ge(bank_free, G)
                transpose_out(pe, TT, lambda i: s[:, i], bank_free, ident, acc, copied, turned)


def combine_branches(nc, d):
    with phase(nc, "loaded", "small_loaded", "biased", "sig_done", "rows_done", "turned", "copied", "stored0",
               "stored1", "dve_steps") as (loaded, small_loaded, biased, sig_done, rows_done, turned, copied, stored0,
                                           stored1, dve_steps), ExitStack() as ctx:
        sb, ps = tensors(nc, ctx)
        gl = sb("cb_gl", [P, TT, 2 * D])
        y = sb("cb_y", [P, 2, TT, D])
        bg = sb("cb_bg", [P, 2 * D])
        ident = sb("cb_ident", [P, P])
        yT = sb("cb_yT", [P, 2, KD, P])
        acc = ps("cb_acc", [P, 2, KD, P])
        with nc.Block() as block:
            @block.sync
            def _(sp):
                sp.dma_start(gl[:], d["zg"].rearrange("(t p) n -> p t n", p=P)[:, :, 2 * D:4 * D]).then_inc(small_loaded, 16)
                sp.dma_start(bg[:], over_partitions(d["b_gate"])).then_inc(small_loaded, 16)
                sp.dma_start(ident[:], d["ident"]).then_inc(small_loaded, 16)
                sp.dma_start(y[:, 0], d["ya"].rearrange("(t p) n -> p t n", p=P)).then_inc(loaded, 16)
                sp.dma_start(y[:, 1], d["ys"].rearrange("(t p) n -> p t n", p=P)).then_inc(loaded, 16)
                out = d["yT"].rearrange("(k p) t -> p k t", p=P)
                for i in range(TT):
                    sp.wait_ge(copied, i + 1)
                    sp.dma_start(out[:, :, i * P:(i + 1) * P], yT[:, i % 2]).then_inc((stored0, stored1)[i % 2], 16)
                sp.wait_ge(stored0, 32)
                sp.wait_ge(stored1, 32)

            @block.scalar
            def _(act):
                for i in range(TT):
                    act.wait_ge(biased, i + 1)
                    act.activation(gl[:, i], gl[:, i], ACT.Sigmoid).then_inc(sig_done, 1)
                for i in range(TT):
                    act.wait_ge(turned, i + 1)
                    if i >= 2:
                        act.wait_ge((stored0, stored1)[i % 2], 16)
                    act.activation(yT[:, i % 2], acc[:, i % 2], ACT.Copy).then_inc(copied, 1)

            @block.vector
            def _(dve):
                step = Steps(dve, dve_steps)
                dve.wait_ge(small_loaded, 48)
                for i in range(TT):
                    dve.tensor_tensor(gl[:, i], gl[:, i], bg[:], ALU.add).then_inc(biased, 1)
                dve.wait_ge(loaded, 32)
                for i in range(TT):
                    dve.wait_ge(sig_done, i + 1)
                    for b in range(2):
                        step(dve.tensor_tensor(y[:, b, i], y[:, b, i], gl[:, i, b * D:(b + 1) * D], ALU.mult), wait=False)
                    step.wait()
                    dve.tensor_tensor(y[:, 0, i], y[:, 0, i], y[:, 1, i], ALU.add).then_inc(rows_done, 1)

            @block.tensor
            def _(pe):
                pe.wait_ge(small_loaded, 48)
                transpose_out(pe, TT, lambda i: y[:, 0, i], rows_done, ident, acc, copied, turned)
PH = 8
TK = 16
NK = 128
HK = PH * TK
SEG = 2 * PH
LOW = -3.0e38


def expert_choice(nc, d):
    with phase(nc, "rows_loaded", "small_loaded", "squared", "rooted", "rows_done", "turned", "turn_copied",
               "scores_done", "scores_copied", "topk_done", "chosen", "maxed", "exp_done", "sel_ready", "sel_turned", "sel_copied",
               "stored", "pool_steps", "dve_steps") as (
            rows_loaded, small_loaded, squared, rooted, rows_done, turned, turn_copied, scores_done, scores_copied,
            topk_done, chosen, maxed, exp_done, sel_ready, sel_turned, sel_copied, stored, pool_steps, dve_steps), ExitStack() as ctx:
        sb, ps = tensors(nc, ctx)
        q = sb("ec_q", [P, TT, SEG, NK])
        sq = sb("ec_sq", [P, SEG, NK])
        ss = sb("ec_ss", [P, TT, SEG])
        mhalf = sb("ec_mhalf", [P, SEG])
        keys = sb("ec_keys", [P, 2, NK])
        ident = sb("ec_ident", [P, P])
        iota = sb("ec_iota", [P, TK])
        qT = sb("ec_qT", [P, SEG, P])
        s = sb("ec_s", [P, 2, SEG, NK])
        s2 = sb("ec_s2", [P, SEG, NK])
        val = sb("ec_val", [P, SEG, TK])
        idx = sb("ec_idx", [P, SEG, TK], U32)
        idxf = sb("ec_idxf", [P, SEG, TK])
        cand = sb("ec_cand", [P, PH, TK, TK])
        cand2 = sb("ec_cand2", [P, PH, TK, TK])
        hot = sb("ec_hot", [P, PH, TK, TK])
        best = sb("ec_best", [P, PH, TK])
        pos = sb("ec_pos", [P, PH, TK], U32)
        part = sb("ec_part", [P, 2, PH, TK], U32)
        partf = sb("ec_partf", [P, 2, PH, TK])
        tot = sb("ec_tot", [P, PH])
        sel = sb("ec_sel", [P, TT, 3, HK])
        selT = sb("ec_selT", [P, 3, T])
        acc = ps("ec_acc", [P, 2, KD, P])
        sc = ps("ec_sc", [P, SEG, NK])
        with nc.Block() as block:
            @block.sync
            def _(sp):
                sp.dma_start(keys[:], d["keysT"]).then_inc(small_loaded, 16)
                sp.dma_start(ident[:], d["ident"]).then_inc(small_loaded, 16)
                sp.dma_start(iota[:], d["iota"][:, 0:TK]).then_inc(small_loaded, 16)
                sp.dma_start(q[:], d["qp"].rearrange("(t p) (s n) -> p t s n", p=P, n=NK)).then_inc(rows_loaded, 16)
                sp.wait_ge(sel_copied, 3)
                sp.dma_start(d["sel"].rearrange("c h t -> h c t"), selT[:]).then_inc(stored, 16)
                sp.wait_ge(stored, 16)

            @block.gpsimd
            def _(pool):
                steps = Steps(pool, pool_steps)
                steps(pool.memset(mhalf[:], -0.5))
                for i in range(TT):
                    pool.wait_ge(squared, i + 1)
                    root_reciprocal(pool, steps, ss[:, i], ss[:, i], 1e-6, mhalf[:]).then_inc(rooted, 1)

            @block.tensor
            def _(pe):
                pe.wait_ge(small_loaded, 48)
                for i in range(TT):
                    pe.wait_ge(rows_done, i + 1)
                    for g in range(2):
                        if i:
                            pe.wait_ge(turn_copied, 2 * (i - 1) + g + 1)
                        for k in range(KD):
                            mm = pe.transpose(acc[:, g, k, :], q[:, i, g * KD + k, :], ident[:])
                        mm.then_inc(turned, 1)
                    pe.wait_ge(turn_copied, 2 * (i + 1))
                    if i:
                        pe.wait_ge(scores_copied, i)
                    for g in range(SEG):
                        mm = pe.matmul(sc[:, g, :], qT[:, g, :], keys[:, g % 2, :], start=True, stop=True)
                    mm.then_inc(scores_done, 1)
                pe.wait_ge(sel_ready, TT)
                pe.wait_ge(scores_copied, TT)
                for c in range(3):
                    for i in range(TT):
                        mm = pe.transpose(sc[:, 4 * c + i, :], sel[:, i, c, :], ident[:])
                    mm.then_inc(sel_turned, 1)

            @block.scalar
            def _(act):
                def softmax_exp(i):
                    act.wait_ge(maxed, i + 1)
                    act.activation(best[:], best[:], ACT.Exp).then_inc(exp_done, 1)

                for i in range(TT):
                    for g in range(2):
                        act.wait_ge(turned, 2 * i + g + 1)
                        if i:
                            act.wait_ge(scores_done, i)
                        act.activation(qT[:, g * KD:(g + 1) * KD, :], acc[:, g], ACT.Copy).then_inc(turn_copied, 1)
                    act.wait_ge(scores_done, i + 1)
                    if i >= 2:
                        act.wait_ge(topk_done, i - 1)
                    act.activation(s[:, i % 2], sc[:], ACT.Copy).then_inc(scores_copied, 1)
                    if i:
                        softmax_exp(i - 1)
                softmax_exp(TT - 1)
                for c in range(3):
                    act.wait_ge(sel_turned, c + 1)
                    act.activation(selT[:, c, :], sc[:, 4 * c:4 * c + 4, :].rearrange("p a b -> p (a b)"),
                                   ACT.Copy).then_inc(sel_copied, 1)

            @block.vector
            def _(dve):
                step = Steps(dve, dve_steps)
                dve.wait_ge(rows_loaded, 16)
                dve.wait_ge(small_loaded, 48)
                for i in range(TT):
                    step(dve.tensor_tensor(sq[:], q[:, i], q[:, i], ALU.mult))
                    step(dve.tensor_reduce(ss[:, i], sq[:], AX.X, ALU.add))
                    dve.tensor_scalar(ss[:, i], ss[:, i], 1.0 / NK, None, ALU.mult).then_inc(squared, 1)
                    dve.wait_ge(rooted, i + 1)
                    dve.tensor_tensor(q[:, i], q[:, i], ss[:, i].unsqueeze(2).to_broadcast([P, SEG, NK]),
                                      ALU.mult).then_inc(rows_done, 1)

                def top16(rows, n, values, indices, rest):
                    for g in range(n):
                        step(dve.max(values[:, g, 0:8], rows(g)), wait=False)
                    step.wait()
                    for g in range(n):
                        step(dve.max_index(indices[:, g, 0:8], values[:, g, 0:8], rows(g)), wait=False)
                        step(dve.match_replace(rest(g), values[:, g, 0:8], rows(g), LOW), wait=False)
                    step.wait()
                    for g in range(n):
                        step(dve.max(values[:, g, 8:16], rest(g)), wait=False)
                    step.wait()
                    for g in range(n):
                        step(dve.max_index(indices[:, g, 8:16], values[:, g, 8:16], rest(g)), wait=False)
                    step.wait()

                for i in range(TT):
                    dve.wait_ge(scores_copied, i + 1)
                    top16(lambda g: s[:, i % 2, g, :], SEG, val, idx, lambda g: s2[:, g, :])
                    dve.sem_inc(topk_done, 1)
                    step(dve.tensor_copy(idxf[:], idx[:]), wait=False)
                    v4 = val[:].rearrange("p (h s) k -> p h s k", s=2)
                    i4 = idxf[:].rearrange("p (h s) k -> p h s k", s=2)
                    step(dve.tensor_tensor(cand[:], v4[:, :, 0, :].unsqueeze(3).to_broadcast([P, PH, TK, TK]),
                                           v4[:, :, 1, :].unsqueeze(2).to_broadcast([P, PH, TK, TK]), ALU.add))
                    top16(lambda h: cand[:, h].rearrange("p a b -> p (a b)"), PH, best, pos,
                          lambda h: cand2[:, h].rearrange("p a b -> p (a b)"))
                    step(dve.tensor_single_scalar(part[:, 0], pos[:], 4, ALU.logical_shift_right), wait=False)
                    step(dve.tensor_single_scalar(part[:, 1], pos[:], 15, ALU.bitwise_and))
                    step(dve.tensor_copy(partf[:], part[:]))
                    for c in range(2):
                        step(dve.tensor_tensor(hot[:], partf[:, c].unsqueeze(3).to_broadcast([P, PH, TK, TK]),
                                               iota[:].unsqueeze(1).unsqueeze(1).to_broadcast([P, PH, TK, TK]),
                                               ALU.is_equal))
                        step(dve.tensor_tensor(hot[:], hot[:], i4[:, :, c, :].unsqueeze(2).to_broadcast([P, PH, TK, TK]),
                                               ALU.mult))
                        step(dve.tensor_reduce(sel[:, i, c, :].rearrange("p (h k) -> p h k", h=PH), hot[:], AX.X, ALU.add))
                    step(dve.tensor_copy(tot[:], best[:, :, 0]))
                    dve.tensor_tensor(best[:], best[:], tot[:].unsqueeze(2).to_broadcast([P, PH, TK]),
                                      ALU.subtract).then_inc(maxed, 1)
                    dve.wait_ge(exp_done, i + 1)
                    step(dve.tensor_reduce(tot[:], best[:], AX.X, ALU.add))
                    step(dve.reciprocal(tot[:], tot[:]))
                    step(dve.tensor_tensor(sel[:, i, 2, :].rearrange("p (h k) -> p h k", h=PH), best[:],
                                           tot[:].unsqueeze(2).to_broadcast([P, PH, TK]), ALU.mult))
                    dve.sem_inc(sel_ready, 1)


def expert_gates(nc, d):
    GT = 8
    RB = 128
    GB = RB // GT
    with phase(nc, "loaded", "a_ready", "b_ready", "bank_done", "copied", "stored0", "stored1") as (
            loaded, a_ready, b_ready, bank_done, copied, stored0, stored1), ExitStack() as ctx:
        sb, ps = tensors(nc, ctx)
        sel = sb("eg_sel", [P, 3, T])
        iota = sb("eg_iota", [P, NK])
        a = sb("eg_a", [P, 2, GT, NK])
        b = sb("eg_b", [P, 2, GT, NK])
        gates = sb("eg_gates", [P, 2, NK, RB])
        acc = ps("eg_acc", [P, 2, 2, GT // 2, NK])
        stored = (stored0, stored1)
        with nc.Block() as block:
            @block.sync
            def _(sp):
                sp.dma_start(sel[:], d["sel"].rearrange("c h t -> h c t")).then_inc(loaded, 16)
                sp.dma_start(iota[:], d["iota"]).then_inc(loaded, 16)
                out = d["G"].rearrange("i j t -> j i t")
                for r in range(T // RB):
                    sp.wait_ge(copied, 4 + 2 * GB * (r + 1))
                    sp.dma_start(out[:, :, r * RB:(r + 1) * RB], gates[:, r % 2]).then_inc(stored[r % 2], 16)
                sp.wait_ge(stored0, 32)
                sp.wait_ge(stored1, 32)

            @block.vector
            def _(dve):
                dve.wait_ge(loaded, 32)
                with dve.Fori(0, T // (2 * GT)) as i:
                    for u in range(2):
                        dve.wait_ge(bank_done, i * 4 + 2 * u + 2)
                        for t in range(GT):
                            at = bass.ds(i * (2 * GT) + u * GT + t, 1)
                            ins = dve.tensor_scalar(a[:, u, t, :], iota[:], sel[:, 0, at], sel[:, 2, at], ALU.is_equal,
                                                    ALU.mult)
                        ins.then_inc(a_ready, 1)
                        at = bass.ds(i * (2 * GT) + u * GT, GT)
                        dve.tensor_tensor(b[:, u], iota[:].unsqueeze(1).to_broadcast([P, GT, NK]),
                                          sel[:, 1, at].unsqueeze(2).to_broadcast([P, GT, NK]),
                                          ALU.is_equal).then_inc(b_ready, 1)

            @block.tensor
            def _(pe):
                pe.sem_inc(bank_done, 4)
                with pe.Fori(0, T // (2 * GT)) as i:
                    for u in range(2):
                        pe.wait_ge(a_ready, i * 2 + u + 1)
                        pe.wait_ge(b_ready, i * 2 + u + 1)
                        for h in range(2):
                            pe.wait_ge(copied, i * 4 + 2 * u + h + 1)
                            for t in range(GT // 2):
                                mm = pe.matmul(acc[:, u, h, t, :], b[:, u, h * (GT // 2) + t, :],
                                               a[:, u, h * (GT // 2) + t, :], start=True, stop=True)
                            mm.then_inc(bank_done, 1)

            @block.scalar
            def _(act):
                act.sem_inc(copied, 4)
                for r in range(T // RB):
                    if r >= 2:
                        act.wait_ge(stored[r % 2], 16 * (r // 2))
                    rows = gates[:, r % 2].rearrange("p i t -> p t i")
                    with act.Fori(0, GB // 2) as i:
                        for u in range(2):
                            for h in range(2):
                                act.wait_ge(bank_done, i * 4 + (4 + 2 * GB * r + 2 * u + h + 1))
                                act.activation(rows[:, bass.ds(i * (2 * GT) + u * GT + h * (GT // 2), GT // 2), :],
                                               acc[:, u, h], ACT.Copy).then_inc(copied, 1)


def experts(nc, d):
    GI = 4
    NG = NK // GI
    HALVES = D // W
    OB = TT * HALVES
    OPEN = 4
    with phase(nc, "x_loaded", "ug0_loaded", "ug1_loaded", "v_loaded", "x_hi", "x_lo", "u_hi", "u_lo", "v_hi", "v_lo",
               "h_done", "gelu_done", "gated", "act_hi", "act_lo", "out_done", "added", "stored") as (
            x_loaded, ug0_loaded, ug1_loaded, v_loaded, x_hi, x_lo, u_hi, u_lo, v_hi, v_lo, h_done, gelu_done, gated,
            act_hi, act_lo, out_done, added, stored), ExitStack() as ctx:
        sb, ps = tensors(nc, ctx)
        xh = sb("ex_xh", [P, KD, T], F32R)
        xl = sb("ex_xl", [P, KD, T], F32R)
        ut = sb("ex_u", [P, 2, GI, KD, NK])
        uh = sb("ex_uh", [P, 2, KD, NK], F32R)
        ul = sb("ex_ul", [P, 2, KD, NK], F32R)
        vt = sb("ex_v", [P, GI, D])
        vh = sb("ex_vh", [P, GI, D], F32R)
        vl = sb("ex_vl", [P, GI, D], F32R)
        gt = sb("ex_g", [P, 2, GI, T])
        ge = sb("ex_ge", [P, 2, T])
        ag = sb("ex_gated", [P, 2, T])
        ah = sb("ex_ah", [P, GI, T], F32R)
        al = sb("ex_al", [P, GI, T], F32R)
        total = sb("ex_total", [P, TT, D])
        hb = ps("ex_hb", [P, 2, T])
        ob = ps("ex_ob", [P, OPEN, W])
        x = total[:].rearrange("p t n -> p (t n)").rearrange("p (k t) -> p k t", k=KD)
        ug_loaded = (ug0_loaded, ug1_loaded)
        u_in = d["uT"].rearrange("i p k j -> p i (k j)")
        v_in = d["peer_v"].rearrange("(i j) n -> j i n", j=NK)
        g_in = d["G"].rearrange("i j t -> j i t")
        with nc.Block() as block:
            @block.sync
            def _(sp):
                sp.dma_start(x, d["h2T"].rearrange("(k p) t -> p k t", p=P)).then_inc(x_loaded, 16)
                with sp.Fori(0, NG // 2) as i:
                    for u in range(2):
                        keys = bass.ds(i * (2 * GI) + u * GI, GI)
                        sp.wait_ge(u_lo, i * (2 * GI) + (u + 1) * GI)
                        sp.dma_start(ut[:, u].rearrange("p i k j -> p i (k j)"), u_in[:, keys, :]).then_inc(ug_loaded[u], 16)
                        sp.wait_ge(gated, i * (2 * GI) + (u + 1) * GI)
                        sp.dma_start(gt[:, u], g_in[:, keys, :]).then_inc(ug_loaded[u], 16)
                        sp.wait_ge(v_lo, i * (2 * GI) + (u + 1) * GI)
                        sp.dma_start(vt[:], v_in[:, keys, :]).then_inc(v_loaded, 16)
                sp.wait_ge(added, OB * (NG + 1))
                sp.dma_start(d["po"].rearrange("(t p) n -> p t n", p=P), total[:]).then_inc(stored, 16)
                sp.wait_ge(stored, 16)

            @block.tensor
            def _(pe):
                pe.sem_inc(h_done, 2)
                pe.sem_inc(out_done, OB)
                pe.wait_ge(x_lo, 1)
                with pe.Fori(0, NG // 2) as i:
                    for u in range(2):
                        for c in range(GI):
                            key = i * (2 * GI) + (u * GI + c)
                            pe.wait_ge(u_lo, key + (2 * GI + 1))
                            pe.wait_ge(gelu_done, key + 1)
                            for k in range(KD):
                                mm = product3(pe, hb[:, c % 2, :], (uh[:, c % 2, k, :], ul[:, c % 2, k, :]),
                                              (xh[:, k, :], xl[:, k, :]), k == 0, k == KD - 1)
                            mm.then_inc(h_done, 1)
                        for first in range(0, OB, OPEN):
                            for keys in (range(GI - 1), range(GI - 1, GI)):
                                key = i * (2 * GI) + (u * GI + keys[-1])
                                if first == 0:
                                    pe.wait_ge(act_lo, key + 3)
                                    pe.wait_ge(v_lo, key + (GI + 1))
                                for n in range(first, first + OPEN):
                                    t, half = divmod(n, HALVES)
                                    if keys[0] == 0:
                                        pe.wait_ge(added, i * (2 * OB) + (u * OB + n + 1 + OPEN))
                                    for c in keys:
                                        tok, cols = slice(t * P, (t + 1) * P), slice(half * W, (half + 1) * W)
                                        mm = product3(pe, ob[:, n % OPEN, :], (ah[:, c, tok], al[:, c, tok]),
                                                      (vh[:, c, cols], vl[:, c, cols]), c == 0, c == GI - 1)
                                    if keys[-1] == GI - 1:
                                        mm.then_inc(out_done, 1)

            @block.scalar
            def _(act):
                def split_u(i, u, c):
                    key = i * (2 * GI) + (u * GI + c)
                    if c == 0:
                        act.wait_ge(ug_loaded[u], i * 32 + 32)
                    act.wait_ge(h_done, key + 1)
                    act.activation(uh[:, c % 2], ut[:, u, c], ACT.Copy).then_inc(u_hi, 1)

                def pair(i, last):
                    for u in range(2):
                        group = i * 2 + u
                        for c in range(GI):
                            key = i * (2 * GI) + (u * GI + c)
                            if c + 2 < GI:
                                split_u(i, u, c + 2)
                            elif not (last and u == 1):
                                split_u(i + u, 1 - u, c + 2 - GI)
                            act.wait_ge(h_done, key + 3)
                            act.wait_ge(gated, key + (2 * GI - 1))
                            act.activation(ge[:, c % 2, :], hb[:, c % 2, :], ACT.Gelu).then_inc(gelu_done, 1)
                            if c == 0:
                                act.wait_ge(v_loaded, group * 16 + 16)
                                act.wait_ge(out_done, group * OB + OB)
                            act.activation(vh[:, c], vt[:, c], ACT.Copy).then_inc(v_hi, 1)
                            act.wait_ge(gated, key + (2 * GI + 1))
                            act.activation(ah[:, c], ag[:, c % 2], ACT.Copy).then_inc(act_hi, 1)

                act.sem_inc(gelu_done, 2)
                act.wait_ge(x_loaded, 16)
                act.activation(xh[:], x, ACT.Copy).then_inc(x_hi, 1)
                split_u(0, 0, 0)
                split_u(0, 0, 1)
                with act.Fori(0, NG // 2 - 1) as i:
                    pair(i, False)
                pair(NG // 2 - 1, True)

            @block.gpsimd
            def _(pool):
                pool.sem_inc(u_lo, 2 * GI)
                with pool.Fori(0, NG // 2) as i:
                    for u in range(2):
                        for c in range(GI):
                            pool.wait_ge(u_hi, i * (2 * GI) + (u * GI + c + 1))
                            pool.tensor_tensor(ul[:, c % 2], ut[:, u, c], uh[:, c % 2].bitcast(F32),
                                               ALU.subtract).then_inc(u_lo, 1)

            @block.vector
            def _(dve):
                dve.sem_inc(v_lo, GI)
                dve.sem_inc(gated, 2 * GI)
                dve.sem_inc(act_lo, 2)
                dve.wait_ge(x_hi, 1)
                dve.tensor_tensor(xl[:], x, xh[:].bitcast(F32), ALU.subtract).then_inc(x_lo, 1)
                dve.wait_ge(x_lo, 1)
                for n in range(OB):
                    t, half = divmod(n, HALVES)
                    dve.memset(total[:, t, half * W:(half + 1) * W], 0.0).then_inc(added, 1)
                with dve.Fori(0, NG // 2) as i:
                    for u in range(2):
                        dve.wait_ge(ug_loaded[u], i * 32 + 32)
                        for c in range(GI):
                            key = i * (2 * GI) + (u * GI + c)
                            dve.wait_ge(gelu_done, key + 3)
                            dve.wait_ge(act_lo, key + 1)
                            dve.tensor_tensor(ag[:, c % 2], ge[:, c % 2, :], gt[:, u, c, :], ALU.mult).then_inc(gated, 1)
                            dve.wait_ge(v_hi, key + 1)
                            dve.tensor_tensor(vl[:, c], vt[:, c], vh[:, c].bitcast(F32), ALU.subtract).then_inc(v_lo, 1)
                            dve.wait_ge(act_hi, key + 1)
                            dve.tensor_tensor(al[:, c], ag[:, c % 2], ah[:, c].bitcast(F32), ALU.subtract).then_inc(act_lo, 1)
                        for n in range(OB):
                            t, half = divmod(n, HALVES)
                            dve.wait_ge(out_done, i * (2 * OB) + (u * OB + n + 1 + OB))
                            dve.wait_ge(added, i * (2 * OB) + (u * OB + n + 1))
                            cols = total[:, t, half * W:(half + 1) * W]
                            dve.tensor_tensor(cols, cols, ob[:, n % OPEN, :], ALU.add).then_inc(added, 1)
def conv_ffn(nc, d, x_in, w_up, conv_w, conv_b, w_down, y_out):
    C = w_down.shape[0] // P
    DB = C // 2
    wv = w_up.rearrange("(k p) n -> p k n", p=P)
    wd = w_down.rearrange("(c p) n -> p c n", p=P)
    assert C % 2 == 0 and DB % 2 == 1
    with phase(nc, "x_loaded", "c_loaded", "w0_loaded", "w1_loaded", "x_hi", "x_lo", "w_hi", "w_lo", "up_done", "base_done",
               "tap_done", "conv_done", "silu_done", "h_done", "h_hi", "h_lo", "block_done", "bank_done", "act_copied",
               "dve_copied", "stored") as (
            x_loaded, c_loaded, w0_loaded, w1_loaded, x_hi, x_lo, w_hi, w_lo, up_done, base_done, tap_done, conv_done,
            silu_done, h_done, h_hi, h_lo, block_done, bank_done, act_copied, dve_copied, stored), ExitStack() as ctx:
        sb, ps = tensors(nc, ctx)
        xh = sb("ff_xh", [P, KD, T], F32R)
        xl = sb("ff_xl", [P, KD, T], F32R)
        raw = sb("ff_raw", [P, 2, 2, D])
        wh = sb("ff_wh", [P, 2, 2, D], F32R)
        wl = sb("ff_wl", [P, 2, 2, D], F32R)
        cw = sb("ff_cw", [P, 2 * C, 3])
        cb = sb("ff_cb", [P, 2 * C])
        cv = sb("ff_cv", [P, 2, 2, T])
        h = sb("ff_h", [P, 2, T])
        hh = sb("ff_hh", [P, C, T], F32R)
        hl = sb("ff_hl", [P, C, T], F32R)
        acc = ps("ff_acc", [P, 2 * TT, W])
        up = acc[:, 0:4].rearrange("p (u s) t -> p u s t", u=2)
        order = [n for half in (1, 0) for n in range(half * 4, half * 4 + 4)]
        y = raw[:].rearrange("p u s n -> p (u s) n")
        x = hh[:].bitcast(F32)[:, 0:KD]
        w_loaded = (w0_loaded, w1_loaded)

        with nc.Block() as block:
            @block.sync
            def _(sp):
                sp.dma_start(x, x_in.rearrange("(k p) t -> p k t", p=P)).then_inc(x_loaded, 16)
                with sp.Fori(0, DB) as i:
                    for u in range(2):
                        sp.wait_ge(w_lo, i * 2 + u + 1)
                        for s in range(2):
                            sp.dma_start(raw[:, u, s].rearrange("p (k j) -> p k j", k=KD),
                                         wv[:, :, bass.ds(i * (2 * P) + (s * C * P + u * P), P)]).then_inc(w_loaded[u], 16)
                for b in range(DB):
                    sp.wait_ge(w_lo, C + b + 1)
                    for s in range(2):
                        sp.dma_start(raw[:, b % 2, s], wd[:, 2 * b + s]).then_inc(w_loaded[b % 2], 16)
                for t in (2, 3, 0, 1):
                    done = (t + 2) % TT + 1
                    sp.wait_ge(act_copied, done)
                    sp.wait_ge(dve_copied, done)
                    sp.dma_start(y_out[t * P:(t + 1) * P, :], y[:, t]).then_inc(stored, 16)
                sp.wait_ge(stored, 16 * TT)

            @block.tensor
            def _(pe):
                pe.wait_ge(x_lo, 1)
                with pe.Fori(0, C // 2) as i:
                    for u in range(2):
                        pe.wait_ge(w_lo, i * 2 + u + 3)
                        for s in range(2):
                            pe.wait_ge(conv_done, i * 4 + 2 * u + s + 1)
                            for k in range(KD):
                                cols = slice(k * P, (k + 1) * P)
                                mm = product3(pe, up[:, u, s, :], (wh[:, u, s, cols], wl[:, u, s, cols]),
                                              (xh[:, k, :], xl[:, k, :]), k == 0, k == KD - 1)
                            mm.then_inc(up_done, 1)
                for c in range(C):
                    b, s = divmod(c, 2)
                    if s == 0:
                        pe.wait_ge(w_lo, C + b + 3)
                    pe.wait_ge(h_lo, c + 1)
                    for n in order:
                        t, half = divmod(n, 2)
                        if c == 0 and n < 4:
                            pe.wait_ge(conv_done, 2 * C + 4 - 3 + n)
                        tok, cols = slice(t * P, (t + 1) * P), slice(half * W, (half + 1) * W)
                        mm = product3(pe, acc[:, n, :], (hh[:, c, tok], hl[:, c, tok]),
                                      (wh[:, b % 2, s, cols], wl[:, b % 2, s, cols]), c == 0, c == C - 1)
                        if c == C - 1:
                            mm.then_inc(bank_done, 1)
                        elif s == 1 and n == order[-1]:
                            mm.then_inc(block_done, 1)

            @block.scalar
            def _(act):
                def split(count, u):
                    act.wait_ge(w_loaded[u], count * 32)
                    act.activation(wh[:, u], raw[:, u], ACT.Copy).then_inc(w_hi, 1)

                act.dma_start(cw[:], conv_w).then_inc(c_loaded, 16)
                act.dma_start(cb[:], conv_b).then_inc(c_loaded, 16)
                act.wait_ge(x_loaded, 16)
                act.activation(xh[:], x, ACT.Copy).then_inc(x_hi, 1)
                split(1, 0)
                split(1, 1)
                act.wait_ge(c_loaded, 32)
                act.wait_ge(x_lo, 1)
                with act.Fori(0, C // 2) as i:
                    for u in range(2):
                        act.wait_ge(h_done, i * 2 + u + 1)
                        for s in range(2):
                            act.wait_ge(up_done, i * 4 + 2 * u + s + 1)
                            ch = bass.ds(i * 2 + (u + s * C), 1)
                            act.activation(cv[:, u, s, :], up[:, u, s, :], ACT.Identity, bias=cb[:, ch],
                                           scale=cw[:, ch, 2]).then_inc(base_done, 1)
                        split(i + 2, u)
                        act.wait_ge(conv_done, i * 4 + 2 * u + 5)
                        act.activation(cv[:, u, 0, :], cv[:, u, 0, :], ACT.Silu).then_inc(silu_done, 1)
                        act.wait_ge(h_done, i * 2 + u + 3)
                        act.activation(hh[:, bass.ds(i * 2 + u, 1), :].rearrange("p o t -> p (o t)"), h[:, u],
                                       ACT.Copy).then_inc(h_hi, 1)
                for b in range(2, DB):
                    act.wait_ge(block_done, b - 1)
                    split((C + b) // 2 + 1, b % 2)
                for j in range(TT):
                    act.wait_ge(bank_done, 2 * j + 1)
                    act.activation(y[:, order[2 * j] // 2, 0:W], acc[:, order[2 * j], :], ACT.Copy).then_inc(act_copied, 1)

            @block.gpsimd
            def _(pool):
                def split(b, u):
                    pool.wait_ge(w_hi, b + 1)
                    pool.tensor_tensor(wl[:, u], raw[:, u], wh[:, u].bitcast(F32), ALU.subtract).then_inc(w_lo, 1)

                pool.sem_inc(w_lo, 2)
                with pool.Fori(0, (C + DB) // 2) as i:
                    split(i * 2, 0)
                    split(i * 2 + 1, 1)
                split(C + DB - 1, 0)

            @block.vector
            def _(dve):
                dve.sem_inc(conv_done, 4)
                dve.sem_inc(h_done, 2)
                dve.wait_ge(x_hi, 1)
                dve.tensor_tensor(xl[:], x, xh[:].bitcast(F32), ALU.subtract).then_inc(x_lo, 1)
                dve.wait_ge(c_loaded, 32)
                with dve.Fori(0, C // 2) as i:
                    for u in range(2):
                        for s in range(2):
                            dve.wait_ge(base_done, i * 4 + 2 * u + s + 1)
                            ch = bass.ds(i * 2 + (u + s * C), 1)
                            z, b = cv[:, u, s, :], up[:, u, s, :]
                            dve.scalar_tensor_tensor(z[:, 1:T], b[:, 0:T - 1], cw[:, ch, 1], z[:, 1:T], ALU.mult,
                                                     ALU.add).then_inc(tap_done, 1)
                            dve.wait_ge(tap_done, i * 4 + 2 * u + s + 1)
                            dve.scalar_tensor_tensor(z[:, 2:T], b[:, 0:T - 2], cw[:, ch, 0], z[:, 2:T], ALU.mult,
                                                     ALU.add).then_inc(conv_done, 1)
                        dve.wait_ge(conv_done, i * 4 + 2 * u + 6)
                        dve.wait_ge(silu_done, i * 2 + u + 1)
                        dve.tensor_tensor(h[:, u], cv[:, u, 0, :], cv[:, u, 1, :], ALU.mult).then_inc(h_done, 1)
                        dve.wait_ge(h_hi, i * 2 + u + 1)
                        chunk = bass.ds(i * 2 + u, 1)
                        dve.tensor_tensor(hl[:, chunk, :].rearrange("p o t -> p (o t)"), h[:, u],
                                          hh[:, chunk, :].bitcast(F32).rearrange("p o t -> p (o t)"),
                                          ALU.subtract).then_inc(h_lo, 1)
                for j in range(TT):
                    dve.wait_ge(bank_done, 2 * j + 2)
                    dve.tensor_copy(y[:, order[2 * j + 1] // 2, W:D], acc[:, order[2 * j + 1], :]).then_inc(dve_copied, 1)


RC = 64
NC_ = T // RC
LOG_DECAY = -float(np.exp(-0.5))


def rwkv_projections(nc, d):
    with phase(nc, "x_loaded", "small_loaded", "w0_loaded", "w1_loaded", "mixed", "bank_done", "copied", "low_done",
               "low_ready", "array_done", "stored0", "stored1", "act_steps", "dve_steps") as (
            x_loaded, small_loaded, w0_loaded, w1_loaded, mixed, bank_done, copied, low_done, low_ready, array_done,
            stored0, stored1, act_steps, dve_steps), ExitStack() as ctx:
        sb, ps = tensors(nc, ctx)
        x = sb("rp_x", [P, KD, T])
        dx = sb("rp_dx", [P, KD, T])
        xm = sb("rp_xm", [P, 2, KD, T])
        mix = sb("rp_mix", [P, 6, KD])
        wt = sb("rp_w", [P, 2, KD, W])
        low = sb("rp_low", [P, KD, 288])
        up = sb("rp_up", [P, 4, D])
        w0 = sb("rp_w0", [P, 2, KD])
        mid = sb("rp_mid", [P, 2, T])
        out = sb("rp_out", [P, 2, KD, T])
        acc = ps("rp_acc", [P, 6, T])
        lowp = ps("rp_lowp", [P, 2, T])
        w_loaded, stored = (w0_loaded, w1_loaded), (stored0, stored1)
        LOW = {3: [(0, 64, 0)], 4: [(64, 64, 1)], 5: [(128, 128, 2), (256, 32, 3)]}
        with nc.Block() as block:
            @block.sync
            def _(sp):
                sp.dma_start(x[:], d["x2T"].rearrange("(k p) t -> p k t", p=P)).then_inc(x_loaded, 16)
                sp.dma_start(mix[:], d["mix_cols"]).then_inc(x_loaded, 16)
                for b in range(6):
                    if b >= 2:
                        sp.wait_ge(bank_done, 4 * (b - 1))
                    src = d["w_rkv"][b // 2].rearrange("(k p) n -> p k n", p=P)[:, :, (b % 2) * W:(b % 2 + 1) * W]
                    sp.dma_start(wt[:, b % 2], src).then_inc(w_loaded[b % 2], 16)
                    if b == 1:
                        sp.dma_start(w0[:], d["w0a0_cols"]).then_inc(small_loaded, 16)
                        for j, (name, n, at) in enumerate((("w1", 64, 0), ("a1", 64, 64), ("g1", 160, 128))):
                            sp.dma_start(low[:, :, at:at + n], d[name].rearrange("(k p) n -> p k n", p=P)).then_inc(
                                small_loaded, 16)
                        sp.dma_start(up[0:64, 0], d["w2"]).then_inc(small_loaded, 16)
                        sp.dma_start(up[0:64, 1], d["a2"]).then_inc(small_loaded, 16)
                        sp.dma_start(up[:, 2], d["g2"][0:P, :]).then_inc(small_loaded, 16)
                        sp.dma_start(up[0:32, 3], d["g2"][P:160, :]).then_inc(small_loaded, 16)
                for n in range(6):
                    sp.wait_ge(array_done, n + 1)
                    sp.dma_start(d["rkvdag"][n].rearrange("(k p) t -> p k t", p=P), out[:, n % 2]).then_inc(stored[n % 2], 16)
                sp.wait_ge(stored0, 48)
                sp.wait_ge(stored1, 48)

            @block.vector
            def _(dve):
                step = Steps(dve, dve_steps)
                dve.wait_ge(x_loaded, 32)
                step(dve.tensor_scalar(dx[:, :, 0:1], x[:, :, 0:1], -1.0, None, ALU.mult), wait=False)
                step(dve.tensor_tensor(dx[:, :, 1:T], x[:, :, 0:T - 1], x[:, :, 1:T], ALU.subtract))
                for n in range(6):
                    if n >= 2:
                        dve.wait_ge(bank_done, KD * (n - 1))
                    for k in range(KD):
                        dve.scalar_tensor_tensor(xm[:, n % 2, k, :], dx[:, k, :], mix[:, n, k:k + 1], x[:, k, :],
                                                 ALU.mult, ALU.add).then_inc(mixed, 1)

            @block.tensor
            def _(pe):
                for n in range(6):
                    pe.wait_ge(mixed, KD * (n + 1))
                    if n >= 3:
                        pe.wait_ge(small_loaded, 128)
                        if n == 5:
                            pe.wait_ge(low_ready, 2)
                        for s, (col, rank, _) in enumerate(LOW[n]):
                            for k in range(KD):
                                mm = pe.matmul(lowp[0:rank, s, :], low[:, k, col:col + rank], xm[:, n % 2, k, :],
                                               start=(k == 0), stop=(k == KD - 1))
                            mm.then_inc(low_done, 1)
                        pe.wait_ge(low_ready, sum(len(LOW[m]) for m in range(3, n + 1)))
                    for m in range(KD):
                        if n < 3 and m % 4 == 0:
                            pe.wait_ge(w_loaded[m // 4], 16 * (n + 1))
                        o = n * KD + m
                        if o >= 6:
                            pe.wait_ge(copied, o - 5)
                        if n < 3:
                            for k in range(KD):
                                mm = pe.matmul(acc[:, o % 6, :], wt[:, m // 4, k, (m % 4) * P:(m % 4 + 1) * P],
                                               xm[:, n % 2, k, :], start=(k == 0), stop=(k == KD - 1))
                        else:
                            for s, (_, rank, at) in enumerate(LOW[n]):
                                mm = pe.matmul(acc[:, o % 6, :], up[0:rank, at, m * P:(m + 1) * P], mid[0:rank, s, :],
                                               start=(s == 0), stop=(s == len(LOW[n]) - 1))
                        mm.then_inc(bank_done, 1)

            @block.scalar
            def _(act):
                step = Steps(act, act_steps)
                lows = 0
                for n in range(6):
                    if n >= 3:
                        for s, (_, rank, _) in enumerate(LOW[n]):
                            lows += 1
                            act.wait_ge(low_done, lows)
                            if n > 3:
                                act.wait_ge(bank_done, KD * n)
                            act.activation(mid[0:rank, s, :], lowp[0:rank, s, :],
                                           (ACT.Tanh, ACT.Copy, ACT.Sigmoid)[n - 3]).then_inc(low_ready, 1)
                    if n >= 2:
                        act.wait_ge(stored[n % 2], 16 * (n // 2))
                    if n == 3:
                        act.wait_ge(small_loaded, 128)
                    for m in range(KD):
                        o = n * KD + m
                        act.wait_ge(bank_done, o + 1)
                        if n in (3, 4):
                            ins = act.activation(out[:, n % 2, m, :], acc[:, o % 6, :], ACT.Sigmoid,
                                                 bias=w0[:, n - 3, m:m + 1])
                        else:
                            ins = act.activation(out[:, n % 2, m, :], acc[:, o % 6, :], ACT.Copy)
                        ins.then_inc(copied, 1)
                    act.wait_ge(copied, KD * (n + 1))
                    if n == 3:
                        step(act.activation(out[:, 1], out[:, 1], ACT.Exp, scale=LOG_DECAY))
                    act.sem_inc(array_done, 1)


def rwkv_prepare(nc, d):
    with phase(nc, "small_loaded", "slot0_loaded", "slot1_loaded", "slot_used", "kk_done", "squared", "summed",
               "rooted", "rk_done", "rk_summed", "out_ready", "stored0", "stored1", "pc_stored",
               "dve_steps", "unit_steps", "parts_done") as (
            small_loaded, slot0_loaded, slot1_loaded, slot_used, kk_done, squared, summed, rooted, rk_done, rk_summed,
            out_ready, stored0, stored1, pc_stored, dve_steps, unit_steps, parts_done), ExitStack() as ctx:
        sb, ps = tensors(nc, ctx)
        a5 = sb("rq_in", [P, 2, 5, T])
        cols = sb("rq_cols", [P, 3, KD])
        start = sb("rq_start", [P, 2, T])
        ones = sb("rq_ones", [P, P])
        w = sb("rq_w", [P, 10, T])
        kk, sq, nrm, kn, b, c, cp, rc, t1, t2 = (w[:, n, :] for n in range(10))
        arbk = sb("rq_arbk", [P, 2, 4, T])
        bonus = sb("rq_bonus", [P, 2, T])
        pc = sb("rq_pc", [P, KD, NC_])
        ssp = ps("rq_ssp", [P, T])
        rkp = ps("rq_rkp", [P, T])
        loaded, stored = (slot0_loaded, slot1_loaded), (stored0, stored1)
        KS = 13
        arrays = d["rkvdag"].rearrange("n (q p) t -> p n q t", p=P)
        with nc.Block() as block:
            @block.sync
            def _(sp):
                sp.dma_start(cols[:], d["k_cols"]).then_inc(small_loaded, 16)
                sp.dma_start(start[:], d["starts"]).then_inc(small_loaded, 16)
                sp.dma_start(ones[:], d["ones64"]).then_inc(small_loaded, 16)
                with sp.Fori(0, KD // 2) as i:
                    for u in range(2):
                        sp.wait_ge(slot_used, i * 2 + u + 1)
                        q = bass.ds(i * 2 + u, 1)
                        sp.dma_start(a5[:, u], arrays[:, 0:5, q, :].rearrange("p n o t -> p n (o t)")).then_inc(loaded[u], 16)

            @block.scalar
            def _(act):
                act.sem_inc(stored0, 32)
                act.sem_inc(stored1, 32)
                with act.Fori(0, KD // 2) as i:
                    for u in range(2):
                        n = i * 2 + u
                        act.wait_ge(kk_done, n + 1)
                        act.activation(sq, kk, ACT.Square).then_inc(squared, 1)
                        act.wait_ge(summed, n + 1)
                        act.activation(nrm, ssp[:], ACT.Sqrt).then_inc(rooted, 1)
                        act.wait_ge(out_ready, n + 1)
                        q = bass.ds(n, 1)
                        act.dma_start(d["arbk"][q].rearrange("o p c t -> p (o c) t"), arbk[:, u]).then_inc(stored[u], 16)
                        act.dma_start(d["bonus"].rearrange("(q p) t -> p q t", p=P)[:, q, :].rearrange(
                            "p o t -> p (o t)"), bonus[:, u]).then_inc(stored[u], 16)
                act.dma_start(d["pc"], pc[:]).then_inc(pc_stored, 16)
                act.wait_ge(pc_stored, 16)
                act.wait_ge(stored0, 32 * (KD // 2) + 32)
                act.wait_ge(stored1, 32 * (KD // 2) + 32)

            @block.tensor
            def _(pe):
                pe.wait_ge(small_loaded, 48)
                with pe.Fori(0, KD // 2) as i:
                    for u in range(2):
                        n = i * 2 + u
                        pe.wait_ge(squared, n + 1)
                        pe.matmul(ssp[:], ones[:], sq, start=True, stop=True).then_inc(summed, 1)
                        pe.wait_ge(rk_done, n + 1)
                        pe.matmul(rkp[:], ones[:], t1, start=True, stop=True).then_inc(rk_summed, 1)

            @block.vector
            def _(dve):
                dve.sem_inc(slot_used, 2)
                dve.wait_ge(small_loaded, 48)
                cp64 = cp.rearrange("p (e t) -> p e t", t=RC)
                c64 = c.rearrange("p (e t) -> p e t", t=RC)
                dve.memset(cp, 1.0).then_inc(parts_done, 1)
                dve.wait_ge(parts_done, 1)
                with dve.Fori(0, KD // 2) as i:
                    for u in range(2):
                        n = i * 2 + u
                        q = bass.ds(n, 1)
                        r, k, v, dec, a = (a5[:, u, j, :] for j in range(5))
                        base = n * KS
                        steps = 0

                        def step(ins, wait=True):
                            nonlocal steps
                            ins.then_inc(dve_steps, 1)
                            steps += 1
                            if wait:
                                dve.wait_ge(dve_steps, base + steps)

                        dve.wait_ge(loaded[u], i * 16 + 16)
                        dve.wait_ge(stored[u], i * 32 + 32)
                        dve.tensor_scalar(kk, k, cols[:, 0, q], None, ALU.mult).then_inc(kk_done, 1)
                        step(dve.tensor_scalar(t2, a, -1.0, cols[:, 1, q], ALU.add, ALU.mult), wait=False)
                        step(dve.tensor_tensor(b, dec, start[:, 0], ALU.mult), wait=False)
                        step(dve.tensor_tensor(rc, dec, start[:, 1], ALU.mult))
                        step(dve.scalar_tensor_tensor(kn, t2, 1.0, k, ALU.add, ALU.mult), wait=False)
                        step(dve.tensor_tensor_scan(c, b, rc, 0.0, ALU.mult, ALU.add))
                        step(dve.tensor_tensor(t1, r, kn, ALU.mult), wait=False)
                        step(dve.tensor_copy(cp64[:, :, 1:RC], c64[:, :, 0:RC - 1]), wait=False)
                        step(dve.reciprocal(rc, c))
                        dve.tensor_scalar(t1, t1, cols[:, 2, q], None, ALU.mult).then_inc(rk_done, 1)
                        step(dve.tensor_copy(pc[:, q, :].rearrange("p o (h e) -> p (o e) h", h=2),
                                             c64[:, :, RC - 1].rearrange("p (e h) -> p e h", h=2)), wait=False)
                        step(dve.tensor_tensor(arbk[:, u, 1], r, c, ALU.mult), wait=False)
                        step(dve.tensor_tensor(arbk[:, u, 3], kn, rc, ALU.mult), wait=False)
                        dve.wait_ge(rooted, n + 1)
                        step(dve.tensor_scalar(nrm, nrm, 1e-12, None, ALU.max))
                        step(dve.reciprocal(nrm, nrm))
                        dve.tensor_tensor(kk, kk, nrm, ALU.mult).then_inc(unit_steps, 1)
                        dve.wait_ge(unit_steps, n * 2 + 1)
                        assert steps == KS
                        dve.scalar_tensor_tensor(arbk[:, u, 0], kk, -1.0, cp, ALU.mult, ALU.mult).then_inc(parts_done, 1)
                        dve.tensor_tensor(b, kk, a, ALU.mult).then_inc(unit_steps, 1)
                        dve.wait_ge(unit_steps, n * 2 + 2)
                        dve.tensor_tensor(arbk[:, u, 2], b, rc, ALU.mult).then_inc(parts_done, 1)
                        dve.wait_ge(rk_summed, n + 1)
                        dve.tensor_tensor(bonus[:, u], rkp[:], v, ALU.mult).then_inc(parts_done, 1)
                        dve.wait_ge(parts_done, n * 3 + 4)
                        dve.sem_inc(out_ready, 1)
                        dve.sem_inc(slot_used, 1)
def rwkv_chunks(nc, d, gt, hs, pc):
    NP = 2 * TT
    LEVELS = 5
    with phase(nc, "small_loaded", "slot0_loaded", "slot1_loaded", "slot_used", "ba_done", "ba_masked", "ka_done",
               "ka_masked", "l_done", "x_ready", "xt_ready", "rows_turned", "rows_copied", "em_ready", "w_done",
               "w_copied", "d_done", "x_added", "mv_done", "mv_copied", "rhs_ready", "az_done", "pads_ready", "pairs_ready", "r_done",
               "y_done", "g_done", "h_done", "r_ready", "y_ready", "g_masked", "h_scaled", "gh_finished", "stored0",
               "stored1", "dve_steps", "pool_steps") as (
            small_loaded, slot0_loaded, slot1_loaded, slot_used, ba_done, ba_masked, ka_done, ka_masked, l_done,
            x_ready, xt_ready, rows_turned, rows_copied, em_ready, w_done, w_copied, d_done, x_added, mv_done, mv_copied,
            rhs_ready, az_done, pads_ready, pairs_ready, r_done, y_done, g_done, h_done, r_ready, y_ready, g_masked,
            h_scaled, gh_finished, stored0, stored1, dve_steps, pool_steps), ExitStack() as ctx:
        sb, ps = tensors(nc, ctx)
        ar = sb("rc_ar", [P, 2, 2, T])
        bk = sb("rc_bk", [P, 2, 2, T])
        vT = sb("rc_vT", [P, 2, T])
        mask2 = sb("rc_mask2", [P, 2, P])
        lmask = sb("rc_lmask", [P, 2, P])
        emask = sb("rc_emask", [P, LEVELS, P])
        bd = sb("rc_bd", [P, P])
        ident = sb("rc_ident", [P, P])
        ba = sb("rc_ba", [P, NP, 2, P])
        ka = sb("rc_ka", [P, NP, 2, P])
        xx = sb("rc_xx", [P, 2, NP, P])
        em = sb("rc_em", [P, LEVELS, NP, P])
        ws = sb("rc_ws", [P, NP, P])
        rows = sb("rc_rows", [P, 4, TT, P])
        rhs = sb("rc_rhs", [P, NP, 2, RC])
        apad = sb("rc_apad", [P, TT, 2, P])
        zpad = sb("rc_zpad", [P, TT, 2, P])
        vpad = sb("rc_vpad", [P, TT, 2, P])
        apair = sb("rc_apair", [P, TT, P])
        zpair = sb("rc_zpair", [P, TT, P])
        ry = sb("rc_ry", [P, 2, 2, T])
        lo = ps("rc_lo", [P, 4, W])
        hi = ps("rc_hi", [P, 4, W])
        loaded, stored = (slot0_loaded, slot1_loaded), (stored0, stored1)

        def banks(t, first, count, **dims):
            return t[:, first:first + count, :].rearrange("p b w -> p (b w)")

        lo_ba = banks(lo, 0, 4).rearrange("p (n s t) -> p n s t", n=NP, s=2)
        hi_ka = banks(hi, 0, 4).rearrange("p (n s t) -> p n s t", n=NP, s=2)
        lo_l = banks(lo, 0, 2).rearrange("p (n t) -> p n t", n=NP)
        lo_w = banks(lo, 2, 2).rearrange("p (n t) -> p n t", n=NP)
        hi_rows = banks(hi, 0, 4).rearrange("p (a i t) -> p a i t", a=4, i=TT)
        hi_d = banks(hi, 0, 4).rearrange("p (x n t) -> p x n t", x=2, n=NP)
        lo_mv = banks(lo, 0, 1).rearrange("p (n t) -> p n t", n=NP)
        hi_az = banks(hi, 0, 2).rearrange("p (n s t) -> p n s t", n=NP, s=2)
        lo_r = banks(lo, 1, 1).rearrange("p (i t) -> p i t", i=TT)
        lo_y = banks(lo, 2, 1).rearrange("p (i t) -> p i t", i=TT)
        hi_g = banks(hi, 2, 2).rearrange("p (e t) -> p e t", e=NC_)
        hi_h = banks(hi, 0, 2).rearrange("p (e t) -> p e t", e=NC_)
        problems = [(c * TT + i, i, c) for i in range(TT) for c in range(2)]
        chunks = [((e % 2) * TT + e // 2, e // 2, slice(RC * (e % 2), RC * (e % 2) + RC)) for e in range(NC_)]

        def heads(t):
            return [t[:, :, c, RC * c:RC * c + RC] for c in range(2)]

        with nc.Block() as block:
            @block.sync
            def _(sp):
                sp.dma_start(mask2[:], d["mask2"]).then_inc(small_loaded, 16)
                sp.dma_start(lmask[:], d["lmask"]).then_inc(small_loaded, 16)
                sp.dma_start(emask[:], d["emask"]).then_inc(small_loaded, 16)
                sp.dma_start(bd[:], d["ones64"]).then_inc(small_loaded, 16)
                sp.dma_start(ident[:], d["ident"]).then_inc(small_loaded, 16)
                sp.dma_start(pc[:], d["pc"]).then_inc(small_loaded, 16)
                src = d["arbk"].rearrange("q p c t -> p q c t")
                v_src = d["rkvdag"][2].rearrange("(q p) t -> p q t", p=P)
                with sp.Fori(0, KD // 2) as i:
                    for u in range(2):
                        sp.wait_ge(slot_used, i * 2 + u + 1)
                        q = bass.ds(i * 2 + u, 1)
                        sp.dma_start(ar[:, u], src[:, q, 0:2, :].rearrange("p o c t -> p (o c) t")).then_inc(loaded[u], 16)
                        sp.dma_start(bk[:, u], src[:, q, 2:4, :].rearrange("p o c t -> p (o c) t")).then_inc(loaded[u], 16)
                        sp.dma_start(vT[:, u], v_src[:, q, :].rearrange("p o t -> p (o t)")).then_inc(loaded[u], 16)

            @block.tensor
            def _(pe):
                pe.wait_ge(small_loaded, 96)
                with pe.Fori(0, KD // 2) as i2:
                    for u in range(2):
                        n = i2 * 2 + u
                        pe.wait_ge(loaded[u], i2 * 48 + 48)
                        pe.wait_ge(y_ready, n + 1)
                        pe.wait_ge(r_ready, n + 1)
                        for p, i, c in problems:
                            h, t = slice(RC * c, RC * c + RC), slice(i * P, (i + 1) * P)
                            mm = pe.matmul(lo_ba[:, p], bk[h, u, 0, t], ar[h, u, :, t], start=True, stop=True)
                        mm.then_inc(ba_done, 1)
                        pe.wait_ge(h_scaled, n + 1)
                        pe.wait_ge(g_masked, n + 1)
                        for p, i, c in problems:
                            h, t = slice(RC * c, RC * c + RC), slice(i * P, (i + 1) * P)
                            mm = pe.matmul(hi_ka[:, p], bk[h, u, 1, t], ar[h, u, :, t], start=True, stop=True)
                        mm.then_inc(ka_done, 1)
                        pe.wait_ge(ba_masked, n + 1)
                        for p, i, c in problems:
                            h, t = slice(RC * c, RC * c + RC), slice(i * P, (i + 1) * P)
                            mm = pe.matmul(lo_l[:, p], ar[h, u, 0, t], bk[h, u, 0, t], start=True, stop=True)
                        mm.then_inc(l_done, 1)
                        pe.wait_ge(ka_masked, n + 1)
                        for a, src in enumerate((ar[:, u, 0], bk[:, u, 0], bk[:, u, 1], vT[:, u])):
                            for i in range(TT):
                                mm = pe.transpose(hi_rows[:, a, i, :], src[:, i * P:(i + 1) * P], ident[:])
                        mm.then_inc(rows_turned, 1)
                        pe.wait_ge(em_ready, n + 1)
                        pe.wait_ge(x_ready, n + 1)
                        pe.wait_ge(xt_ready, n + 1)
                        for lv in range(LEVELS):
                            if lv:
                                pe.wait_ge(x_added, n * LEVELS + lv)
                            for p in range(NP):
                                mm = pe.matmul(lo_w[:, p], em[:, lv, p, :], xx[:, 0, p, :], start=True, stop=True)
                            mm.then_inc(w_done, 1)
                            if lv == 0:
                                pe.wait_ge(rows_copied, n + 1)
                            pe.wait_ge(w_copied, n * LEVELS + lv + 1)
                            for p in range(NP):
                                pe.matmul(hi_d[:, 0, p], xx[:, 1, p, :], ws[:, p, :], start=True, stop=True)
                                mm = pe.matmul(hi_d[:, 1, p], ws[:, p, :], xx[:, 1, p, :], start=True, stop=True)
                            mm.then_inc(d_done, 1)
                        for p, i, c in problems:
                            mm = pe.matmul(lo_mv[:, p], ka[:, p, 0, :], rows[:, 3, i, RC * c:RC * c + RC], start=True,
                                           stop=True)
                        mm.then_inc(mv_done, 1)
                        pe.wait_ge(x_added, n * LEVELS + LEVELS)
                        pe.wait_ge(rhs_ready, n + 1)
                        pe.wait_ge(mv_copied, n + 1)
                        for p, i, c in problems:
                            mm = pe.matmul(hi_az[:, p], xx[:, 1, p, :], rhs[:, p], start=True, stop=True)
                        mm.then_inc(az_done, 1)
                        pe.wait_ge(pads_ready, n * 4 + 4)
                        for i in range(TT):
                            for c in range(2):
                                mm = pe.matmul(lo_r[:, i], apad[:, i, c, :], ba[:, c * TT + i, 1, :], start=(c == 0),
                                               stop=(c == 1))
                        mm.then_inc(r_done, 1)
                        for i in range(TT):
                            for c in range(2):
                                pe.matmul(lo_y[:, i], zpad[:, i, c, :], ba[:, c * TT + i, 1, :], start=(c == 0), stop=False)
                                mm = pe.matmul(lo_y[:, i], vpad[:, i, c, :], ka[:, c * TT + i, 1, :], start=False,
                                               stop=(c == 1))
                        mm.then_inc(y_done, 1)
                        pe.wait_ge(pairs_ready, n * 2 + 2)
                        for e, i, t in chunks:
                            mm = pe.matmul(hi_g[:, e], apair[t, i, :], rows[t, 1, i, :], start=True, stop=True)
                        mm.then_inc(g_done, 1)
                        for e, i, t in chunks:
                            pe.matmul(hi_h[:, e], rows[t, 1, i, :], zpair[t, i, :], start=True, stop=False)
                            mm = pe.matmul(hi_h[:, e], rows[t, 2, i, :], rows[t, 3, i, :], start=False, stop=True)
                        mm.then_inc(h_done, 1)

            @block.vector
            def _(dve):
                dve.sem_inc(r_ready, 1)
                dve.sem_inc(g_masked, 1)
                dve.sem_inc(h_scaled, 1)
                for pad in (apad, zpad, vpad):
                    dve.memset(pad[:], 0.0).then_inc(dve_steps, 1)
                dve.wait_ge(dve_steps, 3)
                dve.wait_ge(small_loaded, 96)
                with dve.Fori(0, KD // 2) as i2:
                    for u in range(2):
                        n = i2 * 2 + u
                        m2 = mask2[:].unsqueeze(1).to_broadcast([P, NP, 2, P])
                        dve.wait_ge(ba_done, n + 1)
                        dve.tensor_tensor(ba[:], lo_ba, m2, ALU.mult).then_inc(ba_masked, 1)
                        dve.wait_ge(ka_done, n + 1)
                        dve.tensor_tensor(ka[:], hi_ka, m2, ALU.mult).then_inc(ka_masked, 1)
                        dve.wait_ge(l_done, n + 1)
                        dve.tensor_tensor(xx[:, 0], lo_l, lmask[:, 0].unsqueeze(1).to_broadcast([P, NP, P]),
                                          ALU.mult).then_inc(dve_steps, 1)
                        dve.wait_ge(dve_steps, n + 4)
                        dve.tensor_tensor(xx[:, 0], xx[:, 0], ident[:].unsqueeze(1).to_broadcast([P, NP, P]),
                                          ALU.add).then_inc(x_ready, 1)
                        dve.wait_ge(x_ready, n + 1)
                        dve.wait_ge(xt_ready, n + 1)
                        for lv in range(LEVELS):
                            dve.wait_ge(d_done, n * LEVELS + lv + 1)
                            dve.tensor_tensor(xx[:], xx[:], hi_d, ALU.add).then_inc(x_added, 1)
                            dve.wait_ge(x_added, n * LEVELS + lv + 1)
                        dve.wait_ge(az_done, n + 1)
                        az = hi_az.rearrange("p (c i) s t -> p i c s t", c=2)
                        for c in range(2):
                            dve.tensor_copy(heads(apad)[c], az[:, :, c, 0, :]).then_inc(pads_ready, 1)
                            dve.tensor_copy(heads(zpad)[c], az[:, :, c, 1, :]).then_inc(pads_ready, 1)
                        dve.wait_ge(r_done, n + 1)
                        dve.wait_ge(stored[u], i2 * 32 + 32)
                        dve.tensor_tensor(ry[:, u, 0, :], lo[:, 1, :], ar[:, u, 1, :], ALU.add).then_inc(r_ready, 1)
                        dve.wait_ge(r_ready, n + 2)
                        dve.sem_inc(slot_used, 1)
                        q = bass.ds(n, 1)
                        dve.wait_ge(g_done, n + 1)
                        dve.wait_ge(gh_finished, n * 2 + 1)
                        dve.tensor_tensor(gt[:, q, :, :].rearrange("p o e t -> p (o e) t"), hi_g,
                                          bd[:].unsqueeze(1).to_broadcast([P, NC_, P]), ALU.mult).then_inc(g_masked, 1)
                        dve.wait_ge(h_done, n + 1)
                        dve.tensor_tensor(hs[:, q, :, :].rearrange("p o e t -> p (o e) t"), hi_h,
                                          pc[:, q, :].rearrange("p o e -> p (o e)").unsqueeze(2).to_broadcast([P, NC_, P]),
                                          ALU.mult).then_inc(h_scaled, 1)

            @block.scalar
            def _(act):
                act.sem_inc(y_ready, 1)
                act.sem_inc(stored0, 32)
                act.sem_inc(stored1, 32)
                with act.Fori(0, KD // 2) as i2:
                    for u in range(2):
                        n = i2 * 2 + u
                        act.wait_ge(rows_turned, n + 1)
                        act.activation(rows[:], hi_rows, ACT.Copy).then_inc(rows_copied, 1)
                        for lv in range(LEVELS):
                            act.wait_ge(w_done, n * LEVELS + lv + 1)
                            act.activation(ws[:], lo_w, ACT.Copy).then_inc(w_copied, 1)
                        act.wait_ge(mv_done, n + 1)
                        act.activation(rhs[:, :, 1, :], lo_mv, ACT.Copy).then_inc(mv_copied, 1)
                        act.wait_ge(y_done, n + 1)
                        act.wait_ge(stored[u], i2 * 32 + 32)
                        act.activation(ry[:, u, 1, :], lo[:, 2, :], ACT.Copy).then_inc(y_ready, 1)
                        act.wait_ge(y_ready, n + 2)
                        act.wait_ge(r_ready, n + 2)
                        q = bass.ds(n, 1)
                        for j in range(2):
                            act.dma_start(d["ry"][j].rearrange("(q p) t -> p q t", p=P)[:, q, :].rearrange(
                                "p o t -> p (o t)"), ry[:, u, j, :]).then_inc(stored[u], 16)
                act.wait_ge(stored0, 32 * (KD // 2) + 32)
                act.wait_ge(stored1, 32 * (KD // 2) + 32)

            @block.gpsimd
            def _(pool):
                pool.sem_inc(slot_used, 2)
                pool.sem_inc(gh_finished, 1)
                pool.wait_ge(small_loaded, 96)
                with pool.Fori(0, KD // 2) as i2:
                    for u in range(2):
                        n = i2 * 2 + u
                        pool.wait_ge(ba_masked, n + 1)
                        pool.tensor_tensor(xx[:, 1], ba[:, :, 0, :], lmask[:, 1].unsqueeze(1).to_broadcast([P, NP, P]),
                                           ALU.mult).then_inc(pool_steps, 1)
                        pool.wait_ge(pool_steps, n * 5 + 1)
                        pool.tensor_tensor(xx[:, 1], xx[:, 1], ident[:].unsqueeze(1).to_broadcast([P, NP, P]),
                                           ALU.add).then_inc(xt_ready, 1)
                        for lv in range(LEVELS):
                            ins = pool.tensor_tensor(em[:, lv], ba[:, :, 0, :],
                                                     emask[:, lv].unsqueeze(1).to_broadcast([P, NP, P]), ALU.mult)
                        ins.then_inc(em_ready, 1)
                        pool.wait_ge(dve_steps, 3)
                        pool.wait_ge(rows_copied, n + 1)
                        for c in range(2):
                            pool.tensor_copy(rhs[:].rearrange("p (c i) s t -> p i c s t", c=2)[:, :, c, 0, :],
                                             rows[:, 0, :, RC * c:RC * c + RC]).then_inc(pool_steps, 1)
                            pool.tensor_copy(heads(vpad)[c], rows[:, 3, :, RC * c:RC * c + RC]).then_inc(pool_steps, 1)
                        pool.wait_ge(pool_steps, n * 5 + 5)
                        pool.sem_inc(rhs_ready, 1)
                        pool.wait_ge(pads_ready, n * 4 + 4)
                        for pad, pair in ((apad, apair), (zpad, zpair)):
                            pool.tensor_tensor(pair[:], pad[:, :, 0, :], pad[:, :, 1, :], ALU.add).then_inc(pairs_ready, 1)
                        q = bass.ds(n, 1)
                        g, h = (t[:, q, :, :].rearrange("p o e t -> p (o e) t") for t in (gt, hs))
                        pool.wait_ge(g_masked, n + 2)
                        pool.tensor_tensor(g, g, ident[:].unsqueeze(1).to_broadcast([P, NC_, P]), ALU.add).then_inc(gh_finished, 1)
                        pool.wait_ge(h_scaled, n + 2)
                        pool.tensor_tensor(h, h, bd[:].unsqueeze(1).to_broadcast([P, NC_, P]), ALU.mult).then_inc(gh_finished, 1)


def rwkv_scan(nc, d, gt, hs, pc):
    with phase(nc, "loaded", "late_loaded", "y_done", "y_added", "s_done", "s_scaled", "s_ready", "mu_done", "centred",
               "squared", "var_done", "rooted", "out_ready", "stored", "dve_steps", "norm_steps") as (
            loaded, late_loaded, y_done, y_added, s_done, s_scaled, s_ready, mu_done, centred, squared, var_done,
            rooted, out_ready, stored, dve_steps, norm_steps), ExitStack() as ctx:
        sb, ps = tensors(nc, ctx)
        ry = sb("rs_ry", [P, 2, KD, T])
        s = sb("rs_s", [P, KD, P])
        bonus = sb("rs_bonus", [P, KD, T])
        gate = sb("rs_gate", [P, KD, T])
        cols = sb("rs_cols", [P, 2, KD])
        mean = sb("rs_mean", [P, P])
        eps = sb("rs_eps", [P, 1])
        sq = sb("rs_sq", [P, 2, T])
        nrm = sb("rs_nrm", [P, 2, T])
        yp = ps("rs_yp", [P, KD, RC])
        sp_ = ps("rs_sp", [P, KD, P])
        mp = ps("rs_mp", [P, 2, T])
        vp = ps("rs_vp", [P, 2, T])
        y = ry[:, 1]

        def at(e):
            return (e % 2) * TT + e // 2

        with nc.Block() as block:
            @block.sync
            def _(sp):
                sp.dma_start(ry[:], d["ry"].rearrange("j (q p) t -> p j q t", p=P)).then_inc(loaded, 16)
                sp.dma_start(mean[:], d["mean64"]).then_inc(late_loaded, 16)
                sp.dma_start(cols[:], d["lnx_cols"]).then_inc(late_loaded, 16)
                sp.dma_start(bonus[:], d["bonus"].rearrange("(q p) t -> p q t", p=P)).then_inc(late_loaded, 16)
                sp.dma_start(gate[:], d["rkvdag"][5].rearrange("(q p) t -> p q t", p=P)).then_inc(late_loaded, 16)
                out = d["tmT"].rearrange("(q p) t -> p q t", p=P)
                for q in range(KD):
                    sp.wait_ge(out_ready, q + 1)
                    sp.dma_start(out[:, q, :], y[:, q, :]).then_inc(stored, 16)
                sp.wait_ge(stored, 16 * KD)

            @block.tensor
            def _(pe):
                pe.wait_ge(loaded, 16)
                for e in range(1, NC_):
                    pe.wait_ge(s_ready, e)
                    if e > 1:
                        pe.wait_ge(y_added, e - 1)
                        pe.wait_ge(s_scaled, e - 1)
                    for q in range(KD):
                        mm = pe.matmul(yp[:, q, :], s[:, q, :], ry[:, 0, q, e * RC:(e + 1) * RC], start=True, stop=True)
                    mm.then_inc(y_done, 1)
                    if e < NC_ - 1:
                        for q in range(KD):
                            mm = pe.matmul(sp_[:, q, :], gt[:, q, at(e), :], s[:, q, :], start=True, stop=True)
                        mm.then_inc(s_done, 1)
                pe.wait_ge(late_loaded, 64)
                pe.wait_ge(y_added, NC_ - 1)
                for q in range(KD + 1):
                    if q < KD:
                        if q >= 2:
                            pe.wait_ge(centred, q - 1)
                        pe.matmul(mp[:, q % 2, :], mean[:], y[:, q, :], start=True, stop=True).then_inc(mu_done, 1)
                    if q:
                        pe.wait_ge(squared, q)
                        if q >= 3:
                            pe.wait_ge(rooted, q - 2)
                        pe.matmul(vp[:, (q - 1) % 2, :], mean[:], sq[:, (q - 1) % 2, :], start=True,
                                  stop=True).then_inc(var_done, 1)

            @block.scalar
            def _(act):
                act.wait_ge(dve_steps, 1)
                for q in range(KD):
                    act.wait_ge(centred, q + 1)
                    if q >= 2:
                        act.wait_ge(var_done, q - 1)
                    act.activation(sq[:, q % 2, :], y[:, q, :], ACT.Square).then_inc(squared, 1)
                    act.wait_ge(var_done, q + 1)
                    if q >= 2:
                        act.wait_ge(out_ready, q - 1)
                    act.activation(nrm[:, q % 2, :], vp[:, q % 2, :], ACT.Sqrt, bias=eps[:]).then_inc(rooted, 1)

            @block.vector
            def _(dve):
                dve.memset(eps[:], 64e-5).then_inc(dve_steps, 1)
                dve.wait_ge(loaded, 16)
                dve.tensor_copy(s[:], hs[:, :, 0, :]).then_inc(s_ready, 1)
                for e in range(1, NC_):
                    if e < NC_ - 1:
                        dve.wait_ge(s_done, e)
                        dve.wait_ge(y_done, e)
                        dve.tensor_tensor(s[:], sp_[:], pc[:, :, at(e)].unsqueeze(2).to_broadcast([P, KD, P]),
                                          ALU.mult).then_inc(s_scaled, 1)
                        dve.wait_ge(s_scaled, e)
                        dve.tensor_tensor(s[:], s[:], hs[:, :, at(e), :], ALU.add).then_inc(s_ready, 1)
                    dve.wait_ge(y_done, e)
                    ye = y[:, :, e * RC:(e + 1) * RC]
                    dve.tensor_tensor(ye, ye, yp[:], ALU.add).then_inc(y_added, 1)
                dve.wait_ge(y_added, NC_ - 1)
                dve.wait_ge(late_loaded, 64)
                step = Steps(dve, norm_steps)

                def centre(q):
                    dve.wait_ge(mu_done, q + 1)
                    dve.tensor_tensor(y[:, q, :], y[:, q, :], mp[:, q % 2, :], ALU.subtract).then_inc(centred, 1)

                centre(0)
                for q in range(KD):
                    if q + 1 < KD:
                        centre(q + 1)
                    yq, r = y[:, q, :], nrm[:, q % 2, :]
                    dve.wait_ge(rooted, q + 1)
                    step(dve.reciprocal(r, r))
                    step(dve.tensor_tensor(yq, yq, r, ALU.mult))
                    step(dve.tensor_scalar(yq, yq, cols[:, 0, q:q + 1], cols[:, 1, q:q + 1], ALU.mult, ALU.add))
                    step(dve.tensor_tensor(yq, yq, bonus[:, q, :], ALU.add))
                    dve.tensor_tensor(yq, yq, gate[:, q, :], ALU.mult).then_inc(out_ready, 1)


def rwkv_recurrence(nc, d):
    with ExitStack() as ctx:
        sb, _ = tensors(nc, ctx)
        gt = sb("rr_gt", [P, KD, NC_, P])
        hs = sb("rr_hs", [P, KD, NC_, P])
        pc = sb("rr_pc", [P, KD, NC_])
        rwkv_chunks(nc, d, gt, hs, pc)
        rwkv_scan(nc, d, gt, hs, pc)
AH = 16
IH = 8
QL, KL = 256, 128
DSA_IN = QL + KL + 64 + IH
CHOSEN = 128
MASKED = -1.0e30
TAKEN = -3.0e38


def sparse_projections(nc, d, o):
    with phase(nc, "x_loaded", "w_loaded", "vec_loaded", "h_done", "h_copied", "summed", "rooted", "rows_done",
               "turned", "turn_copied", "bank_done", "act_copied", "dve_copied", "dve_steps", "pool_steps") as (
            x_loaded, w_loaded, vec_loaded, h_done, h_copied, summed, rooted, rows_done, turned, turn_copied,
            bank_done, act_copied, dve_copied, dve_steps, pool_steps), ExitStack() as ctx:
        sb, ps = tensors(nc, ctx)
        x = sb("sp_x", [P, KD, T])
        win = sb("sp_win", [P, KD, DSA_IN])
        wuq = sb("sp_wuq", [P, 2, D])
        wqi = sb("sp_wqi", [P, 2, IH * 64])
        wuk = sb("sp_wuk", [P, D])
        wuv = sb("sp_wuv", [P, D])
        vec = sb("sp_vec", [P, QL + KL + 128])
        ident = sb("sp_ident", [P, P])
        h = sb("sp_h", [P, TT, DSA_IN])
        ki2 = sb("sp_ki2", [P, TT, 2, 64])
        junk = sb("sp_junk", [P, QL])
        bs = sb("sp_bs", [P, TT, 6])
        mv = sb("sp_mv", [P, TT, 2])
        st = sb("sp_st", [P, TT, 3])
        rt = sb("sp_rt", [P, TT, 3])
        mhalf = sb("sp_mhalf", [P, 2])
        lat = sb("sp_lat", [P, 3, T])
        hp = ps("sp_hp", [P, TT, W])
        op = ps("sp_op", [P, 4, W])
        outs = []
        for m in range(KD):
            outs.append(([(wuq[:, k, m * P:(m + 1) * P], lat[:, k, :]) for k in range(2)], o["qT"][:, m, :]))
        for m in range(IH * 64 // P):
            outs.append(([(wqi[:, k, m * P:(m + 1) * P], lat[:, k, :]) for k in range(2)], o["qiT"][:, m, :]))
        for m in range(KD):
            outs.append(([(wuk[:, m * P:(m + 1) * P], lat[:, 2, :])], o["kT"][:, m, :]))
        for i in range(TT):
            for half in range(2):
                outs.append(([(lat[:, 2, i * P:(i + 1) * P], wuv[:, half * W:(half + 1) * W])],
                             o["v"][:, i, half * W:(half + 1) * W]))
        with nc.Block() as block:
            @block.sync
            def _(sp):
                sp.dma_start(x[:], d["x4T"].rearrange("(k p) t -> p k t", p=P)).then_inc(x_loaded, 16)
                sp.dma_start(win[:], d["dsa_w_in"].rearrange("(k p) n -> p k n", p=P)).then_inc(x_loaded, 16)
                sp.dma_start(vec[:], over_partitions(d["dsa_vecs"])).then_inc(vec_loaded, 16)
                sp.dma_start(ident[:], d["ident"]).then_inc(vec_loaded, 16)
                sp.dma_start(wuq[:], d["dsa_w_uq"].rearrange("(k p) n -> p k n", p=P)).then_inc(w_loaded, 16)
                sp.dma_start(wqi[:], d["dsa_w_qidx"].rearrange("(k p) n -> p k n", p=P)).then_inc(w_loaded, 16)
                sp.dma_start(wuk[:], d["dsa_w_uk"]).then_inc(w_loaded, 16)
                sp.dma_start(wuv[:], d["dsa_w_uv"]).then_inc(w_loaded, 16)

            @block.tensor
            def _(pe):
                pe.wait_ge(x_loaded, 32)
                for i in range(TT):
                    for k in range(KD):
                        mm = pe.matmul(hp[:, i, 0:DSA_IN], x[:, k, i * P:(i + 1) * P], win[:, k, :], start=(k == 0),
                                       stop=(k == KD - 1))
                    mm.then_inc(h_done, 1)
                pe.wait_ge(vec_loaded, 32)
                for i in range(TT):
                    pe.wait_ge(rows_done, i + 1)
                    for c, rows in enumerate((h[:, i, 0:P], h[:, i, P:QL], h[:, i, QL:QL + KL],
                                              ki2[:, i].rearrange("p a b -> p (a b)"))):
                        mm = pe.transpose(hp[:, i, c * P:(c + 1) * P], rows, ident[:])
                    mm.then_inc(turned, 1)
                pe.wait_ge(turn_copied, TT)
                pe.wait_ge(w_loaded, 64)
                for n, (parts, _) in enumerate(outs):
                    if n >= 4:
                        pe.wait_ge((act_copied, dve_copied)[n % 2], n // 2 - 1)
                    for j, (lhs, rhs) in enumerate(parts):
                        mm = pe.matmul(op[:, n % 4, :], lhs, rhs, start=(j == 0), stop=(j == len(parts) - 1))
                    mm.then_inc(bank_done, 1)

            @block.scalar
            def _(act):
                for i in range(TT):
                    act.wait_ge(h_done, i + 1)
                    act.activation(h[:, i, :], hp[:, i, 0:DSA_IN], ACT.Copy).then_inc(h_copied, 1)
                for i in range(TT):
                    act.wait_ge(turned, i + 1)
                    act.activation(lat[:, :, i * P:(i + 1) * P], hp[:, i, 0:3 * P].rearrange("p (c t) -> p c t", c=3),
                                   ACT.Copy)
                    act.activation(o["kiT"][:, i * P:(i + 1) * P], hp[:, i, 3 * P:4 * P], ACT.Copy).then_inc(turn_copied, 1)
                for n in range(0, len(outs), 2):
                    act.wait_ge(bank_done, n + 1)
                    act.activation(outs[n][1], op[:, n % 4, :], ACT.Copy).then_inc(act_copied, 1)

            @block.gpsimd
            def _(pool):
                steps = Steps(pool, pool_steps)
                steps(pool.memset(mhalf[:], -0.5))
                for i in range(TT):
                    pool.wait_ge(summed, i + 1)
                    steps(root_reciprocal(pool, steps, rt[:, i, 0:2], st[:, i, 0:2], 1e-6, mhalf[:]), wait=False)
                    root_reciprocal(pool, steps, rt[:, i, 2:3], st[:, i, 2:3], 1e-5, mhalf[:, 0:1]).then_inc(rooted, 1)

            @block.vector
            def _(dve):
                step = Steps(dve, dve_steps)
                dve.wait_ge(vec_loaded, 32)
                for i in range(TT):
                    dve.wait_ge(h_copied, i + 1)
                    cq, ckv, ki = h[:, i, 0:QL], h[:, i, QL:QL + KL], h[:, i, QL + KL:QL + KL + 64]
                    step(dve.tensor_tensor_reduce(junk[:], cq, cq, 1.0 / QL, 0.0, ALU.mult, ALU.add, st[:, i, 0:1]))
                    step(dve.tensor_tensor_reduce(junk[:, 0:KL], ckv, ckv, 1.0 / KL, 0.0, ALU.mult, ALU.add,
                                                  st[:, i, 1:2]), wait=False)
                    step(dve.bn_stats(bs[:, i, :], ki))
                    step(dve.bn_aggr(mv[:, i, :], bs[:, i, :]))
                    dve.tensor_copy(st[:, i, 2:3], mv[:, i, 1:2]).then_inc(summed, 1)
                    step(dve.tensor_scalar(o["wi"][:, i, :], h[:, i, QL + KL + 64:DSA_IN],
                                           IH ** -0.5 * 64 ** -0.5, None, ALU.mult), wait=False)
                    dve.wait_ge(rooted, i + 1)
                    step(dve.scalar_tensor_tensor(cq, cq, rt[:, i, 0:1], vec[:, 0:QL], ALU.mult, ALU.mult), wait=False)
                    step(dve.scalar_tensor_tensor(ckv, ckv, rt[:, i, 1:2], vec[:, QL:QL + KL], ALU.mult, ALU.mult), wait=False)
                    step(dve.tensor_scalar(ki, ki, mv[:, i, 0:1], rt[:, i, 2:3], ALU.subtract, ALU.mult))
                    step(dve.tensor_tensor(ki, ki, vec[:, QL + KL:QL + KL + 64], ALU.mult))
                    for half in range(2):
                        step(dve.tensor_tensor(ki2[:, i, half, :], ki, vec[:, QL + KL + 64:QL + KL + 128], ALU.add), wait=False)
                    step.wait()
                    dve.sem_inc(rows_done, 1)
                for n in range(1, len(outs), 2):
                    dve.wait_ge(bank_done, n + 1)
                    dve.tensor_copy(outs[n][1], op[:, n % 4, :]).then_inc(dve_copied, 1)


def choose_keys(nc, d, o):
    tiles = range(1, TT)
    with phase(nc, "s_done", "relu_done", "scored", "causal", "chain", "masked", "cleared", "all_done") as (
            s_done, relu_done, scored, causal, chain, masked, cleared, all_done), ExitStack() as ctx:
        sb, ps = tensors(nc, ctx)
        r = sb("ck_r", [P, 2, T])
        sc = sb("ck_sc", [P, TT, T])
        top = sb("ck_top", [P, TT, 8])
        sp_ = ps("ck_sp", [P, 4, T])
        order = [(i, h) for i in tiles for h in range(IH)]
        with nc.Block() as block:
            @block.tensor
            def _(pe):
                for n, (i, h) in enumerate(order):
                    if n >= 4:
                        pe.wait_ge(relu_done, n - 3)
                    rows, keys = slice(64 * (h % 2), 64 * (h % 2) + 64), (i + 1) * P
                    pe.matmul(sp_[:, n % 4, 0:keys], o["qiT"][rows, h // 2, i * P:(i + 1) * P], o["kiT"][rows, 0:keys],
                              start=True, stop=True).then_inc(s_done, 1)

            @block.scalar
            def _(act):
                for n, (i, h) in enumerate(order):
                    keys = (i + 1) * P
                    act.wait_ge(s_done, n + 1)
                    if n >= 2:
                        act.wait_ge(scored, n - 1)
                    act.activation(r[:, n % 2, 0:keys], sp_[:, n % 4, 0:keys], ACT.Relu).then_inc(relu_done, 1)

            @block.gpsimd
            def _(pool):
                pool.memset(o["am"][:, 0, :], 0.0).then_inc(cleared, 1)
                pool.wait_ge(cleared, 1)
                first = o["am"][:, 0, 0:P]
                pool.affine_select(out=first, in_=first, compare_op=ALU.is_ge, fill=MASKED, base=0, pattern=[[-1, P]],
                                   channel_multiplier=1).then_inc(cleared, 1)
                for i in tiles:
                    pool.wait_ge(scored, IH * i)
                    last = sc[:, i, i * P:(i + 1) * P]
                    pool.affine_select(out=last, in_=last, compare_op=ALU.is_ge, fill=MASKED, base=0, pattern=[[-1, P]],
                                       channel_multiplier=1).then_inc(causal, 1)

            @block.vector
            def _(dve):
                for n, (i, h) in enumerate(order):
                    keys = (i + 1) * P
                    dve.wait_ge(relu_done, n + 1)
                    if h == 0:
                        ins = dve.tensor_scalar(sc[:, i, 0:keys], r[:, n % 2, 0:keys], o["wi"][:, i, h:h + 1], None, ALU.mult)
                    else:
                        dve.wait_ge(scored, n)
                        ins = dve.scalar_tensor_tensor(sc[:, i, 0:keys], r[:, n % 2, 0:keys], o["wi"][:, i, h:h + 1],
                                                       sc[:, i, 0:keys], ALU.mult, ALU.add)
                    ins.then_inc(scored, 1)
                dve.wait_ge(causal, TT - 1)
                step = Steps(dve, chain)
                for _ in range(CHOSEN // 8):
                    for i in tiles:
                        step(dve.max(top[:, i, :], sc[:, i, 0:(i + 1) * P]), wait=False)
                    step.wait()
                    for i in tiles:
                        rows = sc[:, i, 0:(i + 1) * P]
                        step(dve.match_replace(rows, top[:, i, :], rows, TAKEN), wait=False)
                    step.wait()
                for i in tiles:
                    dve.tensor_scalar(o["am"][:, i, 0:(i + 1) * P], sc[:, i, 0:(i + 1) * P], -2.0e38, MASKED, ALU.is_gt,
                                      ALU.mult).then_inc(masked, 1)


def bias_table(nc, d):
    M = 640
    with phase(nc, "loaded", "done", "copied", "stored") as (loaded, done, copied, stored), ExitStack() as ctx:
        sb, ps = tensors(nc, ctx)
        rb = sb("bt_rb", [32, AH])
        hot = sb("bt_hot", [32, M])
        fb = sb("bt_fb", [AH, M])
        acc = ps("bt_acc", [P, 2, W])
        with nc.Block() as block:
            @block.sync
            def _(sp):
                sp.dma_start(rb[:], d["rel_bias"]).then_inc(loaded, 16)
                sp.dma_start(hot[:], d["buckets"]).then_inc(loaded, 16)
                sp.wait_ge(copied, 2)
                sp.dma_start(d["fb"], fb[:].unsqueeze(1).to_broadcast([AH, P, M])).then_inc(stored, 16)
                sp.wait_ge(stored, 16)

            @block.tensor
            def _(pe):
                pe.wait_ge(loaded, 32)
                pe.matmul(acc[0:AH, 0, :], rb[:], hot[:, 0:W], start=True, stop=True).then_inc(done, 1)
                pe.matmul(acc[0:AH, 1, 0:M - W], rb[:], hot[:, W:M], start=True, stop=True).then_inc(done, 1)

            @block.vector
            def _(dve):
                dve.wait_ge(done, 2)
                dve.tensor_copy(fb[:, 0:W], acc[0:AH, 0, :]).then_inc(copied, 1)
                dve.tensor_copy(fb[:, W:M], acc[0:AH, 1, 0:M - W]).then_inc(copied, 1)


def sparse_attention(nc, d, o):
    SCALE = 64 ** -0.5
    N = AH * TT
    with phase(nc, "bias_loaded", "ident_loaded", "bias_ready", "s_done", "logits_done", "max_done", "exp_done",
               "p_turned", "p_copied", "o_done", "o_scaled", "o_turned", "o_out", "stored0", "stored1",
               "dve_steps") as (
            bias_loaded, ident_loaded, bias_ready, s_done, logits_done, max_done, exp_done, p_turned, p_copied,
            o_done, o_scaled, o_turned, o_out, stored0, stored1, dve_steps), ExitStack() as ctx:
        sb, ps = tensors(nc, ctx)
        tb = sb("sa_tb", [P, AH, T])
        ident = sb("sa_ident", [P, P])
        bm = sb("sa_bm", [P, 2, T])
        lg = sb("sa_lg", [P, 2, T])
        e = sb("sa_e", [P, 2, T])
        eT = sb("sa_eT", [P, 2, T])
        st = sb("sa_st", [P, N, 2])
        rs = sb("sa_rs", [P, N])
        rows = sb("sa_rows", [P, TT, D])
        oT = sb("sa_oT", [P, 2, KD, P])
        sp_ = ps("sa_sp", [P, 2, T])
        tp = ps("sa_tp", [P, 2, T])
        op = ps("sa_op", [P, 2, T])
        rp = ps("sa_rp", [P, KD, P])
        with nc.Block() as block:
            @block.sync
            def _(sp):
                sp.dma_start(ident[:], d["ident"]).then_inc(ident_loaded, 16)
                fb = d["fb"]
                diagonals = bass.AP(fb.tensor, P - 1, [[640 - 1, P], [P * 640, AH], [1, T]])
                sp.dma_start(tb[:], diagonals).then_inc(bias_loaded, 16)
                out = d["doT"].rearrange("(k p) t -> p k t", p=P)
                for i in range(TT):
                    sp.wait_ge(o_out, i + 1)
                    sp.dma_start(out[:, :, i * P:(i + 1) * P], oT[:, i % 2]).then_inc((stored0, stored1)[i % 2], 16)
                sp.wait_ge(stored0, 32)
                sp.wait_ge(stored1, 32)

            @block.gpsimd
            def _(pool):
                pool.wait_ge(bias_loaded, 16)
                for n in range(N):
                    h, i = divmod(n, TT)
                    if n >= 2:
                        pool.wait_ge(logits_done, n - 1)
                    pool.tensor_tensor(bm[:, n % 2, 0:(i + 1) * P], tb[:, h, 384 - i * P:T], o["am"][:, i, 0:(i + 1) * P],
                                       ALU.add).then_inc(bias_ready, 1)

            @block.tensor
            def _(pe):
                pe.wait_ge(ident_loaded, 16)
                for n in range(N + 2):
                    if n < N:
                        h, i = divmod(n, TT)
                        if n >= 2:
                            pe.wait_ge(logits_done, n - 1)
                        r = slice(64 * (h % 2), 64 * (h % 2) + 64)
                        pe.matmul(sp_[:, n % 2, 0:(i + 1) * P], o["qT"][r, h // 2, i * P:(i + 1) * P],
                                  o["kT"][r, h // 2, 0:(i + 1) * P], start=True, stop=True).then_inc(s_done, 1)
                    if 1 <= n <= N:
                        m = n - 1
                        i = m % TT
                        pe.wait_ge(exp_done, m + 1)
                        if m >= 2:
                            pe.wait_ge(p_copied, m - 1)
                        for c in range(i + 1):
                            mm = pe.transpose(tp[:, m % 2, c * P:(c + 1) * P], e[:, m % 2, c * P:(c + 1) * P], ident[:])
                        mm.then_inc(p_turned, 1)
                    if n >= 2:
                        m = n - 2
                        h, i = divmod(m, TT)
                        pe.wait_ge(p_copied, m + 1)
                        if m >= 2:
                            pe.wait_ge(o_scaled, m - 1)
                        for c in range(i + 1):
                            mm = pe.matmul(op[:, m % 2, 0:64], eT[:, m % 2, c * P:(c + 1) * P],
                                           o["v"][:, c, h * 64:(h + 1) * 64], start=(c == 0), stop=(c == i))
                        mm.then_inc(o_done, 1)
                pe.wait_ge(o_scaled, N)
                for i in range(TT):
                    if i:
                        pe.wait_ge(o_out, i)
                    for c in range(KD):
                        mm = pe.transpose(rp[:, c, :], rows[:, i, c * P:(c + 1) * P], ident[:])
                    mm.then_inc(o_turned, 1)

            @block.vector
            def _(dve):
                step = Steps(dve, dve_steps)

                def scale_o(m):
                    h, i = divmod(m, TT)
                    step(dve.reciprocal(rs[:, m:m + 1], st[:, m, 1:2]))
                    dve.wait_ge(o_done, m + 1)
                    dve.tensor_scalar(rows[:, i, h * 64:(h + 1) * 64], op[:, m % 2, 0:64], rs[:, m:m + 1], None,
                                      ALU.mult).then_inc(o_scaled, 1)

                for n in range(N):
                    h, i = divmod(n, TT)
                    keys = (i + 1) * P
                    dve.wait_ge(s_done, n + 1)
                    dve.wait_ge(bias_ready, n + 1)
                    if n >= 2:
                        dve.wait_ge(exp_done, n - 1)
                    dve.scalar_tensor_tensor(lg[:, n % 2, 0:keys], sp_[:, n % 2, 0:keys], SCALE, bm[:, n % 2, 0:keys],
                                             ALU.mult, ALU.add).then_inc(logits_done, 1)
                    dve.wait_ge(logits_done, n + 1)
                    dve.tensor_reduce(st[:, n, 0:1], lg[:, n % 2, 0:keys], AX.X, ALU.max, negate=True).then_inc(max_done, 1)
                    if n >= 3:
                        scale_o(n - 3)
                for m in range(N - 3, N):
                    scale_o(m)

            @block.scalar
            def _(act):
                for n in range(N + 1):
                    if n < N:
                        keys = (n % TT + 1) * P
                        act.wait_ge(max_done, n + 1)
                        if n >= 2:
                            act.wait_ge(p_turned, n - 1)
                        act.activation(e[:, n % 2, 0:keys], lg[:, n % 2, 0:keys], ACT.Exp, bias=st[:, n, 0:1],
                                       accum_out=st[:, n, 1:2]).then_inc(exp_done, 1)
                    if n:
                        m = n - 1
                        keys = (m % TT + 1) * P
                        act.wait_ge(p_turned, m + 1)
                        if m >= 2:
                            act.wait_ge(o_done, m - 1)
                        act.activation(eT[:, m % 2, 0:keys], tp[:, m % 2, 0:keys], ACT.Copy).then_inc(p_copied, 1)
                for i in range(TT):
                    act.wait_ge(o_turned, i + 1)
                    if i >= 2:
                        act.wait_ge((stored0, stored1)[i % 2], 16)
                    act.activation(oT[:, i % 2], rp[:], ACT.Copy).then_inc(o_out, 1)


def sparse_block(nc, d):
    bias_table(nc, d)
    with ExitStack() as ctx:
        sb, _ = tensors(nc, ctx)
        o = {"qT": sb("so_qT", [P, KD, T]), "kT": sb("so_kT", [P, KD, T]), "v": sb("so_v", [P, TT, D]),
             "qiT": sb("so_qiT", [P, IH // 2, T]), "kiT": sb("so_kiT", [P, T]), "wi": sb("so_wi", [P, TT, IH]),
             "am": sb("so_am", [P, TT, T])}
        sparse_projections(nc, d, o)
        choose_keys(nc, d, o)
        sparse_attention(nc, d, o)


def whole_block(nc, d):
    modulation(nc, d)
    premix(nc, d)
    own = d["hT"][:, CTX:LK]
    project(nc, own, d["w_in"][:, 0:D], d["q"])
    project(nc, d["hT"], d["w_in"][:, D:3 * D], d["kv"])
    project(nc, own, d["w_in"][:, 3 * D:7 * D], d["zg"])
    diff_attention(nc, d)
    spatial_gating(nc, d)
    project(nc, d["oT"], d["w_branch_attn"], d["ya"])
    project(nc, d["sT"], d["w_branch_sgu"], d["ys"])
    combine_branches(nc, d)
    project(nc, d["yT"], d["w_out"], d["yo"])
    join_rms(nc, d, "x", "yo", "g_post_mix", 2, "x1", "h2T", "g_pre_ffn", 3)
    project(nc, d["h2T"], d["peer_w_query"], d["qp"])
    expert_choice(nc, d)
    expert_gates(nc, d)
    experts(nc, d)
    join_rms(nc, d, "x1", "po", "g_post_ffn", 5, "x2", "x2T")
    rwkv_projections(nc, d)
    rwkv_prepare(nc, d)
    rwkv_recurrence(nc, d)
    project(nc, d["tmT"], d["w_o"], d["ho"])
    join_ln(nc, d, "x2", "ho", d["ln_g"][0:1], d["ln_b"][0:1], "x3", "x3T")
    conv_ffn(nc, d, d["x3T"], d["w_up"][0], d["conv_w"][0], d["conv_b"][0], d["w_down"][0], d["f1"])
    join_ln(nc, d, "x3", "f1", d["ln_g"][1:2], d["ln_b"][1:2], "x4", "x4T")
    sparse_block(nc, d)
    project(nc, d["doT"], d["dsa_w_o"], d["do"])
    join_ln(nc, d, "x4", "do", d["ln_g"][2:3], d["ln_b"][2:3], "x5", "x5T")
    conv_ffn(nc, d, d["x5T"], d["w_up"][1], d["conv_w"][1], d["conv_b"][1], d["w_down"][1], d["f2"])
    join_ln(nc, d, "x5", "f2", d["ln_g"][3:4], d["ln_b"][3:4], "out")


SCRATCH = {
    "mod": (1, 8 * D), "hT": (D, LK), "q": (T, D), "kv": (LK, 2 * D), "zg": (T, 4 * D), "oT": (D, T), "sT": (D, T),
    "ya": (T, D), "ys": (T, D), "yT": (D, T), "yo": (T, D), "x1": (T, D), "h2T": (D, T), "qp": (T, SEG * NK),
    "sel": (3, HK, T), "G": (NK, NK, T), "po": (T, D), "x2": (T, D), "x2T": (D, T), "rkvdag": (6, D, T),
    "arbk": (KD, P, 4, T), "bonus": (D, T), "pc": (P, KD, NC_), "ry": (2, D, T), "tmT": (D, T), "ho": (T, D),
    "x3": (T, D), "x3T": (D, T), "f1": (T, D), "x4": (T, D), "x4T": (D, T), "fb": (AH, P, 640), "doT": (D, T),
    "do": (T, D), "x5": (T, D), "x5T": (D, T), "f2": (T, D),
}


def constants():
    f = np.float32
    c = {"ident": np.eye(P, dtype=f), "iota": np.tile(np.arange(P, dtype=f), (P, 1))}
    t = np.arange(T)
    inv = f(10000.0) ** (-np.arange(16, dtype=f) / f(16))
    ang = np.concatenate([(t // 64).astype(f)[:, None] * inv, (t % 64).astype(f)[:, None] * inv], 1)
    c["rope"] = np.stack([np.cos(ang), np.sin(ang)]).astype(f).reshape(2, TT, P, 32).transpose(2, 0, 1, 3)
    start = (np.arange(T) % RC == 0).astype(f)
    c["starts"] = np.tile(np.stack([1 - start, start])[None], (P, 1, 1)).astype(f)
    c["ones64"] = np.kron(np.eye(2, dtype=f), np.ones((64, 64), f))
    c["mean64"] = c["ones64"] / f(64)
    s, t = np.arange(P)[:, None], np.arange(P)[None]
    same = s // RC == t // RC
    c["mask2"] = np.stack([(s < t) & same, (s <= t) & same], 1).astype(f)

    def join(m):
        return ((s // (2 * m) == t // (2 * m)) & (s // m < t // m)).astype(f)

    c["lmask"] = np.stack([join(1).T, join(1)], 1)
    c["emask"] = np.stack([join(m) for m in (2, 4, 8, 16, 32)], 1)
    dist = np.maximum(T - 1 - np.arange(640), 0)
    far = 16 + (np.log(np.maximum(dist, 1).astype(f) / f(16)) / f(np.log(8.0)) * f(16)).astype(np.int32)
    c["buckets"] = (np.arange(32)[:, None] == np.where(dist < 16, dist, np.minimum(far, 31))[None]).astype(f)
    return c


def lay_out(a):
    def cols(v):
        return v.reshape(KD, P).T

    out = {
        "x": a["x"][0], "ctx": a["ctx"][0], "w_ada": a["w_ada"][0], "b_ada": a["b_ada"],
        "c_cols": np.stack([cols(a["c"][0]), cols(a["c_ctx"])], 2), "w_in": a["w_in"][0],
        "lambda4": np.concatenate([a["lambda_q1"], a["lambda_k1"], a["lambda_q2"], a["lambda_k2"]], 1),
        "sgu_wT": a["sgu_w"][0].transpose(2, 0, 1), "sgu_bT": a["sgu_b"][0].T,
        "w_branch_attn": a["w_branch_attn"][0], "w_branch_sgu": a["w_branch_sgu"][0], "w_out": a["w_out"][0],
        "peer_w_query": a["peer_w_query"][0], "keysT": a["peer_sub_keys"][0].transpose(2, 0, 1),
        "uT": a["peer_u"][0].reshape(NK, NK, KD, P).transpose(0, 3, 2, 1), "peer_v": a["peer_v"][0],
        "mix_cols": a["rwkv_mix_2"][0].reshape(6, KD, P).transpose(2, 0, 1), "w_rkv": a["rwkv_w_rkv_2"][0],
        "w0a0_cols": np.stack([cols(a["rwkv_w0_2"][0]), cols(a["rwkv_a0_2"][0])], 1),
        "k_cols": np.stack([cols(a["rwkv_k_k_2"][0]), cols(a["rwkv_k_a_2"][0]), cols(a["rwkv_r_k_2"][0].reshape(-1))], 1),
        "lnx_cols": np.stack([cols(a["rwkv_lnx_g_2"][0]), cols(a["rwkv_lnx_b_2"][0])], 1), "w_o": a["rwkv_w_o_2"][0],
        "ln_g": a["ln_g_2"].reshape(4, D), "ln_b": a["ln_b_2"].reshape(4, D),
        "w_up": a["ffn_w_up_2"], "w_down": a["ffn_w_down_2"],
        "conv_w": a["ffn_conv_w_2"].reshape(2, 3, -1, P).transpose(0, 3, 2, 1),
        "conv_b": a["ffn_conv_b_2"].reshape(2, -1, P).transpose(0, 2, 1),
        "dsa_w_in": a["dsa_w_in_2"][0], "dsa_w_uq": a["dsa_w_uq_2"][0], "dsa_w_qidx": a["dsa_w_qidx_2"][0],
        "dsa_vecs": np.concatenate([a["dsa_q_norm_g_2"], a["dsa_kv_norm_g_2"], a["dsa_kidx_g_2"], a["dsa_kidx_b_2"]], 1),
        "dsa_w_uk": a["dsa_w_uk_2"][0].transpose(2, 0, 1).reshape(P, D),
        "dsa_w_uv": a["dsa_w_uv_2"][0].transpose(1, 0, 2).reshape(P, D),
        "dsa_w_o": a["dsa_w_o_2"][0], "rel_bias": a["rel_bias_2"],
    }
    for n in ("w1", "a1", "g1", "w2", "a2", "g2"):
        out[n] = a[f"rwkv_{n}_2"][0]
    for n in ("g_pre_mix", "g_post_mix", "g_pre_ffn", "g_post_ffn", "b_gate", "subln_g", "sgu_ln_g", "sgu_ln_b"):
        out[n] = a[n]
    return out


def kernel(**inputs):
    import concourse.bacc as bacc
    from concourse.bass_utils import run_bass_kernel_spmd as run

    nc = bacc.Bacc("TRN2", target_bir_lowering=False, num_devices=1)
    arrays, d = {}, {}
    sent = {**lay_out({n: np.asarray(v) for n, v in inputs.items()}), **constants()}
    for n, v in sent.items():
        arrays["in_" + n] = np.ascontiguousarray(v)
        d[n] = nc.dram_tensor("in_" + n, v.shape, F32, kind="ExternalInput").ap()
    for n, shape in SCRATCH.items():
        d[n] = nc.dram_tensor("scratch_" + n, list(shape), F32).ap()
    d["out"] = nc.dram_tensor("out_0_dram", (T, D), F32, kind="ExternalOutput").ap()
    whole_block(nc, d)
    r = run(nc, [arrays], core_ids=[0])
    return r.results[0]["out_0_dram"].reshape(1, T, D)
```

```python
from contextlib import ExitStack, contextmanager

import numpy as np

import concourse.bass as bass
from concourse import mybir

F32 = mybir.dt.float32
F32R = mybir.dt.float32r
U32 = mybir.dt.uint32
ALU = mybir.AluOpType
ACT = mybir.ActivationFunctionType
AX = mybir.AxisListType

P = 128
D = 1024
T = 512
CTX = 256
KD = D // P
TT = T // P
W = 512
HEADS = 16
DH = 64
LK = T + CTX
SEM_BASE = 110


@contextmanager
def phase(nc, *names):
    with ExitStack() as ctx:
        sems = [ctx.enter_context(nc.semaphore(n, num=SEM_BASE + i)) for i, n in enumerate(names)]
        yield sems
        nc.all_engine_barrier(sems_to_clear=range(SEM_BASE, SEM_BASE + len(names)))


class Steps:

    def __init__(self, eng, sem):
        self.eng, self.sem, self.n = eng, sem, 0

    def __call__(self, ins, wait=True):
        ins.then_inc(self.sem, 1)
        self.n += 1
        if wait:
            self.eng.wait_ge(self.sem, self.n)

    def wait(self):
        self.eng.wait_ge(self.sem, self.n)


def tensors(nc, ctx):
    def sb(name, shape, dt=F32):
        return ctx.enter_context(nc.sbuf_tensor(name, shape, dt, allow_name_mangling=True))

    def ps(name, shape, dt=F32):
        return ctx.enter_context(nc.psum_tensor(name, shape, dt, allow_name_mangling=True))

    return sb, ps


def root_reciprocal(pool, steps, out, src, eps, mhalf):
    steps(pool.tensor_scalar(out, src, eps, None, ALU.add))
    return pool.tensor_tensor(out, out, mhalf, ALU.pow)


def over_partitions(row):
    return row.to_broadcast([P, row.shape[1]])


def modulation(nc, d):
    NB, BW = 6, 1024
    w = d["w_ada"].rearrange("(k p) n -> p k n", p=P)
    with phase(nc, "c_loaded", "silu_done", "w0_loaded", "w1_loaded", "w_used", "bank_done", "added", "stored") as (
            c_loaded, silu_done, w0_loaded, w1_loaded, w_used, bank_done, added, stored), ExitStack() as ctx:
        sb, ps = tensors(nc, ctx)
        cc = sb("ada_c", [P, KD, 2])
        cs = sb("ada_silu", [P, KD, 2])
        wt = sb("ada_w", [P, 2, KD, BW])
        b2 = sb("ada_b", [2, NB * BW])
        rows = sb("ada_rows", [2, NB * BW])
        acc = ps("ada_acc", [P, 2, 2, W])
        w_loaded = (w0_loaded, w1_loaded)
        with nc.Block() as block:
            @block.sync
            def _(sp):
                sp.dma_start(cc[:], d["c_cols"]).then_inc(c_loaded, 16)
                sp.dma_start(b2[:], d["b_ada"].to_broadcast([2, NB * BW])).then_inc(c_loaded, 16)
                with sp.Fori(0, NB // 2) as i:
                    for u in range(2):
                        sp.wait_ge(w_used, i * 2 + u + 1)
                        sp.dma_start(wt[:, u], w[:, :, bass.ds(i * (2 * BW) + u * BW, BW)]).then_inc(w_loaded[u], 16)
                sp.wait_ge(added, NB * 2 + 4)
                sp.dma_start(d["mod"][0:1, 0:6 * D], rows[0:1, :]).then_inc(stored, 16)
                sp.dma_start(d["mod"][0:1, 6 * D:8 * D], rows[1:2, 0:2 * D]).then_inc(stored, 16)
                sp.wait_ge(stored, 32)

            @block.scalar
            def _(act):
                act.wait_ge(c_loaded, 32)
                act.activation(cs[:], cc[:], ACT.Silu).then_inc(silu_done, 1)

            @block.tensor
            def _(pe):
                pe.sem_inc(w_used, 2)
                pe.wait_ge(silu_done, 1)
                with pe.Fori(0, NB // 2) as i:
                    for u in range(2):
                        pe.wait_ge(w_loaded[u], i * 16 + 16)
                        for s in range(2):
                            pe.wait_ge(added, i * 4 + 2 * u + s + 1)
                            for k in range(KD):
                                mm = pe.matmul(acc[0:2, u, s, :], cs[:, k, :], wt[:, u, k, s * W:(s + 1) * W],
                                               start=(k == 0), stop=(k == KD - 1))
                            mm.then_inc(bank_done, 1)
                        pe.wait_ge(bank_done, i * 4 + 2 * u + 2)
                        pe.sem_inc(w_used, 1)

            @block.vector
            def _(dve):
                dve.sem_inc(added, 4)
                dve.wait_ge(c_loaded, 32)
                with dve.Fori(0, NB // 2) as i:
                    for u in range(2):
                        for s in range(2):
                            dve.wait_ge(bank_done, i * 4 + 2 * u + s + 1)
                            col = bass.ds(i * (2 * BW) + u * BW + s * W, W)
                            dve.tensor_tensor(rows[:, col], acc[0:2, u, s, :], b2[:, col], ALU.add).then_inc(added, 1)


def product3(pe, out, left, right, start, stop):
    pe.matmul(out, left[0], right[0], start=start, stop=False)
    pe.matmul(out, left[0], right[1], start=False, stop=False)
    return pe.matmul(out, left[1], right[0], start=False, stop=stop)


def project(nc, xT, *products):
    K, tokens = xT.shape
    KC = K // P
    KH = KC // 2
    halves = (slice(0, KH), slice(KH, KC))
    tiles = tokens // P
    sets = 2 if 2 * tiles <= 8 else 1
    parts, NP = [], 0
    for w, out in products:
        n = w.shape[1] // (2 * W)
        parts.append((NP, n, w.rearrange("(k p) n -> p k n", p=P), out.rearrange("(t p) n -> p t n", p=P)))
        NP += n
    with phase(nc, "xa_loaded", "xb_loaded", "w0a_loaded", "w0b_loaded", "w1a_loaded", "w1b_loaded", "x_hi", "x_lo",
               "w_hi", "wa_lo", "wb_lo", "block_done", "bank_done", "copied", "stored0", "stored1") as (
            xa_loaded, xb_loaded, w0a_loaded, w0b_loaded, w1a_loaded, w1b_loaded, x_hi, x_lo, w_hi, wa_lo, wb_lo,
            block_done, bank_done, copied, stored0, stored1), ExitStack() as ctx:
        sb, ps = tensors(nc, ctx)
        xh = sb("pr_xh", [P, KC, tokens], F32R)
        xl = sb("pr_xl", [P, KC, tokens], F32R)
        raw = sb("pr_raw", [P, 2, KC, W])
        wh = sb("pr_wh", [P, 2, KC, W], F32R)
        wl = sb("pr_wl", [P, 2, KC, W], F32R)
        stage = sb("pr_stage", [P, 2, tiles, W])
        acc = ps("pr_acc", [P, sets, tiles, W])
        x = stage[:].rearrange("p u t n -> p (u t n)").rearrange("p (k t) -> p k t", k=KC)
        x_loaded, w_loaded = (xa_loaded, xb_loaded), ((w0a_loaded, w0b_loaded), (w1a_loaded, w1b_loaded))
        w_lo, stored = (wa_lo, wb_lo), (stored0, stored1)
        with nc.Block() as block:
            @block.sync
            def _(sp):
                def load(pair, i, wv, u, h):
                    sp.wait_ge(w_lo[h], pair * 2 + u + 1)
                    sp.dma_start(raw[:, u, halves[h]], wv[:, halves[h], bass.ds(i * (2 * W) + u * W, W)]).then_inc(
                        w_loaded[u][h], 16)

                xv = xT.rearrange("(k p) t -> p k t", p=P)
                for h in range(2):
                    sp.dma_start(x[:, halves[h]], xv[:, halves[h]]).then_inc(x_loaded[h], 16)
                    sp.wait_ge(w_lo[h], 1)
                    sp.dma_start(raw[:, 0, halves[h]], parts[0][2][:, halves[h], 0:W]).then_inc(w_loaded[0][h], 16)
                for h in range(2):
                    sp.wait_ge(w_lo[h], 2)
                    sp.dma_start(raw[:, 1, halves[h]], parts[0][2][:, halves[h], W:2 * W]).then_inc(w_loaded[1][h], 16)
                for before, n, wv, _ in parts:
                    first = int(before == 0)
                    if n > first:
                        with sp.Fori(first, n) as i:
                            for u in range(2):
                                for h in range(2):
                                    load(i + before, i, wv, u, h)

            @block.scalar
            def _(act):
                def hi(pair, u):
                    act.wait_ge(block_done, pair * 2 + u + 1)
                    for h in range(2):
                        act.wait_ge(w_loaded[u][h], pair * 16 + 16)
                        act.activation(wh[:, u, halves[h]], raw[:, u, halves[h]], ACT.Copy).then_inc(w_hi, 1)

                def store(pair, i, rows, u):
                    act.wait_ge(copied, pair * (2 * tiles) + ((u + 1) * tiles + sets * tiles))
                    act.dma_start(rows[:, :, bass.ds(i * (2 * W) + u * W, W)], stage[:, u]).then_inc(stored[u], 16)

                act.sem_inc(stored0, 16)
                act.sem_inc(stored1, 16)
                act.wait_ge(block_done, 1)
                for h in range(2):
                    act.wait_ge(x_loaded[h], 16)
                    act.activation(xh[:, halves[h]], x[:, halves[h]], ACT.Copy).then_inc(x_hi, 1)
                    act.wait_ge(w_loaded[0][h], 16)
                    act.activation(wh[:, 0, halves[h]], raw[:, 0, halves[h]], ACT.Copy).then_inc(w_hi, 1)
                for before, n, _, rows in parts:
                    loop = n - int(before + n == NP)
                    if loop:
                        with act.Fori(0, loop) as i:
                            hi(i + before, 1)
                            store(i + before, i, rows, 0)
                            hi(i + (before + 1), 0)
                            store(i + before, i, rows, 1)
                hi(NP - 1, 1)
                for u in range(2):
                    store(NP - 1, parts[-1][1] - 1, parts[-1][3], u)
                act.wait_ge(stored0, 16 * NP + 16)
                act.wait_ge(stored1, 16 * NP + 16)

            @block.gpsimd
            def _(pool):
                pool.sem_inc(wa_lo, 2)
                with pool.Fori(0, NP) as i:
                    for u in range(2):
                        pool.wait_ge(w_hi, i * 4 + (2 * u + 1))
                        pool.tensor_tensor(wl[:, u, 0:KH], raw[:, u, 0:KH], wh[:, u, 0:KH].bitcast(F32),
                                           ALU.subtract).then_inc(wa_lo, 1)

            @block.tensor
            def _(pe):
                def half(pair, u, h):
                    pe.wait_ge(x_lo, h + 1)
                    pe.wait_ge(w_lo[h], pair * 2 + (u + 3))
                    for t in range(tiles):
                        if h == 0:
                            pe.wait_ge(copied, pair * (2 * tiles) + (u * tiles + t + 1))
                        tok = slice(t * P, (t + 1) * P)
                        for k in range(h * KH, (h + 1) * KH):
                            mm = product3(pe, acc[:, u % sets, t, :], (xh[:, k, tok], xl[:, k, tok]),
                                          (wh[:, u, k, :], wl[:, u, k, :]), k == 0, k == KC - 1)
                        if h:
                            mm.then_inc(bank_done, 1)

                pe.sem_inc(block_done, 2)
                with pe.Fori(0, NP) as i:
                    for u in range(2):
                        half(i, u, 0)
                        half(i, u, 1)
                        pe.wait_ge(bank_done, i * (2 * tiles) + (u + 1) * tiles)
                        pe.sem_inc(block_done, 1)

            @block.vector
            def _(dve):
                dve.sem_inc(copied, sets * tiles)
                dve.sem_inc(wb_lo, 2)
                for h in range(2):
                    dve.wait_ge(x_hi, h + 1)
                    dve.tensor_tensor(xl[:, halves[h]], x[:, halves[h]], xh[:, halves[h]].bitcast(F32),
                                      ALU.subtract).then_inc(x_lo, 1)
                dve.wait_ge(x_lo, 2)
                with dve.Fori(0, NP) as i:
                    for u in range(2):
                        dve.wait_ge(w_hi, i * 4 + (2 * u + 2))
                        dve.tensor_tensor(wl[:, u, KH:KC], raw[:, u, KH:KC], wh[:, u, KH:KC].bitcast(F32),
                                          ALU.subtract).then_inc(wb_lo, 1)
                        dve.wait_ge(stored[u], i * 16 + 16)
                        for t in range(tiles):
                            dve.wait_ge(bank_done, i * (2 * tiles) + u * tiles + t + 1)
                            dve.tensor_copy(stage[:, u, t, :], acc[:, u % sets, t, :]).then_inc(copied, 1)


def transpose_out(pe, tiles, src, ready, ident, acc, copied, done):
    for i in range(tiles):
        pe.wait_ge(ready, i + 1)
        if i >= 2:
            pe.wait_ge(copied, i - 1)
        rows = src(i)
        for k in range(KD):
            mm = pe.transpose(acc[:, i % 2, k, :], rows[:, k * P:(k + 1) * P], ident[:])
        mm.then_inc(done, 1)


def premix(nc, d):
    CT = CTX // P
    tiles = CT + TT
    with phase(nc, "vec_loaded", "rows_loaded", "gain_done", "squared", "rows_done", "turned", "copied", "stored0", "stored1",
               "rooted", "pool_steps", "dve_steps") as (vec_loaded, rows_loaded, gain_done, squared, rows_done, turned, copied,
                                          stored0, stored1, rooted, pool_steps, dve_steps), ExitStack() as ctx:
        sb, ps = tensors(nc, ctx)
        x = sb("pm_x", [P, tiles, D])
        junk = sb("pm_junk", [P, D])
        ss = sb("pm_ss", [P, tiles])
        rstd = sb("pm_rstd", [P, tiles])
        mhalf = sb("pm_mhalf", [P, tiles])
        g = sb("pm_g", [P, D])
        gain = sb("pm_gain", [P, 2, D])
        shift = sb("pm_shift", [P, 2, D])
        ident = sb("pm_ident", [P, P])
        h = sb("pm_h", [P, tiles, D])
        hT = sb("pm_hT", [P, 2, KD, P])
        acc = ps("pm_acc", [P, 2, KD, P])
        with nc.Block() as block:
            @block.sync
            def _(sp):
                sp.dma_start(x[:, 0:CT], d["ctx"].rearrange("(t p) n -> p t n", p=P)).then_inc(rows_loaded, 16)
                sp.dma_start(x[:, CT:tiles], d["x"].rearrange("(t p) n -> p t n", p=P)).then_inc(rows_loaded, 16)
                sp.dma_start(ident[:], d["ident"]).then_inc(rows_loaded, 16)
                sp.dma_start(g[:], over_partitions(d["g_pre_mix"])).then_inc(vec_loaded, 16)
                for s, at in enumerate((6, 0)):
                    sp.dma_start(shift[:, s], over_partitions(d["mod"][:, at * D:(at + 1) * D])).then_inc(vec_loaded, 16)
                    sp.dma_start(gain[:, s], over_partitions(d["mod"][:, (at + 1) * D:(at + 2) * D])).then_inc(vec_loaded, 16)
                hT_out = d["hT"].rearrange("(k p) t -> p k t", p=P)
                for i in range(tiles):
                    sp.wait_ge(copied, i + 1)
                    sp.dma_start(hT_out[:, :, i * P:(i + 1) * P], hT[:, i % 2]).then_inc((stored0, stored1)[i % 2], 16)
                sp.wait_ge(stored0, 16 * tiles // 2)
                sp.wait_ge(stored1, 16 * tiles // 2)

            @block.scalar
            def _(act):
                act.wait_ge(rows_loaded, 48)
                for i in range(tiles):
                    if i:
                        act.wait_ge(squared, i)
                    act.activation(junk[:], x[:, i], ACT.Square, scale=D ** -0.5, accum_out=ss[:, i:i + 1]).then_inc(squared, 1)
                for i in range(tiles):
                    act.wait_ge(turned, i + 1)
                    if i >= 2:
                        act.wait_ge((stored0, stored1)[i % 2], 16 * (i // 2))
                    act.activation(hT[:, i % 2], acc[:, i % 2], ACT.Copy).then_inc(copied, 1)

            @block.vector
            def _(dve):
                step = Steps(dve, dve_steps)
                dve.wait_ge(vec_loaded, 80)
                for s in range(2):
                    step(dve.scalar_tensor_tensor(gain[:, s], gain[:, s], 1.0, g[:], ALU.add, ALU.mult))
                dve.wait_ge(rooted, 1)
                for i in range(tiles):
                    s = int(i >= CT)
                    step(dve.scalar_tensor_tensor(h[:, i], x[:, i], rstd[:, i:i + 1], gain[:, s], ALU.mult, ALU.mult))
                    dve.tensor_tensor(h[:, i], h[:, i], shift[:, s], ALU.add).then_inc(rows_done, 1)

            @block.gpsimd
            def _(pool):
                steps = Steps(pool, pool_steps)
                steps(pool.memset(mhalf[:], -0.5))
                pool.wait_ge(squared, tiles)
                root_reciprocal(pool, steps, rstd[:], ss[:], 1e-6, mhalf[:]).then_inc(rooted, 1)

            @block.tensor
            def _(pe):
                pe.wait_ge(rows_loaded, 48)
                transpose_out(pe, tiles, lambda i: h[:, i], rows_done, ident, acc, copied, turned)


def join_rms(nc, d, x_in, y_in, g_post, gate_at, x_out, hT_out, g_pre=None, shift_at=None):
    order = [(w, i) for n in range(TT + 2) for w, i in (("y", n), ("x", n - 2)) if 0 <= i < TT and (w == "y" or g_pre)]
    place = {what: n + 1 for n, what in enumerate(order)}
    with phase(nc, "row0_loaded", "row1_loaded", "row2_loaded", "row3_loaded", "vec_loaded", "rows_done", "x_done", "turned",
               "copied", "stored0", "stored1", "x_stored", "summed", "rooted", "pool_steps", "dve_steps") as (
            row0_loaded, row1_loaded, row2_loaded, row3_loaded, vec_loaded, rows_done, x_done, turned, copied, stored0,
            stored1, x_stored, summed, rooted, pool_steps, dve_steps), ExitStack() as ctx:
        sb, ps = tensors(nc, ctx)
        x = sb("jr_x", [P, TT, D])
        y = sb("jr_y", [P, TT, D])
        h = sb("jr_h", [P, TT, D])
        junk = sb("jr_junk", [P, 2 * TT, D])
        st = sb("jr_st", [P, TT, 4])
        mhalf = sb("jr_mhalf", [P, 1])
        gp = sb("jr_gp", [P, D])
        gt = sb("jr_gt", [P, D])
        gain = sb("jr_gain", [P, D])
        shift = sb("jr_shift", [P, D])
        g2 = sb("jr_g2", [P, D])
        ident = sb("jr_ident", [P, P])
        hT = sb("jr_hT", [P, 2, KD, P])
        acc = ps("jr_acc", [P, 2, KD, P])
        loaded = (row0_loaded, row1_loaded, row2_loaded, row3_loaded)

        def vec(at):
            return over_partitions(d["mod"][:, at * D:(at + 1) * D])

        with nc.Block() as block:
            @block.sync
            def _(sp):
                for i in range(TT):
                    sp.dma_start(y[:, i], d[y_in][i * P:(i + 1) * P, :]).then_inc(loaded[i], 16)
                    sp.dma_start(x[:, i], d[x_in][i * P:(i + 1) * P, :]).then_inc(loaded[i], 16)
                turned_out = d[hT_out].rearrange("(k p) t -> p k t", p=P)
                for i in range(TT):
                    sp.wait_ge(x_done, i + 1)
                    sp.dma_start(d[x_out][i * P:(i + 1) * P, :], x[:, i]).then_inc(x_stored, 16)
                    sp.wait_ge(copied, i + 1)
                    sp.dma_start(turned_out[:, :, i * P:(i + 1) * P], hT[:, i % 2]).then_inc((stored0, stored1)[i % 2], 16)
                sp.wait_ge(x_stored, 16 * TT)
                sp.wait_ge(stored0, 16 * TT // 2)
                sp.wait_ge(stored1, 16 * TT // 2)

            @block.scalar
            def _(act):
                def copy_out(i):
                    act.wait_ge(turned, i + 1)
                    if i >= 2:
                        act.wait_ge((stored0, stored1)[i % 2], 16 * (i // 2))
                    act.activation(hT[:, i % 2], acc[:, i % 2], ACT.Copy).then_inc(copied, 1)

                act.dma_start(gp[:], over_partitions(d[g_post])).then_inc(vec_loaded, 16)
                act.dma_start(gt[:], vec(gate_at)).then_inc(vec_loaded, 16)
                act.dma_start(ident[:], d["ident"]).then_inc(vec_loaded, 16)
                if g_pre:
                    act.dma_start(g2[:], over_partitions(d[g_pre])).then_inc(vec_loaded, 16)
                    act.dma_start(shift[:], vec(shift_at)).then_inc(vec_loaded, 16)
                    act.dma_start(gain[:], vec(shift_at + 1)).then_inc(vec_loaded, 16)
                for n, (what, i) in enumerate(order):
                    if what == "y":
                        act.wait_ge(loaded[i], 32)
                        rows, to = y[:, i], st[:, i, 0:1]
                    else:
                        act.wait_ge(x_done, i + 1)
                        rows, to = x[:, i], st[:, i, 2:3]
                    act.activation(junk[:, n], rows, ACT.Square, scale=D ** -0.5, accum_out=to).then_inc(summed, 1)
                    if what == "x" and i >= 1:
                        copy_out(i - 1)
                for i in range(TT - 1 if g_pre else 0, TT):
                    copy_out(i)

            @block.vector
            def _(dve):
                step = Steps(dve, dve_steps)
                dve.wait_ge(vec_loaded, 96 if g_pre else 48)
                step(dve.tensor_tensor(gt[:], gt[:], gp[:], ALU.mult))
                if g_pre:
                    step(dve.scalar_tensor_tensor(gain[:], gain[:], 1.0, g2[:], ALU.add, ALU.mult))
                for what, i in order:
                    dve.wait_ge(rooted, place[what, i])
                    if what == "y":
                        step(dve.scalar_tensor_tensor(y[:, i], y[:, i], st[:, i, 1:2], gt[:], ALU.mult, ALU.mult))
                        dve.wait_ge(loaded[i], 32)
                        dve.tensor_tensor(x[:, i], x[:, i], y[:, i], ALU.add).then_inc(x_done, 1)
                    else:
                        step(dve.scalar_tensor_tensor(h[:, i], x[:, i], st[:, i, 3:4], gain[:], ALU.mult, ALU.mult))
                        dve.tensor_tensor(h[:, i], h[:, i], shift[:], ALU.add).then_inc(rows_done, 1)

            @block.gpsimd
            def _(pool):
                steps = Steps(pool, pool_steps)
                steps(pool.memset(mhalf[:], -0.5))
                for what, i in order:
                    pool.wait_ge(summed, place[what, i])
                    at = 0 if what == "y" else 2
                    root_reciprocal(pool, steps, st[:, i, at + 1:at + 2], st[:, i, at:at + 1], 1e-6,
                                    mhalf[:]).then_inc(rooted, 1)

            @block.tensor
            def _(pe):
                pe.wait_ge(vec_loaded, 96 if g_pre else 48)
                if g_pre:
                    transpose_out(pe, TT, lambda i: h[:, i], rows_done, ident, acc, copied, turned)
                else:
                    transpose_out(pe, TT, lambda i: x[:, i], x_done, ident, acc, copied, turned)


def join_ln(nc, d, x_in, y_in, g, b, x_out, xT_out=None):
    ALPHA = 4.0 ** 0.25
    with phase(nc, "row0_loaded", "row1_loaded", "row2_loaded", "row3_loaded", "vec_loaded", "x_done", "turned", "copied",
               "stored0", "stored1", "x_stored", "averaged", "rooted", "scaled", "normed", "pool_steps",
               "dve_steps") as (
            row0_loaded, row1_loaded, row2_loaded, row3_loaded, vec_loaded, x_done, turned, copied, stored0, stored1,
            x_stored, averaged, rooted, scaled, normed, pool_steps, dve_steps), ExitStack() as ctx:
        sb, ps = tensors(nc, ctx)
        x = sb("jl_x", [P, TT, D])
        y = sb("jl_y", [P, TT, D])
        st = sb("jl_st", [P, TT, 2, 6])
        mv = sb("jl_mv", [P, TT, 2])
        rs = sb("jl_rs", [P, TT, 2])
        mhalf = sb("jl_mhalf", [P, 1])
        gv = sb("jl_g", [P, D])
        bv = sb("jl_b", [P, D])
        ident = sb("jl_ident", [P, P])
        xT = sb("jl_xT", [P, 2, KD, P])
        acc = ps("jl_acc", [P, 2, KD, P])
        loaded = (row0_loaded, row1_loaded, row2_loaded, row3_loaded)
        with nc.Block() as block:
            @block.sync
            def _(sp):
                for i in range(TT):
                    sp.dma_start(x[:, i], d[x_in][i * P:(i + 1) * P, :]).then_inc(loaded[i], 16)
                    sp.dma_start(y[:, i], d[y_in][i * P:(i + 1) * P, :]).then_inc(loaded[i], 16)
                for i in range(TT):
                    sp.wait_ge(x_done, i + 1)
                    sp.dma_start(d[x_out][i * P:(i + 1) * P, :], x[:, i]).then_inc(x_stored, 16)
                    if xT_out:
                        sp.wait_ge(copied, i + 1)
                        sp.dma_start(d[xT_out].rearrange("(k p) t -> p k t", p=P)[:, :, i * P:(i + 1) * P],
                                     xT[:, i % 2]).then_inc((stored0, stored1)[i % 2], 16)
                sp.wait_ge(x_stored, 16 * TT)
                if xT_out:
                    sp.wait_ge(stored0, 16 * TT // 2)
                    sp.wait_ge(stored1, 16 * TT // 2)

            def finish(dve, step, i):
                if i == 0:
                    dve.wait_ge(vec_loaded, 48)
                dve.wait_ge(normed, i + 1)
                step(dve.tensor_tensor(y[:, i], y[:, i], gv[:], ALU.mult))
                dve.tensor_tensor(x[:, i], y[:, i], bv[:], ALU.add).then_inc(x_done, 1)

            @block.vector
            def _(dve):
                step = Steps(dve, dve_steps)

                def average(i):
                    dve.wait_ge(loaded[i], 32)
                    step(dve.scalar_tensor_tensor(y[:, i], x[:, i], ALPHA, y[:, i], ALU.mult, ALU.add))
                    for s in range(2):
                        step(dve.bn_stats(st[:, i, s, :], y[:, i, s * W:(s + 1) * W]), wait=False)
                    step.wait()
                    dve.bn_aggr(mv[:, i, :], st[:, i].rearrange("p s c -> p (s c)")).then_inc(averaged, 1)

                average(0)
                for i in range(TT):
                    if i + 1 < TT:
                        average(i + 1)
                    dve.wait_ge(averaged, i + 1)
                    dve.wait_ge(rooted, i + 1)
                    dve.scalar_tensor_tensor(rs[:, i, 1:2], mv[:, i, 0:1], -1.0, rs[:, i, 0:1], ALU.mult,
                                             ALU.mult).then_inc(scaled, 1)
                    if i:
                        finish(dve, step, i - 1)
                finish(dve, step, TT - 1)

            @block.gpsimd
            def _(pool):
                steps = Steps(pool, pool_steps)
                steps(pool.memset(mhalf[:], -0.5))
                for i in range(TT):
                    pool.wait_ge(averaged, i + 1)
                    root_reciprocal(pool, steps, rs[:, i, 0:1], mv[:, i, 1:2], 1e-5, mhalf[:]).then_inc(rooted, 1)

            if xT_out:
                @block.tensor
                def _(pe):
                    pe.wait_ge(vec_loaded, 48)
                    transpose_out(pe, TT, lambda i: x[:, i], x_done, ident, acc, copied, turned)

            @block.scalar
            def _(act):
                act.dma_start(gv[:], over_partitions(g)).then_inc(vec_loaded, 16)
                act.dma_start(bv[:], over_partitions(b)).then_inc(vec_loaded, 16)
                act.dma_start(ident[:], d["ident"]).then_inc(vec_loaded, 16)
                for i in range(TT + 1):
                    if i < TT:
                        act.wait_ge(scaled, i + 1)
                        act.activation(y[:, i], y[:, i], ACT.Identity, scale=rs[:, i, 0:1], bias=rs[:, i, 1:2]).then_inc(normed, 1)
                    if i and xT_out:
                        act.wait_ge(turned, i)
                        if i >= 3:
                            act.wait_ge((stored0, stored1)[(i - 1) % 2], 16 * ((i - 1) // 2))
                        act.activation(xT[:, (i - 1) % 2], acc[:, (i - 1) % 2], ACT.Copy).then_inc(copied, 1)
def diff_attention(nc, d):
    VH = 8
    KT = LK // P
    SCALE = DH ** -0.5
    N = VH * TT
    with phase(nc, "ctx_loaded", "kv_loaded", "q_loaded", "small_loaded", "turn_ready", "turned", "turn_copied",
               "lam_summed", "lam_exp", "lam_done", "k_rotated", "q_rotated", "scores_done", "max_done", "exp_done",
               "probs_done", "probs_turned", "probs_copied", "o_done", "o_copied", "squared", "rooted", "rows_done",
               "o_turned", "o_out", "stored0", "stored1", "pool_steps", "dve_steps") as (
            ctx_loaded, kv_loaded, q_loaded, small_loaded, turn_ready, turned, turn_copied, lam_summed, lam_exp,
            lam_done, k_rotated, q_rotated, scores_done, max_done, exp_done, probs_done, probs_turned, probs_copied,
            o_done, o_copied, squared, rooted, rows_done, o_turned, o_out, stored0, stored1, pool_steps,
            dve_steps), ExitStack() as ctx:
        sb, ps = tensors(nc, ctx)
        q = sb("at_q", [P, TT, D])
        k = sb("at_k", [P, KT, D])
        v = sb("at_v", [P, KT, D])
        qT = sb("at_qT", [P, KD, T])
        kT = sb("at_kT", [P, KD, LK])
        cs = sb("at_cos", [P, 2, TT, 32])
        lam4 = sb("at_lam4", [P, 4, DH])
        lam = sb("at_lam", [P, 8])
        ident = sb("at_ident", [P, P])
        gs = sb("at_gs", [P, P])
        tmp = sb("at_tmp", [P, 2, 2, W])
        e = sb("at_e", [P, 2, 2, LK])
        a = sb("at_a", [P, 2, LK])
        aT = sb("at_aT", [P, 2, LK])
        st = sb("at_st", [P, N, 4])
        rs = sb("at_rs", [P, 2, N])
        mhalf = sb("at_mhalf", [P, VH])
        o = sb("at_o", [P, TT, D])
        ss = sb("at_ss", [P, TT, VH])
        sc = ps("at_sc", [P, 2, 1024])
        tr = [ps("at_tr", [P, 1024]), ps("at_ops", [P, 1024])]
        oT = e[:].rearrange("p a b c -> p (a b c)")[:, 0:2 * D].rearrange("p (a k t) -> p a k t", a=2, k=KD)
        ctx_rows = d["kv"][0:CTX, :].rearrange("(t p) n -> p t n", p=P)
        own_rows = d["kv"][CTX:LK, :].rearrange("(t p) n -> p t n", p=P)
        order = [("k", 0), ("k", 1)] + [(x, i) for i in range(TT) for x in ("k", "q")]

        def rotate(eng, steps, rows, i, n, done):
            x = rows.rearrange("p (h a s f) -> p h a s f", h=HEADS, a=2, s=2)
            x1, x2 = x[:, :, :, 0, :], x[:, :, :, 1, :]
            cos, sin = (cs[:, n2, i, :].rearrange("p (a f) -> p a f", a=2).unsqueeze(1).to_broadcast([P, HEADS, 2, 16])
                        for n2 in range(2))
            t1, t2 = (tmp[:, n, n2, :].rearrange("p (h a f) -> p h a f", h=HEADS, a=2) for n2 in range(2))
            steps(eng.tensor_tensor(t1, x1, sin, ALU.mult), wait=False)
            steps(eng.tensor_tensor(t2, x2, sin, ALU.mult), wait=False)
            steps.wait()
            steps(eng.tensor_tensor(x1, x1, cos, ALU.mult), wait=False)
            steps(eng.tensor_tensor(x2, x2, cos, ALU.mult), wait=False)
            steps.wait()
            steps(eng.tensor_tensor(x1, x1, t2, ALU.subtract), wait=False)
            steps(eng.tensor_tensor(x2, x2, t1, ALU.add), wait=False)
            steps.wait()
            eng.sem_inc(done, 1)

        with nc.Block() as block:
            @block.sync
            def _(sp):
                sp.dma_start(k[:, 0:2], ctx_rows[:, :, 0:D]).then_inc(ctx_loaded, 16)
                sp.dma_start(ident[:], d["ident"]).then_inc(ctx_loaded, 16)
                sp.dma_start(cs[:], d["rope"]).then_inc(small_loaded, 16)
                sp.dma_start(lam4[:], d["lambda4"].to_broadcast([P, 4 * DH])).then_inc(small_loaded, 16)
                sp.dma_start(gs[:], over_partitions(d["subln_g"])).then_inc(small_loaded, 16)
                sp.dma_start(q[:], d["q"].rearrange("(t p) n -> p t n", p=P)).then_inc(q_loaded, 16)
                sp.dma_start(k[:, 2:KT], own_rows[:, :, 0:D]).then_inc(kv_loaded, 16)
                sp.dma_start(v[:, 0:2], ctx_rows[:, :, D:2 * D]).then_inc(kv_loaded, 16)
                sp.dma_start(v[:, 2:KT], own_rows[:, :, D:2 * D]).then_inc(kv_loaded, 16)
                out = d["oT"].rearrange("(k p) t -> p k t", p=P)
                for i in range(TT):
                    sp.wait_ge(o_out, i + 1)
                    sp.dma_start(out[:, :, i * P:(i + 1) * P], oT[:, i % 2]).then_inc((stored0, stored1)[i % 2], 16)
                sp.wait_ge(stored0, 32)
                sp.wait_ge(stored1, 32)

            @block.gpsimd
            def _(pool):
                steps = Steps(pool, pool_steps)
                steps(pool.memset(mhalf[:], -0.5))
                pool.wait_ge(small_loaded, 48)
                pool.wait_ge(kv_loaded, 48)
                for i in range(TT):
                    rotate(pool, steps, k[:, 2 + i], i, 1, k_rotated)
                for i in range(TT):
                    pool.wait_ge(squared, i + 1)
                    root_reciprocal(pool, steps, ss[:, i], ss[:, i], 1e-6, mhalf[:]).then_inc(rooted, 1)

            @block.tensor
            def _(pe):
                pe.wait_ge(ctx_loaded, 32)
                for n, (what, i) in enumerate(order):
                    if what == "q":
                        pe.wait_ge(q_rotated, i + 1)
                    elif i >= 2 or n >= 2:
                        pe.wait_ge(k_rotated, i + 1)
                    if n >= 2:
                        pe.wait_ge(turn_copied, n - 1)
                    rows = q[:, i] if what == "q" else k[:, i if n < 2 else 2 + i]
                    for c in range(KD):
                        mm = pe.transpose(tr[n % 2][:, c * P:(c + 1) * P], rows[:, c * P:(c + 1) * P], ident[:])
                    mm.then_inc(turned, 1)
                pe.wait_ge(turn_copied, len(order))
                pe.wait_ge(kv_loaded, 48)
                for n in range(N + 3):
                    if n < N:
                        h, i = divmod(n, TT)
                        for c in range(2):
                            if n:
                                pe.wait_ge(exp_done, 2 * (n - 1) + c + 1)
                            rows = slice(DH * c, DH * c + DH)
                            lhs = qT[rows, h, i * P:(i + 1) * P]
                            pe.matmul(sc[:, c, 0:W], lhs, kT[rows, h, 0:W], start=True, stop=True)
                            pe.matmul(sc[:, c, W:LK], lhs, kT[rows, h, W:LK], start=True,
                                      stop=True).then_inc(scores_done, 1)
                    if 2 <= n <= N + 1:
                        m = n - 2
                        pe.wait_ge(probs_done, m + 1)
                        if m:
                            pe.wait_ge(probs_copied, m)
                        for c in range(KT):
                            mm = pe.transpose(tr[0][:, c * P:(c + 1) * P], a[:, m % 2, c * P:(c + 1) * P], ident[:])
                        mm.then_inc(probs_turned, 1)
                    if n >= 3:
                        m = n - 3
                        h = m // TT
                        pe.wait_ge(probs_copied, m + 1)
                        if m >= 2:
                            pe.wait_ge(o_copied, m - 1)
                        for c in range(KT):
                            mm = pe.matmul(tr[1][:, (m % 2) * W:(m % 2) * W + P], aT[:, m % 2, c * P:(c + 1) * P],
                                           v[:, c, h * P:(h + 1) * P], start=(c == 0), stop=(c == KT - 1))
                        mm.then_inc(o_done, 1)
                pe.wait_ge(o_copied, N)
                for i in range(TT):
                    pe.wait_ge(rows_done, i + 1)
                    if i >= 2:
                        pe.wait_ge(o_out, i - 1)
                    for c in range(KD):
                        mm = pe.transpose(tr[i % 2][:, c * P:(c + 1) * P], o[:, i, c * P:(c + 1) * P], ident[:])
                    mm.then_inc(o_turned, 1)

            @block.scalar
            def _(act):
                act.wait_ge(lam_summed, 1)
                act.activation(lam[:, 2:4], lam[:, 0:2], ACT.Exp).then_inc(lam_exp, 1)
                for n, (what, i) in enumerate(order):
                    act.wait_ge(turned, n + 1)
                    to = qT[:, :, i * P:(i + 1) * P] if what == "q" else kT[:, :, (i if n < 2 else 2 + i) * P:
                                                                            (i + 1 if n < 2 else 3 + i) * P]
                    act.activation(to, tr[n % 2][:].rearrange("p (k t) -> p k t", k=KD), ACT.Copy,
                                   scale=-SCALE if what == "q" else 1.0).then_inc(turn_copied, 1)
                for n in range(N + 2):
                    if n < N:
                        if n >= 2:
                            act.wait_ge(probs_done, n - 1)
                        for c in range(2):
                            act.wait_ge(max_done, 2 * n + c + 1)
                            act.activation(e[:, n % 2, c], sc[:, c, 0:LK], ACT.Exp, bias=st[:, n, c:c + 1], scale=-1.0,
                                           accum_out=st[:, n, 2 + c:3 + c]).then_inc(exp_done, 1)
                    if n >= 2:
                        m = n - 2
                        act.wait_ge(probs_turned, m + 1)
                        if m >= 2:
                            act.wait_ge(o_done, m - 1)
                        act.activation(aT[:, m % 2], tr[0][:, 0:LK], ACT.Copy).then_inc(probs_copied, 1)
                for i in range(TT):
                    act.wait_ge(o_turned, i + 1)
                    if i >= 2:
                        act.wait_ge((stored0, stored1)[i % 2], 16)
                    act.activation(oT[:, i % 2].rearrange("p k t -> p (k t)"), tr[i % 2][:], ACT.Copy).then_inc(o_out, 1)

            @block.vector
            def _(dve):
                step = Steps(dve, dve_steps)
                dve.wait_ge(small_loaded, 48)
                for c in range(2):
                    step(dve.tensor_tensor_reduce(tmp[:, 0, c, 0:DH], lam4[:, 2 * c], lam4[:, 2 * c + 1], 1.0, 0.0,
                                                  ALU.mult, ALU.add, lam[:, c:c + 1]), wait=False)
                step.wait()
                dve.sem_inc(lam_summed, 1)
                dve.wait_ge(lam_exp, 1)
                step(dve.tensor_tensor(lam[:, 4:5], lam[:, 3:4], lam[:, 2:3], ALU.subtract))
                step(dve.tensor_scalar(lam[:, 5:6], lam[:, 4:5], -0.2, None, ALU.add))
                step(dve.tensor_scalar(gs[:], gs[:], 0.8, None, ALU.mult))
                dve.wait_ge(q_loaded, 16)
                for i in range(TT):
                    rotate(dve, step, q[:, i], i, 0, q_rotated)

                def combine(m):
                    dve.wait_ge(exp_done, 2 * m + 2)
                    step(dve.reciprocal(rs[:, :, m], st[:, m, 2:4]))
                    step(dve.scalar_tensor_tensor(rs[:, 1, m:m + 1], rs[:, 1, m:m + 1], lam[:, 5:6], st[:, m, 2:3],
                                                  ALU.mult, ALU.mult))
                    if m >= 2:
                        dve.wait_ge(probs_turned, m - 1)
                    dve.scalar_tensor_tensor(a[:, m % 2], e[:, m % 2, 1], rs[:, 1, m:m + 1], e[:, m % 2, 0], ALU.mult,
                                             ALU.add).then_inc(probs_done, 1)

                def copy_o(m):
                    h, i = divmod(m, TT)
                    dve.wait_ge(o_done, m + 1)
                    dve.tensor_scalar(o[:, i, h * P:(h + 1) * P], tr[1][:, (m % 2) * W:(m % 2) * W + P],
                                      rs[:, 0, m:m + 1], None, ALU.mult).then_inc(o_copied, 1)

                for n in range(N):
                    for c in range(2):
                        dve.wait_ge(scores_done, 2 * n + c + 1)
                        dve.tensor_reduce(st[:, n, c:c + 1], sc[:, c, 0:LK], AX.X, ALU.min).then_inc(max_done, 1)
                    if n:
                        combine(n - 1)
                    if n >= 4:
                        copy_o(n - 4)
                combine(N - 1)
                for m in range(N - 4, N):
                    copy_o(m)
                dve.wait_ge(o_copied, N)
                for i in range(TT):
                    rows = o[:, i].rearrange("p (h c) -> p h c", h=VH)
                    sq = q[:, i]
                    step(dve.tensor_tensor(sq, o[:, i], o[:, i], ALU.mult))
                    step(dve.tensor_reduce(ss[:, i], sq.rearrange("p (h c) -> p h c", h=VH), AX.X, ALU.add))
                    dve.tensor_scalar(ss[:, i], ss[:, i], 1.0 / P, None, ALU.mult).then_inc(squared, 1)
                    dve.wait_ge(rooted, i + 1)
                    step(dve.tensor_tensor(rows, rows, ss[:, i].unsqueeze(2).to_broadcast([P, VH, P]), ALU.mult))
                    dve.tensor_tensor(rows, rows, gs[:].unsqueeze(1).to_broadcast([P, VH, P]), ALU.mult).then_inc(rows_done, 1)


def spatial_gating(nc, d):
    G = 8
    with phase(nc, "z_loaded", "small_loaded", "gelu_done", "averaged", "rooted", "v_done", "mixed", "bank_free",
               "turned", "copied", "stored0", "stored1", "pool_steps", "dve_steps") as (
            z_loaded, small_loaded, gelu_done, averaged, rooted, v_done, mixed, bank_free, turned, copied, stored0,
            stored1, pool_steps, dve_steps), ExitStack() as ctx:
        sb, ps = tensors(nc, ctx)
        z = sb("sg_z", [P, TT, 2 * D])
        ws = sb("sg_ws", [P, G, P])
        bs = sb("sg_bs", [P, G])
        gv = sb("sg_g", [P, D])
        bv = sb("sg_b", [P, D])
        s = sb("sg_s", [P, TT, D])
        st = sb("sg_st", [P, TT, 2, 6])
        mv = sb("sg_mv", [P, TT, 2])
        rs = sb("sg_rs", [P, TT])
        mhalf = sb("sg_mhalf", [P, 1])
        ident = sb("sg_ident", [P, P])
        sT = sb("sg_sT", [P, 2, KD, P])
        mix = ps("sg_mix", [P, 4, TT, P])
        acc = ps("sg_acc", [P, 2, KD, P])
        with nc.Block() as block:
            @block.sync
            def _(sp):
                sp.dma_start(z[:], d["zg"].rearrange("(t p) n -> p t n", p=P)[:, :, 0:2 * D]).then_inc(z_loaded, 16)
                sp.dma_start(ws[:], d["sgu_wT"]).then_inc(small_loaded, 16)
                sp.dma_start(bs[:], d["sgu_bT"]).then_inc(small_loaded, 16)
                sp.dma_start(gv[:], over_partitions(d["sgu_ln_g"])).then_inc(small_loaded, 16)
                sp.dma_start(bv[:], over_partitions(d["sgu_ln_b"])).then_inc(small_loaded, 16)
                sp.dma_start(ident[:], d["ident"]).then_inc(small_loaded, 16)
                out = d["sT"].rearrange("(k p) t -> p k t", p=P)
                for i in range(TT):
                    sp.wait_ge(copied, i + 1)
                    sp.dma_start(out[:, :, i * P:(i + 1) * P], sT[:, i % 2]).then_inc((stored0, stored1)[i % 2], 16)
                sp.wait_ge(stored0, 32)
                sp.wait_ge(stored1, 32)

            @block.scalar
            def _(act):
                act.wait_ge(z_loaded, 16)
                for i in range(TT):
                    act.activation(z[:, i], z[:, i], ACT.Gelu).then_inc(gelu_done, 1)
                for i in range(TT):
                    act.wait_ge(turned, i + 1)
                    if i >= 2:
                        act.wait_ge((stored0, stored1)[i % 2], 16)
                    act.activation(sT[:, i % 2], acc[:, i % 2], ACT.Copy).then_inc(copied, 1)

            @block.gpsimd
            def _(pool):
                steps = Steps(pool, pool_steps)
                steps(pool.memset(mhalf[:], -0.5))
                for i in range(TT):
                    pool.wait_ge(averaged, i + 1)
                    root_reciprocal(pool, steps, rs[:, i:i + 1], mv[:, i, 1:2], 1e-5, mhalf[:]).then_inc(rooted, 1)

            @block.vector
            def _(dve):
                step = Steps(dve, dve_steps)
                dve.wait_ge(small_loaded, 80)
                for i in range(TT):
                    dve.wait_ge(gelu_done, i + 1)
                    v = z[:, i, D:2 * D]
                    for h in range(2):
                        step(dve.bn_stats(st[:, i, h, :], v[:, h * W:(h + 1) * W]), wait=False)
                    step.wait()
                    dve.bn_aggr(mv[:, i, :], st[:, i].rearrange("p s c -> p (s c)")).then_inc(averaged, 1)
                    dve.wait_ge(rooted, i + 1)
                    step(dve.tensor_scalar(v, v, mv[:, i, 0:1], rs[:, i:i + 1], ALU.subtract, ALU.mult))
                    step(dve.tensor_tensor(v, v, gv[:], ALU.mult))
                    dve.tensor_tensor(v, v, bv[:], ALU.add).then_inc(v_done, 1)
                for g in range(G):
                    cols = slice(g * P, (g + 1) * P)
                    dve.wait_ge(mixed, g + 1)
                    dve.scalar_tensor_tensor(s[:, :, cols], mix[:, g % 4], bs[:, g:g + 1], z[:, :, cols], ALU.add,
                                             ALU.mult).then_inc(bank_free, 1)

            @block.tensor
            def _(pe):
                pe.wait_ge(small_loaded, 80)
                pe.wait_ge(v_done, TT)
                for g in range(G):
                    if g >= 4:
                        pe.wait_ge(bank_free, g - 3)
                    pe.matmul(mix[:, g % 4], ws[:, g, :], z[:, :, D + g * P:D + (g + 1) * P], start=True,
                              stop=True).then_inc(mixed, 1)
                pe.wait_ge(bank_free, G)
                transpose_out(pe, TT, lambda i: s[:, i], bank_free, ident, acc, copied, turned)


def combine_branches(nc, d):
    with phase(nc, "loaded", "small_loaded", "biased", "sig_done", "rows_done", "turned", "copied", "stored0",
               "stored1", "dve_steps") as (loaded, small_loaded, biased, sig_done, rows_done, turned, copied, stored0,
                                           stored1, dve_steps), ExitStack() as ctx:
        sb, ps = tensors(nc, ctx)
        gl = sb("cb_gl", [P, TT, 2 * D])
        y = sb("cb_y", [P, 2, TT, D])
        bg = sb("cb_bg", [P, 2 * D])
        ident = sb("cb_ident", [P, P])
        yT = sb("cb_yT", [P, 2, KD, P])
        acc = ps("cb_acc", [P, 2, KD, P])
        with nc.Block() as block:
            @block.sync
            def _(sp):
                sp.dma_start(gl[:], d["zg"].rearrange("(t p) n -> p t n", p=P)[:, :, 2 * D:4 * D]).then_inc(small_loaded, 16)
                sp.dma_start(bg[:], over_partitions(d["b_gate"])).then_inc(small_loaded, 16)
                sp.dma_start(ident[:], d["ident"]).then_inc(small_loaded, 16)
                sp.dma_start(y[:, 0], d["ya"].rearrange("(t p) n -> p t n", p=P)).then_inc(loaded, 16)
                sp.dma_start(y[:, 1], d["ys"].rearrange("(t p) n -> p t n", p=P)).then_inc(loaded, 16)
                out = d["yT"].rearrange("(k p) t -> p k t", p=P)
                for i in range(TT):
                    sp.wait_ge(copied, i + 1)
                    sp.dma_start(out[:, :, i * P:(i + 1) * P], yT[:, i % 2]).then_inc((stored0, stored1)[i % 2], 16)
                sp.wait_ge(stored0, 32)
                sp.wait_ge(stored1, 32)

            @block.scalar
            def _(act):
                for i in range(TT):
                    act.wait_ge(biased, i + 1)
                    act.activation(gl[:, i], gl[:, i], ACT.Sigmoid).then_inc(sig_done, 1)
                for i in range(TT):
                    act.wait_ge(turned, i + 1)
                    if i >= 2:
                        act.wait_ge((stored0, stored1)[i % 2], 16)
                    act.activation(yT[:, i % 2], acc[:, i % 2], ACT.Copy).then_inc(copied, 1)

            @block.vector
            def _(dve):
                step = Steps(dve, dve_steps)
                dve.wait_ge(small_loaded, 48)
                for i in range(TT):
                    dve.tensor_tensor(gl[:, i], gl[:, i], bg[:], ALU.add).then_inc(biased, 1)
                dve.wait_ge(loaded, 32)
                for i in range(TT):
                    dve.wait_ge(sig_done, i + 1)
                    for b in range(2):
                        step(dve.tensor_tensor(y[:, b, i], y[:, b, i], gl[:, i, b * D:(b + 1) * D], ALU.mult), wait=False)
                    step.wait()
                    dve.tensor_tensor(y[:, 0, i], y[:, 0, i], y[:, 1, i], ALU.add).then_inc(rows_done, 1)

            @block.tensor
            def _(pe):
                pe.wait_ge(small_loaded, 48)
                transpose_out(pe, TT, lambda i: y[:, 0, i], rows_done, ident, acc, copied, turned)
PH = 8
TK = 16
NK = 128
HK = PH * TK
SEG = 2 * PH
LOW = -3.0e38


def expert_choice(nc, d):
    with phase(nc, "row0_loaded", "row1_loaded", "row2_loaded", "row3_loaded", "small_loaded", "squared", "rooted",
               "turned", "turn_copied", "scores_done", "scores_copied", "topk_done", "hot_ready", "hot_scaled", "maxed",
               "exp_done", "sel_ready", "sel_turned", "sel_copied", "stored", "pool_steps", "dve_steps") as (
            row0_loaded, row1_loaded, row2_loaded, row3_loaded, small_loaded, squared, rooted, turned, turn_copied,
            scores_done, scores_copied, topk_done, hot_ready, hot_scaled, maxed, exp_done, sel_ready, sel_turned,
            sel_copied, stored, pool_steps, dve_steps), ExitStack() as ctx:
        sb, ps = tensors(nc, ctx)
        q = sb("ec_q", [P, TT, SEG, NK])
        junk = sb("ec_junk", [P, SEG, NK])
        ss = sb("ec_ss", [P, TT, SEG])
        mhalf = sb("ec_mhalf", [P, SEG])
        keys = sb("ec_keys", [P, 2, NK])
        ident = sb("ec_ident", [P, P])
        iota = sb("ec_iota", [P, TK])
        qT = sb("ec_qT", [P, SEG, P])
        s = sb("ec_s", [P, 2, SEG, NK])
        s2 = sb("ec_s2", [P, SEG, NK])
        val = sb("ec_val", [P, SEG, TK])
        idx = sb("ec_idx", [P, SEG, TK], U32)
        idxf = sb("ec_idxf", [P, 2, SEG, TK])
        cand = sb("ec_cand", [P, PH, TK, TK])
        cand2 = sb("ec_cand2", [P, PH, TK, TK])
        hot = sb("ec_hot", [P, 2, PH, TK, TK])
        best = sb("ec_best", [P, 2, PH, TK])
        pos = sb("ec_pos", [P, PH, TK], U32)
        part = sb("ec_part", [P, 2, PH, TK], U32)
        partf = sb("ec_partf", [P, 2, PH, TK])
        tot = sb("ec_tot", [P, PH])
        sel = sb("ec_sel", [P, TT, 3, HK])
        selT = sb("ec_selT", [P, 3, T])
        acc = ps("ec_acc", [P, 2, KD, P])
        sc = ps("ec_sc", [P, SEG, NK])
        loaded = (row0_loaded, row1_loaded, row2_loaded, row3_loaded)
        with nc.Block() as block:
            @block.sync
            def _(sp):
                q_rows = d["qp"].rearrange("(t p) (s n) -> p t s n", p=P, n=NK)
                sp.dma_start(q[:, 0], q_rows[:, 0]).then_inc(loaded[0], 16)
                sp.dma_start(ident[:], d["ident"]).then_inc(small_loaded, 16)
                sp.dma_start(keys[:], d["keysT"]).then_inc(small_loaded, 16)
                sp.dma_start(iota[:], d["iota"][:, 0:TK]).then_inc(small_loaded, 16)
                for i in range(1, TT):
                    sp.dma_start(q[:, i], q_rows[:, i]).then_inc(loaded[i], 16)
                sp.wait_ge(sel_copied, 3)
                sp.dma_start(d["sel"].rearrange("c h t -> h c t"), selT[:]).then_inc(stored, 16)
                sp.wait_ge(stored, 16)

            @block.gpsimd
            def _(pool):
                steps = Steps(pool, pool_steps)
                steps(pool.memset(mhalf[:], -0.5))

                def root(i):
                    pool.wait_ge(squared, SEG * (i + 1))
                    root_reciprocal(pool, steps, ss[:, i], ss[:, i], 1e-6, mhalf[:]).then_inc(rooted, 1)

                root(0)
                for i in range(TT):
                    if i + 1 < TT:
                        root(i + 1)
                    for c in range(2):
                        n = 2 * i + c
                        pool.wait_ge(hot_ready, n + 1)
                        keys_at = idxf[:, i % 2].rearrange("p (h s) k -> p h s k", s=2)[:, :, c, :]
                        pool.tensor_tensor(hot[:, c], hot[:, c], keys_at.unsqueeze(2).to_broadcast([P, PH, TK, TK]),
                                           ALU.mult).then_inc(hot_scaled, 1)

            @block.tensor
            def _(pe):
                pe.wait_ge(small_loaded, 48)
                for i in range(TT):
                    pe.wait_ge(loaded[i], 16)
                    for g in range(2):
                        if i:
                            pe.wait_ge(turn_copied, 2 * (i - 1) + g + 1)
                        for k in range(KD):
                            mm = pe.transpose(acc[:, g, k, :], q[:, i, g * KD + k, :], ident[:])
                        mm.then_inc(turned, 1)
                    pe.wait_ge(turn_copied, 2 * (i + 1))
                    if i:
                        pe.wait_ge(scores_copied, i)
                    for g in range(SEG):
                        mm = pe.matmul(sc[:, g, :], qT[:, g, :], keys[:, g % 2, :], start=True, stop=True)
                    mm.then_inc(scores_done, 1)
                pe.wait_ge(sel_ready, TT)
                pe.wait_ge(scores_copied, TT)
                for c in range(3):
                    for i in range(TT):
                        mm = pe.transpose(sc[:, 4 * c + i, :], sel[:, i, c, :], ident[:])
                    mm.then_inc(sel_turned, 1)

            @block.scalar
            def _(act):
                def squares(i):
                    act.wait_ge(loaded[i], 16)
                    for g in range(SEG):
                        if i:
                            act.wait_ge(squared, SEG * (i - 1) + g + 1)
                        act.activation(junk[:, g], q[:, i, g], ACT.Square, scale=NK ** -0.5,
                                       accum_out=ss[:, i, g:g + 1]).then_inc(squared, 1)

                def softmax_exp(i):
                    act.wait_ge(maxed, i + 1)
                    act.activation(best[:, i % 2], best[:, i % 2], ACT.Exp).then_inc(exp_done, 1)

                squares(0)
                for i in range(TT):
                    for g in range(2):
                        act.wait_ge(turned, 2 * i + g + 1)
                        if i:
                            act.wait_ge(scores_done, i)
                        act.activation(qT[:, g * KD:(g + 1) * KD, :], acc[:, g], ACT.Copy).then_inc(turn_copied, 1)
                    act.wait_ge(scores_done, i + 1)
                    act.wait_ge(rooted, i + 1)
                    if i >= 2:
                        act.wait_ge(topk_done, i - 1)
                    for g in range(SEG):
                        ins = act.activation(s[:, i % 2, g], sc[:, g], ACT.Copy, scale=ss[:, i, g:g + 1])
                    ins.then_inc(scores_copied, 1)
                    if i + 1 < TT:
                        squares(i + 1)
                    if i:
                        softmax_exp(i - 1)
                softmax_exp(TT - 1)
                for c in range(3):
                    act.wait_ge(sel_turned, c + 1)
                    act.activation(selT[:, c, :], sc[:, 4 * c:4 * c + 4, :].rearrange("p a b -> p (a b)"),
                                   ACT.Copy).then_inc(sel_copied, 1)

            @block.vector
            def _(dve):
                step = Steps(dve, dve_steps)
                dve.wait_ge(small_loaded, 48)

                def top16(rows, n, values, indices, rest):
                    for g in range(n):
                        step(dve.max(values[:, g, 0:8], rows(g)), wait=False)
                    step.wait()
                    for g in range(n):
                        step(dve.max_index(indices[:, g, 0:8], values[:, g, 0:8], rows(g)), wait=False)
                        step(dve.match_replace(rest(g), values[:, g, 0:8], rows(g), LOW), wait=False)
                    step.wait()
                    for g in range(n):
                        step(dve.max(values[:, g, 8:16], rest(g)), wait=False)
                    step.wait()
                    for g in range(n):
                        step(dve.max_index(indices[:, g, 8:16], values[:, g, 8:16], rest(g)), wait=False)
                    step.wait()

                def finish(i):
                    for c in range(2):
                        dve.wait_ge(hot_scaled, 2 * i + c + 1)
                        step(dve.tensor_reduce(sel[:, i, c, :].rearrange("p (h k) -> p h k", h=PH), hot[:, c], AX.X,
                                               ALU.add), wait=False)
                    dve.wait_ge(exp_done, i + 1)
                    step(dve.tensor_reduce(tot[:], best[:, i % 2], AX.X, ALU.add))
                    step(dve.reciprocal(tot[:], tot[:]))
                    step(dve.tensor_tensor(sel[:, i, 2, :].rearrange("p (h k) -> p h k", h=PH), best[:, i % 2],
                                           tot[:].unsqueeze(2).to_broadcast([P, PH, TK]), ALU.mult))
                    dve.sem_inc(sel_ready, 1)

                for i in range(TT):
                    dve.wait_ge(scores_copied, i + 1)
                    top16(lambda g: s[:, i % 2, g, :], SEG, val, idx, lambda g: s2[:, g, :])
                    dve.sem_inc(topk_done, 1)
                    step(dve.tensor_copy(idxf[:, i % 2], idx[:]), wait=False)
                    v4 = val[:].rearrange("p (h s) k -> p h s k", s=2)
                    step(dve.tensor_tensor(cand[:], v4[:, :, 0, :].unsqueeze(3).to_broadcast([P, PH, TK, TK]),
                                           v4[:, :, 1, :].unsqueeze(2).to_broadcast([P, PH, TK, TK]), ALU.add))
                    if i:
                        finish(i - 1)
                    top = best[:, i % 2]
                    top16(lambda h: cand[:, h].rearrange("p a b -> p (a b)"), PH, top, pos,
                          lambda h: cand2[:, h].rearrange("p a b -> p (a b)"))
                    step(dve.tensor_copy(tot[:], top[:, :, 0]))
                    dve.tensor_tensor(top, top, tot[:].unsqueeze(2).to_broadcast([P, PH, TK]),
                                      ALU.subtract).then_inc(maxed, 1)
                    step(dve.tensor_single_scalar(part[:, 0], pos[:], 4, ALU.logical_shift_right), wait=False)
                    step(dve.tensor_single_scalar(part[:, 1], pos[:], 15, ALU.bitwise_and))
                    step(dve.tensor_copy(partf[:], part[:]))
                    for c in range(2):
                        dve.tensor_tensor(hot[:, c], partf[:, c].unsqueeze(3).to_broadcast([P, PH, TK, TK]),
                                          iota[:].unsqueeze(1).unsqueeze(1).to_broadcast([P, PH, TK, TK]),
                                          ALU.is_equal).then_inc(hot_ready, 1)
                finish(TT - 1)


def expert_gates(nc, d):
    GT = 8
    GP = GT - 1
    RB = 128
    GB = RB // GT
    with phase(nc, "loaded", "hot_ready", "a_ready", "b_ready", "bank_done", "copied", "stored0", "stored1") as (
            loaded, hot_ready, a_ready, b_ready, bank_done, copied, stored0, stored1), ExitStack() as ctx:
        sb, ps = tensors(nc, ctx)
        sel = sb("eg_sel", [P, 3, T])
        iota = sb("eg_iota", [P, NK])
        a = sb("eg_a", [P, 2, GT, NK])
        b = sb("eg_b", [P, 2, GT, NK])
        gates = sb("eg_gates", [P, 2, NK, RB])
        acc = ps("eg_acc", [P, 2, 2, GT // 2, NK])
        stored = (stored0, stored1)
        with nc.Block() as block:
            @block.sync
            def _(sp):
                sp.dma_start(sel[:], d["sel"].rearrange("c h t -> h c t")).then_inc(loaded, 16)
                sp.dma_start(iota[:], d["iota"]).then_inc(loaded, 16)
                out = d["G"].rearrange("i j t -> j i t")
                for r in range(T // RB):
                    sp.wait_ge(copied, 4 + 2 * GB * (r + 1))
                    sp.dma_start(out[:, :, r * RB:(r + 1) * RB], gates[:, r % 2]).then_inc(stored[r % 2], 16)
                sp.wait_ge(stored0, 32)
                sp.wait_ge(stored1, 32)

            @block.vector
            def _(dve):
                dve.wait_ge(loaded, 32)
                with dve.Fori(0, T // (2 * GT)) as i:
                    for u in range(2):
                        dve.wait_ge(bank_done, i * 4 + 2 * u + 2)
                        at = bass.ds(i * (2 * GT) + u * GT, GP)
                        dve.tensor_tensor(a[:, u, 0:GP], iota[:].unsqueeze(1).to_broadcast([P, GP, NK]),
                                          sel[:, 0, at].unsqueeze(2).to_broadcast([P, GP, NK]),
                                          ALU.is_equal).then_inc(hot_ready, 1)
                        at = bass.ds(i * (2 * GT) + (u * GT + GP), 1)
                        dve.tensor_scalar(a[:, u, GP, :], iota[:], sel[:, 0, at], sel[:, 2, at], ALU.is_equal, ALU.mult)
                        at = bass.ds(i * (2 * GT) + u * GT, GT)
                        dve.tensor_tensor(b[:, u], iota[:].unsqueeze(1).to_broadcast([P, GT, NK]),
                                          sel[:, 1, at].unsqueeze(2).to_broadcast([P, GT, NK]),
                                          ALU.is_equal).then_inc(b_ready, 1)

            @block.gpsimd
            def _(pool):
                pool.wait_ge(loaded, 32)
                with pool.Fori(0, T // (2 * GT)) as i:
                    for u in range(2):
                        pool.wait_ge(hot_ready, i * 2 + u + 1)
                        at = bass.ds(i * (2 * GT) + u * GT, GP)
                        pool.tensor_tensor(a[:, u, 0:GP], a[:, u, 0:GP], sel[:, 2, at].unsqueeze(2).to_broadcast([P, GP, NK]),
                                           ALU.mult).then_inc(a_ready, 1)

            @block.tensor
            def _(pe):
                pe.sem_inc(bank_done, 4)
                with pe.Fori(0, T // (2 * GT)) as i:
                    for u in range(2):
                        pe.wait_ge(a_ready, i * 2 + u + 1)
                        pe.wait_ge(b_ready, i * 2 + u + 1)
                        for h in range(2):
                            pe.wait_ge(copied, i * 4 + 2 * u + h + 1)
                            for t in range(GT // 2):
                                mm = pe.matmul(acc[:, u, h, t, :], b[:, u, h * (GT // 2) + t, :],
                                               a[:, u, h * (GT // 2) + t, :], start=True, stop=True)
                            mm.then_inc(bank_done, 1)

            @block.scalar
            def _(act):
                act.sem_inc(copied, 4)
                for r in range(T // RB):
                    if r >= 2:
                        act.wait_ge(stored[r % 2], 16 * (r // 2))
                    rows = gates[:, r % 2].rearrange("p i t -> p t i")
                    with act.Fori(0, GB // 2) as i:
                        for u in range(2):
                            for h in range(2):
                                act.wait_ge(bank_done, i * 4 + (4 + 2 * GB * r + 2 * u + h + 1))
                                act.activation(rows[:, bass.ds(i * (2 * GT) + u * GT + h * (GT // 2), GT // 2), :],
                                               acc[:, u, h], ACT.Copy).then_inc(copied, 1)


def experts(nc, d):
    GI = 4
    NG = NK // GI
    HALVES = D // W
    OB = TT * HALVES
    OPEN = 4
    with phase(nc, "x_loaded", "ug0_loaded", "ug1_loaded", "v_loaded", "x_hi", "x_lo", "u_hi", "u_lo", "v_hi", "v_lo",
               "h_done", "gelu_done", "gated", "act_hi", "act_lo", "out_done", "added", "stored") as (
            x_loaded, ug0_loaded, ug1_loaded, v_loaded, x_hi, x_lo, u_hi, u_lo, v_hi, v_lo, h_done, gelu_done, gated,
            act_hi, act_lo, out_done, added, stored), ExitStack() as ctx:
        sb, ps = tensors(nc, ctx)
        xh = sb("ex_xh", [P, KD, T], F32R)
        xl = sb("ex_xl", [P, KD, T], F32R)
        ut = sb("ex_u", [P, 2, GI, KD, NK])
        uh = sb("ex_uh", [P, 2, KD, NK], F32R)
        ul = sb("ex_ul", [P, 2, KD, NK], F32R)
        vt = sb("ex_v", [P, GI, D])
        vh = sb("ex_vh", [P, GI, D], F32R)
        vl = sb("ex_vl", [P, GI, D], F32R)
        gt = sb("ex_g", [P, 2, GI, T])
        ge = sb("ex_ge", [P, 2, T])
        ag = sb("ex_gated", [P, 2, T])
        ah = sb("ex_ah", [P, GI, T], F32R)
        al = sb("ex_al", [P, GI, T], F32R)
        total = sb("ex_total", [P, TT, D])
        hb = ps("ex_hb", [P, 2, T])
        ob = ps("ex_ob", [P, OPEN, W])
        x = total[:].rearrange("p t n -> p (t n)").rearrange("p (k t) -> p k t", k=KD)
        ug_loaded = (ug0_loaded, ug1_loaded)
        u_in = d["uT"].rearrange("i p k j -> p i (k j)")
        v_in = d["peer_v"].rearrange("(i j) n -> j i n", j=NK)
        g_in = d["G"].rearrange("i j t -> j i t")
        with nc.Block() as block:
            @block.sync
            def _(sp):
                sp.dma_start(x, d["h2T"].rearrange("(k p) t -> p k t", p=P)).then_inc(x_loaded, 16)
                with sp.Fori(0, NG // 2) as i:
                    for u in range(2):
                        keys = bass.ds(i * (2 * GI) + u * GI, GI)
                        sp.wait_ge(u_lo, i * (2 * GI) + (u + 1) * GI)
                        sp.dma_start(ut[:, u].rearrange("p i k j -> p i (k j)"), u_in[:, keys, :]).then_inc(ug_loaded[u], 16)
                        sp.wait_ge(gated, i * (2 * GI) + (u + 1) * GI)
                        sp.dma_start(gt[:, u], g_in[:, keys, :]).then_inc(ug_loaded[u], 16)
                        sp.wait_ge(v_lo, i * (2 * GI) + (u + 1) * GI)
                        sp.dma_start(vt[:], v_in[:, keys, :]).then_inc(v_loaded, 16)
                sp.wait_ge(added, OB * (NG + 1))
                sp.dma_start(d["po"].rearrange("(t p) n -> p t n", p=P), total[:]).then_inc(stored, 16)
                sp.wait_ge(stored, 16)

            @block.tensor
            def _(pe):
                pe.sem_inc(h_done, 2)
                pe.sem_inc(out_done, OB)
                pe.wait_ge(x_lo, 1)
                with pe.Fori(0, NG // 2) as i:
                    for u in range(2):
                        for c in range(GI):
                            key = i * (2 * GI) + (u * GI + c)
                            pe.wait_ge(u_lo, key + (2 * GI + 1))
                            pe.wait_ge(gelu_done, key + 1)
                            for k in range(KD):
                                mm = product3(pe, hb[:, c % 2, :], (uh[:, c % 2, k, :], ul[:, c % 2, k, :]),
                                              (xh[:, k, :], xl[:, k, :]), k == 0, k == KD - 1)
                            mm.then_inc(h_done, 1)
                        for first in range(0, OB, OPEN):
                            for keys in (range(GI - 1), range(GI - 1, GI)):
                                key = i * (2 * GI) + (u * GI + keys[-1])
                                if first == 0:
                                    pe.wait_ge(act_lo, key + 3)
                                    pe.wait_ge(v_lo, key + (GI + 1))
                                for n in range(first, first + OPEN):
                                    t, half = divmod(n, HALVES)
                                    if keys[0] == 0:
                                        pe.wait_ge(added, i * (2 * OB) + (u * OB + n + 1 + OPEN))
                                    for c in keys:
                                        tok, cols = slice(t * P, (t + 1) * P), slice(half * W, (half + 1) * W)
                                        mm = product3(pe, ob[:, n % OPEN, :], (ah[:, c, tok], al[:, c, tok]),
                                                      (vh[:, c, cols], vl[:, c, cols]), c == 0, c == GI - 1)
                                    if keys[-1] == GI - 1:
                                        mm.then_inc(out_done, 1)

            @block.scalar
            def _(act):
                def split_u(i, u, c):
                    key = i * (2 * GI) + (u * GI + c)
                    if c == 0:
                        act.wait_ge(ug_loaded[u], i * 32 + 32)
                    act.wait_ge(h_done, key + 1)
                    act.activation(uh[:, c % 2], ut[:, u, c], ACT.Copy).then_inc(u_hi, 1)

                def pair(i, last):
                    for u in range(2):
                        group = i * 2 + u
                        for c in range(GI):
                            key = i * (2 * GI) + (u * GI + c)
                            if c + 2 < GI:
                                split_u(i, u, c + 2)
                            elif not (last and u == 1):
                                split_u(i + u, 1 - u, c + 2 - GI)
                            act.wait_ge(h_done, key + 3)
                            act.wait_ge(gated, key + (2 * GI - 1))
                            act.activation(ge[:, c % 2, :], hb[:, c % 2, :], ACT.Gelu).then_inc(gelu_done, 1)
                            if c == 0:
                                act.wait_ge(v_loaded, group * 16 + 16)
                                act.wait_ge(out_done, group * OB + OB)
                            act.activation(vh[:, c], vt[:, c], ACT.Copy).then_inc(v_hi, 1)
                            act.wait_ge(gated, key + (2 * GI + 1))
                            act.activation(ah[:, c], ag[:, c % 2], ACT.Copy).then_inc(act_hi, 1)

                act.sem_inc(gelu_done, 2)
                act.wait_ge(x_loaded, 16)
                act.activation(xh[:], x, ACT.Copy).then_inc(x_hi, 1)
                split_u(0, 0, 0)
                split_u(0, 0, 1)
                with act.Fori(0, NG // 2 - 1) as i:
                    pair(i, False)
                pair(NG // 2 - 1, True)

            @block.gpsimd
            def _(pool):
                pool.sem_inc(u_lo, 2 * GI)
                with pool.Fori(0, NG // 2) as i:
                    for u in range(2):
                        for c in range(GI):
                            pool.wait_ge(u_hi, i * (2 * GI) + (u * GI + c + 1))
                            pool.tensor_tensor(ul[:, c % 2], ut[:, u, c], uh[:, c % 2].bitcast(F32),
                                               ALU.subtract).then_inc(u_lo, 1)

            @block.vector
            def _(dve):
                dve.sem_inc(v_lo, GI)
                dve.sem_inc(gated, 2 * GI)
                dve.sem_inc(act_lo, 2)
                dve.wait_ge(x_hi, 1)
                dve.tensor_tensor(xl[:], x, xh[:].bitcast(F32), ALU.subtract).then_inc(x_lo, 1)
                dve.wait_ge(x_lo, 1)
                for n in range(OB):
                    t, half = divmod(n, HALVES)
                    dve.memset(total[:, t, half * W:(half + 1) * W], 0.0).then_inc(added, 1)
                with dve.Fori(0, NG // 2) as i:
                    for u in range(2):
                        dve.wait_ge(ug_loaded[u], i * 32 + 32)
                        for c in range(GI):
                            key = i * (2 * GI) + (u * GI + c)
                            dve.wait_ge(gelu_done, key + 3)
                            dve.wait_ge(act_lo, key + 1)
                            dve.tensor_tensor(ag[:, c % 2], ge[:, c % 2, :], gt[:, u, c, :], ALU.mult).then_inc(gated, 1)
                            dve.wait_ge(v_hi, key + 1)
                            dve.tensor_tensor(vl[:, c], vt[:, c], vh[:, c].bitcast(F32), ALU.subtract).then_inc(v_lo, 1)
                            dve.wait_ge(act_hi, key + 1)
                            dve.tensor_tensor(al[:, c], ag[:, c % 2], ah[:, c].bitcast(F32), ALU.subtract).then_inc(act_lo, 1)
                        for n in range(OB):
                            t, half = divmod(n, HALVES)
                            dve.wait_ge(out_done, i * (2 * OB) + (u * OB + n + 1 + OB))
                            dve.wait_ge(added, i * (2 * OB) + (u * OB + n + 1))
                            cols = total[:, t, half * W:(half + 1) * W]
                            dve.tensor_tensor(cols, cols, ob[:, n % OPEN, :], ALU.add).then_inc(added, 1)
def conv_ffn(nc, d, x_in, w_up, conv_w, conv_b, w_down, y_out):
    C = w_down.shape[0] // P
    DB = C // 2
    wv = w_up.rearrange("(k p) n -> p k n", p=P)
    wd = w_down.rearrange("(c p) n -> p c n", p=P)
    assert C % 2 == 0 and DB % 2 == 1
    with phase(nc, "x_loaded", "c_loaded", "w0_loaded", "w1_loaded", "x_hi", "x_lo", "w_hi", "w_lo", "up_done", "base_done",
               "tap_done", "conv_done", "silu_done", "h_done", "h_hi", "h_lo", "block_done", "bank_done", "act_copied",
               "dve_copied", "stored") as (
            x_loaded, c_loaded, w0_loaded, w1_loaded, x_hi, x_lo, w_hi, w_lo, up_done, base_done, tap_done, conv_done,
            silu_done, h_done, h_hi, h_lo, block_done, bank_done, act_copied, dve_copied, stored), ExitStack() as ctx:
        sb, ps = tensors(nc, ctx)
        xh = sb("ff_xh", [P, KD, T], F32R)
        xl = sb("ff_xl", [P, KD, T], F32R)
        raw = sb("ff_raw", [P, 2, 2, D])
        wh = sb("ff_wh", [P, 2, 2, D], F32R)
        wl = sb("ff_wl", [P, 2, 2, D], F32R)
        cw = sb("ff_cw", [P, 2 * C, 3])
        cb = sb("ff_cb", [P, 2 * C])
        cv = sb("ff_cv", [P, 2, 2, T])
        h = sb("ff_h", [P, 2, T])
        hh = sb("ff_hh", [P, C, T], F32R)
        hl = sb("ff_hl", [P, C, T], F32R)
        acc = ps("ff_acc", [P, 2 * TT, W])
        up = acc[:, 0:4].rearrange("p (u s) t -> p u s t", u=2)
        order = [n for half in (1, 0) for n in range(half * 4, half * 4 + 4)]
        y = raw[:].rearrange("p u s n -> p (u s) n")
        x = hh[:].bitcast(F32)[:, 0:KD]
        w_loaded = (w0_loaded, w1_loaded)

        with nc.Block() as block:
            @block.sync
            def _(sp):
                sp.dma_start(x, x_in.rearrange("(k p) t -> p k t", p=P)).then_inc(x_loaded, 16)
                with sp.Fori(0, DB) as i:
                    for u in range(2):
                        sp.wait_ge(w_lo, i * 2 + u + 1)
                        for s in range(2):
                            sp.dma_start(raw[:, u, s].rearrange("p (k j) -> p k j", k=KD),
                                         wv[:, :, bass.ds(i * (2 * P) + (s * C * P + u * P), P)]).then_inc(w_loaded[u], 16)
                for b in range(DB):
                    sp.wait_ge(w_lo, C + b + 1)
                    for s in range(2):
                        sp.dma_start(raw[:, b % 2, s], wd[:, 2 * b + s]).then_inc(w_loaded[b % 2], 16)
                for t in (2, 3, 0, 1):
                    done = (t + 2) % TT + 1
                    sp.wait_ge(act_copied, done)
                    sp.wait_ge(dve_copied, done)
                    sp.dma_start(y_out[t * P:(t + 1) * P, :], y[:, t]).then_inc(stored, 16)
                sp.wait_ge(stored, 16 * TT)

            @block.tensor
            def _(pe):
                pe.wait_ge(x_lo, 1)
                with pe.Fori(0, C // 2) as i:
                    for u in range(2):
                        pe.wait_ge(w_lo, i * 2 + u + 3)
                        for s in range(2):
                            pe.wait_ge(conv_done, i * 4 + 2 * u + s + 1)
                            for k in range(KD):
                                cols = slice(k * P, (k + 1) * P)
                                mm = product3(pe, up[:, u, s, :], (wh[:, u, s, cols], wl[:, u, s, cols]),
                                              (xh[:, k, :], xl[:, k, :]), k == 0, k == KD - 1)
                            mm.then_inc(up_done, 1)
                for c in range(C):
                    b, s = divmod(c, 2)
                    if s == 0:
                        pe.wait_ge(w_lo, C + b + 3)
                    pe.wait_ge(h_lo, c + 1)
                    for n in order:
                        t, half = divmod(n, 2)
                        if c == 0 and n < 4:
                            pe.wait_ge(conv_done, 2 * C + 4 - 3 + n)
                        tok, cols = slice(t * P, (t + 1) * P), slice(half * W, (half + 1) * W)
                        mm = product3(pe, acc[:, n, :], (hh[:, c, tok], hl[:, c, tok]),
                                      (wh[:, b % 2, s, cols], wl[:, b % 2, s, cols]), c == 0, c == C - 1)
                        if c == C - 1:
                            mm.then_inc(bank_done, 1)
                        elif s == 1 and n == order[-1]:
                            mm.then_inc(block_done, 1)

            @block.scalar
            def _(act):
                def split(count, u):
                    act.wait_ge(w_loaded[u], count * 32)
                    act.activation(wh[:, u], raw[:, u], ACT.Copy).then_inc(w_hi, 1)

                act.dma_start(cw[:], conv_w).then_inc(c_loaded, 16)
                act.dma_start(cb[:], conv_b).then_inc(c_loaded, 16)
                act.wait_ge(x_loaded, 16)
                act.activation(xh[:], x, ACT.Copy).then_inc(x_hi, 1)
                split(1, 0)
                split(1, 1)
                act.wait_ge(c_loaded, 32)
                act.wait_ge(x_lo, 1)
                with act.Fori(0, C // 2) as i:
                    for u in range(2):
                        act.wait_ge(h_done, i * 2 + u + 1)
                        for s in range(2):
                            act.wait_ge(up_done, i * 4 + 2 * u + s + 1)
                            ch = bass.ds(i * 2 + (u + s * C), 1)
                            act.activation(cv[:, u, s, :], up[:, u, s, :], ACT.Identity, bias=cb[:, ch],
                                           scale=cw[:, ch, 2]).then_inc(base_done, 1)
                        split(i + 2, u)
                        act.wait_ge(conv_done, i * 4 + 2 * u + 5)
                        act.activation(cv[:, u, 0, :], cv[:, u, 0, :], ACT.Silu).then_inc(silu_done, 1)
                        act.wait_ge(h_done, i * 2 + u + 3)
                        act.activation(hh[:, bass.ds(i * 2 + u, 1), :].rearrange("p o t -> p (o t)"), h[:, u],
                                       ACT.Copy).then_inc(h_hi, 1)
                for b in range(2, DB):
                    act.wait_ge(block_done, b - 1)
                    split((C + b) // 2 + 1, b % 2)
                for j in range(TT):
                    act.wait_ge(bank_done, 2 * j + 1)
                    act.activation(y[:, order[2 * j] // 2, 0:W], acc[:, order[2 * j], :], ACT.Copy).then_inc(act_copied, 1)

            @block.gpsimd
            def _(pool):
                def split(b, u):
                    pool.wait_ge(w_hi, b + 1)
                    pool.tensor_tensor(wl[:, u], raw[:, u], wh[:, u].bitcast(F32), ALU.subtract).then_inc(w_lo, 1)

                pool.sem_inc(w_lo, 2)
                with pool.Fori(0, (C + DB) // 2) as i:
                    split(i * 2, 0)
                    split(i * 2 + 1, 1)
                split(C + DB - 1, 0)

            @block.vector
            def _(dve):
                dve.sem_inc(conv_done, 4)
                dve.sem_inc(h_done, 2)
                dve.wait_ge(x_hi, 1)
                dve.tensor_tensor(xl[:], x, xh[:].bitcast(F32), ALU.subtract).then_inc(x_lo, 1)
                dve.wait_ge(c_loaded, 32)
                with dve.Fori(0, C // 2) as i:
                    for u in range(2):
                        for s in range(2):
                            dve.wait_ge(base_done, i * 4 + 2 * u + s + 1)
                            ch = bass.ds(i * 2 + (u + s * C), 1)
                            z, b = cv[:, u, s, :], up[:, u, s, :]
                            dve.scalar_tensor_tensor(z[:, 1:T], b[:, 0:T - 1], cw[:, ch, 1], z[:, 1:T], ALU.mult,
                                                     ALU.add).then_inc(tap_done, 1)
                            dve.wait_ge(tap_done, i * 4 + 2 * u + s + 1)
                            dve.scalar_tensor_tensor(z[:, 2:T], b[:, 0:T - 2], cw[:, ch, 0], z[:, 2:T], ALU.mult,
                                                     ALU.add).then_inc(conv_done, 1)
                        dve.wait_ge(conv_done, i * 4 + 2 * u + 6)
                        dve.wait_ge(silu_done, i * 2 + u + 1)
                        dve.tensor_tensor(h[:, u], cv[:, u, 0, :], cv[:, u, 1, :], ALU.mult).then_inc(h_done, 1)
                        dve.wait_ge(h_hi, i * 2 + u + 1)
                        chunk = bass.ds(i * 2 + u, 1)
                        dve.tensor_tensor(hl[:, chunk, :].rearrange("p o t -> p (o t)"), h[:, u],
                                          hh[:, chunk, :].bitcast(F32).rearrange("p o t -> p (o t)"),
                                          ALU.subtract).then_inc(h_lo, 1)
                for j in range(TT):
                    dve.wait_ge(bank_done, 2 * j + 2)
                    dve.tensor_copy(y[:, order[2 * j + 1] // 2, W:D], acc[:, order[2 * j + 1], :]).then_inc(dve_copied, 1)


RC = 64
NC_ = T // RC
LOG_DECAY = -float(np.exp(-0.5))


def rwkv_projections(nc, d):
    with phase(nc, "x_loaded", "small_loaded", "w0_loaded", "w1_loaded", "mixed", "bank_done", "copied", "low_done",
               "low_ready", "array_done", "stored0", "stored1", "act_steps", "dve_steps") as (
            x_loaded, small_loaded, w0_loaded, w1_loaded, mixed, bank_done, copied, low_done, low_ready, array_done,
            stored0, stored1, act_steps, dve_steps), ExitStack() as ctx:
        sb, ps = tensors(nc, ctx)
        x = sb("rp_x", [P, KD, T])
        dx = sb("rp_dx", [P, KD, T])
        xm = sb("rp_xm", [P, 2, KD, T])
        mix = sb("rp_mix", [P, 6, KD])
        wt = sb("rp_w", [P, 2, KD, W])
        low = sb("rp_low", [P, KD, 288])
        up = sb("rp_up", [P, 4, D])
        w0 = sb("rp_w0", [P, 2, KD])
        mid = sb("rp_mid", [P, 2, T])
        out = sb("rp_out", [P, 2, KD, T])
        acc = ps("rp_acc", [P, 6, T])
        lowp = ps("rp_lowp", [P, 2, T])
        w_loaded, stored = (w0_loaded, w1_loaded), (stored0, stored1)
        LOW = {3: [(0, 64, 0)], 4: [(64, 64, 1)], 5: [(128, 128, 2), (256, 32, 3)]}
        with nc.Block() as block:
            @block.sync
            def _(sp):
                sp.dma_start(x[:], d["x2T"].rearrange("(k p) t -> p k t", p=P)).then_inc(x_loaded, 16)
                sp.dma_start(mix[:], d["mix_cols"]).then_inc(x_loaded, 16)
                for b in range(6):
                    if b >= 2:
                        sp.wait_ge(bank_done, 4 * (b - 1))
                    src = d["w_rkv"][b // 2].rearrange("(k p) n -> p k n", p=P)[:, :, (b % 2) * W:(b % 2 + 1) * W]
                    sp.dma_start(wt[:, b % 2], src).then_inc(w_loaded[b % 2], 16)
                    if b == 1:
                        sp.dma_start(w0[:], d["w0a0_cols"]).then_inc(small_loaded, 16)
                        for j, (name, n, at) in enumerate((("w1", 64, 0), ("a1", 64, 64), ("g1", 160, 128))):
                            sp.dma_start(low[:, :, at:at + n], d[name].rearrange("(k p) n -> p k n", p=P)).then_inc(
                                small_loaded, 16)
                        sp.dma_start(up[0:64, 0], d["w2"]).then_inc(small_loaded, 16)
                        sp.dma_start(up[0:64, 1], d["a2"]).then_inc(small_loaded, 16)
                        sp.dma_start(up[:, 2], d["g2"][0:P, :]).then_inc(small_loaded, 16)
                        sp.dma_start(up[0:32, 3], d["g2"][P:160, :]).then_inc(small_loaded, 16)
                for n in range(6):
                    sp.wait_ge(array_done, n + 1)
                    sp.dma_start(d["rkvdag"][n].rearrange("(k p) t -> p k t", p=P), out[:, n % 2]).then_inc(stored[n % 2], 16)
                sp.wait_ge(stored0, 48)
                sp.wait_ge(stored1, 48)

            @block.vector
            def _(dve):
                step = Steps(dve, dve_steps)
                dve.wait_ge(x_loaded, 32)
                step(dve.tensor_scalar(dx[:, :, 0:1], x[:, :, 0:1], -1.0, None, ALU.mult), wait=False)
                step(dve.tensor_tensor(dx[:, :, 1:T], x[:, :, 0:T - 1], x[:, :, 1:T], ALU.subtract))
                for n in range(6):
                    if n >= 2:
                        dve.wait_ge(bank_done, KD * (n - 1))
                    for k in range(KD):
                        dve.scalar_tensor_tensor(xm[:, n % 2, k, :], dx[:, k, :], mix[:, n, k:k + 1], x[:, k, :],
                                                 ALU.mult, ALU.add).then_inc(mixed, 1)

            @block.tensor
            def _(pe):
                for n in range(6):
                    pe.wait_ge(mixed, KD * (n + 1))
                    if n >= 3:
                        pe.wait_ge(small_loaded, 128)
                        if n == 5:
                            pe.wait_ge(low_ready, 2)
                        for s, (col, rank, _) in enumerate(LOW[n]):
                            for k in range(KD):
                                mm = pe.matmul(lowp[0:rank, s, :], low[:, k, col:col + rank], xm[:, n % 2, k, :],
                                               start=(k == 0), stop=(k == KD - 1))
                            mm.then_inc(low_done, 1)
                        pe.wait_ge(low_ready, sum(len(LOW[m]) for m in range(3, n + 1)))
                    for m in range(KD):
                        if n < 3 and m % 4 == 0:
                            pe.wait_ge(w_loaded[m // 4], 16 * (n + 1))
                        o = n * KD + m
                        if o >= 6:
                            pe.wait_ge(copied, o - 5)
                        if n < 3:
                            for k in range(KD):
                                mm = pe.matmul(acc[:, o % 6, :], wt[:, m // 4, k, (m % 4) * P:(m % 4 + 1) * P],
                                               xm[:, n % 2, k, :], start=(k == 0), stop=(k == KD - 1))
                        else:
                            for s, (_, rank, at) in enumerate(LOW[n]):
                                mm = pe.matmul(acc[:, o % 6, :], up[0:rank, at, m * P:(m + 1) * P], mid[0:rank, s, :],
                                               start=(s == 0), stop=(s == len(LOW[n]) - 1))
                        mm.then_inc(bank_done, 1)

            @block.scalar
            def _(act):
                step = Steps(act, act_steps)
                lows = 0
                for n in range(6):
                    if n >= 3:
                        for s, (_, rank, _) in enumerate(LOW[n]):
                            lows += 1
                            act.wait_ge(low_done, lows)
                            if n > 3:
                                act.wait_ge(bank_done, KD * n)
                            act.activation(mid[0:rank, s, :], lowp[0:rank, s, :],
                                           (ACT.Tanh, ACT.Copy, ACT.Sigmoid)[n - 3]).then_inc(low_ready, 1)
                    if n >= 2:
                        act.wait_ge(stored[n % 2], 16 * (n // 2))
                    if n == 3:
                        act.wait_ge(small_loaded, 128)
                    for m in range(KD):
                        o = n * KD + m
                        act.wait_ge(bank_done, o + 1)
                        if n in (3, 4):
                            ins = act.activation(out[:, n % 2, m, :], acc[:, o % 6, :], ACT.Sigmoid,
                                                 bias=w0[:, n - 3, m:m + 1])
                        else:
                            ins = act.activation(out[:, n % 2, m, :], acc[:, o % 6, :], ACT.Copy)
                        ins.then_inc(copied, 1)
                    act.wait_ge(copied, KD * (n + 1))
                    if n == 3:
                        step(act.activation(out[:, 1], out[:, 1], ACT.Exp, scale=LOG_DECAY))
                    act.sem_inc(array_done, 1)


def rwkv_prepare(nc, d):
    with phase(nc, "small_loaded", "slot0_loaded", "slot1_loaded", "slot_used", "kk_done", "squared", "summed",
               "rooted", "rk_done", "rk_summed", "out_ready", "stored0", "stored1", "pc_stored",
               "dve_steps", "unit_steps", "parts_done") as (
            small_loaded, slot0_loaded, slot1_loaded, slot_used, kk_done, squared, summed, rooted, rk_done, rk_summed,
            out_ready, stored0, stored1, pc_stored, dve_steps, unit_steps, parts_done), ExitStack() as ctx:
        sb, ps = tensors(nc, ctx)
        a5 = sb("rq_in", [P, 2, 5, T])
        cols = sb("rq_cols", [P, 3, KD])
        start = sb("rq_start", [P, 2, T])
        ones = sb("rq_ones", [P, P])
        w = sb("rq_w", [P, 10, T])
        kk, sq, nrm, kn, b, c, cp, rc, t1, t2 = (w[:, n, :] for n in range(10))
        arbk = sb("rq_arbk", [P, 2, 4, T])
        bonus = sb("rq_bonus", [P, 2, T])
        pc = sb("rq_pc", [P, KD, NC_])
        ssp = ps("rq_ssp", [P, T])
        rkp = ps("rq_rkp", [P, T])
        loaded, stored = (slot0_loaded, slot1_loaded), (stored0, stored1)
        KS = 13
        arrays = d["rkvdag"].rearrange("n (q p) t -> p n q t", p=P)
        with nc.Block() as block:
            @block.sync
            def _(sp):
                sp.dma_start(cols[:], d["k_cols"]).then_inc(small_loaded, 16)
                sp.dma_start(start[:], d["starts"]).then_inc(small_loaded, 16)
                sp.dma_start(ones[:], d["ones64"]).then_inc(small_loaded, 16)
                with sp.Fori(0, KD // 2) as i:
                    for u in range(2):
                        sp.wait_ge(slot_used, i * 2 + u + 1)
                        q = bass.ds(i * 2 + u, 1)
                        sp.dma_start(a5[:, u], arrays[:, 0:5, q, :].rearrange("p n o t -> p n (o t)")).then_inc(loaded[u], 16)

            @block.scalar
            def _(act):
                act.sem_inc(stored0, 32)
                act.sem_inc(stored1, 32)
                with act.Fori(0, KD // 2) as i:
                    for u in range(2):
                        n = i * 2 + u
                        act.wait_ge(kk_done, n + 1)
                        act.activation(sq, kk, ACT.Square).then_inc(squared, 1)
                        act.wait_ge(summed, n + 1)
                        act.activation(nrm, ssp[:], ACT.Sqrt).then_inc(rooted, 1)
                        act.wait_ge(out_ready, n + 1)
                        q = bass.ds(n, 1)
                        act.dma_start(d["arbk"][q].rearrange("o p c t -> p (o c) t"), arbk[:, u]).then_inc(stored[u], 16)
                        act.dma_start(d["bonus"].rearrange("(q p) t -> p q t", p=P)[:, q, :].rearrange(
                            "p o t -> p (o t)"), bonus[:, u]).then_inc(stored[u], 16)
                act.dma_start(d["pc"], pc[:]).then_inc(pc_stored, 16)
                act.wait_ge(pc_stored, 16)
                act.wait_ge(stored0, 32 * (KD // 2) + 32)
                act.wait_ge(stored1, 32 * (KD // 2) + 32)

            @block.tensor
            def _(pe):
                pe.wait_ge(small_loaded, 48)
                with pe.Fori(0, KD // 2) as i:
                    for u in range(2):
                        n = i * 2 + u
                        pe.wait_ge(squared, n + 1)
                        pe.matmul(ssp[:], ones[:], sq, start=True, stop=True).then_inc(summed, 1)
                        pe.wait_ge(rk_done, n + 1)
                        pe.matmul(rkp[:], ones[:], t1, start=True, stop=True).then_inc(rk_summed, 1)

            @block.vector
            def _(dve):
                dve.sem_inc(slot_used, 2)
                dve.wait_ge(small_loaded, 48)
                cp64 = cp.rearrange("p (e t) -> p e t", t=RC)
                c64 = c.rearrange("p (e t) -> p e t", t=RC)
                dve.memset(cp, 1.0).then_inc(parts_done, 1)
                dve.wait_ge(parts_done, 1)
                with dve.Fori(0, KD // 2) as i:
                    for u in range(2):
                        n = i * 2 + u
                        q = bass.ds(n, 1)
                        r, k, v, dec, a = (a5[:, u, j, :] for j in range(5))
                        base = n * KS
                        steps = 0

                        def step(ins, wait=True):
                            nonlocal steps
                            ins.then_inc(dve_steps, 1)
                            steps += 1
                            if wait:
                                dve.wait_ge(dve_steps, base + steps)

                        dve.wait_ge(loaded[u], i * 16 + 16)
                        dve.wait_ge(stored[u], i * 32 + 32)
                        dve.tensor_scalar(kk, k, cols[:, 0, q], None, ALU.mult).then_inc(kk_done, 1)
                        step(dve.tensor_scalar(t2, a, -1.0, cols[:, 1, q], ALU.add, ALU.mult), wait=False)
                        step(dve.tensor_tensor(b, dec, start[:, 0], ALU.mult), wait=False)
                        step(dve.tensor_tensor(rc, dec, start[:, 1], ALU.mult))
                        step(dve.scalar_tensor_tensor(kn, t2, 1.0, k, ALU.add, ALU.mult), wait=False)
                        step(dve.tensor_tensor_scan(c, b, rc, 0.0, ALU.mult, ALU.add))
                        step(dve.tensor_tensor(t1, r, kn, ALU.mult), wait=False)
                        step(dve.tensor_copy(cp64[:, :, 1:RC], c64[:, :, 0:RC - 1]), wait=False)
                        step(dve.reciprocal(rc, c))
                        dve.tensor_scalar(t1, t1, cols[:, 2, q], None, ALU.mult).then_inc(rk_done, 1)
                        step(dve.tensor_copy(pc[:, q, :].rearrange("p o (h e) -> p (o e) h", h=2),
                                             c64[:, :, RC - 1].rearrange("p (e h) -> p e h", h=2)), wait=False)
                        step(dve.tensor_tensor(arbk[:, u, 1], r, c, ALU.mult), wait=False)
                        step(dve.tensor_tensor(arbk[:, u, 3], kn, rc, ALU.mult), wait=False)
                        dve.wait_ge(rooted, n + 1)
                        step(dve.tensor_scalar(nrm, nrm, 1e-12, None, ALU.max))
                        step(dve.reciprocal(nrm, nrm))
                        dve.tensor_tensor(kk, kk, nrm, ALU.mult).then_inc(unit_steps, 1)
                        dve.wait_ge(unit_steps, n * 2 + 1)
                        assert steps == KS
                        dve.scalar_tensor_tensor(arbk[:, u, 0], kk, -1.0, cp, ALU.mult, ALU.mult).then_inc(parts_done, 1)
                        dve.tensor_tensor(b, kk, a, ALU.mult).then_inc(unit_steps, 1)
                        dve.wait_ge(unit_steps, n * 2 + 2)
                        dve.tensor_tensor(arbk[:, u, 2], b, rc, ALU.mult).then_inc(parts_done, 1)
                        dve.wait_ge(rk_summed, n + 1)
                        dve.tensor_tensor(bonus[:, u], rkp[:], v, ALU.mult).then_inc(parts_done, 1)
                        dve.wait_ge(parts_done, n * 3 + 4)
                        dve.sem_inc(out_ready, 1)
                        dve.sem_inc(slot_used, 1)
def rwkv_chunks(nc, d, gt, hs, pc):
    NP = 2 * TT
    LEVELS = 5
    with phase(nc, "small_loaded", "slot0_loaded", "slot1_loaded", "slot_used", "ba_done", "ba_masked", "ka_done",
               "ka_masked", "l_done", "x_ready", "xt_ready", "rows_turned", "rows_copied", "em_ready", "w_done",
               "w_copied", "d_done", "x_added", "mv_done", "mv_copied", "rhs_ready", "az_done", "pads_ready", "pairs_ready", "r_done",
               "y_done", "g_done", "h_done", "r_ready", "y_ready", "g_masked", "h_scaled", "gh_finished", "stored0",
               "stored1", "dve_steps", "pool_steps") as (
            small_loaded, slot0_loaded, slot1_loaded, slot_used, ba_done, ba_masked, ka_done, ka_masked, l_done,
            x_ready, xt_ready, rows_turned, rows_copied, em_ready, w_done, w_copied, d_done, x_added, mv_done, mv_copied,
            rhs_ready, az_done, pads_ready, pairs_ready, r_done, y_done, g_done, h_done, r_ready, y_ready, g_masked,
            h_scaled, gh_finished, stored0, stored1, dve_steps, pool_steps), ExitStack() as ctx:
        sb, ps = tensors(nc, ctx)
        ar = sb("rc_ar", [P, 2, 2, T])
        bk = sb("rc_bk", [P, 2, 2, T])
        vT = sb("rc_vT", [P, 2, T])
        mask2 = sb("rc_mask2", [P, 2, P])
        lmask = sb("rc_lmask", [P, 2, P])
        emask = sb("rc_emask", [P, LEVELS, P])
        bd = sb("rc_bd", [P, P])
        ident = sb("rc_ident", [P, P])
        ba = sb("rc_ba", [P, NP, 2, P])
        ka = sb("rc_ka", [P, NP, 2, P])
        xx = sb("rc_xx", [P, 2, NP, P])
        em = sb("rc_em", [P, LEVELS, NP, P])
        ws = sb("rc_ws", [P, NP, P])
        rows = sb("rc_rows", [P, 4, TT, P])
        rhs = sb("rc_rhs", [P, NP, 2, RC])
        apad = sb("rc_apad", [P, TT, 2, P])
        zpad = sb("rc_zpad", [P, TT, 2, P])
        vpad = sb("rc_vpad", [P, TT, 2, P])
        apair = sb("rc_apair", [P, TT, P])
        zpair = sb("rc_zpair", [P, TT, P])
        ry = sb("rc_ry", [P, 2, 2, T])
        lo = ps("rc_lo", [P, 4, W])
        hi = ps("rc_hi", [P, 4, W])
        loaded, stored = (slot0_loaded, slot1_loaded), (stored0, stored1)

        def banks(t, first, count, **dims):
            return t[:, first:first + count, :].rearrange("p b w -> p (b w)")

        lo_ba = banks(lo, 0, 4).rearrange("p (n s t) -> p n s t", n=NP, s=2)
        hi_ka = banks(hi, 0, 4).rearrange("p (n s t) -> p n s t", n=NP, s=2)
        lo_l = banks(lo, 0, 2).rearrange("p (n t) -> p n t", n=NP)
        lo_w = banks(lo, 2, 2).rearrange("p (n t) -> p n t", n=NP)
        hi_rows = banks(hi, 0, 4).rearrange("p (a i t) -> p a i t", a=4, i=TT)
        hi_d = [banks(hi, 2 * c, 2).rearrange("p (x n t) -> p x n t", x=2, n=TT) for c in range(2)]
        lo_mv = banks(lo, 0, 1).rearrange("p (n t) -> p n t", n=NP)
        hi_az = banks(hi, 0, 2).rearrange("p (n s t) -> p n s t", n=NP, s=2)
        lo_r = banks(lo, 1, 1).rearrange("p (i t) -> p i t", i=TT)
        lo_y = banks(lo, 2, 1).rearrange("p (i t) -> p i t", i=TT)
        hi_g = banks(hi, 2, 2).rearrange("p (e t) -> p e t", e=NC_)
        hi_h = banks(hi, 0, 2).rearrange("p (e t) -> p e t", e=NC_)
        problems = [(c * TT + i, i, c) for i in range(TT) for c in range(2)]
        chunks = [((e % 2) * TT + e // 2, e // 2, slice(RC * (e % 2), RC * (e % 2) + RC)) for e in range(NC_)]

        def of_head(c):
            return range(TT * c, TT * c + TT)

        def heads(t):
            return [t[:, :, c, RC * c:RC * c + RC] for c in range(2)]

        with nc.Block() as block:
            @block.sync
            def _(sp):
                sp.dma_start(mask2[:], d["mask2"]).then_inc(small_loaded, 16)
                sp.dma_start(lmask[:], d["lmask"]).then_inc(small_loaded, 16)
                sp.dma_start(emask[:], d["emask"]).then_inc(small_loaded, 16)
                sp.dma_start(bd[:], d["ones64"]).then_inc(small_loaded, 16)
                sp.dma_start(ident[:], d["ident"]).then_inc(small_loaded, 16)
                sp.dma_start(pc[:], d["pc"]).then_inc(small_loaded, 16)
                src = d["arbk"].rearrange("q p c t -> p q c t")
                v_src = d["rkvdag"][2].rearrange("(q p) t -> p q t", p=P)
                with sp.Fori(0, KD // 2) as i:
                    for u in range(2):
                        sp.wait_ge(slot_used, i * 2 + u + 1)
                        q = bass.ds(i * 2 + u, 1)
                        sp.dma_start(ar[:, u], src[:, q, 0:2, :].rearrange("p o c t -> p (o c) t")).then_inc(loaded[u], 16)
                        sp.dma_start(bk[:, u], src[:, q, 2:4, :].rearrange("p o c t -> p (o c) t")).then_inc(loaded[u], 16)
                        sp.dma_start(vT[:, u], v_src[:, q, :].rearrange("p o t -> p (o t)")).then_inc(loaded[u], 16)

            @block.tensor
            def _(pe):
                pe.wait_ge(small_loaded, 96)
                with pe.Fori(0, KD // 2) as i2:
                    for u in range(2):
                        n = i2 * 2 + u
                        pe.wait_ge(loaded[u], i2 * 48 + 48)
                        pe.wait_ge(y_ready, n + 1)
                        pe.wait_ge(r_ready, n + 1)
                        for p, i, c in problems:
                            h, t = slice(RC * c, RC * c + RC), slice(i * P, (i + 1) * P)
                            mm = pe.matmul(lo_ba[:, p], bk[h, u, 0, t], ar[h, u, :, t], start=True, stop=True)
                        mm.then_inc(ba_done, 1)
                        pe.wait_ge(h_scaled, n + 1)
                        pe.wait_ge(g_masked, n + 1)
                        for p, i, c in problems:
                            h, t = slice(RC * c, RC * c + RC), slice(i * P, (i + 1) * P)
                            mm = pe.matmul(hi_ka[:, p], bk[h, u, 1, t], ar[h, u, :, t], start=True, stop=True)
                        mm.then_inc(ka_done, 1)
                        pe.wait_ge(ba_masked, n + 1)
                        for p, i, c in problems:
                            h, t = slice(RC * c, RC * c + RC), slice(i * P, (i + 1) * P)
                            mm = pe.matmul(lo_l[:, p], ar[h, u, 0, t], bk[h, u, 0, t], start=True, stop=True)
                        mm.then_inc(l_done, 1)
                        pe.wait_ge(ka_masked, n + 1)
                        for a, src in enumerate((ar[:, u, 0], bk[:, u, 0], bk[:, u, 1], vT[:, u])):
                            for i in range(TT):
                                mm = pe.transpose(hi_rows[:, a, i, :], src[:, i * P:(i + 1) * P], ident[:])
                        mm.then_inc(rows_turned, 1)
                        pe.wait_ge(x_ready, n + 1)
                        pe.wait_ge(xt_ready, n + 1)
                        for lv in range(LEVELS):
                            for c in range(2):
                                if lv:
                                    pe.wait_ge(x_added, n * (2 * LEVELS) + (2 * lv - 1 + c))
                                if c == 0:
                                    pe.wait_ge(em_ready, n * LEVELS + (lv + 1))
                                for p in of_head(c):
                                    mm = pe.matmul(lo_w[:, p], em[:, lv, p, :], xx[:, 0, p, :], start=True, stop=True)
                                mm.then_inc(w_done, 1)
                            if lv == 0:
                                pe.wait_ge(rows_copied, n + 1)
                            for c in range(2):
                                pe.wait_ge(w_copied, n * (2 * LEVELS) + (2 * lv + c + 1))
                                for p in of_head(c):
                                    if lv < LEVELS - 1:
                                        pe.matmul(hi_d[c][:, 0, p % TT], xx[:, 1, p, :], ws[:, p, :], start=True, stop=True)
                                    mm = pe.matmul(hi_d[c][:, 1, p % TT], ws[:, p, :], xx[:, 1, p, :], start=True,
                                                   stop=True)
                                mm.then_inc(d_done, 1)
                        for p, i, c in problems:
                            mm = pe.matmul(lo_mv[:, p], ka[:, p, 0, :], rows[:, 3, i, RC * c:RC * c + RC], start=True,
                                           stop=True)
                        mm.then_inc(mv_done, 1)
                        pe.wait_ge(x_added, n * (2 * LEVELS) + 2 * LEVELS)
                        pe.wait_ge(rhs_ready, n + 1)
                        pe.wait_ge(mv_copied, n + 1)
                        for p, i, c in problems:
                            mm = pe.matmul(hi_az[:, p], xx[:, 1, p, :], rhs[:, p], start=True, stop=True)
                        mm.then_inc(az_done, 1)
                        pe.wait_ge(pads_ready, n * 4 + 4)
                        for i in range(TT):
                            for c in range(2):
                                mm = pe.matmul(lo_r[:, i], apad[:, i, c, :], ba[:, c * TT + i, 1, :], start=(c == 0),
                                               stop=(c == 1))
                        mm.then_inc(r_done, 1)
                        for i in range(TT):
                            for c in range(2):
                                pe.matmul(lo_y[:, i], zpad[:, i, c, :], ba[:, c * TT + i, 1, :], start=(c == 0), stop=False)
                                mm = pe.matmul(lo_y[:, i], vpad[:, i, c, :], ka[:, c * TT + i, 1, :], start=False,
                                               stop=(c == 1))
                        mm.then_inc(y_done, 1)
                        pe.wait_ge(pairs_ready, n * 2 + 2)
                        for e, i, t in chunks:
                            mm = pe.matmul(hi_g[:, e], apair[t, i, :], rows[t, 1, i, :], start=True, stop=True)
                        mm.then_inc(g_done, 1)
                        for e, i, t in chunks:
                            pe.matmul(hi_h[:, e], rows[t, 1, i, :], zpair[t, i, :], start=True, stop=False)
                            mm = pe.matmul(hi_h[:, e], rows[t, 2, i, :], rows[t, 3, i, :], start=False, stop=True)
                        mm.then_inc(h_done, 1)

            @block.vector
            def _(dve):
                dve.sem_inc(r_ready, 1)
                dve.sem_inc(g_masked, 1)
                dve.sem_inc(h_scaled, 1)
                for pad in (apad, zpad, vpad):
                    dve.memset(pad[:], 0.0).then_inc(dve_steps, 1)
                dve.wait_ge(dve_steps, 3)
                dve.wait_ge(small_loaded, 96)
                with dve.Fori(0, KD // 2) as i2:
                    for u in range(2):
                        n = i2 * 2 + u
                        m2 = mask2[:].unsqueeze(1).to_broadcast([P, NP, 2, P])
                        dve.wait_ge(ba_done, n + 1)
                        dve.tensor_tensor(ba[:], lo_ba, m2, ALU.mult).then_inc(ba_masked, 1)
                        dve.wait_ge(ka_done, n + 1)
                        dve.tensor_tensor(ka[:], hi_ka, m2, ALU.mult).then_inc(ka_masked, 1)
                        dve.wait_ge(ba_masked, n + 1)
                        dve.tensor_tensor(xx[:, 1], ba[:, :, 0, :], lmask[:, 1].unsqueeze(1).to_broadcast([P, NP, P]),
                                          ALU.mult).then_inc(dve_steps, 1)
                        dve.wait_ge(dve_steps, n * 2 + 4)
                        dve.tensor_tensor(xx[:, 1], xx[:, 1], ident[:].unsqueeze(1).to_broadcast([P, NP, P]),
                                          ALU.add).then_inc(xt_ready, 1)
                        dve.wait_ge(l_done, n + 1)
                        dve.tensor_tensor(xx[:, 0], lo_l, lmask[:, 0].unsqueeze(1).to_broadcast([P, NP, P]),
                                          ALU.mult).then_inc(dve_steps, 1)
                        dve.wait_ge(dve_steps, n * 2 + 5)
                        dve.tensor_tensor(xx[:, 0], xx[:, 0], ident[:].unsqueeze(1).to_broadcast([P, NP, P]),
                                          ALU.add).then_inc(x_ready, 1)
                        dve.wait_ge(x_ready, n + 1)
                        dve.wait_ge(xt_ready, n + 1)
                        for lv in range(LEVELS):
                            for c in range(2):
                                if lv:
                                    dve.wait_ge(x_added, n * (2 * LEVELS) + (2 * lv - 1 + c))
                                dve.wait_ge(d_done, n * (2 * LEVELS) + (2 * lv + c + 1))
                                own = slice(TT * c, TT * c + TT)
                                both = slice(0 if lv < LEVELS - 1 else 1, 2)
                                dve.tensor_tensor(xx[:, both, own], xx[:, both, own], hi_d[c][:, both],
                                                  ALU.add).then_inc(x_added, 1)
                        dve.wait_ge(az_done, n + 1)
                        az = hi_az.rearrange("p (c i) s t -> p i c s t", c=2)
                        for c in range(2):
                            dve.tensor_copy(heads(apad)[c], az[:, :, c, 0, :]).then_inc(pads_ready, 1)
                            dve.tensor_copy(heads(zpad)[c], az[:, :, c, 1, :]).then_inc(pads_ready, 1)
                        dve.wait_ge(r_done, n + 1)
                        dve.wait_ge(stored[u], i2 * 32 + 32)
                        dve.tensor_tensor(ry[:, u, 0, :], lo[:, 1, :], ar[:, u, 1, :], ALU.add).then_inc(r_ready, 1)
                        dve.wait_ge(r_ready, n + 2)
                        dve.sem_inc(slot_used, 1)
                        q = bass.ds(n, 1)
                        dve.wait_ge(g_done, n + 1)
                        dve.wait_ge(gh_finished, n * 2 + 1)
                        dve.tensor_tensor(gt[:, q, :, :].rearrange("p o e t -> p (o e) t"), hi_g,
                                          bd[:].unsqueeze(1).to_broadcast([P, NC_, P]), ALU.mult).then_inc(g_masked, 1)
                        dve.wait_ge(h_done, n + 1)
                        dve.tensor_tensor(hs[:, q, :, :].rearrange("p o e t -> p (o e) t"), hi_h,
                                          pc[:, q, :].rearrange("p o e -> p (o e)").unsqueeze(2).to_broadcast([P, NC_, P]),
                                          ALU.mult).then_inc(h_scaled, 1)

            @block.scalar
            def _(act):
                act.sem_inc(y_ready, 1)
                act.sem_inc(stored0, 32)
                act.sem_inc(stored1, 32)
                with act.Fori(0, KD // 2) as i2:
                    for u in range(2):
                        n = i2 * 2 + u
                        act.wait_ge(rows_turned, n + 1)
                        act.activation(rows[:], hi_rows, ACT.Copy).then_inc(rows_copied, 1)
                        for lv in range(LEVELS):
                            for c in range(2):
                                act.wait_ge(w_done, n * (2 * LEVELS) + (2 * lv + c + 1))
                                own = slice(TT * c, TT * c + TT)
                                act.activation(ws[:, own], lo_w[:, own], ACT.Copy).then_inc(w_copied, 1)
                        act.wait_ge(mv_done, n + 1)
                        act.activation(rhs[:, :, 1, :], lo_mv, ACT.Copy).then_inc(mv_copied, 1)
                        act.wait_ge(y_done, n + 1)
                        act.wait_ge(stored[u], i2 * 32 + 32)
                        act.activation(ry[:, u, 1, :], lo[:, 2, :], ACT.Copy).then_inc(y_ready, 1)
                        act.wait_ge(y_ready, n + 2)
                        act.wait_ge(r_ready, n + 2)
                        q = bass.ds(n, 1)
                        for j in range(2):
                            act.dma_start(d["ry"][j].rearrange("(q p) t -> p q t", p=P)[:, q, :].rearrange(
                                "p o t -> p (o t)"), ry[:, u, j, :]).then_inc(stored[u], 16)
                act.wait_ge(stored0, 32 * (KD // 2) + 32)
                act.wait_ge(stored1, 32 * (KD // 2) + 32)

            @block.gpsimd
            def _(pool):
                pool.sem_inc(slot_used, 2)
                pool.sem_inc(gh_finished, 1)
                pool.wait_ge(small_loaded, 96)
                with pool.Fori(0, KD // 2) as i2:
                    for u in range(2):
                        n = i2 * 2 + u
                        pool.wait_ge(ba_masked, n + 1)
                        for lv in range(LEVELS):
                            pool.tensor_tensor(em[:, lv], ba[:, :, 0, :], emask[:, lv].unsqueeze(1).to_broadcast([P, NP, P]),
                                               ALU.mult).then_inc(em_ready, 1)
                        pool.wait_ge(dve_steps, 3)
                        pool.wait_ge(rows_copied, n + 1)
                        for c in range(2):
                            pool.tensor_copy(rhs[:].rearrange("p (c i) s t -> p i c s t", c=2)[:, :, c, 0, :],
                                             rows[:, 0, :, RC * c:RC * c + RC]).then_inc(pool_steps, 1)
                            pool.tensor_copy(heads(vpad)[c], rows[:, 3, :, RC * c:RC * c + RC]).then_inc(pool_steps, 1)
                        pool.wait_ge(pool_steps, n * 4 + 4)
                        pool.sem_inc(rhs_ready, 1)
                        pool.wait_ge(pads_ready, n * 4 + 4)
                        for pad, pair in ((apad, apair), (zpad, zpair)):
                            pool.tensor_tensor(pair[:], pad[:, :, 0, :], pad[:, :, 1, :], ALU.add).then_inc(pairs_ready, 1)
                        q = bass.ds(n, 1)
                        g, h = (t[:, q, :, :].rearrange("p o e t -> p (o e) t") for t in (gt, hs))
                        pool.wait_ge(g_masked, n + 2)
                        pool.tensor_tensor(g, g, ident[:].unsqueeze(1).to_broadcast([P, NC_, P]), ALU.add).then_inc(gh_finished, 1)
                        pool.wait_ge(h_scaled, n + 2)
                        pool.tensor_tensor(h, h, bd[:].unsqueeze(1).to_broadcast([P, NC_, P]), ALU.mult).then_inc(gh_finished, 1)


def rwkv_scan(nc, d, gt, hs, pc):
    with phase(nc, "loaded", "late_loaded", "y_done", "y_added", "s_done", "s_scaled", "s_ready", "mu_done", "centred",
               "squared", "var_done", "rooted", "out_ready", "stored", "dve_steps", "norm_steps") as (
            loaded, late_loaded, y_done, y_added, s_done, s_scaled, s_ready, mu_done, centred, squared, var_done,
            rooted, out_ready, stored, dve_steps, norm_steps), ExitStack() as ctx:
        sb, ps = tensors(nc, ctx)
        ry = sb("rs_ry", [P, 2, KD, T])
        s = sb("rs_s", [P, KD, P])
        bonus = sb("rs_bonus", [P, KD, T])
        gate = sb("rs_gate", [P, KD, T])
        cols = sb("rs_cols", [P, 2, KD])
        mean = sb("rs_mean", [P, P])
        eps = sb("rs_eps", [P, 1])
        sq = sb("rs_sq", [P, 2, T])
        nrm = sb("rs_nrm", [P, 2, T])
        yp = ps("rs_yp", [P, KD, RC])
        sp_ = ps("rs_sp", [P, KD, P])
        mp = ps("rs_mp", [P, 2, T])
        vp = ps("rs_vp", [P, 2, T])
        y = ry[:, 1]

        def at(e):
            return (e % 2) * TT + e // 2

        with nc.Block() as block:
            @block.sync
            def _(sp):
                sp.dma_start(ry[:], d["ry"].rearrange("j (q p) t -> p j q t", p=P)).then_inc(loaded, 16)
                sp.dma_start(mean[:], d["mean64"]).then_inc(late_loaded, 16)
                sp.dma_start(cols[:], d["lnx_cols"]).then_inc(late_loaded, 16)
                sp.dma_start(bonus[:], d["bonus"].rearrange("(q p) t -> p q t", p=P)).then_inc(late_loaded, 16)
                sp.dma_start(gate[:], d["rkvdag"][5].rearrange("(q p) t -> p q t", p=P)).then_inc(late_loaded, 16)
                out = d["tmT"].rearrange("(q p) t -> p q t", p=P)
                for q in range(KD):
                    sp.wait_ge(out_ready, q + 1)
                    sp.dma_start(out[:, q, :], y[:, q, :]).then_inc(stored, 16)
                sp.wait_ge(stored, 16 * KD)

            @block.tensor
            def _(pe):
                pe.wait_ge(loaded, 16)
                for e in range(1, NC_):
                    pe.wait_ge(s_ready, e)
                    if e > 1:
                        pe.wait_ge(y_added, e - 1)
                        pe.wait_ge(s_scaled, e - 1)
                    for q in range(KD):
                        mm = pe.matmul(yp[:, q, :], s[:, q, :], ry[:, 0, q, e * RC:(e + 1) * RC], start=True, stop=True)
                    mm.then_inc(y_done, 1)
                    if e < NC_ - 1:
                        for q in range(KD):
                            mm = pe.matmul(sp_[:, q, :], gt[:, q, at(e), :], s[:, q, :], start=True, stop=True)
                        mm.then_inc(s_done, 1)
                pe.wait_ge(late_loaded, 64)
                pe.wait_ge(y_added, NC_ - 1)
                for q in range(KD + 1):
                    if q < KD:
                        if q >= 2:
                            pe.wait_ge(centred, q - 1)
                        pe.matmul(mp[:, q % 2, :], mean[:], y[:, q, :], start=True, stop=True).then_inc(mu_done, 1)
                    if q:
                        pe.wait_ge(squared, q)
                        if q >= 3:
                            pe.wait_ge(rooted, q - 2)
                        pe.matmul(vp[:, (q - 1) % 2, :], mean[:], sq[:, (q - 1) % 2, :], start=True,
                                  stop=True).then_inc(var_done, 1)

            @block.scalar
            def _(act):
                act.wait_ge(dve_steps, 1)
                for q in range(KD):
                    act.wait_ge(centred, q + 1)
                    if q >= 2:
                        act.wait_ge(var_done, q - 1)
                    act.activation(sq[:, q % 2, :], y[:, q, :], ACT.Square).then_inc(squared, 1)
                    act.wait_ge(var_done, q + 1)
                    if q >= 2:
                        act.wait_ge(out_ready, q - 1)
                    act.activation(nrm[:, q % 2, :], vp[:, q % 2, :], ACT.Sqrt, bias=eps[:]).then_inc(rooted, 1)

            @block.vector
            def _(dve):
                dve.memset(eps[:], 64e-5).then_inc(dve_steps, 1)
                dve.wait_ge(loaded, 16)
                dve.tensor_copy(s[:], hs[:, :, 0, :]).then_inc(s_ready, 1)
                for e in range(1, NC_):
                    if e < NC_ - 1:
                        dve.wait_ge(s_done, e)
                        dve.wait_ge(y_done, e)
                        dve.tensor_tensor(s[:], sp_[:], pc[:, :, at(e)].unsqueeze(2).to_broadcast([P, KD, P]),
                                          ALU.mult).then_inc(s_scaled, 1)
                        dve.wait_ge(s_scaled, e)
                        dve.tensor_tensor(s[:], s[:], hs[:, :, at(e), :], ALU.add).then_inc(s_ready, 1)
                    dve.wait_ge(y_done, e)
                    ye = y[:, :, e * RC:(e + 1) * RC]
                    dve.tensor_tensor(ye, ye, yp[:], ALU.add).then_inc(y_added, 1)
                dve.wait_ge(y_added, NC_ - 1)
                dve.wait_ge(late_loaded, 64)
                step = Steps(dve, norm_steps)

                def centre(q):
                    dve.wait_ge(mu_done, q + 1)
                    dve.tensor_tensor(y[:, q, :], y[:, q, :], mp[:, q % 2, :], ALU.subtract).then_inc(centred, 1)

                centre(0)
                for q in range(KD):
                    if q + 1 < KD:
                        centre(q + 1)
                    yq, r = y[:, q, :], nrm[:, q % 2, :]
                    dve.wait_ge(rooted, q + 1)
                    step(dve.reciprocal(r, r))
                    step(dve.tensor_tensor(yq, yq, r, ALU.mult))
                    step(dve.tensor_scalar(yq, yq, cols[:, 0, q:q + 1], cols[:, 1, q:q + 1], ALU.mult, ALU.add))
                    step(dve.tensor_tensor(yq, yq, bonus[:, q, :], ALU.add))
                    dve.tensor_tensor(yq, yq, gate[:, q, :], ALU.mult).then_inc(out_ready, 1)


def rwkv_recurrence(nc, d):
    with ExitStack() as ctx:
        sb, _ = tensors(nc, ctx)
        gt = sb("rr_gt", [P, KD, NC_, P])
        hs = sb("rr_hs", [P, KD, NC_, P])
        pc = sb("rr_pc", [P, KD, NC_])
        rwkv_chunks(nc, d, gt, hs, pc)
        rwkv_scan(nc, d, gt, hs, pc)
AH = 16
IH = 8
QL, KL = 256, 128
DSA_IN = QL + KL + 64 + IH
CHOSEN = 128
MASKED = -1.0e30
TAKEN = -3.0e38


def sparse_projections(nc, d, o):
    M = 640
    with phase(nc, "bias_loaded", "bias_done", "bias_copied", "bias_stored", "x_loaded", "w_loaded", "vec_loaded", "h_done", "h_copied", "summed", "rooted", "rows_done",
               "turned", "turn_copied", "bank_done", "act_copied", "dve_copied", "dve_steps", "pool_steps") as (
            bias_loaded, bias_done, bias_copied, bias_stored, x_loaded, w_loaded, vec_loaded, h_done, h_copied, summed, rooted, rows_done, turned, turn_copied,
            bank_done, act_copied, dve_copied, dve_steps, pool_steps), ExitStack() as ctx:
        sb, ps = tensors(nc, ctx)
        x = sb("sp_x", [P, KD, T])
        win = sb("sp_win", [P, KD, DSA_IN])
        wuq = sb("sp_wuq", [P, 2, D])
        wqi = sb("sp_wqi", [P, 2, IH * 64])
        wuk = sb("sp_wuk", [P, D])
        wuv = sb("sp_wuv", [P, D])
        vec = sb("sp_vec", [P, QL + KL + 128])
        ident = sb("sp_ident", [P, P])
        h = sb("sp_h", [P, TT, DSA_IN])
        ki2 = sb("sp_ki2", [P, TT, 2, 64])
        junk = sb("sp_junk", [P, QL])
        bs = sb("sp_bs", [P, TT, 6])
        mv = sb("sp_mv", [P, TT, 2])
        st = sb("sp_st", [P, TT, 3])
        rt = sb("sp_rt", [P, TT, 3])
        mhalf = sb("sp_mhalf", [P, 2])
        lat = sb("sp_lat", [P, 3, T])
        rb = sb("sp_rb", [32, AH])
        hot = sb("sp_hot", [32, M])
        fb = sb("sp_fb", [AH, M])
        hp = ps("sp_hp", [P, TT, W])
        op = ps("sp_op", [P, 4, W])
        outs = []
        for m in range(KD):
            outs.append(([(wuq[:, k, m * P:(m + 1) * P], lat[:, k, :]) for k in range(2)], o["qT"][:, m, :]))
        for m in range(IH * 64 // P):
            outs.append(([(wqi[:, k, m * P:(m + 1) * P], lat[:, k, :]) for k in range(2)], o["qiT"][:, m, :]))
        for m in range(KD):
            outs.append(([(wuk[:, m * P:(m + 1) * P], lat[:, 2, :])], o["kT"][:, m, :]))
        for i in range(TT):
            for half in range(2):
                outs.append(([(lat[:, 2, i * P:(i + 1) * P], wuv[:, half * W:(half + 1) * W])],
                             o["v"][:, i, half * W:(half + 1) * W]))
        with nc.Block() as block:
            @block.sync
            def _(sp):
                sp.dma_start(rb[:], d["rel_bias"]).then_inc(bias_loaded, 16)
                sp.dma_start(hot[:], d["buckets"]).then_inc(bias_loaded, 16)
                sp.dma_start(x[:], d["x4T"].rearrange("(k p) t -> p k t", p=P)).then_inc(x_loaded, 16)
                sp.dma_start(win[:], d["dsa_w_in"].rearrange("(k p) n -> p k n", p=P)).then_inc(x_loaded, 16)
                sp.dma_start(vec[:], over_partitions(d["dsa_vecs"])).then_inc(vec_loaded, 16)
                sp.dma_start(ident[:], d["ident"]).then_inc(vec_loaded, 16)
                sp.dma_start(wuq[:], d["dsa_w_uq"].rearrange("(k p) n -> p k n", p=P)).then_inc(w_loaded, 16)
                sp.dma_start(wqi[:], d["dsa_w_qidx"].rearrange("(k p) n -> p k n", p=P)).then_inc(w_loaded, 16)
                sp.dma_start(wuk[:], d["dsa_w_uk"]).then_inc(w_loaded, 16)
                sp.dma_start(wuv[:], d["dsa_w_uv"]).then_inc(w_loaded, 16)
                sp.wait_ge(bias_copied, 2)
                sp.dma_start(d["fb"], fb[:].unsqueeze(1).to_broadcast([AH, P, M])).then_inc(bias_stored, 16)
                sp.wait_ge(bias_stored, 16)

            @block.tensor
            def _(pe):
                pe.wait_ge(bias_loaded, 32)
                pe.matmul(op[0:AH, 0, :], rb[:], hot[:, 0:W], start=True, stop=True).then_inc(bias_done, 1)
                pe.matmul(op[0:AH, 1, 0:M - W], rb[:], hot[:, W:M], start=True, stop=True).then_inc(bias_done, 1)
                pe.wait_ge(x_loaded, 32)
                for i in range(TT):
                    for k in range(KD):
                        mm = pe.matmul(hp[:, i, 0:DSA_IN], x[:, k, i * P:(i + 1) * P], win[:, k, :], start=(k == 0),
                                       stop=(k == KD - 1))
                    mm.then_inc(h_done, 1)
                pe.wait_ge(vec_loaded, 32)
                for i in range(TT):
                    pe.wait_ge(rows_done, i + 1)
                    for c, rows in enumerate((h[:, i, 0:P], h[:, i, P:QL], h[:, i, QL:QL + KL],
                                              ki2[:, i].rearrange("p a b -> p (a b)"))):
                        mm = pe.transpose(hp[:, i, c * P:(c + 1) * P], rows, ident[:])
                    mm.then_inc(turned, 1)
                pe.wait_ge(turn_copied, TT)
                pe.wait_ge(w_loaded, 64)
                pe.wait_ge(bias_copied, 2)
                for n, (parts, _) in enumerate(outs):
                    if n >= 4:
                        pe.wait_ge((act_copied, dve_copied)[n % 2], n // 2 - 1)
                    for j, (lhs, rhs) in enumerate(parts):
                        mm = pe.matmul(op[:, n % 4, :], lhs, rhs, start=(j == 0), stop=(j == len(parts) - 1))
                    mm.then_inc(bank_done, 1)

            @block.scalar
            def _(act):
                for i in range(TT):
                    act.wait_ge(h_done, i + 1)
                    act.activation(h[:, i, :], hp[:, i, 0:DSA_IN], ACT.Copy).then_inc(h_copied, 1)
                for i in range(TT):
                    act.wait_ge(turned, i + 1)
                    act.activation(lat[:, :, i * P:(i + 1) * P], hp[:, i, 0:3 * P].rearrange("p (c t) -> p c t", c=3),
                                   ACT.Copy)
                    act.activation(o["kiT"][:, i * P:(i + 1) * P], hp[:, i, 3 * P:4 * P], ACT.Copy).then_inc(turn_copied, 1)
                for n in range(0, len(outs), 2):
                    act.wait_ge(bank_done, n + 1)
                    act.activation(outs[n][1], op[:, n % 4, :], ACT.Copy).then_inc(act_copied, 1)

            @block.gpsimd
            def _(pool):
                steps = Steps(pool, pool_steps)
                steps(pool.memset(mhalf[:], -0.5))
                for i in range(TT):
                    pool.wait_ge(summed, i + 1)
                    steps(root_reciprocal(pool, steps, rt[:, i, 0:2], st[:, i, 0:2], 1e-6, mhalf[:]), wait=False)
                    root_reciprocal(pool, steps, rt[:, i, 2:3], st[:, i, 2:3], 1e-5, mhalf[:, 0:1]).then_inc(rooted, 1)

            @block.vector
            def _(dve):
                step = Steps(dve, dve_steps)
                dve.wait_ge(bias_done, 2)
                dve.tensor_copy(fb[:, 0:W], op[0:AH, 0, :]).then_inc(bias_copied, 1)
                dve.tensor_copy(fb[:, W:M], op[0:AH, 1, 0:M - W]).then_inc(bias_copied, 1)
                dve.wait_ge(vec_loaded, 32)
                for i in range(TT):
                    dve.wait_ge(h_copied, i + 1)
                    cq, ckv, ki = h[:, i, 0:QL], h[:, i, QL:QL + KL], h[:, i, QL + KL:QL + KL + 64]
                    step(dve.tensor_tensor_reduce(junk[:], cq, cq, 1.0 / QL, 0.0, ALU.mult, ALU.add, st[:, i, 0:1]))
                    step(dve.tensor_tensor_reduce(junk[:, 0:KL], ckv, ckv, 1.0 / KL, 0.0, ALU.mult, ALU.add,
                                                  st[:, i, 1:2]), wait=False)
                    step(dve.bn_stats(bs[:, i, :], ki))
                    step(dve.bn_aggr(mv[:, i, :], bs[:, i, :]))
                    dve.tensor_copy(st[:, i, 2:3], mv[:, i, 1:2]).then_inc(summed, 1)
                    step(dve.tensor_scalar(o["wi"][:, i, :], h[:, i, QL + KL + 64:DSA_IN],
                                           IH ** -0.5 * 64 ** -0.5, None, ALU.mult), wait=False)
                    dve.wait_ge(rooted, i + 1)
                    step(dve.scalar_tensor_tensor(cq, cq, rt[:, i, 0:1], vec[:, 0:QL], ALU.mult, ALU.mult), wait=False)
                    step(dve.scalar_tensor_tensor(ckv, ckv, rt[:, i, 1:2], vec[:, QL:QL + KL], ALU.mult, ALU.mult), wait=False)
                    step(dve.tensor_scalar(ki, ki, mv[:, i, 0:1], rt[:, i, 2:3], ALU.subtract, ALU.mult))
                    step(dve.tensor_tensor(ki, ki, vec[:, QL + KL:QL + KL + 64], ALU.mult))
                    for half in range(2):
                        step(dve.tensor_tensor(ki2[:, i, half, :], ki, vec[:, QL + KL + 64:QL + KL + 128], ALU.add), wait=False)
                    step.wait()
                    dve.sem_inc(rows_done, 1)
                for n in range(1, len(outs), 2):
                    dve.wait_ge(bank_done, n + 1)
                    dve.tensor_copy(outs[n][1], op[:, n % 4, :]).then_inc(dve_copied, 1)


def choose_keys(nc, d, o):
    tiles = range(1, TT)
    with phase(nc, "s_done", "relu_done", "scored", "causal", "chain", "masked", "cleared", "all_done") as (
            s_done, relu_done, scored, causal, chain, masked, cleared, all_done), ExitStack() as ctx:
        sb, ps = tensors(nc, ctx)
        r = sb("ck_r", [P, 2, T])
        sc = sb("ck_sc", [P, TT, T])
        top = sb("ck_top", [P, TT, 8])
        sp_ = ps("ck_sp", [P, 4, T])
        order = [(i, h) for i in tiles for h in range(IH)]
        with nc.Block() as block:
            @block.tensor
            def _(pe):
                for n, (i, h) in enumerate(order):
                    if n >= 4:
                        pe.wait_ge(relu_done, n - 3)
                    rows, keys = slice(64 * (h % 2), 64 * (h % 2) + 64), (i + 1) * P
                    pe.matmul(sp_[:, n % 4, 0:keys], o["qiT"][rows, h // 2, i * P:(i + 1) * P], o["kiT"][rows, 0:keys],
                              start=True, stop=True).then_inc(s_done, 1)

            @block.scalar
            def _(act):
                for n, (i, h) in enumerate(order):
                    keys = (i + 1) * P
                    act.wait_ge(s_done, n + 1)
                    if n >= 2:
                        act.wait_ge(scored, n - 1)
                    act.activation(r[:, n % 2, 0:keys], sp_[:, n % 4, 0:keys], ACT.Relu).then_inc(relu_done, 1)

            @block.gpsimd
            def _(pool):
                pool.memset(o["am"][:, 0, :], 0.0).then_inc(cleared, 1)
                pool.wait_ge(cleared, 1)
                first = o["am"][:, 0, 0:P]
                pool.affine_select(out=first, in_=first, compare_op=ALU.is_ge, fill=MASKED, base=0, pattern=[[-1, P]],
                                   channel_multiplier=1).then_inc(cleared, 1)
                for i in tiles:
                    pool.wait_ge(scored, IH * i)
                    last = sc[:, i, i * P:(i + 1) * P]
                    pool.affine_select(out=last, in_=last, compare_op=ALU.is_ge, fill=MASKED, base=0, pattern=[[-1, P]],
                                       channel_multiplier=1).then_inc(causal, 1)

            @block.vector
            def _(dve):
                for n, (i, h) in enumerate(order):
                    keys = (i + 1) * P
                    dve.wait_ge(relu_done, n + 1)
                    if h == 0:
                        ins = dve.tensor_scalar(sc[:, i, 0:keys], r[:, n % 2, 0:keys], o["wi"][:, i, h:h + 1], None, ALU.mult)
                    else:
                        dve.wait_ge(scored, n)
                        ins = dve.scalar_tensor_tensor(sc[:, i, 0:keys], r[:, n % 2, 0:keys], o["wi"][:, i, h:h + 1],
                                                       sc[:, i, 0:keys], ALU.mult, ALU.add)
                    ins.then_inc(scored, 1)
                dve.wait_ge(causal, TT - 1)
                step = Steps(dve, chain)
                for _ in range(CHOSEN // 8):
                    for i in tiles:
                        step(dve.max(top[:, i, :], sc[:, i, 0:(i + 1) * P]), wait=False)
                    step.wait()
                    for i in tiles:
                        rows = sc[:, i, 0:(i + 1) * P]
                        step(dve.match_replace(rows, top[:, i, :], rows, TAKEN), wait=False)
                    step.wait()
                for i in tiles:
                    dve.tensor_scalar(o["am"][:, i, 0:(i + 1) * P], sc[:, i, 0:(i + 1) * P], -2.0e38, MASKED, ALU.is_gt,
                                      ALU.mult).then_inc(masked, 1)


def sparse_attention(nc, d, o):
    SCALE = 64 ** -0.5
    N = AH * TT
    SL = 4
    TURN, PV = 3, 4
    with phase(nc, "bias_loaded", "ident_loaded", "bias_ready", "s_done", "logits_done", "max_done", "exp_done",
               "p_turned", "p_copied", "o_done", "o_scaled", "o_turned", "o_out", "stored0", "stored1",
               "dve_steps") as (
            bias_loaded, ident_loaded, bias_ready, s_done, logits_done, max_done, exp_done, p_turned, p_copied,
            o_done, o_scaled, o_turned, o_out, stored0, stored1, dve_steps), ExitStack() as ctx:
        sb, ps = tensors(nc, ctx)
        tb = sb("sa_tb", [P, AH, T])
        ident = sb("sa_ident", [P, P])
        bm = sb("sa_bm", [P, 2, T])
        lg = sb("sa_lg", [P, SL, T])
        e = sb("sa_e", [P, SL, T])
        eT = sb("sa_eT", [P, SL, T])
        st = sb("sa_st", [P, N, 2])
        rs = sb("sa_rs", [P, N])
        rows = sb("sa_rows", [P, TT, D])
        oT = sb("sa_oT", [P, 2, KD, P])
        sp_ = ps("sa_sp", [P, 2, T])
        tp = ps("sa_tp", [P, 2, T])
        op = ps("sa_op", [P, 2, T])
        rp = ps("sa_rp", [P, KD, P])
        with nc.Block() as block:
            @block.sync
            def _(sp):
                sp.dma_start(ident[:], d["ident"]).then_inc(ident_loaded, 16)
                fb = d["fb"]
                diagonals = bass.AP(fb.tensor, P - 1, [[640 - 1, P], [P * 640, AH], [1, T]])
                sp.dma_start(tb[:], diagonals).then_inc(bias_loaded, 16)
                out = d["doT"].rearrange("(k p) t -> p k t", p=P)
                for i in range(TT):
                    sp.wait_ge(o_out, i + 1)
                    sp.dma_start(out[:, :, i * P:(i + 1) * P], oT[:, i % 2]).then_inc((stored0, stored1)[i % 2], 16)
                sp.wait_ge(stored0, 32)
                sp.wait_ge(stored1, 32)

            @block.gpsimd
            def _(pool):
                pool.wait_ge(bias_loaded, 16)
                for n in range(N):
                    h, i = divmod(n, TT)
                    if n >= 2:
                        pool.wait_ge(logits_done, n - 1)
                    pool.tensor_tensor(bm[:, n % 2, 0:(i + 1) * P], tb[:, h, 384 - i * P:T], o["am"][:, i, 0:(i + 1) * P],
                                       ALU.add).then_inc(bias_ready, 1)

            @block.tensor
            def _(pe):
                pe.wait_ge(ident_loaded, 16)
                for n in range(N + PV):
                    if n < N:
                        h, i = divmod(n, TT)
                        if n >= 2:
                            pe.wait_ge(logits_done, n - 1)
                        r = slice(64 * (h % 2), 64 * (h % 2) + 64)
                        pe.matmul(sp_[:, n % 2, 0:(i + 1) * P], o["qT"][r, h // 2, i * P:(i + 1) * P],
                                  o["kT"][r, h // 2, 0:(i + 1) * P], start=True, stop=True).then_inc(s_done, 1)
                    if TURN <= n < N + TURN:
                        m = n - TURN
                        i = m % TT
                        pe.wait_ge(exp_done, m + 1)
                        if m >= 2:
                            pe.wait_ge(p_copied, m - 1)
                        for c in range(i + 1):
                            mm = pe.transpose(tp[:, m % 2, c * P:(c + 1) * P], e[:, m % SL, c * P:(c + 1) * P], ident[:])
                        mm.then_inc(p_turned, 1)
                    if n >= PV:
                        m = n - PV
                        h, i = divmod(m, TT)
                        pe.wait_ge(p_copied, m + 1)
                        if m >= 2:
                            pe.wait_ge(o_scaled, m - 1)
                        for c in range(i + 1):
                            mm = pe.matmul(op[:, m % 2, 0:64], eT[:, m % SL, c * P:(c + 1) * P],
                                           o["v"][:, c, h * 64:(h + 1) * 64], start=(c == 0), stop=(c == i))
                        mm.then_inc(o_done, 1)
                pe.wait_ge(o_scaled, N)
                for i in range(TT):
                    if i:
                        pe.wait_ge(o_out, i)
                    for c in range(KD):
                        mm = pe.transpose(rp[:, c, :], rows[:, i, c * P:(c + 1) * P], ident[:])
                    mm.then_inc(o_turned, 1)

            @block.vector
            def _(dve):
                step = Steps(dve, dve_steps)

                def scale_o(m):
                    h, i = divmod(m, TT)
                    step(dve.reciprocal(rs[:, m:m + 1], st[:, m, 1:2]))
                    dve.wait_ge(o_done, m + 1)
                    dve.tensor_scalar(rows[:, i, h * 64:(h + 1) * 64], op[:, m % 2, 0:64], rs[:, m:m + 1], None,
                                      ALU.mult).then_inc(o_scaled, 1)

                for n in range(N + PV + 1):
                    if n < N:
                        keys = (n % TT + 1) * P
                        dve.wait_ge(s_done, n + 1)
                        dve.wait_ge(bias_ready, n + 1)
                        if n >= SL:
                            dve.wait_ge(exp_done, n - SL + 1)
                        dve.scalar_tensor_tensor(lg[:, n % SL, 0:keys], sp_[:, n % 2, 0:keys], SCALE,
                                                 bm[:, n % 2, 0:keys], ALU.mult, ALU.add).then_inc(logits_done, 1)
                    if 1 <= n <= N:
                        m = n - 1
                        dve.wait_ge(logits_done, m + 1)
                        dve.tensor_reduce(st[:, m, 0:1], lg[:, m % SL, 0:(m % TT + 1) * P], AX.X, ALU.max,
                                          negate=True).then_inc(max_done, 1)
                    if n > PV:
                        scale_o(n - PV - 1)

            @block.scalar
            def _(act):
                for n in range(N + TURN):
                    if n >= TURN:
                        m = n - TURN
                        keys = (m % TT + 1) * P
                        act.wait_ge(p_turned, m + 1)
                        if m >= SL:
                            act.wait_ge(o_done, m - SL + 1)
                        act.activation(eT[:, m % SL, 0:keys], tp[:, m % 2, 0:keys], ACT.Copy).then_inc(p_copied, 1)
                    if n < N:
                        keys = (n % TT + 1) * P
                        act.wait_ge(max_done, n + 1)
                        if n >= SL:
                            act.wait_ge(p_turned, n - SL + 1)
                        act.activation(e[:, n % SL, 0:keys], lg[:, n % SL, 0:keys], ACT.Exp, bias=st[:, n, 0:1],
                                       accum_out=st[:, n, 1:2]).then_inc(exp_done, 1)
                for i in range(TT):
                    act.wait_ge(o_turned, i + 1)
                    if i >= 2:
                        act.wait_ge((stored0, stored1)[i % 2], 16)
                    act.activation(oT[:, i % 2], rp[:], ACT.Copy).then_inc(o_out, 1)


def sparse_block(nc, d):
    with ExitStack() as ctx:
        sb, _ = tensors(nc, ctx)
        o = {"qT": sb("so_qT", [P, KD, T]), "kT": sb("so_kT", [P, KD, T]), "v": sb("so_v", [P, TT, D]),
             "qiT": sb("so_qiT", [P, IH // 2, T]), "kiT": sb("so_kiT", [P, T]), "wi": sb("so_wi", [P, TT, IH]),
             "am": sb("so_am", [P, TT, T])}
        sparse_projections(nc, d, o)
        choose_keys(nc, d, o)
        sparse_attention(nc, d, o)


def whole_block(nc, d):
    modulation(nc, d)
    premix(nc, d)
    own = d["hT"][:, CTX:LK]
    project(nc, own, (d["w_in"][:, 0:D], d["q"]), (d["w_in"][:, 3 * D:7 * D], d["zg"]))
    project(nc, d["hT"], (d["w_in"][:, D:3 * D], d["kv"]))
    diff_attention(nc, d)
    spatial_gating(nc, d)
    project(nc, d["oT"], (d["w_branch_attn"], d["ya"]))
    project(nc, d["sT"], (d["w_branch_sgu"], d["ys"]))
    combine_branches(nc, d)
    project(nc, d["yT"], (d["w_out"], d["yo"]))
    join_rms(nc, d, "x", "yo", "g_post_mix", 2, "x1", "h2T", "g_pre_ffn", 3)
    project(nc, d["h2T"], (d["peer_w_query"], d["qp"]))
    expert_choice(nc, d)
    expert_gates(nc, d)
    experts(nc, d)
    join_rms(nc, d, "x1", "po", "g_post_ffn", 5, "x2", "x2T")
    rwkv_projections(nc, d)
    rwkv_prepare(nc, d)
    rwkv_recurrence(nc, d)
    project(nc, d["tmT"], (d["w_o"], d["ho"]))
    join_ln(nc, d, "x2", "ho", d["ln_g"][0:1], d["ln_b"][0:1], "x3", "x3T")
    conv_ffn(nc, d, d["x3T"], d["w_up"][0], d["conv_w"][0], d["conv_b"][0], d["w_down"][0], d["f1"])
    join_ln(nc, d, "x3", "f1", d["ln_g"][1:2], d["ln_b"][1:2], "x4", "x4T")
    sparse_block(nc, d)
    project(nc, d["doT"], (d["dsa_w_o"], d["do"]))
    join_ln(nc, d, "x4", "do", d["ln_g"][2:3], d["ln_b"][2:3], "x5", "x5T")
    conv_ffn(nc, d, d["x5T"], d["w_up"][1], d["conv_w"][1], d["conv_b"][1], d["w_down"][1], d["f2"])
    join_ln(nc, d, "x5", "f2", d["ln_g"][3:4], d["ln_b"][3:4], "out")


SCRATCH = {
    "mod": (1, 8 * D), "hT": (D, LK), "q": (T, D), "kv": (LK, 2 * D), "zg": (T, 4 * D), "oT": (D, T), "sT": (D, T),
    "ya": (T, D), "ys": (T, D), "yT": (D, T), "yo": (T, D), "x1": (T, D), "h2T": (D, T), "qp": (T, SEG * NK),
    "sel": (3, HK, T), "G": (NK, NK, T), "po": (T, D), "x2": (T, D), "x2T": (D, T), "rkvdag": (6, D, T),
    "arbk": (KD, P, 4, T), "bonus": (D, T), "pc": (P, KD, NC_), "ry": (2, D, T), "tmT": (D, T), "ho": (T, D),
    "x3": (T, D), "x3T": (D, T), "f1": (T, D), "x4": (T, D), "x4T": (D, T), "fb": (AH, P, 640), "doT": (D, T),
    "do": (T, D), "x5": (T, D), "x5T": (D, T), "f2": (T, D),
}


def constants():
    f = np.float32
    c = {"ident": np.eye(P, dtype=f), "iota": np.tile(np.arange(P, dtype=f), (P, 1))}
    t = np.arange(T)
    inv = f(10000.0) ** (-np.arange(16, dtype=f) / f(16))
    ang = np.concatenate([(t // 64).astype(f)[:, None] * inv, (t % 64).astype(f)[:, None] * inv], 1)
    c["rope"] = np.stack([np.cos(ang), np.sin(ang)]).astype(f).reshape(2, TT, P, 32).transpose(2, 0, 1, 3)
    start = (np.arange(T) % RC == 0).astype(f)
    c["starts"] = np.tile(np.stack([1 - start, start])[None], (P, 1, 1)).astype(f)
    c["ones64"] = np.kron(np.eye(2, dtype=f), np.ones((64, 64), f))
    c["mean64"] = c["ones64"] / f(64)
    s, t = np.arange(P)[:, None], np.arange(P)[None]
    same = s // RC == t // RC
    c["mask2"] = np.stack([(s < t) & same, (s <= t) & same], 1).astype(f)

    def join(m):
        return ((s // (2 * m) == t // (2 * m)) & (s // m < t // m)).astype(f)

    c["lmask"] = np.stack([join(1).T, join(1)], 1)
    c["emask"] = np.stack([join(m) for m in (2, 4, 8, 16, 32)], 1)
    dist = np.maximum(T - 1 - np.arange(640), 0)
    far = 16 + (np.log(np.maximum(dist, 1).astype(f) / f(16)) / f(np.log(8.0)) * f(16)).astype(np.int32)
    c["buckets"] = (np.arange(32)[:, None] == np.where(dist < 16, dist, np.minimum(far, 31))[None]).astype(f)
    return c


def lay_out(a):
    def cols(v):
        return v.reshape(KD, P).T

    out = {
        "x": a["x"][0], "ctx": a["ctx"][0], "w_ada": a["w_ada"][0], "b_ada": a["b_ada"],
        "c_cols": np.stack([cols(a["c"][0]), cols(a["c_ctx"])], 2), "w_in": a["w_in"][0],
        "lambda4": np.concatenate([a["lambda_q1"], a["lambda_k1"], a["lambda_q2"], a["lambda_k2"]], 1),
        "sgu_wT": a["sgu_w"][0].transpose(2, 0, 1), "sgu_bT": a["sgu_b"][0].T,
        "w_branch_attn": a["w_branch_attn"][0], "w_branch_sgu": a["w_branch_sgu"][0], "w_out": a["w_out"][0],
        "peer_w_query": a["peer_w_query"][0], "keysT": a["peer_sub_keys"][0].transpose(2, 0, 1),
        "uT": a["peer_u"][0].reshape(NK, NK, KD, P).transpose(0, 3, 2, 1), "peer_v": a["peer_v"][0],
        "mix_cols": a["rwkv_mix_2"][0].reshape(6, KD, P).transpose(2, 0, 1), "w_rkv": a["rwkv_w_rkv_2"][0],
        "w0a0_cols": np.stack([cols(a["rwkv_w0_2"][0]), cols(a["rwkv_a0_2"][0])], 1),
        "k_cols": np.stack([cols(a["rwkv_k_k_2"][0]), cols(a["rwkv_k_a_2"][0]), cols(a["rwkv_r_k_2"][0].reshape(-1))], 1),
        "lnx_cols": np.stack([cols(a["rwkv_lnx_g_2"][0]), cols(a["rwkv_lnx_b_2"][0])], 1), "w_o": a["rwkv_w_o_2"][0],
        "ln_g": a["ln_g_2"].reshape(4, D), "ln_b": a["ln_b_2"].reshape(4, D),
        "w_up": a["ffn_w_up_2"], "w_down": a["ffn_w_down_2"],
        "conv_w": a["ffn_conv_w_2"].reshape(2, 3, -1, P).transpose(0, 3, 2, 1),
        "conv_b": a["ffn_conv_b_2"].reshape(2, -1, P).transpose(0, 2, 1),
        "dsa_w_in": a["dsa_w_in_2"][0], "dsa_w_uq": a["dsa_w_uq_2"][0], "dsa_w_qidx": a["dsa_w_qidx_2"][0],
        "dsa_vecs": np.concatenate([a["dsa_q_norm_g_2"], a["dsa_kv_norm_g_2"], a["dsa_kidx_g_2"], a["dsa_kidx_b_2"]], 1),
        "dsa_w_uk": a["dsa_w_uk_2"][0].transpose(2, 0, 1).reshape(P, D),
        "dsa_w_uv": a["dsa_w_uv_2"][0].transpose(1, 0, 2).reshape(P, D),
        "dsa_w_o": a["dsa_w_o_2"][0], "rel_bias": a["rel_bias_2"],
    }
    for n in ("w1", "a1", "g1", "w2", "a2", "g2"):
        out[n] = a[f"rwkv_{n}_2"][0]
    for n in ("g_pre_mix", "g_post_mix", "g_pre_ffn", "g_post_ffn", "b_gate", "subln_g", "sgu_ln_g", "sgu_ln_b"):
        out[n] = a[n]
    return out


def kernel(**inputs):
    import concourse.bacc as bacc
    from concourse.bass_utils import run_bass_kernel_spmd as run

    nc = bacc.Bacc("TRN2", target_bir_lowering=False, num_devices=1)
    arrays, d = {}, {}
    sent = {**lay_out({n: np.asarray(v) for n, v in inputs.items()}), **constants()}
    for n, v in sent.items():
        arrays["in_" + n] = np.ascontiguousarray(v)
        d[n] = nc.dram_tensor("in_" + n, v.shape, F32, kind="ExternalInput").ap()
    for n, shape in SCRATCH.items():
        d[n] = nc.dram_tensor("scratch_" + n, list(shape), F32).ap()
    d["out"] = nc.dram_tensor("out_0_dram", (T, D), F32, kind="ExternalOutput").ap()
    whole_block(nc, d)
    r = run(nc, [arrays], core_ids=[0])
    return r.results[0]["out_0_dram"].reshape(1, T, D)
```

```python
from contextlib import ExitStack, contextmanager

import numpy as np

import concourse.bass as bass
from concourse import mybir

F32 = mybir.dt.float32
F32R = mybir.dt.float32r
U32 = mybir.dt.uint32
ALU = mybir.AluOpType
ACT = mybir.ActivationFunctionType
AX = mybir.AxisListType

P = 128
D = 1024
T = 512
CTX = 256
KD = D // P
TT = T // P
W = 512
HEADS = 16
DH = 64
LK = T + CTX
SEM_BASE = 110


@contextmanager
def phase(nc, *names):
    with ExitStack() as ctx:
        sems = [ctx.enter_context(nc.semaphore(n, num=SEM_BASE + i)) for i, n in enumerate(names)]
        yield sems
        nc.all_engine_barrier(sems_to_clear=range(SEM_BASE, SEM_BASE + len(names)))


class Steps:

    def __init__(self, eng, sem):
        self.eng, self.sem, self.n = eng, sem, 0

    def __call__(self, ins, wait=True):
        ins.then_inc(self.sem, 1)
        self.n += 1
        if wait:
            self.eng.wait_ge(self.sem, self.n)

    def wait(self):
        self.eng.wait_ge(self.sem, self.n)


def tensors(nc, ctx):
    def sb(name, shape, dt=F32):
        return ctx.enter_context(nc.sbuf_tensor(name, shape, dt, allow_name_mangling=True))

    def ps(name, shape, dt=F32):
        return ctx.enter_context(nc.psum_tensor(name, shape, dt, allow_name_mangling=True))

    return sb, ps


def root_reciprocal(pool, steps, out, src, eps, mhalf):
    steps(pool.tensor_scalar(out, src, eps, None, ALU.add))
    return pool.tensor_tensor(out, out, mhalf, ALU.pow)


def over_partitions(row):
    return row.to_broadcast([P, row.shape[1]])


def modulation(nc, d, x, rstd):
    tiles = LK // P
    NB, BW = 12, W
    w = d["w_ada"].rearrange("(k p) n -> p k n", p=P)
    with phase(nc, "c_loaded", "silu_done", "w0_loaded", "w1_loaded", "w_used", "bank_done", "added", "stored",
               "rows_loaded", "squared", "pool_steps") as (
            c_loaded, silu_done, w0_loaded, w1_loaded, w_used, bank_done, added, stored, rows_loaded, squared,
            pool_steps), ExitStack() as ctx:
        sb, ps = tensors(nc, ctx)
        cc = sb("ada_c", [P, KD, 2])
        cs = sb("ada_silu", [P, KD, 2])
        wt = sb("ada_w", [P, 2, KD, BW])
        b2 = sb("ada_b", [2, NB * BW])
        rows = sb("ada_rows", [2, NB * BW])
        junk = sb("ada_junk", [P, D])
        ss = sb("ada_ss", [P, tiles])
        mhalf = sb("ada_mhalf", [P, tiles])
        acc = ps("ada_acc", [P, 2, W])
        w_loaded = (w0_loaded, w1_loaded)
        with nc.Block() as block:
            @block.sync
            def _(sp):
                sp.dma_start(cc[:], d["c_cols"]).then_inc(c_loaded, 16)
                sp.dma_start(b2[:], d["b_ada"].to_broadcast([2, NB * BW])).then_inc(c_loaded, 16)
                with sp.Fori(0, NB // 2) as i:
                    for u in range(2):
                        sp.wait_ge(w_used, i * 2 + u + 1)
                        sp.dma_start(wt[:, u], w[:, :, bass.ds(i * (2 * BW) + u * BW, BW)]).then_inc(w_loaded[u], 16)
                sp.wait_ge(added, NB + 2)
                sp.dma_start(d["mod"][0:1, 0:6 * D], rows[0:1, :]).then_inc(stored, 16)
                sp.dma_start(d["mod"][0:1, 6 * D:8 * D], rows[1:2, 0:2 * D]).then_inc(stored, 16)
                sp.wait_ge(stored, 32)

            @block.scalar
            def _(act):
                act.wait_ge(c_loaded, 32)
                act.activation(cs[:], cc[:], ACT.Silu).then_inc(silu_done, 1)
                act.wait_ge(w1_loaded, 16)
                act.dma_start(x[:, 0:CTX // P], d["ctx"].rearrange("(t p) n -> p t n", p=P)).then_inc(rows_loaded, 16)
                act.dma_start(x[:, CTX // P:tiles], d["x"].rearrange("(t p) n -> p t n", p=P)).then_inc(rows_loaded, 16)
                act.wait_ge(rows_loaded, 32)
                for i in range(tiles):
                    if i:
                        act.wait_ge(squared, i)
                    act.activation(junk[:], x[:, i], ACT.Square, scale=D ** -0.5, accum_out=ss[:, i:i + 1]).then_inc(squared, 1)

            @block.gpsimd
            def _(pool):
                steps = Steps(pool, pool_steps)
                steps(pool.memset(mhalf[:], -0.5))
                pool.wait_ge(squared, tiles)
                steps(root_reciprocal(pool, steps, rstd[:], ss[:], 1e-6, mhalf[:]))

            @block.tensor
            def _(pe):
                pe.sem_inc(w_used, 2)
                pe.wait_ge(silu_done, 1)
                with pe.Fori(0, NB // 2) as i:
                    for u in range(2):
                        pe.wait_ge(w_loaded[u], i * 16 + 16)
                        pe.wait_ge(added, i * 2 + u + 1)
                        for k in range(KD):
                            mm = pe.matmul(acc[0:2, u, :], cs[:, k, :], wt[:, u, k, :], start=(k == 0), stop=(k == KD - 1))
                        mm.then_inc(bank_done, 1)
                        pe.wait_ge(bank_done, i * 2 + u + 1)
                        pe.sem_inc(w_used, 1)

            @block.vector
            def _(dve):
                dve.sem_inc(added, 2)
                dve.wait_ge(c_loaded, 32)
                with dve.Fori(0, NB // 2) as i:
                    for u in range(2):
                        dve.wait_ge(bank_done, i * 2 + u + 1)
                        col = bass.ds(i * (2 * BW) + u * BW, BW)
                        dve.tensor_tensor(rows[:, col], acc[0:2, u, :], b2[:, col], ALU.add).then_inc(added, 1)


def product3(pe, out, left, right, start, stop):
    pe.matmul(out, left[0], right[0], start=start, stop=False)
    pe.matmul(out, left[0], right[1], start=False, stop=False)
    return pe.matmul(out, left[1], right[0], start=False, stop=stop)


def split_pair(nc, ctx, name, tokens=T):
    sb, _ = tensors(nc, ctx)
    return tuple(sb(f"{name}_{part}", [P, KD, tokens], F32R) for part in ("hi", "lo"))


def project(nc, xT, split, *products, keep=None):
    xh, xl = split
    _, KC, tokens = xh.shape
    KH = KC // 2
    halves = (slice(0, KH), slice(KH, KC))
    tiles = tokens // P
    sets = 2 if 2 * tiles <= 8 else 1
    parts, NP = [], 0
    for w, out in products:
        n = w.shape[1] // (2 * W)
        parts.append((NP, n, w.rearrange("(k p) n -> p k n", p=P),
                      None if out is None else out.rearrange("(t p) n -> p t n", p=P)))
        NP += n
    assert keep is None or NP == 1
    with phase(nc, "xa_loaded", "xb_loaded", "w0a_loaded", "w0b_loaded", "w1a_loaded", "w1b_loaded", "x_hi", "x_lo",
               "w_hi", "wa_lo", "wb_lo", "block_done", "bank_done", "copied", "stored0", "stored1") as (
            xa_loaded, xb_loaded, w0a_loaded, w0b_loaded, w1a_loaded, w1b_loaded, x_hi, x_lo, w_hi, wa_lo, wb_lo,
            block_done, bank_done, copied, stored0, stored1), ExitStack() as ctx:
        sb, ps = tensors(nc, ctx)
        raw = sb("pr_raw", [P, 2, KC, W])
        wh = sb("pr_wh", [P, 2, KC, W], F32R)
        wl = sb("pr_wl", [P, 2, KC, W], F32R)
        stage = sb("pr_stage", [P, 2, tiles, W]) if keep is None else keep
        acc = ps("pr_acc", [P, sets, tiles, W])
        x = stage[:].rearrange("p u t n -> p (u t n)").rearrange("p (k t) -> p k t", k=KC)
        x_loaded, w_loaded = (xa_loaded, xb_loaded), ((w0a_loaded, w0b_loaded), (w1a_loaded, w1b_loaded))
        w_lo, stored = (wa_lo, wb_lo), (stored0, stored1)
        with nc.Block() as block:
            @block.sync
            def _(sp):
                def load(pair, i, wv, u, h):
                    sp.wait_ge(w_lo[h], pair * 2 + u + 1)
                    sp.dma_start(raw[:, u, halves[h]], wv[:, halves[h], bass.ds(i * (2 * W) + u * W, W)]).then_inc(
                        w_loaded[u][h], 16)

                for h in range(2):
                    if xT is not None:
                        sp.dma_start(x[:, halves[h]], xT.rearrange("(k p) t -> p k t", p=P)[:, halves[h]]).then_inc(
                            x_loaded[h], 16)
                    sp.wait_ge(w_lo[h], 1)
                    sp.dma_start(raw[:, 0, halves[h]], parts[0][2][:, halves[h], 0:W]).then_inc(w_loaded[0][h], 16)
                for h in range(2):
                    sp.wait_ge(w_lo[h], 2)
                    sp.dma_start(raw[:, 1, halves[h]], parts[0][2][:, halves[h], W:2 * W]).then_inc(w_loaded[1][h], 16)
                for before, n, wv, _ in parts:
                    first = int(before == 0)
                    if n > first:
                        with sp.Fori(first, n) as i:
                            for u in range(2):
                                for h in range(2):
                                    load(i + before, i, wv, u, h)

            @block.scalar
            def _(act):
                def hi(pair, u):
                    act.wait_ge(block_done, pair * 2 + u + 1)
                    for h in range(2):
                        act.wait_ge(w_loaded[u][h], pair * 16 + 16)
                        act.activation(wh[:, u, halves[h]], raw[:, u, halves[h]], ACT.Copy).then_inc(w_hi, 1)

                def store(pair, i, rows, u):
                    act.wait_ge(copied, pair * (2 * tiles) + ((u + 1) * tiles + sets * tiles))
                    act.dma_start(rows[:, :, bass.ds(i * (2 * W) + u * W, W)], stage[:, u]).then_inc(stored[u], 16)

                act.sem_inc(stored0, 16)
                act.sem_inc(stored1, 16)
                act.wait_ge(block_done, 1)
                for h in range(2):
                    if xT is not None:
                        act.wait_ge(x_loaded[h], 16)
                        act.activation(xh[:, halves[h]], x[:, halves[h]], ACT.Copy).then_inc(x_hi, 1)
                    act.wait_ge(w_loaded[0][h], 16)
                    act.activation(wh[:, 0, halves[h]], raw[:, 0, halves[h]], ACT.Copy).then_inc(w_hi, 1)
                for before, n, _, rows in parts:
                    loop = n - int(before + n == NP)
                    if loop:
                        with act.Fori(0, loop) as i:
                            hi(i + before, 1)
                            store(i + before, i, rows, 0)
                            hi(i + (before + 1), 0)
                            store(i + before, i, rows, 1)
                hi(NP - 1, 1)
                if keep is None:
                    for u in range(2):
                        store(NP - 1, parts[-1][1] - 1, parts[-1][3], u)
                    act.wait_ge(stored0, 16 * NP + 16)
                    act.wait_ge(stored1, 16 * NP + 16)

            @block.gpsimd
            def _(pool):
                pool.sem_inc(wa_lo, 2)
                with pool.Fori(0, NP) as i:
                    for u in range(2):
                        pool.wait_ge(w_hi, i * 4 + (2 * u + 1))
                        pool.tensor_tensor(wl[:, u, 0:KH], raw[:, u, 0:KH], wh[:, u, 0:KH].bitcast(F32),
                                           ALU.subtract).then_inc(wa_lo, 1)

            @block.tensor
            def _(pe):
                def half(pair, u, h):
                    if xT is not None:
                        pe.wait_ge(x_lo, h + 1)
                    pe.wait_ge(w_lo[h], pair * 2 + (u + 3))
                    for t in range(tiles):
                        if h == 0:
                            pe.wait_ge(copied, pair * (2 * tiles) + (u * tiles + t + 1))
                        tok = slice(t * P, (t + 1) * P)
                        for k in range(h * KH, (h + 1) * KH):
                            mm = product3(pe, acc[:, u % sets, t, :], (xh[:, k, tok], xl[:, k, tok]),
                                          (wh[:, u, k, :], wl[:, u, k, :]), k == 0, k == KC - 1)
                        if h:
                            mm.then_inc(bank_done, 1)

                pe.sem_inc(block_done, 2)
                with pe.Fori(0, NP) as i:
                    for u in range(2):
                        half(i, u, 0)
                        half(i, u, 1)
                        pe.wait_ge(bank_done, i * (2 * tiles) + (u + 1) * tiles)
                        pe.sem_inc(block_done, 1)

            @block.vector
            def _(dve):
                dve.sem_inc(copied, sets * tiles)
                dve.sem_inc(wb_lo, 2)
                if xT is not None:
                    for h in range(2):
                        dve.wait_ge(x_hi, h + 1)
                        dve.tensor_tensor(xl[:, halves[h]], x[:, halves[h]], xh[:, halves[h]].bitcast(F32),
                                          ALU.subtract).then_inc(x_lo, 1)
                    dve.wait_ge(x_lo, 2)
                with dve.Fori(0, NP) as i:
                    for u in range(2):
                        dve.wait_ge(w_hi, i * 4 + (2 * u + 2))
                        dve.tensor_tensor(wl[:, u, KH:KC], raw[:, u, KH:KC], wh[:, u, KH:KC].bitcast(F32),
                                          ALU.subtract).then_inc(wb_lo, 1)
                        dve.wait_ge(stored[u], i * 16 + 16)
                        for t in range(tiles):
                            dve.wait_ge(bank_done, i * (2 * tiles) + u * tiles + t + 1)
                            dve.tensor_copy(stage[:, u, t, :], acc[:, u % sets, t, :]).then_inc(copied, 1)


def transpose_out(pe, tiles, src, ready, ident, acc, copied, done):
    for i in range(tiles):
        pe.wait_ge(ready, i + 1)
        if i >= 2:
            pe.wait_ge(copied, i - 1)
        rows = src(i)
        for k in range(KD):
            mm = pe.transpose(acc[:, i % 2, k, :], rows[:, k * P:(k + 1) * P], ident[:])
        mm.then_inc(done, 1)


def split_lo(dve, split, i, acc, hi_done, copied):
    cols = slice(i * P, (i + 1) * P)
    dve.wait_ge(hi_done, i + 1)
    dve.tensor_tensor(split[1][:, :, cols], acc[:, i % 2], split[0][:, :, cols].bitcast(F32), ALU.subtract).then_inc(copied, 1)


def premix(nc, d, x, rstd, split):
    CT = CTX // P
    tiles = CT + TT
    with phase(nc, "vec_loaded", "ident_loaded", "rows_done", "turned", "hi_done", "copied", "dve_steps") as (
            vec_loaded, ident_loaded, rows_done, turned, hi_done, copied, dve_steps), ExitStack() as ctx:
        sb, ps = tensors(nc, ctx)
        g = sb("pm_g", [P, D])
        gain = sb("pm_gain", [P, 2, D])
        shift = sb("pm_shift", [P, 2, D])
        ident = sb("pm_ident", [P, P])
        h = sb("pm_h", [P, tiles, D])
        acc = ps("pm_acc", [P, 2, KD, P])
        with nc.Block() as block:
            @block.sync
            def _(sp):
                sp.dma_start(ident[:], d["ident"]).then_inc(ident_loaded, 16)
                sp.dma_start(g[:], over_partitions(d["g_pre_mix"])).then_inc(vec_loaded, 16)
                for s, at in enumerate((6, 0)):
                    sp.dma_start(shift[:, s], over_partitions(d["mod"][:, at * D:(at + 1) * D])).then_inc(vec_loaded, 16)
                    sp.dma_start(gain[:, s], over_partitions(d["mod"][:, (at + 1) * D:(at + 2) * D])).then_inc(vec_loaded, 16)

            @block.scalar
            def _(act):
                for i in range(tiles):
                    act.wait_ge(turned, i + 1)
                    act.activation(split[0][:, :, i * P:(i + 1) * P], acc[:, i % 2], ACT.Copy).then_inc(hi_done, 1)

            @block.vector
            def _(dve):
                step = Steps(dve, dve_steps)
                dve.wait_ge(vec_loaded, 80)
                for s in range(2):
                    step(dve.scalar_tensor_tensor(gain[:, s], gain[:, s], 1.0, g[:], ALU.add, ALU.mult))
                for i in range(tiles):
                    s = int(i >= CT)
                    step(dve.scalar_tensor_tensor(h[:, i], x[:, i], rstd[:, i:i + 1], gain[:, s], ALU.mult, ALU.mult))
                    dve.tensor_tensor(h[:, i], h[:, i], shift[:, s], ALU.add).then_inc(rows_done, 1)
                    if i >= 2:
                        split_lo(dve, split, i - 2, acc, hi_done, copied)
                for i in range(tiles - 2, tiles):
                    split_lo(dve, split, i, acc, hi_done, copied)

            @block.tensor
            def _(pe):
                pe.wait_ge(ident_loaded, 16)
                transpose_out(pe, tiles, lambda i: h[:, i], rows_done, ident, acc, copied, turned)


def join_rms(nc, d, x_in, y, g_post, gate_at, x_out, hT_out=None, split=None, g_pre=None, shift_at=None):
    order = [(w, i) for n in range(TT + 2) for w, i in (("y", n), ("x", n - 2)) if 0 <= i < TT and (w == "y" or g_pre)]
    place = {what: n + 1 for n, what in enumerate(order)}
    with phase(nc, "row0_loaded", "row1_loaded", "row2_loaded", "row3_loaded", "vec_loaded", "rows_done", "x_done", "turned",
               "hi_done", "copied", "stored0", "stored1", "x_stored", "summed", "rooted", "pool_steps", "dve_steps") as (
            row0_loaded, row1_loaded, row2_loaded, row3_loaded, vec_loaded, rows_done, x_done, turned, hi_done, copied, stored0,
            stored1, x_stored, summed, rooted, pool_steps, dve_steps), ExitStack() as ctx:
        sb, ps = tensors(nc, ctx)
        x = sb("jr_x", [P, TT, D])
        h = sb("jr_h", [P, TT, D])
        junk = sb("jr_junk", [P, 2 * TT, 2, W])
        st = sb("jr_st", [P, TT, 4])
        mhalf = sb("jr_mhalf", [P, 1])
        gp = sb("jr_gp", [P, D])
        gt = sb("jr_gt", [P, D])
        gain = sb("jr_gain", [P, D])
        shift = sb("jr_shift", [P, D])
        g2 = sb("jr_g2", [P, D])
        ident = sb("jr_ident", [P, P])
        hT = sb("jr_hT", [P, 2, KD, P])
        acc = ps("jr_acc", [P, 2, KD, P])
        loaded = (row0_loaded, row1_loaded, row2_loaded, row3_loaded)

        def halves(rows):
            return rows.rearrange("p (u w) -> p u w", u=2)

        def vec(at):
            return over_partitions(d["mod"][:, at * D:(at + 1) * D])

        with nc.Block() as block:
            @block.sync
            def _(sp):
                for i in range(TT):
                    sp.dma_start(x[:, i], d[x_in][i * P:(i + 1) * P, :]).then_inc(loaded[i], 16)
                for i in range(TT):
                    sp.wait_ge(x_done, i + 1)
                    sp.dma_start(d[x_out][i * P:(i + 1) * P, :], x[:, i]).then_inc(x_stored, 16)
                    if hT_out:
                        sp.wait_ge(copied, i + 1)
                        sp.dma_start(d[hT_out].rearrange("(k p) t -> p k t", p=P)[:, :, i * P:(i + 1) * P],
                                     hT[:, i % 2]).then_inc((stored0, stored1)[i % 2], 16)
                sp.wait_ge(x_stored, 16 * TT)
                if hT_out:
                    sp.wait_ge(stored0, 16 * TT // 2)
                    sp.wait_ge(stored1, 16 * TT // 2)

            @block.scalar
            def _(act):
                def copy_out(i):
                    act.wait_ge(turned, i + 1)
                    if split:
                        act.activation(split[0][:, :, i * P:(i + 1) * P], acc[:, i % 2], ACT.Copy).then_inc(hi_done, 1)
                    else:
                        if i >= 2:
                            act.wait_ge((stored0, stored1)[i % 2], 16 * (i // 2))
                        act.activation(hT[:, i % 2], acc[:, i % 2], ACT.Copy).then_inc(copied, 1)

                act.dma_start(gp[:], over_partitions(d[g_post])).then_inc(vec_loaded, 16)
                act.dma_start(gt[:], vec(gate_at)).then_inc(vec_loaded, 16)
                act.dma_start(ident[:], d["ident"]).then_inc(vec_loaded, 16)
                if g_pre:
                    act.dma_start(g2[:], over_partitions(d[g_pre])).then_inc(vec_loaded, 16)
                    act.dma_start(shift[:], vec(shift_at)).then_inc(vec_loaded, 16)
                    act.dma_start(gain[:], vec(shift_at + 1)).then_inc(vec_loaded, 16)
                for n, (what, i) in enumerate(order):
                    if what == "y":
                        rows, to = y[:, i], st[:, i, 0:1]
                    else:
                        act.wait_ge(x_done, i + 1)
                        rows, to = halves(x[:, i]), st[:, i, 2:3]
                    act.activation(junk[:, n], rows, ACT.Square, scale=D ** -0.5, accum_out=to).then_inc(summed, 1)
                    if what == "x" and i >= 1:
                        copy_out(i - 1)
                for i in range(TT - 1 if g_pre else 0, TT):
                    copy_out(i)

            @block.vector
            def _(dve):
                step = Steps(dve, dve_steps)
                dve.wait_ge(vec_loaded, 96 if g_pre else 48)
                step(dve.tensor_tensor(gt[:], gt[:], gp[:], ALU.mult))
                if g_pre:
                    step(dve.scalar_tensor_tensor(gain[:], gain[:], 1.0, g2[:], ALU.add, ALU.mult))
                for what, i in order:
                    dve.wait_ge(rooted, place[what, i])
                    if what == "y":
                        step(dve.scalar_tensor_tensor(y[:, i], y[:, i], st[:, i, 1:2], halves(gt[:]), ALU.mult, ALU.mult))
                        dve.wait_ge(loaded[i], 16)
                        dve.tensor_tensor(halves(x[:, i]), halves(x[:, i]), y[:, i], ALU.add).then_inc(x_done, 1)
                    else:
                        step(dve.scalar_tensor_tensor(h[:, i], x[:, i], st[:, i, 3:4], gain[:], ALU.mult, ALU.mult))
                        dve.tensor_tensor(h[:, i], h[:, i], shift[:], ALU.add).then_inc(rows_done, 1)
                        if i >= 2:
                            split_lo(dve, split, i - 2, acc, hi_done, copied)
                if split:
                    for i in range(TT - 2, TT):
                        split_lo(dve, split, i, acc, hi_done, copied)

            @block.gpsimd
            def _(pool):
                steps = Steps(pool, pool_steps)
                steps(pool.memset(mhalf[:], -0.5))
                for what, i in order:
                    pool.wait_ge(summed, place[what, i])
                    at = 0 if what == "y" else 2
                    root_reciprocal(pool, steps, st[:, i, at + 1:at + 2], st[:, i, at:at + 1], 1e-6,
                                    mhalf[:]).then_inc(rooted, 1)

            @block.tensor
            def _(pe):
                pe.wait_ge(vec_loaded, 96 if g_pre else 48)
                if g_pre:
                    transpose_out(pe, TT, lambda i: h[:, i], rows_done, ident, acc, copied, turned)
                else:
                    transpose_out(pe, TT, lambda i: x[:, i], x_done, ident, acc, copied, turned)


def join_ln(nc, d, x_in, y, g, b, x_out, xT_out=None, split=None):
    ALPHA = 4.0 ** 0.25
    with phase(nc, "row0_loaded", "row1_loaded", "row2_loaded", "row3_loaded", "vec_loaded", "x_done", "turned", "hi_done", "copied",
               "stored0", "stored1", "x_stored", "averaged", "rooted", "scaled", "normed", "pool_steps",
               "dve_steps") as (
            row0_loaded, row1_loaded, row2_loaded, row3_loaded, vec_loaded, x_done, turned, hi_done, copied,
            stored0, stored1, x_stored, averaged, rooted, scaled, normed, pool_steps, dve_steps), ExitStack() as ctx:
        sb, ps = tensors(nc, ctx)
        x = sb("jl_x", [P, TT, D])
        st = sb("jl_st", [P, TT, 2, 6])
        mv = sb("jl_mv", [P, TT, 2])
        rs = sb("jl_rs", [P, TT, 2])
        mhalf = sb("jl_mhalf", [P, 1])
        gv = sb("jl_g", [P, D])
        bv = sb("jl_b", [P, D])
        ident = sb("jl_ident", [P, P])
        xT = sb("jl_xT", [P, 2, KD, P])
        acc = ps("jl_acc", [P, 2, KD, P])
        loaded = (row0_loaded, row1_loaded, row2_loaded, row3_loaded)

        def halves(rows):
            return rows.rearrange("p (u w) -> p u w", u=2)

        with nc.Block() as block:
            @block.sync
            def _(sp):
                for i in range(TT):
                    sp.dma_start(x[:, i], d[x_in][i * P:(i + 1) * P, :]).then_inc(loaded[i], 16)
                for i in range(TT):
                    sp.wait_ge(x_done, i + 1)
                    sp.dma_start(d[x_out][i * P:(i + 1) * P, :], x[:, i]).then_inc(x_stored, 16)
                    if xT_out:
                        sp.wait_ge(copied, i + 1)
                        sp.dma_start(d[xT_out].rearrange("(k p) t -> p k t", p=P)[:, :, i * P:(i + 1) * P],
                                     xT[:, i % 2]).then_inc((stored0, stored1)[i % 2], 16)
                sp.wait_ge(x_stored, 16 * TT)
                if xT_out:
                    sp.wait_ge(stored0, 16 * TT // 2)
                    sp.wait_ge(stored1, 16 * TT // 2)

            def finish(dve, step, i):
                if i == 0:
                    dve.wait_ge(vec_loaded, 48)
                dve.wait_ge(normed, i + 1)
                step(dve.tensor_tensor(y[:, i], y[:, i], halves(gv[:]), ALU.mult))
                dve.tensor_tensor(halves(x[:, i]), y[:, i], halves(bv[:]), ALU.add).then_inc(x_done, 1)

            @block.vector
            def _(dve):
                step = Steps(dve, dve_steps)

                def average(i):
                    dve.wait_ge(loaded[i], 16)
                    step(dve.scalar_tensor_tensor(y[:, i], halves(x[:, i]), ALPHA, y[:, i], ALU.mult, ALU.add))
                    for s in range(2):
                        step(dve.bn_stats(st[:, i, s, :], y[:, i, s]), wait=False)
                    step.wait()
                    dve.bn_aggr(mv[:, i, :], st[:, i].rearrange("p s c -> p (s c)")).then_inc(averaged, 1)

                average(0)
                for i in range(TT):
                    if i + 1 < TT:
                        average(i + 1)
                    dve.wait_ge(averaged, i + 1)
                    dve.wait_ge(rooted, i + 1)
                    dve.scalar_tensor_tensor(rs[:, i, 1:2], mv[:, i, 0:1], -1.0, rs[:, i, 0:1], ALU.mult,
                                             ALU.mult).then_inc(scaled, 1)
                    if i:
                        finish(dve, step, i - 1)
                    if split and i == TT - 1:
                        split_lo(dve, split, 0, acc, hi_done, copied)
                finish(dve, step, TT - 1)
                if split:
                    for i in range(1, TT):
                        split_lo(dve, split, i, acc, hi_done, copied)

            @block.gpsimd
            def _(pool):
                steps = Steps(pool, pool_steps)
                steps(pool.memset(mhalf[:], -0.5))
                for i in range(TT):
                    pool.wait_ge(averaged, i + 1)
                    root_reciprocal(pool, steps, rs[:, i, 0:1], mv[:, i, 1:2], 1e-5, mhalf[:]).then_inc(rooted, 1)

            if xT_out or split:
                @block.tensor
                def _(pe):
                    pe.wait_ge(vec_loaded, 48)
                    transpose_out(pe, TT, lambda i: x[:, i], x_done, ident, acc, copied, turned)

            @block.scalar
            def _(act):
                act.dma_start(gv[:], over_partitions(g)).then_inc(vec_loaded, 16)
                act.dma_start(bv[:], over_partitions(b)).then_inc(vec_loaded, 16)
                act.dma_start(ident[:], d["ident"]).then_inc(vec_loaded, 16)
                for i in range(TT + 1):
                    if i < TT:
                        act.wait_ge(scaled, i + 1)
                        act.activation(y[:, i], y[:, i], ACT.Identity, scale=rs[:, i, 0:1], bias=rs[:, i, 1:2]).then_inc(normed, 1)
                    if i and split:
                        act.wait_ge(turned, i)
                        act.activation(split[0][:, :, (i - 1) * P:i * P], acc[:, (i - 1) % 2], ACT.Copy).then_inc(hi_done, 1)
                    elif i and xT_out:
                        act.wait_ge(turned, i)
                        if i >= 3:
                            act.wait_ge((stored0, stored1)[(i - 1) % 2], 16 * ((i - 1) // 2))
                        act.activation(xT[:, (i - 1) % 2], acc[:, (i - 1) % 2], ACT.Copy).then_inc(copied, 1)
def diff_attention(nc, d):
    VH = 8
    KT = LK // P
    SCALE = DH ** -0.5
    N = VH * TT
    with phase(nc, "ctx_loaded", "kv_loaded", "q_loaded", "small_loaded", "turn_ready", "turned", "turn_copied",
               "lam_summed", "lam_exp", "lam_done", "pool_rotated", "dve_rotated", "scores_done", "max_done", "exp_done",
               "probs_done", "probs_turned", "probs_copied", "o_done", "o_copied", "squared", "rooted", "rows_done",
               "o_turned", "o_out", "stored0", "stored1", "pool_steps", "dve_steps") as (
            ctx_loaded, kv_loaded, q_loaded, small_loaded, turn_ready, turned, turn_copied, lam_summed, lam_exp,
            lam_done, pool_rotated, dve_rotated, scores_done, max_done, exp_done, probs_done, probs_turned, probs_copied,
            o_done, o_copied, squared, rooted, rows_done, o_turned, o_out, stored0, stored1, pool_steps,
            dve_steps), ExitStack() as ctx:
        sb, ps = tensors(nc, ctx)
        q = sb("at_q", [P, TT, D])
        k = sb("at_k", [P, KT, D])
        v = sb("at_v", [P, KT, D])
        qT = sb("at_qT", [P, KD, T])
        kT = sb("at_kT", [P, KD, LK])
        cs = sb("at_cos", [P, 2, TT, 32])
        lam4 = sb("at_lam4", [P, 4, DH])
        lam = sb("at_lam", [P, 8])
        ident = sb("at_ident", [P, P])
        gs = sb("at_gs", [P, P])
        tmp = sb("at_tmp", [P, 2, 2, W])
        e = sb("at_e", [P, 2, 2, LK])
        a = sb("at_a", [P, 2, LK])
        aT = sb("at_aT", [P, 2, LK])
        st = sb("at_st", [P, N, 4])
        rs = sb("at_rs", [P, 2, N])
        mhalf = sb("at_mhalf", [P, VH])
        o = sb("at_o", [P, TT, D])
        ss = sb("at_ss", [P, TT, VH])
        sc = ps("at_sc", [P, 2, 1024])
        tr = [ps("at_tr", [P, 1024]), ps("at_ops", [P, 1024])]
        oT = e[:].rearrange("p a b c -> p (a b c)")[:, 0:2 * D].rearrange("p (a k t) -> p a k t", a=2, k=KD)
        ctx_rows = d["kv"][0:CTX, :].rearrange("(t p) n -> p t n", p=P)
        own_rows = d["kv"][CTX:LK, :].rearrange("(t p) n -> p t n", p=P)
        by_dve = [("q", 0), ("q", 1), ("k", 2), ("q", 2), ("k", 3), ("q", 3)]
        by_pool = [("k", 0), ("k", 1)]
        order = [("c", 0), ("c", 1)] + by_dve[0:3] + by_pool[0:1] + by_dve[3:5] + by_pool[1:2] + by_dve[5:6]

        def tile_of(what, i):
            if what == "q":
                return q[:, i], qT[:, :, i * P:(i + 1) * P]
            j = i if what == "c" else 2 + i
            return k[:, j], kT[:, :, j * P:(j + 1) * P]

        def rotate(eng, steps, rows, i, n, done):
            x = rows.rearrange("p (h a s f) -> p h a s f", h=HEADS, a=2, s=2)
            x1, x2 = x[:, :, :, 0, :], x[:, :, :, 1, :]
            cos, sin = (cs[:, n2, i, :].rearrange("p (a f) -> p a f", a=2).unsqueeze(1).to_broadcast([P, HEADS, 2, 16])
                        for n2 in range(2))
            t1, t2 = (tmp[:, n, n2, :].rearrange("p (h a f) -> p h a f", h=HEADS, a=2) for n2 in range(2))
            steps(eng.tensor_tensor(t1, x1, sin, ALU.mult), wait=False)
            steps(eng.tensor_tensor(t2, x2, sin, ALU.mult), wait=False)
            steps.wait()
            steps(eng.tensor_tensor(x1, x1, cos, ALU.mult), wait=False)
            steps(eng.tensor_tensor(x2, x2, cos, ALU.mult), wait=False)
            steps.wait()
            steps(eng.tensor_tensor(x1, x1, t2, ALU.subtract), wait=False)
            steps(eng.tensor_tensor(x2, x2, t1, ALU.add), wait=False)
            steps.wait()
            eng.sem_inc(done, 1)

        with nc.Block() as block:
            @block.sync
            def _(sp):
                sp.dma_start(k[:, 0:2], ctx_rows[:, :, 0:D]).then_inc(ctx_loaded, 16)
                sp.dma_start(ident[:], d["ident"]).then_inc(ctx_loaded, 16)
                sp.dma_start(cs[:], d["rope"]).then_inc(small_loaded, 16)
                sp.dma_start(lam4[:], d["lambda4"].to_broadcast([P, 4 * DH])).then_inc(small_loaded, 16)
                sp.dma_start(gs[:], over_partitions(d["subln_g"])).then_inc(small_loaded, 16)
                sp.dma_start(q[:], d["q"].rearrange("(t p) n -> p t n", p=P)).then_inc(q_loaded, 16)
                sp.dma_start(k[:, 2:KT], own_rows[:, :, 0:D]).then_inc(kv_loaded, 16)
                sp.dma_start(v[:, 0:2], ctx_rows[:, :, D:2 * D]).then_inc(kv_loaded, 16)
                sp.dma_start(v[:, 2:KT], own_rows[:, :, D:2 * D]).then_inc(kv_loaded, 16)
                out = d["oT"].rearrange("(k p) t -> p k t", p=P)
                for i in range(TT):
                    sp.wait_ge(o_out, i + 1)
                    sp.dma_start(out[:, :, i * P:(i + 1) * P], oT[:, i % 2]).then_inc((stored0, stored1)[i % 2], 16)
                sp.wait_ge(stored0, 32)
                sp.wait_ge(stored1, 32)

            @block.gpsimd
            def _(pool):
                steps = Steps(pool, pool_steps)
                steps(pool.memset(mhalf[:], -0.5))
                pool.wait_ge(small_loaded, 48)
                pool.wait_ge(kv_loaded, 48)
                for what, i in by_pool:
                    rotate(pool, steps, tile_of(what, i)[0], i, 1, pool_rotated)
                for i in range(TT):
                    pool.wait_ge(squared, N - TT + i + 1)
                    root_reciprocal(pool, steps, ss[:, i], ss[:, i], 1e-6, mhalf[:]).then_inc(rooted, 1)

            @block.tensor
            def _(pe):
                pe.wait_ge(ctx_loaded, 32)
                for n, (what, i) in enumerate(order):
                    if (what, i) in by_dve:
                        pe.wait_ge(dve_rotated, by_dve.index((what, i)) + 1)
                    elif (what, i) in by_pool:
                        pe.wait_ge(pool_rotated, by_pool.index((what, i)) + 1)
                    if n >= 2:
                        pe.wait_ge(turn_copied, n - 1)
                    rows = tile_of(what, i)[0]
                    for c in range(KD):
                        mm = pe.transpose(tr[n % 2][:, c * P:(c + 1) * P], rows[:, c * P:(c + 1) * P], ident[:])
                    mm.then_inc(turned, 1)
                pe.wait_ge(turn_copied, len(order))
                pe.wait_ge(kv_loaded, 48)
                for n in range(N + 3):
                    if n < N:
                        h, i = divmod(n, TT)
                        for c in range(2):
                            if n:
                                pe.wait_ge(exp_done, 2 * (n - 1) + c + 1)
                            rows = slice(DH * c, DH * c + DH)
                            lhs = qT[rows, h, i * P:(i + 1) * P]
                            pe.matmul(sc[:, c, 0:W], lhs, kT[rows, h, 0:W], start=True, stop=True)
                            pe.matmul(sc[:, c, W:LK], lhs, kT[rows, h, W:LK], start=True,
                                      stop=True).then_inc(scores_done, 1)
                    if 2 <= n <= N + 1:
                        m = n - 2
                        pe.wait_ge(probs_done, m + 1)
                        if m:
                            pe.wait_ge(probs_copied, m)
                        for c in range(KT):
                            mm = pe.transpose(tr[0][:, c * P:(c + 1) * P], a[:, m % 2, c * P:(c + 1) * P], ident[:])
                        mm.then_inc(probs_turned, 1)
                    if n >= 3:
                        m = n - 3
                        h = m // TT
                        pe.wait_ge(probs_copied, m + 1)
                        if m >= 2:
                            pe.wait_ge(o_copied, m - 1)
                        for c in range(KT):
                            mm = pe.matmul(tr[1][:, (m % 2) * W:(m % 2) * W + P], aT[:, m % 2, c * P:(c + 1) * P],
                                           v[:, c, h * P:(h + 1) * P], start=(c == 0), stop=(c == KT - 1))
                        mm.then_inc(o_done, 1)
                pe.wait_ge(o_copied, N)
                for i in range(TT):
                    pe.wait_ge(rows_done, i + 1)
                    if i >= 2:
                        pe.wait_ge(o_out, i - 1)
                    for c in range(KD):
                        mm = pe.transpose(tr[i % 2][:, c * P:(c + 1) * P], o[:, i, c * P:(c + 1) * P], ident[:])
                    mm.then_inc(o_turned, 1)

            @block.scalar
            def _(act):
                def square(m):
                    h, i = divmod(m, TT)
                    act.wait_ge(o_copied, m + 1)
                    act.activation(q[:, i, h * P:(h + 1) * P], o[:, i, h * P:(h + 1) * P], ACT.Square, scale=P ** -0.5,
                                   accum_out=ss[:, i, h:h + 1]).then_inc(squared, 1)

                act.wait_ge(lam_summed, 1)
                act.activation(lam[:, 2:4], lam[:, 0:2], ACT.Exp).then_inc(lam_exp, 1)
                for n, (what, i) in enumerate(order):
                    act.wait_ge(turned, n + 1)
                    act.activation(tile_of(what, i)[1], tr[n % 2][:].rearrange("p (k t) -> p k t", k=KD), ACT.Copy,
                                   scale=-SCALE if what == "q" else 1.0).then_inc(turn_copied, 1)
                for n in range(N + 2):
                    if n < N:
                        if n >= 2:
                            act.wait_ge(probs_done, n - 1)
                        for c in range(2):
                            act.wait_ge(max_done, 2 * n + c + 1)
                            act.activation(e[:, n % 2, c], sc[:, c, 0:LK], ACT.Exp, bias=st[:, n, c:c + 1], scale=-1.0,
                                           accum_out=st[:, n, 2 + c:3 + c]).then_inc(exp_done, 1)
                    if n >= 2:
                        m = n - 2
                        act.wait_ge(probs_turned, m + 1)
                        if m >= 2:
                            act.wait_ge(o_done, m - 1)
                        act.activation(aT[:, m % 2], tr[0][:, 0:LK], ACT.Copy).then_inc(probs_copied, 1)
                    if n >= 6:
                        square(n - 6)
                for m in range(N - 4, N):
                    square(m)
                for i in range(TT):
                    act.wait_ge(o_turned, i + 1)
                    if i >= 2:
                        act.wait_ge((stored0, stored1)[i % 2], 16)
                    act.activation(oT[:, i % 2].rearrange("p k t -> p (k t)"), tr[i % 2][:], ACT.Copy).then_inc(o_out, 1)

            @block.vector
            def _(dve):
                step = Steps(dve, dve_steps)
                dve.wait_ge(small_loaded, 48)
                for c in range(2):
                    step(dve.tensor_tensor_reduce(tmp[:, 0, c, 0:DH], lam4[:, 2 * c], lam4[:, 2 * c + 1], 1.0, 0.0,
                                                  ALU.mult, ALU.add, lam[:, c:c + 1]), wait=False)
                step.wait()
                dve.sem_inc(lam_summed, 1)
                dve.wait_ge(lam_exp, 1)
                step(dve.tensor_tensor(lam[:, 4:5], lam[:, 3:4], lam[:, 2:3], ALU.subtract))
                step(dve.tensor_scalar(lam[:, 5:6], lam[:, 4:5], -0.2, None, ALU.add))
                step(dve.tensor_scalar(gs[:], gs[:], 0.8, None, ALU.mult))
                dve.wait_ge(q_loaded, 16)
                for what, i in by_dve:
                    if what == "k":
                        dve.wait_ge(kv_loaded, 48)
                    rotate(dve, step, tile_of(what, i)[0], i, 0, dve_rotated)

                def combine(m):
                    dve.wait_ge(exp_done, 2 * m + 2)
                    step(dve.reciprocal(rs[:, :, m], st[:, m, 2:4]))
                    step(dve.scalar_tensor_tensor(rs[:, 1, m:m + 1], rs[:, 1, m:m + 1], lam[:, 5:6], st[:, m, 2:3],
                                                  ALU.mult, ALU.mult))
                    if m >= 2:
                        dve.wait_ge(probs_turned, m - 1)
                    dve.scalar_tensor_tensor(a[:, m % 2], e[:, m % 2, 1], rs[:, 1, m:m + 1], e[:, m % 2, 0], ALU.mult,
                                             ALU.add).then_inc(probs_done, 1)

                def copy_o(m):
                    h, i = divmod(m, TT)
                    dve.wait_ge(o_done, m + 1)
                    dve.tensor_scalar(o[:, i, h * P:(h + 1) * P], tr[1][:, (m % 2) * W:(m % 2) * W + P],
                                      rs[:, 0, m:m + 1], None, ALU.mult).then_inc(o_copied, 1)

                for n in range(N):
                    for c in range(2):
                        dve.wait_ge(scores_done, 2 * n + c + 1)
                        dve.tensor_reduce(st[:, n, c:c + 1], sc[:, c, 0:LK], AX.X, ALU.min).then_inc(max_done, 1)
                    if n:
                        combine(n - 1)
                    if n >= 4:
                        copy_o(n - 4)
                combine(N - 1)
                for m in range(N - 4, N):
                    copy_o(m)
                dve.wait_ge(o_copied, N)
                for i in range(TT):
                    dve.wait_ge(rooted, i + 1)
                    for h in range(VH):
                        rows = o[:, i, h * P:(h + 1) * P]
                        ins = dve.scalar_tensor_tensor(rows, rows, ss[:, i, h:h + 1], gs[:], ALU.mult, ALU.mult)
                    ins.then_inc(rows_done, 1)


def spatial_gating(nc, d, split):
    G = 8
    with phase(nc, "z_loaded", "small_loaded", "gelu_done", "averaged", "rooted", "v_done", "mixed", "bank_free",
               "turned", "hi_done", "copied", "pool_steps", "dve_steps") as (
            z_loaded, small_loaded, gelu_done, averaged, rooted, v_done, mixed, bank_free, turned, hi_done, copied,
            pool_steps, dve_steps), ExitStack() as ctx:
        sb, ps = tensors(nc, ctx)
        z = sb("sg_z", [P, TT, 2 * D])
        ws = sb("sg_ws", [P, G, P])
        bs = sb("sg_bs", [P, G])
        gv = sb("sg_g", [P, D])
        bv = sb("sg_b", [P, D])
        s = sb("sg_s", [P, TT, D])
        st = sb("sg_st", [P, TT, 2, 6])
        mv = sb("sg_mv", [P, TT, 2])
        rs = sb("sg_rs", [P, TT])
        mhalf = sb("sg_mhalf", [P, 1])
        ident = sb("sg_ident", [P, P])
        mix = ps("sg_mix", [P, 4, TT, P])
        acc = ps("sg_acc", [P, 2, KD, P])
        with nc.Block() as block:
            @block.sync
            def _(sp):
                sp.dma_start(z[:], d["zg"].rearrange("(t p) n -> p t n", p=P)[:, :, 0:2 * D]).then_inc(z_loaded, 16)
                sp.dma_start(ws[:], d["sgu_wT"]).then_inc(small_loaded, 16)
                sp.dma_start(bs[:], d["sgu_bT"]).then_inc(small_loaded, 16)
                sp.dma_start(gv[:], over_partitions(d["sgu_ln_g"])).then_inc(small_loaded, 16)
                sp.dma_start(bv[:], over_partitions(d["sgu_ln_b"])).then_inc(small_loaded, 16)
                sp.dma_start(ident[:], d["ident"]).then_inc(small_loaded, 16)

            @block.scalar
            def _(act):
                act.wait_ge(z_loaded, 16)
                for i in range(TT):
                    act.activation(z[:, i], z[:, i], ACT.Gelu).then_inc(gelu_done, 1)
                for i in range(TT):
                    act.wait_ge(turned, i + 1)
                    act.activation(split[0][:, :, i * P:(i + 1) * P], acc[:, i % 2], ACT.Copy).then_inc(hi_done, 1)

            @block.gpsimd
            def _(pool):
                steps = Steps(pool, pool_steps)
                steps(pool.memset(mhalf[:], -0.5))
                for i in range(TT):
                    pool.wait_ge(averaged, i + 1)
                    root_reciprocal(pool, steps, rs[:, i:i + 1], mv[:, i, 1:2], 1e-5, mhalf[:]).then_inc(rooted, 1)

            @block.vector
            def _(dve):
                step = Steps(dve, dve_steps)
                dve.wait_ge(small_loaded, 80)
                for i in range(TT):
                    dve.wait_ge(gelu_done, i + 1)
                    v = z[:, i, D:2 * D]
                    for h in range(2):
                        step(dve.bn_stats(st[:, i, h, :], v[:, h * W:(h + 1) * W]), wait=False)
                    step.wait()
                    dve.bn_aggr(mv[:, i, :], st[:, i].rearrange("p s c -> p (s c)")).then_inc(averaged, 1)
                    dve.wait_ge(rooted, i + 1)
                    step(dve.tensor_scalar(v, v, mv[:, i, 0:1], rs[:, i:i + 1], ALU.subtract, ALU.mult))
                    step(dve.tensor_tensor(v, v, gv[:], ALU.mult))
                    dve.tensor_tensor(v, v, bv[:], ALU.add).then_inc(v_done, 1)
                for g in range(G):
                    cols = slice(g * P, (g + 1) * P)
                    dve.wait_ge(mixed, g + 1)
                    dve.scalar_tensor_tensor(s[:, :, cols], mix[:, g % 4], bs[:, g:g + 1], z[:, :, cols], ALU.add,
                                             ALU.mult).then_inc(bank_free, 1)
                for i in range(TT):
                    split_lo(dve, split, i, acc, hi_done, copied)

            @block.tensor
            def _(pe):
                pe.wait_ge(small_loaded, 80)
                pe.wait_ge(v_done, TT)
                for g in range(G):
                    if g >= 4:
                        pe.wait_ge(bank_free, g - 3)
                    pe.matmul(mix[:, g % 4], ws[:, g, :], z[:, :, D + g * P:D + (g + 1) * P], start=True,
                              stop=True).then_inc(mixed, 1)
                pe.wait_ge(bank_free, G)
                transpose_out(pe, TT, lambda i: s[:, i], bank_free, ident, acc, copied, turned)


def combine_branches(nc, d, ya, ys, split):
    with phase(nc, "small_loaded", "biased", "sig_done", "rows_done", "turned", "hi_done", "copied", "dve_steps") as (
            small_loaded, biased, sig_done, rows_done, turned, hi_done, copied, dve_steps), ExitStack() as ctx:
        sb, ps = tensors(nc, ctx)
        gl = sb("cb_gl", [P, TT, 2 * D])
        y = sb("cb_y", [P, TT, D])
        bg = sb("cb_bg", [P, 2 * D])
        ident = sb("cb_ident", [P, P])
        acc = ps("cb_acc", [P, 2, KD, P])
        with nc.Block() as block:
            @block.sync
            def _(sp):
                sp.dma_start(gl[:], d["zg"].rearrange("(t p) n -> p t n", p=P)[:, :, 2 * D:4 * D]).then_inc(small_loaded, 16)
                sp.dma_start(bg[:], over_partitions(d["b_gate"])).then_inc(small_loaded, 16)
                sp.dma_start(ident[:], d["ident"]).then_inc(small_loaded, 16)

            @block.scalar
            def _(act):
                for i in range(TT):
                    act.wait_ge(biased, i + 1)
                    act.activation(gl[:, i], gl[:, i], ACT.Sigmoid).then_inc(sig_done, 1)
                for i in range(TT):
                    act.wait_ge(turned, i + 1)
                    act.activation(split[0][:, :, i * P:(i + 1) * P], acc[:, i % 2], ACT.Copy).then_inc(hi_done, 1)

            @block.vector
            def _(dve):
                step = Steps(dve, dve_steps)
                dve.wait_ge(small_loaded, 48)
                for i in range(TT):
                    dve.tensor_tensor(gl[:, i], gl[:, i], bg[:], ALU.add).then_inc(biased, 1)
                for i in range(TT):
                    dve.wait_ge(sig_done, i + 1)
                    for b, branch in enumerate((ya, ys)):
                        gate = gl[:, i, b * D:(b + 1) * D].rearrange("p (u w) -> p u w", u=2)
                        step(dve.tensor_tensor(branch[:, i], branch[:, i], gate, ALU.mult), wait=False)
                    step.wait()
                    dve.tensor_tensor(y[:, i].rearrange("p (u w) -> p u w", u=2), ya[:, i], ys[:, i],
                                      ALU.add).then_inc(rows_done, 1)
                for i in range(TT):
                    split_lo(dve, split, i, acc, hi_done, copied)

            @block.tensor
            def _(pe):
                pe.wait_ge(small_loaded, 48)
                transpose_out(pe, TT, lambda i: y[:, i], rows_done, ident, acc, copied, turned)
PH = 8
TK = 16
NK = 128
HK = PH * TK
SEG = 2 * PH
LOW = -3.0e38
RB = 64


def expert_choice(nc, d, selT):
    with phase(nc, "row0_loaded", "row1_loaded", "row2_loaded", "row3_loaded", "small_loaded", "squared", "rooted",
               "turned", "turn_copied", "scores_done", "scores_copied", "topk_done", "hot_ready", "hot_scaled", "maxed",
               "exp_done", "sel_ready", "sel_turned", "sel_copied", "pool_steps", "dve_steps") as (
            row0_loaded, row1_loaded, row2_loaded, row3_loaded, small_loaded, squared, rooted, turned, turn_copied,
            scores_done, scores_copied, topk_done, hot_ready, hot_scaled, maxed, exp_done, sel_ready, sel_turned,
            sel_copied, pool_steps, dve_steps), ExitStack() as ctx:
        sb, ps = tensors(nc, ctx)
        q = sb("ec_q", [P, TT, SEG, NK])
        junk = sb("ec_junk", [P, SEG, NK])
        ss = sb("ec_ss", [P, TT, SEG])
        mhalf = sb("ec_mhalf", [P, SEG])
        keys = sb("ec_keys", [P, 2, NK])
        ident = sb("ec_ident", [P, P])
        iota = sb("ec_iota", [P, TK])
        qT = sb("ec_qT", [P, SEG, P])
        s = sb("ec_s", [P, 2, SEG, NK])
        s2 = sb("ec_s2", [P, SEG, NK])
        val = sb("ec_val", [P, SEG, TK])
        idx = sb("ec_idx", [P, SEG, TK], U32)
        idxf = sb("ec_idxf", [P, 2, SEG, TK])
        cand = sb("ec_cand", [P, PH, TK, TK])
        cand2 = sb("ec_cand2", [P, PH, TK, TK])
        hot = sb("ec_hot", [P, 2, PH, TK, TK])
        best = sb("ec_best", [P, 2, PH, TK])
        pos = sb("ec_pos", [P, PH, TK], U32)
        part = sb("ec_part", [P, 2, PH, TK], U32)
        partf = sb("ec_partf", [P, 2, PH, TK])
        tot = sb("ec_tot", [P, PH])
        sel = sb("ec_sel", [P, TT, 3, HK])
        acc = ps("ec_acc", [P, 2, KD, P])
        sc = ps("ec_sc", [P, SEG, NK])
        loaded = (row0_loaded, row1_loaded, row2_loaded, row3_loaded)
        with nc.Block() as block:
            @block.sync
            def _(sp):
                q_rows = d["qp"].rearrange("(t p) (s n) -> p t s n", p=P, n=NK)
                sp.dma_start(q[:, 0], q_rows[:, 0]).then_inc(loaded[0], 16)
                sp.dma_start(ident[:], d["ident"]).then_inc(small_loaded, 16)
                sp.dma_start(keys[:], d["keysT"]).then_inc(small_loaded, 16)
                sp.dma_start(iota[:], d["iota"][:, 0:TK]).then_inc(small_loaded, 16)
                for i in range(1, TT):
                    sp.dma_start(q[:, i], q_rows[:, i]).then_inc(loaded[i], 16)

            @block.gpsimd
            def _(pool):
                steps = Steps(pool, pool_steps)
                steps(pool.memset(mhalf[:], -0.5))

                def root(i):
                    pool.wait_ge(squared, SEG * (i + 1))
                    root_reciprocal(pool, steps, ss[:, i], ss[:, i], 1e-6, mhalf[:]).then_inc(rooted, 1)

                root(0)
                for i in range(TT):
                    if i + 1 < TT:
                        root(i + 1)
                    for c in range(2):
                        n = 2 * i + c
                        pool.wait_ge(hot_ready, n + 1)
                        keys_at = idxf[:, i % 2].rearrange("p (h s) k -> p h s k", s=2)[:, :, c, :]
                        pool.tensor_tensor(hot[:, c], hot[:, c], keys_at.unsqueeze(2).to_broadcast([P, PH, TK, TK]),
                                           ALU.mult).then_inc(hot_scaled, 1)

            @block.tensor
            def _(pe):
                pe.wait_ge(small_loaded, 48)
                for i in range(TT):
                    pe.wait_ge(loaded[i], 16)
                    for g in range(2):
                        if i:
                            pe.wait_ge(turn_copied, 2 * (i - 1) + g + 1)
                        for k in range(KD):
                            mm = pe.transpose(acc[:, g, k, :], q[:, i, g * KD + k, :], ident[:])
                        mm.then_inc(turned, 1)
                    pe.wait_ge(turn_copied, 2 * (i + 1))
                    if i:
                        pe.wait_ge(scores_copied, i)
                    for g in range(SEG):
                        mm = pe.matmul(sc[:, g, :], qT[:, g, :], keys[:, g % 2, :], start=True, stop=True)
                    mm.then_inc(scores_done, 1)
                pe.wait_ge(sel_ready, TT)
                pe.wait_ge(scores_copied, TT)
                for c in range(3):
                    for i in range(TT):
                        mm = pe.transpose(sc[:, 4 * c + i, :], sel[:, i, c, :], ident[:])
                    mm.then_inc(sel_turned, 1)

            @block.scalar
            def _(act):
                def squares(i):
                    act.wait_ge(loaded[i], 16)
                    for g in range(SEG):
                        if i:
                            act.wait_ge(squared, SEG * (i - 1) + g + 1)
                        act.activation(junk[:, g], q[:, i, g], ACT.Square, scale=NK ** -0.5,
                                       accum_out=ss[:, i, g:g + 1]).then_inc(squared, 1)

                def softmax_exp(i):
                    act.wait_ge(maxed, i + 1)
                    act.activation(best[:, i % 2], best[:, i % 2], ACT.Exp).then_inc(exp_done, 1)

                squares(0)
                for i in range(TT):
                    for g in range(2):
                        act.wait_ge(turned, 2 * i + g + 1)
                        if i:
                            act.wait_ge(scores_done, i)
                        act.activation(qT[:, g * KD:(g + 1) * KD, :], acc[:, g], ACT.Copy).then_inc(turn_copied, 1)
                    act.wait_ge(scores_done, i + 1)
                    act.wait_ge(rooted, i + 1)
                    if i >= 2:
                        act.wait_ge(topk_done, i - 1)
                    for g in range(SEG):
                        ins = act.activation(s[:, i % 2, g], sc[:, g], ACT.Copy, scale=ss[:, i, g:g + 1])
                    ins.then_inc(scores_copied, 1)
                    if i + 1 < TT:
                        squares(i + 1)
                    if i:
                        softmax_exp(i - 1)
                softmax_exp(TT - 1)
                for c in range(3):
                    act.wait_ge(sel_turned, c + 1)
                    act.activation(selT[:, c, :], sc[:, 4 * c:4 * c + 4, :].rearrange("p a b -> p (a b)"),
                                   ACT.Copy).then_inc(sel_copied, 1)

            @block.vector
            def _(dve):
                step = Steps(dve, dve_steps)
                dve.wait_ge(small_loaded, 48)

                def top16(rows, n, values, indices, rest):
                    for g in range(n):
                        step(dve.max(values[:, g, 0:8], rows(g)), wait=False)
                    step.wait()
                    for g in range(n):
                        step(dve.max_index(indices[:, g, 0:8], values[:, g, 0:8], rows(g)), wait=False)
                        step(dve.match_replace(rest(g), values[:, g, 0:8], rows(g), LOW), wait=False)
                    step.wait()
                    for g in range(n):
                        step(dve.max(values[:, g, 8:16], rest(g)), wait=False)
                    step.wait()
                    for g in range(n):
                        step(dve.max_index(indices[:, g, 8:16], values[:, g, 8:16], rest(g)), wait=False)
                    step.wait()

                def finish(i):
                    for c in range(2):
                        dve.wait_ge(hot_scaled, 2 * i + c + 1)
                        step(dve.tensor_reduce(sel[:, i, c, :].rearrange("p (h k) -> p h k", h=PH), hot[:, c], AX.X,
                                               ALU.add), wait=False)
                    dve.wait_ge(exp_done, i + 1)
                    step(dve.tensor_reduce(tot[:], best[:, i % 2], AX.X, ALU.add))
                    step(dve.reciprocal(tot[:], tot[:]))
                    step(dve.tensor_tensor(sel[:, i, 2, :].rearrange("p (h k) -> p h k", h=PH), best[:, i % 2],
                                           tot[:].unsqueeze(2).to_broadcast([P, PH, TK]), ALU.mult))
                    dve.sem_inc(sel_ready, 1)

                for i in range(TT):
                    dve.wait_ge(scores_copied, i + 1)
                    top16(lambda g: s[:, i % 2, g, :], SEG, val, idx, lambda g: s2[:, g, :])
                    dve.sem_inc(topk_done, 1)
                    step(dve.tensor_copy(idxf[:, i % 2], idx[:]), wait=False)
                    v4 = val[:].rearrange("p (h s) k -> p h s k", s=2)
                    step(dve.tensor_tensor(cand[:], v4[:, :, 0, :].unsqueeze(3).to_broadcast([P, PH, TK, TK]),
                                           v4[:, :, 1, :].unsqueeze(2).to_broadcast([P, PH, TK, TK]), ALU.add))
                    if i:
                        finish(i - 1)
                    top = best[:, i % 2]
                    top16(lambda h: cand[:, h].rearrange("p a b -> p (a b)"), PH, top, pos,
                          lambda h: cand2[:, h].rearrange("p a b -> p (a b)"))
                    step(dve.tensor_copy(tot[:], top[:, :, 0]))
                    dve.tensor_tensor(top, top, tot[:].unsqueeze(2).to_broadcast([P, PH, TK]),
                                      ALU.subtract).then_inc(maxed, 1)
                    step(dve.tensor_single_scalar(part[:, 0], pos[:], 4, ALU.logical_shift_right), wait=False)
                    step(dve.tensor_single_scalar(part[:, 1], pos[:], 15, ALU.bitwise_and))
                    step(dve.tensor_copy(partf[:], part[:]))
                    for c in range(2):
                        dve.tensor_tensor(hot[:, c], partf[:, c].unsqueeze(3).to_broadcast([P, PH, TK, TK]),
                                          iota[:].unsqueeze(1).unsqueeze(1).to_broadcast([P, PH, TK, TK]),
                                          ALU.is_equal).then_inc(hot_ready, 1)
                finish(TT - 1)


def expert_gates(nc, d, sel):
    GT = 8
    GP = GT - 1
    GB = RB // GT
    with phase(nc, "loaded", "hot_ready", "a_ready", "b_ready", "bank_done", "copied", "stored0", "stored1") as (
            loaded, hot_ready, a_ready, b_ready, bank_done, copied, stored0, stored1), ExitStack() as ctx:
        sb, ps = tensors(nc, ctx)
        iota = sb("eg_iota", [P, NK])
        a = sb("eg_a", [P, 2, GT, NK])
        b = sb("eg_b", [P, 2, GT, NK])
        gates = sb("eg_gates", [P, 2, NK, RB])
        acc = ps("eg_acc", [P, 2, 2, GT // 2, NK])
        stored = (stored0, stored1)
        with nc.Block() as block:
            @block.sync
            def _(sp):
                sp.dma_start(iota[:], d["iota"]).then_inc(loaded, 16)
                for r in range(T // RB):
                    sp.wait_ge(copied, 4 + 2 * GB * (r + 1))
                    sp.dma_start(d["G"][r], gates[:, r % 2]).then_inc(stored[r % 2], 16)
                sp.wait_ge(stored0, 16 * (T // RB // 2))
                sp.wait_ge(stored1, 16 * (T // RB // 2))

            @block.vector
            def _(dve):
                dve.wait_ge(loaded, 16)
                with dve.Fori(0, T // (2 * GT)) as i:
                    for u in range(2):
                        dve.wait_ge(bank_done, i * 4 + 2 * u + 2)
                        at = bass.ds(i * (2 * GT) + u * GT, GP)
                        dve.tensor_tensor(a[:, u, 0:GP], iota[:].unsqueeze(1).to_broadcast([P, GP, NK]),
                                          sel[:, 0, at].unsqueeze(2).to_broadcast([P, GP, NK]),
                                          ALU.is_equal).then_inc(hot_ready, 1)
                        at = bass.ds(i * (2 * GT) + (u * GT + GP), 1)
                        dve.tensor_scalar(a[:, u, GP, :], iota[:], sel[:, 0, at], sel[:, 2, at], ALU.is_equal, ALU.mult)
                        at = bass.ds(i * (2 * GT) + u * GT, GT)
                        dve.tensor_tensor(b[:, u], iota[:].unsqueeze(1).to_broadcast([P, GT, NK]),
                                          sel[:, 1, at].unsqueeze(2).to_broadcast([P, GT, NK]),
                                          ALU.is_equal).then_inc(b_ready, 1)

            @block.gpsimd
            def _(pool):
                pool.wait_ge(loaded, 16)
                with pool.Fori(0, T // (2 * GT)) as i:
                    for u in range(2):
                        pool.wait_ge(hot_ready, i * 2 + u + 1)
                        at = bass.ds(i * (2 * GT) + u * GT, GP)
                        pool.tensor_tensor(a[:, u, 0:GP], a[:, u, 0:GP], sel[:, 2, at].unsqueeze(2).to_broadcast([P, GP, NK]),
                                           ALU.mult).then_inc(a_ready, 1)

            @block.tensor
            def _(pe):
                pe.sem_inc(bank_done, 4)
                with pe.Fori(0, T // (2 * GT)) as i:
                    for u in range(2):
                        pe.wait_ge(a_ready, i * 2 + u + 1)
                        pe.wait_ge(b_ready, i * 2 + u + 1)
                        for h in range(2):
                            pe.wait_ge(copied, i * 4 + 2 * u + h + 1)
                            for t in range(GT // 2):
                                mm = pe.matmul(acc[:, u, h, t, :], b[:, u, h * (GT // 2) + t, :],
                                               a[:, u, h * (GT // 2) + t, :], start=True, stop=True)
                            mm.then_inc(bank_done, 1)

            @block.scalar
            def _(act):
                act.sem_inc(copied, 4)
                for r in range(T // RB):
                    if r >= 2:
                        act.wait_ge(stored[r % 2], 16 * (r // 2))
                    rows = gates[:, r % 2].rearrange("p i t -> p t i")
                    with act.Fori(0, GB // 2) as i:
                        for u in range(2):
                            for h in range(2):
                                act.wait_ge(bank_done, i * 4 + (4 + 2 * GB * r + 2 * u + h + 1))
                                act.activation(rows[:, bass.ds(i * (2 * GT) + u * GT + h * (GT // 2), GT // 2), :],
                                               acc[:, u, h], ACT.Copy).then_inc(copied, 1)


def experts(nc, d, x, total):
    GI = 4
    NG = NK // GI
    HALVES = D // W
    OB = TT * HALVES
    OPEN = 4
    with phase(nc, "ug0_loaded", "ug1_loaded", "v_loaded", "u_hi", "u_lo", "v_hi", "v_lo",
               "h_done", "gelu_done", "gated", "act_hi", "act_lo", "out_done", "added") as (
            ug0_loaded, ug1_loaded, v_loaded, u_hi, u_lo, v_hi, v_lo, h_done, gelu_done, gated,
            act_hi, act_lo, out_done, added), ExitStack() as ctx:
        sb, ps = tensors(nc, ctx)
        xh, xl = x
        ut = sb("ex_u", [P, 2, GI, KD, NK])
        uh = sb("ex_uh", [P, 2, KD, NK], F32R)
        ul = sb("ex_ul", [P, 2, KD, NK], F32R)
        vt = sb("ex_v", [P, GI, D])
        vh = sb("ex_vh", [P, GI, D], F32R)
        vl = sb("ex_vl", [P, GI, D], F32R)
        gt = sb("ex_g", [P, 2, T // RB, GI, RB])
        ge = sb("ex_ge", [P, 2, T])
        ag = sb("ex_gated", [P, 2, T])
        ah = sb("ex_ah", [P, GI, T], F32R)
        al = sb("ex_al", [P, GI, T], F32R)
        hb = ps("ex_hb", [P, 2, T])
        ob = ps("ex_ob", [P, OPEN, W])
        ug_loaded = (ug0_loaded, ug1_loaded)
        u_in = d["uT"].rearrange("i p k j -> p i (k j)")
        v_in = d["peer_v"].rearrange("(i j) n -> j i n", j=NK)
        g_in = d["G"].rearrange("r j i t -> j r i t")
        with nc.Block() as block:
            @block.sync
            def _(sp):
                with sp.Fori(0, NG // 2) as i:
                    for u in range(2):
                        keys = bass.ds(i * (2 * GI) + u * GI, GI)
                        sp.wait_ge(u_lo, i * (2 * GI) + (u + 1) * GI)
                        sp.dma_start(ut[:, u].rearrange("p i k j -> p i (k j)"), u_in[:, keys, :]).then_inc(ug_loaded[u], 16)
                        sp.wait_ge(gated, i * (2 * GI) + (u + 1) * GI)
                        sp.dma_start(gt[:, u], g_in[:, :, keys, :]).then_inc(ug_loaded[u], 16)
                        sp.wait_ge(v_lo, i * (2 * GI) + (u + 1) * GI)
                        sp.dma_start(vt[:], v_in[:, keys, :]).then_inc(v_loaded, 16)

            @block.tensor
            def _(pe):
                pe.sem_inc(h_done, 2)
                pe.sem_inc(out_done, OB)
                with pe.Fori(0, NG // 2) as i:
                    for u in range(2):
                        for c in range(GI):
                            key = i * (2 * GI) + (u * GI + c)
                            pe.wait_ge(u_lo, key + (2 * GI + 1))
                            pe.wait_ge(gelu_done, key + 1)
                            for k in range(KD):
                                mm = product3(pe, hb[:, c % 2, :], (uh[:, c % 2, k, :], ul[:, c % 2, k, :]),
                                              (xh[:, k, :], xl[:, k, :]), k == 0, k == KD - 1)
                            mm.then_inc(h_done, 1)
                        for first in range(0, OB, OPEN):
                            for keys in (range(GI - 1), range(GI - 1, GI)):
                                key = i * (2 * GI) + (u * GI + keys[-1])
                                if first == 0:
                                    pe.wait_ge(act_lo, key + 3)
                                    pe.wait_ge(v_lo, key + (GI + 1))
                                for n in range(first, first + OPEN):
                                    t, half = divmod(n, HALVES)
                                    if keys[0] == 0:
                                        pe.wait_ge(added, i * (2 * OB) + (u * OB + n + 1 + OPEN))
                                    for c in keys:
                                        tok, cols = slice(t * P, (t + 1) * P), slice(half * W, (half + 1) * W)
                                        mm = product3(pe, ob[:, n % OPEN, :], (ah[:, c, tok], al[:, c, tok]),
                                                      (vh[:, c, cols], vl[:, c, cols]), c == 0, c == GI - 1)
                                    if keys[-1] == GI - 1:
                                        mm.then_inc(out_done, 1)

            @block.scalar
            def _(act):
                def split_u(i, u, c):
                    key = i * (2 * GI) + (u * GI + c)
                    if c == 0:
                        act.wait_ge(ug_loaded[u], i * 32 + 32)
                    act.wait_ge(h_done, key + 1)
                    act.activation(uh[:, c % 2], ut[:, u, c], ACT.Copy).then_inc(u_hi, 1)

                def pair(i, last):
                    for u in range(2):
                        group = i * 2 + u
                        for c in range(GI):
                            key = i * (2 * GI) + (u * GI + c)
                            if c + 2 < GI:
                                split_u(i, u, c + 2)
                            elif not (last and u == 1):
                                split_u(i + u, 1 - u, c + 2 - GI)
                            act.wait_ge(h_done, key + 3)
                            act.wait_ge(gated, key + (2 * GI - 1))
                            act.activation(ge[:, c % 2, :], hb[:, c % 2, :], ACT.Gelu).then_inc(gelu_done, 1)
                            if c == 0:
                                act.wait_ge(v_loaded, group * 16 + 16)
                                act.wait_ge(out_done, group * OB + OB)
                            act.activation(vh[:, c], vt[:, c], ACT.Copy).then_inc(v_hi, 1)
                            act.wait_ge(gated, key + (2 * GI + 1))
                            act.activation(ah[:, c], ag[:, c % 2], ACT.Copy).then_inc(act_hi, 1)

                act.sem_inc(gelu_done, 2)
                split_u(0, 0, 0)
                split_u(0, 0, 1)
                with act.Fori(0, NG // 2 - 1) as i:
                    pair(i, False)
                pair(NG // 2 - 1, True)

            @block.gpsimd
            def _(pool):
                pool.sem_inc(u_lo, 2 * GI)
                with pool.Fori(0, NG // 2) as i:
                    for u in range(2):
                        for c in range(GI):
                            pool.wait_ge(u_hi, i * (2 * GI) + (u * GI + c + 1))
                            pool.tensor_tensor(ul[:, c % 2], ut[:, u, c], uh[:, c % 2].bitcast(F32),
                                               ALU.subtract).then_inc(u_lo, 1)

            @block.vector
            def _(dve):
                dve.sem_inc(v_lo, GI)
                dve.sem_inc(gated, 2 * GI)
                dve.sem_inc(act_lo, 2)
                for n in range(OB):
                    t, half = divmod(n, HALVES)
                    dve.memset(total[:, t, half * W:(half + 1) * W], 0.0).then_inc(added, 1)
                with dve.Fori(0, NG // 2) as i:
                    for u in range(2):
                        dve.wait_ge(ug_loaded[u], i * 32 + 32)
                        for c in range(GI):
                            key = i * (2 * GI) + (u * GI + c)
                            dve.wait_ge(gelu_done, key + 3)
                            dve.wait_ge(act_lo, key + 1)
                            dve.tensor_tensor(ag[:, c % 2].rearrange("p (r t) -> p r t", t=RB),
                                              ge[:, c % 2, :].rearrange("p (r t) -> p r t", t=RB), gt[:, u, :, c, :],
                                              ALU.mult).then_inc(gated, 1)
                            dve.wait_ge(v_hi, key + 1)
                            dve.tensor_tensor(vl[:, c], vt[:, c], vh[:, c].bitcast(F32), ALU.subtract).then_inc(v_lo, 1)
                            dve.wait_ge(act_hi, key + 1)
                            dve.tensor_tensor(al[:, c], ag[:, c % 2], ah[:, c].bitcast(F32), ALU.subtract).then_inc(act_lo, 1)
                        for n in range(OB):
                            t, half = divmod(n, HALVES)
                            dve.wait_ge(out_done, i * (2 * OB) + (u * OB + n + 1 + OB))
                            dve.wait_ge(added, i * (2 * OB) + (u * OB + n + 1))
                            cols = total[:, t, half * W:(half + 1) * W]
                            dve.tensor_tensor(cols, cols, ob[:, n % OPEN, :], ALU.add).then_inc(added, 1)
def conv_ffn(nc, d, x, w_up, conv_w, conv_b, w_down, raw):
    C = w_down.shape[0] // P
    DB = C // 2
    wv = w_up.rearrange("(k p) n -> p k n", p=P)
    wd = w_down.rearrange("(c p) n -> p c n", p=P)
    assert C % 2 == 0 and DB % 2 == 1
    with phase(nc, "c_loaded", "w0_loaded", "w1_loaded", "w_hi", "w_lo", "up_done", "base_done",
               "tap_done", "conv_done", "silu_done", "h_done", "h_hi", "h_lo", "block_done", "bank_done", "act_copied",
               "dve_copied") as (
            c_loaded, w0_loaded, w1_loaded, w_hi, w_lo, up_done, base_done, tap_done, conv_done,
            silu_done, h_done, h_hi, h_lo, block_done, bank_done, act_copied, dve_copied), ExitStack() as ctx:
        sb, ps = tensors(nc, ctx)
        xh, xl = x
        wh = sb("ff_wh", [P, 2, 2, D], F32R)
        wl = sb("ff_wl", [P, 2, 2, D], F32R)
        cw = sb("ff_cw", [P, 2 * C, 3])
        cb = sb("ff_cb", [P, 2 * C])
        cv = sb("ff_cv", [P, 2, 2, T])
        h = sb("ff_h", [P, 2, T])
        hh = sb("ff_hh", [P, C, T], F32R)
        hl = sb("ff_hl", [P, C, T], F32R)
        acc = ps("ff_acc", [P, 2 * TT, W])
        up = acc[:, 0:4].rearrange("p (u s) t -> p u s t", u=2)
        order = [n for half in (1, 0) for n in range(half * 4, half * 4 + 4)]
        y = raw[:].rearrange("p u s n -> p (u s) n")
        w_loaded = (w0_loaded, w1_loaded)

        with nc.Block() as block:
            @block.sync
            def _(sp):
                with sp.Fori(0, DB) as i:
                    for u in range(2):
                        sp.wait_ge(w_lo, i * 2 + u + 1)
                        for s in range(2):
                            sp.dma_start(raw[:, u, s].rearrange("p (k j) -> p k j", k=KD),
                                         wv[:, :, bass.ds(i * (2 * P) + (s * C * P + u * P), P)]).then_inc(w_loaded[u], 16)
                for b in range(DB):
                    sp.wait_ge(w_lo, C + b + 1)
                    for s in range(2):
                        sp.dma_start(raw[:, b % 2, s], wd[:, 2 * b + s]).then_inc(w_loaded[b % 2], 16)

            @block.tensor
            def _(pe):
                with pe.Fori(0, C // 2) as i:
                    for u in range(2):
                        pe.wait_ge(w_lo, i * 2 + u + 3)
                        for s in range(2):
                            pe.wait_ge(conv_done, i * 4 + 2 * u + s + 1)
                            for k in range(KD):
                                cols = slice(k * P, (k + 1) * P)
                                mm = product3(pe, up[:, u, s, :], (wh[:, u, s, cols], wl[:, u, s, cols]),
                                              (xh[:, k, :], xl[:, k, :]), k == 0, k == KD - 1)
                            mm.then_inc(up_done, 1)
                for c in range(C):
                    b, s = divmod(c, 2)
                    if s == 0:
                        pe.wait_ge(w_lo, C + b + 3)
                    pe.wait_ge(h_lo, c + 1)
                    for n in order:
                        t, half = divmod(n, 2)
                        if c == 0 and n < 4:
                            pe.wait_ge(conv_done, 2 * C + 4 - 3 + n)
                        tok, cols = slice(t * P, (t + 1) * P), slice(half * W, (half + 1) * W)
                        mm = product3(pe, acc[:, n, :], (hh[:, c, tok], hl[:, c, tok]),
                                      (wh[:, b % 2, s, cols], wl[:, b % 2, s, cols]), c == 0, c == C - 1)
                        if c == C - 1:
                            mm.then_inc(bank_done, 1)
                        elif s == 1 and n == order[-1]:
                            mm.then_inc(block_done, 1)

            @block.scalar
            def _(act):
                def split(count, u):
                    act.wait_ge(w_loaded[u], count * 32)
                    act.activation(wh[:, u], raw[:, u], ACT.Copy).then_inc(w_hi, 1)

                act.dma_start(cw[:], conv_w).then_inc(c_loaded, 16)
                act.dma_start(cb[:], conv_b).then_inc(c_loaded, 16)
                split(1, 0)
                split(1, 1)
                act.wait_ge(c_loaded, 32)
                with act.Fori(0, C // 2) as i:
                    for u in range(2):
                        act.wait_ge(h_done, i * 2 + u + 1)
                        for s in range(2):
                            act.wait_ge(up_done, i * 4 + 2 * u + s + 1)
                            ch = bass.ds(i * 2 + (u + s * C), 1)
                            act.activation(cv[:, u, s, :], up[:, u, s, :], ACT.Identity, bias=cb[:, ch],
                                           scale=cw[:, ch, 2]).then_inc(base_done, 1)
                        split(i + 2, u)
                        act.wait_ge(conv_done, i * 4 + 2 * u + 5)
                        act.activation(cv[:, u, 0, :], cv[:, u, 0, :], ACT.Silu).then_inc(silu_done, 1)
                        act.wait_ge(h_done, i * 2 + u + 3)
                        act.activation(hh[:, bass.ds(i * 2 + u, 1), :].rearrange("p o t -> p (o t)"), h[:, u],
                                       ACT.Copy).then_inc(h_hi, 1)
                for b in range(2, DB):
                    act.wait_ge(block_done, b - 1)
                    split((C + b) // 2 + 1, b % 2)
                for j in range(TT):
                    act.wait_ge(bank_done, 2 * j + 1)
                    act.activation(y[:, order[2 * j] // 2, 0:W], acc[:, order[2 * j], :], ACT.Copy).then_inc(act_copied, 1)

            @block.gpsimd
            def _(pool):
                def split(b, u):
                    pool.wait_ge(w_hi, b + 1)
                    pool.tensor_tensor(wl[:, u], raw[:, u], wh[:, u].bitcast(F32), ALU.subtract).then_inc(w_lo, 1)

                pool.sem_inc(w_lo, 2)
                with pool.Fori(0, (C + DB) // 2) as i:
                    split(i * 2, 0)
                    split(i * 2 + 1, 1)
                split(C + DB - 1, 0)

            @block.vector
            def _(dve):
                dve.sem_inc(conv_done, 4)
                dve.sem_inc(h_done, 2)
                dve.wait_ge(c_loaded, 32)
                with dve.Fori(0, C // 2) as i:
                    for u in range(2):
                        for s in range(2):
                            dve.wait_ge(base_done, i * 4 + 2 * u + s + 1)
                            ch = bass.ds(i * 2 + (u + s * C), 1)
                            z, b = cv[:, u, s, :], up[:, u, s, :]
                            dve.scalar_tensor_tensor(z[:, 1:T], b[:, 0:T - 1], cw[:, ch, 1], z[:, 1:T], ALU.mult,
                                                     ALU.add).then_inc(tap_done, 1)
                            dve.wait_ge(tap_done, i * 4 + 2 * u + s + 1)
                            dve.scalar_tensor_tensor(z[:, 2:T], b[:, 0:T - 2], cw[:, ch, 0], z[:, 2:T], ALU.mult,
                                                     ALU.add).then_inc(conv_done, 1)
                        dve.wait_ge(conv_done, i * 4 + 2 * u + 6)
                        dve.wait_ge(silu_done, i * 2 + u + 1)
                        dve.tensor_tensor(h[:, u], cv[:, u, 0, :], cv[:, u, 1, :], ALU.mult).then_inc(h_done, 1)
                        dve.wait_ge(h_hi, i * 2 + u + 1)
                        chunk = bass.ds(i * 2 + u, 1)
                        dve.tensor_tensor(hl[:, chunk, :].rearrange("p o t -> p (o t)"), h[:, u],
                                          hh[:, chunk, :].bitcast(F32).rearrange("p o t -> p (o t)"),
                                          ALU.subtract).then_inc(h_lo, 1)
                for j in range(TT):
                    dve.wait_ge(bank_done, 2 * j + 2)
                    dve.tensor_copy(y[:, order[2 * j + 1] // 2, W:D], acc[:, order[2 * j + 1], :]).then_inc(dve_copied, 1)


RC = 64
NC_ = T // RC
LOG_DECAY = -float(np.exp(-0.5))


def rwkv_inputs(nc, d):
    LOW = {3: ((0, 64, 0),), 4: ((64, 64, 1),), 5: ((128, 128, 2), (256, 32, 3))}
    ORDER = (1, 4, 3, 0, 2, 5)
    AT = {n: j for j, n in enumerate(ORDER)}
    with phase(nc, "x_loaded", "low_loaded", "small_loaded", "w0_loaded", "w1_loaded", "mixed", "low_done", "low_ready",
               "bank_done", "copied", "decay_step", "squared", "summed", "rooted", "nrm_used", "rk_done", "rk_summed", "out_ready",
               "slot_used", "stored0", "stored1", "pc_stored", "mix_steps", "dve_steps", "unit_steps", "parts_done") as (
            x_loaded, low_loaded, small_loaded, w0_loaded, w1_loaded, mixed, low_done, low_ready, bank_done, copied,
            decay_step, squared, summed, rooted, nrm_used, rk_done, rk_summed, out_ready, slot_used, stored0, stored1,
            pc_stored, mix_steps, dve_steps, unit_steps, parts_done), ExitStack() as ctx:
        sb, ps = tensors(nc, ctx)
        xm = sb("ri_xm", [P, 3, KD, T])
        mix = sb("ri_mix", [P, 6, KD])
        low = sb("ri_low", [P, KD, 288])
        mid = sb("ri_mid", [P, 4, T])
        wt = sb("ri_w", [P, 2, 3, KD, P])
        wu = sb("ri_wu", [P, 2, 4, P])
        w0 = sb("ri_w0", [P, 2, KD])
        cols = sb("ri_cols", [P, 3, KD])
        start = sb("ri_start", [P, 2, T])
        ones = sb("ri_ones", [P, P])
        pc = sb("ri_pc", [P, KD, NC_])
        work = sb("ri_work", [P, 32, T])
        x, dx, xl = work[:, 0:8], work[:, 8:16], work[:, 16:32].rearrange("p (u k) t -> p u k t", u=2)
        a5 = work[:, 0:10].rearrange("p (u n) t -> p u n t", u=2)
        kk, sq, nrm, kn, b, c, cp, rc, t1, t2 = (work[:, n, :] for n in range(10, 20))
        arbk = work[:, 20:28].rearrange("p (u n) t -> p u n t", u=2)
        bonus, gate = work[:, 28:30], work[:, 30:32]
        acc = ps("ri_acc", [P, 6, T])
        two = ps("ri_two", [P, 2, T])
        w_loaded, stored = (w0_loaded, w1_loaded), (stored0, stored1)
        STORES, LOADS = 4, 7
        KS = 11
        with nc.Block() as block:
            @block.sync
            def _(sp):
                def load(i, u):
                    at = bass.ds(i * (2 * P) + u * P, P)
                    for j in range(3):
                        sp.dma_start(wt[:, u, j], d["w_rkv"][j].rearrange("(k p) n -> p k n", p=P)[:, :, at]).then_inc(
                            w_loaded[u], 16)
                    sp.dma_start(wu[0:64, u, 0], d["w2"][:, at]).then_inc(w_loaded[u], 16)
                    sp.dma_start(wu[0:64, u, 1], d["a2"][:, at]).then_inc(w_loaded[u], 16)
                    sp.dma_start(wu[:, u, 2], d["g2"][0:P, at]).then_inc(w_loaded[u], 16)
                    sp.dma_start(wu[0:32, u, 3], d["g2"][P:160, at]).then_inc(w_loaded[u], 16)

                def rows(name, n):
                    return name.rearrange("(q p) t -> p q t", p=P)[:, bass.ds(n, 1), :].rearrange("p o t -> p (o t)")

                def store(i, u):
                    n = i * 2 + u
                    sp.wait_ge(out_ready, n + 1)
                    sp.dma_start(d["arbk"][bass.ds(n, 1)].rearrange("o p c t -> p (o c) t"), arbk[:, u]).then_inc(stored[u], 16)
                    sp.dma_start(rows(d["bonus"], n), bonus[:, u]).then_inc(stored[u], 16)
                    sp.dma_start(rows(d["vg"][0], n), a5[:, u, 2]).then_inc(stored[u], 16)
                    sp.dma_start(rows(d["vg"][1], n), gate[:, u]).then_inc(stored[u], 16)

                sp.dma_start(x, d["x2T"].rearrange("(k p) t -> p k t", p=P)).then_inc(x_loaded, 16)
                sp.dma_start(mix[:], d["mix_cols"]).then_inc(x_loaded, 16)
                for name, n, at in (("w1", 64, 0), ("a1", 64, 64), ("g1", 160, 128)):
                    sp.dma_start(low[:, :, at:at + n], d[name].rearrange("(k p) n -> p k n", p=P)).then_inc(low_loaded, 16)
                load(0, 0)
                load(0, 1)
                sp.dma_start(w0[:], d["w0a0_cols"]).then_inc(small_loaded, 16)
                sp.dma_start(cols[:], d["k_cols"]).then_inc(small_loaded, 16)
                sp.dma_start(start[:], d["starts"]).then_inc(small_loaded, 16)
                sp.dma_start(ones[:], d["ones64"]).then_inc(small_loaded, 16)
                with sp.Fori(0, KD // 2 - 1) as i:
                    for u in range(2):
                        store(i, u)
                        load(i + 1, u)
                for u in range(2):
                    store(KD // 2 - 1, u)
                sp.dma_start(d["pc"], pc[:]).then_inc(pc_stored, 16)
                sp.wait_ge(pc_stored, 16)
                for u in range(2):
                    sp.wait_ge(stored[u], 16 * STORES * (KD // 2 + 1))

            @block.tensor
            def _(pe):
                pe.wait_ge(low_loaded, 48)
                for j, n in enumerate((3, 4, 5)):
                    pe.wait_ge(mixed, KD * (j + 1))
                    for s, (col, rank, slot) in enumerate(LOW[n]):
                        if n == 5:
                            pe.wait_ge(low_ready, s + 1)
                        for k in range(KD):
                            mm = pe.matmul(two[0:rank, (1 if n == 4 else s), :], low[:, k, col:col + rank],
                                           xl[:, j % 2, k, :], start=(k == 0), stop=(k == KD - 1))
                        mm.then_inc(low_done, 1)
                pe.wait_ge(small_loaded, 64)
                pe.wait_ge(mixed, 6 * KD)
                pe.wait_ge(low_ready, 4)
                with pe.Fori(0, KD // 2) as i:
                    for u in range(2):
                        n = i * 2 + u
                        pe.wait_ge(w_loaded[u], i * (16 * LOADS) + 16 * LOADS)
                        for j, what in enumerate(ORDER):
                            pe.wait_ge(copied, i * 12 + (6 * u + j + 1))
                            if what < 3:
                                for k in range(KD):
                                    mm = pe.matmul(acc[:, j, :], wt[:, u, what, k, :], xm[:, what, k, :], start=(k == 0),
                                                   stop=(k == KD - 1))
                            else:
                                parts = LOW[what]
                                for s, (_, rank, slot) in enumerate(parts):
                                    mm = pe.matmul(acc[:, j, :], wu[0:rank, u, slot, :], mid[0:rank, slot, :],
                                                   start=(s == 0), stop=(s == len(parts) - 1))
                            mm.then_inc(bank_done, 1)
                            if what == 0:
                                pe.wait_ge(squared, n + 1)
                                pe.wait_ge(rooted, n + 1)
                                pe.matmul(two[:, 0, :], ones[:], sq, start=True, stop=True).then_inc(summed, 1)
                        pe.wait_ge(rk_done, n + 1)
                        pe.matmul(two[:, 1, :], ones[:], t1, start=True, stop=True).then_inc(rk_summed, 1)

            @block.scalar
            def _(act):
                act.sem_inc(stored0, 16 * STORES)
                act.sem_inc(stored1, 16 * STORES)
                act.sem_inc(copied, 6)
                act.sem_inc(rooted, 1)
                low_funcs = (ACT.Tanh, ACT.Copy, ACT.Sigmoid, ACT.Sigmoid)
                for slot, (bank, rank) in enumerate(((0, 64), (1, 64), (0, 128), (1, 32))):
                    act.wait_ge(low_done, slot + 1)
                    act.activation(mid[0:rank, slot, :], two[0:rank, bank, :], low_funcs[slot]).then_inc(low_ready, 1)
                act.wait_ge(small_loaded, 64)
                act.wait_ge(mixed, 6 * KD)
                with act.Fori(0, KD // 2) as i:
                    for u in range(2):
                        n = i * 2 + u
                        q = bass.ds(n, 1)
                        act.wait_ge(slot_used, n + 1)
                        act.wait_ge(stored[u], i * (16 * STORES) + 16 * STORES)
                        for j, what in enumerate(ORDER):
                            act.wait_ge(bank_done, i * 12 + (6 * u + j + 1))
                            if what in (3, 4):
                                out = a5[:, u, what]
                                ins = act.activation(out, acc[:, j, :], ACT.Sigmoid, bias=w0[:, what - 3, q])
                                if what == 3:
                                    ins.then_inc(decay_step, 1)
                                    act.wait_ge(decay_step, n + 1)
                                    ins = act.activation(out, out, ACT.Exp, scale=LOG_DECAY)
                            else:
                                ins = act.activation(gate[:, u] if what == 5 else a5[:, u, what], acc[:, j, :], ACT.Copy)
                            ins.then_inc(copied, 1)
                            if what == 1:
                                act.wait_ge(copied, i * 12 + (6 * u + 7))
                                act.activation(sq, a5[:, u, 1], ACT.Square, scale=cols[:, 0, q]).then_inc(squared, 1)
                            if what == 0:
                                act.wait_ge(summed, n + 1)
                                act.wait_ge(nrm_used, n + 1)
                                act.activation(nrm, two[:, 0, :], ACT.Sqrt).then_inc(rooted, 1)

            @block.vector
            def _(dve):
                dve.sem_inc(slot_used, 2)
                dve.sem_inc(nrm_used, 1)
                dve.wait_ge(x_loaded, 32)
                dve.tensor_scalar(dx[:, :, 0:1], x[:, :, 0:1], -1.0, None, ALU.mult).then_inc(mix_steps, 1)
                dve.tensor_tensor(dx[:, :, 1:T], x[:, :, 0:T - 1], x[:, :, 1:T], ALU.subtract).then_inc(mix_steps, 1)
                dve.wait_ge(mix_steps, 2)
                for j, what in enumerate((3, 4, 5, 1, 0, 2)):
                    if what == 5:
                        dve.wait_ge(low_done, 1)
                    out = xl[:, j % 2] if what >= 3 else xm[:, what]
                    for k in range(KD):
                        dve.scalar_tensor_tensor(out[:, k], dx[:, k], mix[:, what, k:k + 1], x[:, k], ALU.mult,
                                                 ALU.add).then_inc(mixed, 1)
                dve.wait_ge(small_loaded, 64)
                dve.wait_ge(mixed, 6 * KD)
                dve.wait_ge(low_done, 4)
                cp64 = cp.rearrange("p (e t) -> p e t", t=RC)
                c64 = c.rearrange("p (e t) -> p e t", t=RC)
                dve.memset(cp, 1.0).then_inc(parts_done, 1)
                dve.wait_ge(parts_done, 1)
                with dve.Fori(0, KD // 2) as i:
                    for u in range(2):
                        n = i * 2 + u
                        q = bass.ds(n, 1)
                        r, k, v, dec, a = (a5[:, u, j, :] for j in range(5))
                        base = n * KS
                        steps = 0

                        def step(ins, wait=True):
                            nonlocal steps
                            ins.then_inc(dve_steps, 1)
                            steps += 1
                            if wait:
                                dve.wait_ge(dve_steps, base + steps)

                        def ready(what):
                            dve.wait_ge(copied, i * 12 + (6 * u + AT[what] + 7))

                        dve.wait_ge(stored[u], i * (16 * STORES) + 16 * STORES)
                        ready(1)
                        step(dve.tensor_scalar(kk, k, cols[:, 0, q], None, ALU.mult), wait=False)
                        ready(4)
                        step(dve.tensor_scalar(t2, a, -1.0, cols[:, 1, q], ALU.add, ALU.mult))
                        step(dve.scalar_tensor_tensor(kn, t2, 1.0, k, ALU.add, ALU.mult), wait=False)
                        ready(3)
                        step(dve.tensor_tensor(b, dec, start[:, 0], ALU.mult), wait=False)
                        step(dve.tensor_tensor(rc, dec, start[:, 1], ALU.mult))
                        step(dve.tensor_tensor_scan(c, b, rc, 0.0, ALU.mult, ALU.add))
                        ready(0)
                        dve.tensor_tensor(t1, r, kn, ALU.mult).then_inc(unit_steps, 1)
                        step(dve.reciprocal(rc, c), wait=False)
                        dve.wait_ge(unit_steps, n * 3 + 1)
                        dve.tensor_scalar(t1, t1, cols[:, 2, q], None, ALU.mult).then_inc(rk_done, 1)
                        step(dve.tensor_copy(cp64[:, :, 1:RC], c64[:, :, 0:RC - 1]), wait=False)
                        step(dve.tensor_copy(pc[:, q, :].rearrange("p o (h e) -> p (o e) h", h=2),
                                             c64[:, :, RC - 1].rearrange("p (e h) -> p e h", h=2)))
                        dve.tensor_tensor(arbk[:, u, 1], r, c, ALU.mult).then_inc(parts_done, 1)
                        dve.tensor_tensor(arbk[:, u, 3], kn, rc, ALU.mult).then_inc(parts_done, 1)
                        dve.wait_ge(rooted, n + 2)
                        step(dve.tensor_scalar(nrm, nrm, 1e-12, None, ALU.max))
                        step(dve.reciprocal(nrm, nrm))
                        dve.tensor_tensor(kk, kk, nrm, ALU.mult).then_inc(unit_steps, 1)
                        dve.wait_ge(unit_steps, n * 3 + 2)
                        dve.sem_inc(nrm_used, 1)
                        dve.scalar_tensor_tensor(arbk[:, u, 0], kk, -1.0, cp, ALU.mult, ALU.mult).then_inc(parts_done, 1)
                        dve.tensor_tensor(b, kk, a, ALU.mult).then_inc(unit_steps, 1)
                        dve.wait_ge(unit_steps, n * 3 + 3)
                        dve.tensor_tensor(arbk[:, u, 2], b, rc, ALU.mult).then_inc(parts_done, 1)
                        ready(2)
                        dve.wait_ge(rk_summed, n + 1)
                        dve.tensor_tensor(bonus[:, u], two[:, 1, :], v, ALU.mult).then_inc(parts_done, 1)
                        dve.wait_ge(parts_done, n * 5 + 6)
                        ready(5)
                        dve.sem_inc(out_ready, 1)
                        dve.sem_inc(slot_used, 1)
                        assert steps == KS, steps
def rwkv_chunks(nc, d, gt, hs, pc):
    NP = 2 * TT
    LEVELS = 5
    with phase(nc, "small_loaded", "slot0_loaded", "slot1_loaded", "slot_used", "ba_done", "ba_masked", "ka_done",
               "ka_masked", "l_done", "x_ready", "xt_ready", "rows_turned", "rows_copied", "em_ready", "w_done",
               "w_copied", "d_done", "x_added", "mv_done", "mv_copied", "rhs_ready", "az_done", "pads_ready", "pairs_ready", "r_done",
               "y_done", "g_done", "h_done", "r_ready", "y_ready", "g_masked", "h_scaled", "gh_finished", "stored0",
               "stored1", "dve_steps", "pool_steps") as (
            small_loaded, slot0_loaded, slot1_loaded, slot_used, ba_done, ba_masked, ka_done, ka_masked, l_done,
            x_ready, xt_ready, rows_turned, rows_copied, em_ready, w_done, w_copied, d_done, x_added, mv_done, mv_copied,
            rhs_ready, az_done, pads_ready, pairs_ready, r_done, y_done, g_done, h_done, r_ready, y_ready, g_masked,
            h_scaled, gh_finished, stored0, stored1, dve_steps, pool_steps), ExitStack() as ctx:
        sb, ps = tensors(nc, ctx)
        ar = sb("rc_ar", [P, 2, 2, T])
        bk = sb("rc_bk", [P, 2, 2, T])
        vT = sb("rc_vT", [P, 2, T])
        mask2 = sb("rc_mask2", [P, 2, P])
        lmask = sb("rc_lmask", [P, 2, P])
        emask = sb("rc_emask", [P, LEVELS, P])
        bd = sb("rc_bd", [P, P])
        ident = sb("rc_ident", [P, P])
        ba = sb("rc_ba", [P, NP, 2, P])
        ka = sb("rc_ka", [P, NP, 2, P])
        xx = sb("rc_xx", [P, 2, NP, P])
        em = sb("rc_em", [P, LEVELS, NP, P])
        ws = sb("rc_ws", [P, NP, P])
        rows = sb("rc_rows", [P, 4, TT, P])
        rhs = sb("rc_rhs", [P, NP, 2, RC])
        apad = sb("rc_apad", [P, TT, 2, P])
        zpad = sb("rc_zpad", [P, TT, 2, P])
        vpad = sb("rc_vpad", [P, TT, 2, P])
        apair = sb("rc_apair", [P, TT, P])
        zpair = sb("rc_zpair", [P, TT, P])
        ry = sb("rc_ry", [P, 2, 2, T])
        lo = ps("rc_lo", [P, 4, W])
        hi = ps("rc_hi", [P, 4, W])
        loaded, stored = (slot0_loaded, slot1_loaded), (stored0, stored1)

        def banks(t, first, count, **dims):
            return t[:, first:first + count, :].rearrange("p b w -> p (b w)")

        lo_ba = banks(lo, 0, 4).rearrange("p (n s t) -> p n s t", n=NP, s=2)
        hi_ka = banks(hi, 0, 4).rearrange("p (n s t) -> p n s t", n=NP, s=2)
        lo_l = banks(lo, 0, 2).rearrange("p (n t) -> p n t", n=NP)
        lo_w = banks(lo, 2, 2).rearrange("p (n t) -> p n t", n=NP)
        hi_rows = banks(hi, 0, 4).rearrange("p (a i t) -> p a i t", a=4, i=TT)
        hi_d = [banks(hi, 2 * c, 2).rearrange("p (x n t) -> p x n t", x=2, n=TT) for c in range(2)]
        lo_mv = banks(lo, 0, 1).rearrange("p (n t) -> p n t", n=NP)
        hi_az = banks(hi, 0, 2).rearrange("p (n s t) -> p n s t", n=NP, s=2)
        lo_r = banks(lo, 1, 1).rearrange("p (i t) -> p i t", i=TT)
        lo_y = banks(lo, 2, 1).rearrange("p (i t) -> p i t", i=TT)
        hi_g = banks(hi, 2, 2).rearrange("p (e t) -> p e t", e=NC_)
        hi_h = banks(hi, 0, 2).rearrange("p (e t) -> p e t", e=NC_)
        problems = [(c * TT + i, i, c) for i in range(TT) for c in range(2)]
        chunks = [((e % 2) * TT + e // 2, e // 2, slice(RC * (e % 2), RC * (e % 2) + RC)) for e in range(NC_)]

        def of_head(c):
            return range(TT * c, TT * c + TT)

        def heads(t):
            return [t[:, :, c, RC * c:RC * c + RC] for c in range(2)]

        with nc.Block() as block:
            @block.sync
            def _(sp):
                sp.dma_start(mask2[:], d["mask2"]).then_inc(small_loaded, 16)
                sp.dma_start(lmask[:], d["lmask"]).then_inc(small_loaded, 16)
                sp.dma_start(emask[:], d["emask"]).then_inc(small_loaded, 16)
                sp.dma_start(bd[:], d["ones64"]).then_inc(small_loaded, 16)
                sp.dma_start(ident[:], d["ident"]).then_inc(small_loaded, 16)
                sp.dma_start(pc[:], d["pc"]).then_inc(small_loaded, 16)
                src = d["arbk"].rearrange("q p c t -> p q c t")
                v_src = d["vg"][0].rearrange("(q p) t -> p q t", p=P)
                with sp.Fori(0, KD // 2) as i:
                    for u in range(2):
                        sp.wait_ge(slot_used, i * 2 + u + 1)
                        q = bass.ds(i * 2 + u, 1)
                        sp.dma_start(ar[:, u], src[:, q, 0:2, :].rearrange("p o c t -> p (o c) t")).then_inc(loaded[u], 16)
                        sp.dma_start(bk[:, u], src[:, q, 2:4, :].rearrange("p o c t -> p (o c) t")).then_inc(loaded[u], 16)
                        sp.dma_start(vT[:, u], v_src[:, q, :].rearrange("p o t -> p (o t)")).then_inc(loaded[u], 16)

            @block.tensor
            def _(pe):
                pe.wait_ge(small_loaded, 96)
                with pe.Fori(0, KD // 2) as i2:
                    for u in range(2):
                        n = i2 * 2 + u
                        pe.wait_ge(loaded[u], i2 * 48 + 48)
                        pe.wait_ge(y_ready, n + 1)
                        pe.wait_ge(r_ready, n + 1)
                        for p, i, c in problems:
                            h, t = slice(RC * c, RC * c + RC), slice(i * P, (i + 1) * P)
                            mm = pe.matmul(lo_ba[:, p], bk[h, u, 0, t], ar[h, u, :, t], start=True, stop=True)
                        mm.then_inc(ba_done, 1)
                        pe.wait_ge(h_scaled, n + 1)
                        pe.wait_ge(g_masked, n + 1)
                        for p, i, c in problems:
                            h, t = slice(RC * c, RC * c + RC), slice(i * P, (i + 1) * P)
                            mm = pe.matmul(hi_ka[:, p], bk[h, u, 1, t], ar[h, u, :, t], start=True, stop=True)
                        mm.then_inc(ka_done, 1)
                        pe.wait_ge(ba_masked, n + 1)
                        for p, i, c in problems:
                            h, t = slice(RC * c, RC * c + RC), slice(i * P, (i + 1) * P)
                            mm = pe.matmul(lo_l[:, p], ar[h, u, 0, t], bk[h, u, 0, t], start=True, stop=True)
                        mm.then_inc(l_done, 1)
                        pe.wait_ge(ka_masked, n + 1)
                        for a, src in enumerate((ar[:, u, 0], bk[:, u, 0], bk[:, u, 1], vT[:, u])):
                            for i in range(TT):
                                mm = pe.transpose(hi_rows[:, a, i, :], src[:, i * P:(i + 1) * P], ident[:])
                        mm.then_inc(rows_turned, 1)
                        pe.wait_ge(x_ready, n + 1)
                        pe.wait_ge(xt_ready, n + 1)
                        for lv in range(LEVELS):
                            for c in range(2):
                                if lv:
                                    pe.wait_ge(x_added, n * (2 * LEVELS) + (2 * lv - 1 + c))
                                if c == 0:
                                    pe.wait_ge(em_ready, n * LEVELS + (lv + 1))
                                for p in of_head(c):
                                    mm = pe.matmul(lo_w[:, p], em[:, lv, p, :], xx[:, 0, p, :], start=True, stop=True)
                                mm.then_inc(w_done, 1)
                            if lv == 0:
                                pe.wait_ge(rows_copied, n + 1)
                            for c in range(2):
                                pe.wait_ge(w_copied, n * (2 * LEVELS) + (2 * lv + c + 1))
                                for p in of_head(c):
                                    if lv < LEVELS - 1:
                                        pe.matmul(hi_d[c][:, 0, p % TT], xx[:, 1, p, :], ws[:, p, :], start=True, stop=True)
                                    mm = pe.matmul(hi_d[c][:, 1, p % TT], ws[:, p, :], xx[:, 1, p, :], start=True,
                                                   stop=True)
                                mm.then_inc(d_done, 1)
                        for p, i, c in problems:
                            mm = pe.matmul(lo_mv[:, p], ka[:, p, 0, :], rows[:, 3, i, RC * c:RC * c + RC], start=True,
                                           stop=True)
                        mm.then_inc(mv_done, 1)
                        pe.wait_ge(x_added, n * (2 * LEVELS) + 2 * LEVELS)
                        pe.wait_ge(rhs_ready, n + 1)
                        pe.wait_ge(mv_copied, n + 1)
                        for p, i, c in problems:
                            mm = pe.matmul(hi_az[:, p], xx[:, 1, p, :], rhs[:, p], start=True, stop=True)
                        mm.then_inc(az_done, 1)
                        pe.wait_ge(pads_ready, n * 4 + 4)
                        for i in range(TT):
                            for c in range(2):
                                mm = pe.matmul(lo_r[:, i], apad[:, i, c, :], ba[:, c * TT + i, 1, :], start=(c == 0),
                                               stop=(c == 1))
                        mm.then_inc(r_done, 1)
                        for i in range(TT):
                            for c in range(2):
                                pe.matmul(lo_y[:, i], zpad[:, i, c, :], ba[:, c * TT + i, 1, :], start=(c == 0), stop=False)
                                mm = pe.matmul(lo_y[:, i], vpad[:, i, c, :], ka[:, c * TT + i, 1, :], start=False,
                                               stop=(c == 1))
                        mm.then_inc(y_done, 1)
                        pe.wait_ge(pairs_ready, n * 2 + 2)
                        for e, i, t in chunks:
                            mm = pe.matmul(hi_g[:, e], apair[t, i, :], rows[t, 1, i, :], start=True, stop=True)
                        mm.then_inc(g_done, 1)
                        for e, i, t in chunks:
                            pe.matmul(hi_h[:, e], rows[t, 1, i, :], zpair[t, i, :], start=True, stop=False)
                            mm = pe.matmul(hi_h[:, e], rows[t, 2, i, :], rows[t, 3, i, :], start=False, stop=True)
                        mm.then_inc(h_done, 1)

            @block.vector
            def _(dve):
                dve.sem_inc(r_ready, 1)
                dve.sem_inc(g_masked, 1)
                dve.sem_inc(h_scaled, 1)
                for pad in (apad, zpad, vpad):
                    dve.memset(pad[:], 0.0).then_inc(dve_steps, 1)
                dve.wait_ge(dve_steps, 3)
                dve.wait_ge(small_loaded, 96)
                with dve.Fori(0, KD // 2) as i2:
                    for u in range(2):
                        n = i2 * 2 + u
                        m2 = mask2[:].unsqueeze(1).to_broadcast([P, NP, 2, P])
                        dve.wait_ge(ba_done, n + 1)
                        dve.tensor_tensor(ba[:], lo_ba, m2, ALU.mult).then_inc(ba_masked, 1)
                        dve.wait_ge(ka_done, n + 1)
                        dve.tensor_tensor(ka[:], hi_ka, m2, ALU.mult).then_inc(ka_masked, 1)
                        dve.wait_ge(ba_masked, n + 1)
                        dve.tensor_tensor(xx[:, 1], ba[:, :, 0, :], lmask[:, 1].unsqueeze(1).to_broadcast([P, NP, P]),
                                          ALU.mult).then_inc(dve_steps, 1)
                        dve.wait_ge(dve_steps, n * 2 + 4)
                        dve.tensor_tensor(xx[:, 1], xx[:, 1], ident[:].unsqueeze(1).to_broadcast([P, NP, P]),
                                          ALU.add).then_inc(xt_ready, 1)
                        dve.wait_ge(l_done, n + 1)
                        dve.tensor_tensor(xx[:, 0], lo_l, lmask[:, 0].unsqueeze(1).to_broadcast([P, NP, P]),
                                          ALU.mult).then_inc(dve_steps, 1)
                        dve.wait_ge(dve_steps, n * 2 + 5)
                        dve.tensor_tensor(xx[:, 0], xx[:, 0], ident[:].unsqueeze(1).to_broadcast([P, NP, P]),
                                          ALU.add).then_inc(x_ready, 1)
                        dve.wait_ge(x_ready, n + 1)
                        dve.wait_ge(xt_ready, n + 1)
                        for lv in range(LEVELS):
                            for c in range(2):
                                if lv:
                                    dve.wait_ge(x_added, n * (2 * LEVELS) + (2 * lv - 1 + c))
                                dve.wait_ge(d_done, n * (2 * LEVELS) + (2 * lv + c + 1))
                                own = slice(TT * c, TT * c + TT)
                                both = slice(0 if lv < LEVELS - 1 else 1, 2)
                                dve.tensor_tensor(xx[:, both, own], xx[:, both, own], hi_d[c][:, both],
                                                  ALU.add).then_inc(x_added, 1)
                        dve.wait_ge(az_done, n + 1)
                        az = hi_az.rearrange("p (c i) s t -> p i c s t", c=2)
                        for c in range(2):
                            dve.tensor_copy(heads(apad)[c], az[:, :, c, 0, :]).then_inc(pads_ready, 1)
                            dve.tensor_copy(heads(zpad)[c], az[:, :, c, 1, :]).then_inc(pads_ready, 1)
                        dve.wait_ge(r_done, n + 1)
                        dve.wait_ge(stored[u], i2 * 32 + 32)
                        dve.tensor_tensor(ry[:, u, 0, :], lo[:, 1, :], ar[:, u, 1, :], ALU.add).then_inc(r_ready, 1)
                        dve.wait_ge(r_ready, n + 2)
                        dve.sem_inc(slot_used, 1)
                        q = bass.ds(n, 1)
                        dve.wait_ge(g_done, n + 1)
                        dve.wait_ge(gh_finished, n * 2 + 1)
                        dve.tensor_tensor(gt[:, q, :, :].rearrange("p o e t -> p (o e) t"), hi_g,
                                          bd[:].unsqueeze(1).to_broadcast([P, NC_, P]), ALU.mult).then_inc(g_masked, 1)
                        dve.wait_ge(h_done, n + 1)
                        dve.tensor_tensor(hs[:, q, :, :].rearrange("p o e t -> p (o e) t"), hi_h,
                                          pc[:, q, :].rearrange("p o e -> p (o e)").unsqueeze(2).to_broadcast([P, NC_, P]),
                                          ALU.mult).then_inc(h_scaled, 1)

            @block.scalar
            def _(act):
                act.sem_inc(y_ready, 1)
                act.sem_inc(stored0, 32)
                act.sem_inc(stored1, 32)
                with act.Fori(0, KD // 2) as i2:
                    for u in range(2):
                        n = i2 * 2 + u
                        act.wait_ge(rows_turned, n + 1)
                        act.activation(rows[:], hi_rows, ACT.Copy).then_inc(rows_copied, 1)
                        for lv in range(LEVELS):
                            for c in range(2):
                                act.wait_ge(w_done, n * (2 * LEVELS) + (2 * lv + c + 1))
                                own = slice(TT * c, TT * c + TT)
                                act.activation(ws[:, own], lo_w[:, own], ACT.Copy).then_inc(w_copied, 1)
                        act.wait_ge(mv_done, n + 1)
                        act.activation(rhs[:, :, 1, :], lo_mv, ACT.Copy).then_inc(mv_copied, 1)
                        act.wait_ge(y_done, n + 1)
                        act.wait_ge(stored[u], i2 * 32 + 32)
                        act.activation(ry[:, u, 1, :], lo[:, 2, :], ACT.Copy).then_inc(y_ready, 1)
                        act.wait_ge(y_ready, n + 2)
                        act.wait_ge(r_ready, n + 2)
                        q = bass.ds(n, 1)
                        for j in range(2):
                            act.dma_start(d["ry"][j].rearrange("(q p) t -> p q t", p=P)[:, q, :].rearrange(
                                "p o t -> p (o t)"), ry[:, u, j, :]).then_inc(stored[u], 16)
                act.wait_ge(stored0, 32 * (KD // 2) + 32)
                act.wait_ge(stored1, 32 * (KD // 2) + 32)

            @block.gpsimd
            def _(pool):
                pool.sem_inc(slot_used, 2)
                pool.sem_inc(gh_finished, 1)
                pool.wait_ge(small_loaded, 96)
                with pool.Fori(0, KD // 2) as i2:
                    for u in range(2):
                        n = i2 * 2 + u
                        pool.wait_ge(ba_masked, n + 1)
                        for lv in range(LEVELS):
                            pool.tensor_tensor(em[:, lv], ba[:, :, 0, :], emask[:, lv].unsqueeze(1).to_broadcast([P, NP, P]),
                                               ALU.mult).then_inc(em_ready, 1)
                        pool.wait_ge(dve_steps, 3)
                        pool.wait_ge(rows_copied, n + 1)
                        for c in range(2):
                            pool.tensor_copy(rhs[:].rearrange("p (c i) s t -> p i c s t", c=2)[:, :, c, 0, :],
                                             rows[:, 0, :, RC * c:RC * c + RC]).then_inc(pool_steps, 1)
                            pool.tensor_copy(heads(vpad)[c], rows[:, 3, :, RC * c:RC * c + RC]).then_inc(pool_steps, 1)
                        pool.wait_ge(pool_steps, n * 4 + 4)
                        pool.sem_inc(rhs_ready, 1)
                        pool.wait_ge(pads_ready, n * 4 + 4)
                        for pad, pair in ((apad, apair), (zpad, zpair)):
                            pool.tensor_tensor(pair[:], pad[:, :, 0, :], pad[:, :, 1, :], ALU.add).then_inc(pairs_ready, 1)
                        q = bass.ds(n, 1)
                        g, h = (t[:, q, :, :].rearrange("p o e t -> p (o e) t") for t in (gt, hs))
                        pool.wait_ge(g_masked, n + 2)
                        pool.tensor_tensor(g, g, ident[:].unsqueeze(1).to_broadcast([P, NC_, P]), ALU.add).then_inc(gh_finished, 1)
                        pool.wait_ge(h_scaled, n + 2)
                        pool.tensor_tensor(h, h, bd[:].unsqueeze(1).to_broadcast([P, NC_, P]), ALU.mult).then_inc(gh_finished, 1)


def rwkv_scan(nc, d, gt, hs, pc):
    HQ = KD // 2
    with phase(nc, "loaded", "mean_loaded", "late_loaded", "y_done", "y_added", "s_done", "s_scaled", "s_ready", "mu_done", "centred",
               "squared", "var_done", "var_copied", "inverted", "pre_steps", "factor_ready", "scaled", "out_ready", "stored",
               "cleared") as (
            loaded, mean_loaded, late_loaded, y_done, y_added, s_done, s_scaled, s_ready, mu_done, centred, squared, var_done,
            var_copied, inverted, pre_steps, factor_ready, scaled, out_ready, stored, cleared), ExitStack() as ctx:
        sb, ps = tensors(nc, ctx)
        ry = sb("rs_ry", [P, 2, KD, T])
        s = sb("rs_s", [P, KD, P])
        bonus = sb("rs_bonus", [P, KD, T])
        gate = sb("rs_gate", [P, KD, T])
        cols = sb("rs_cols", [P, 2, KD])
        mean = sb("rs_mean", [P, P])
        eps = sb("rs_eps", [P, 1])
        sq = sb("rs_sq", [P, 2, KD, RC])
        dev = sb("rs_dev", [P, 2, KD, RC])
        yp = ps("rs_yp", [P, KD, RC])
        sp_ = ps("rs_sp", [P, KD, P])
        mp = ps("rs_mp", [P, 2, KD, RC])
        vp = ps("rs_vp", [P, 2, KD, RC])
        y = ry[:, 1]

        def at(e):
            return (e % 2) * TT + e // 2

        def of(t, e):
            return t[:, :, e * RC:(e + 1) * RC]

        with nc.Block() as block:
            @block.sync
            def _(sp):
                sp.dma_start(ry[:], d["ry"].rearrange("j (q p) t -> p j q t", p=P)).then_inc(loaded, 16)
                out = d["tmT"].rearrange("(q p) t -> p q t", p=P)
                for i in range(TT):
                    sp.wait_ge(out_ready, 2 * (i + 1))
                    sp.dma_start(out[:, :, i * P:(i + 1) * P], y[:, :, i * P:(i + 1) * P]).then_inc(stored, 16)
                sp.wait_ge(stored, 16 * TT)

            @block.tensor
            def _(pe):
                pe.wait_ge(loaded, 16)
                pe.wait_ge(mean_loaded, 16)
                for e in range(1, NC_ + 2):
                    if e < NC_ - 1:
                        for half in range(2):
                            pe.wait_ge(s_ready, 2 * (e - 1) + half + 1)
                            for q in range(half * HQ, (half + 1) * HQ):
                                mm = pe.matmul(sp_[:, q, :], gt[:, q, at(e), :], s[:, q, :], start=True, stop=True)
                            mm.then_inc(s_done, 1)
                    if e < NC_:
                        pe.wait_ge(s_ready, 2 * e)
                        if e > 1:
                            pe.wait_ge(y_added, e - 1)
                        for q in range(KD):
                            mm = pe.matmul(yp[:, q, :], s[:, q, :], of(ry[:, 0], e)[:, q], start=True, stop=True)
                        mm.then_inc(y_done, 1)
                    m = e - 1
                    if m < NC_:
                        if m:
                            pe.wait_ge(y_added, m)
                        if m >= 2:
                            pe.wait_ge(centred, m - 1)
                        pe.matmul(mp[:, m % 2], mean[:], of(y, m), start=True, stop=True).then_inc(mu_done, 1)
                    v = e - 2
                    if v >= 0:
                        pe.wait_ge(squared, v + 1)
                        if v >= 2:
                            pe.wait_ge(var_copied, v - 1)
                        pe.matmul(vp[:, v % 2], mean[:], sq[:, v % 2], start=True, stop=True).then_inc(var_done, 1)

            @block.scalar
            def _(act):
                act.dma_start(mean[:], d["mean64"]).then_inc(mean_loaded, 16)
                act.dma_start(cols[:], d["lnx_cols"]).then_inc(late_loaded, 16)
                act.dma_start(bonus[:], d["bonus"].rearrange("(q p) t -> p q t", p=P)).then_inc(late_loaded, 16)
                act.dma_start(gate[:], d["vg"][1].rearrange("(q p) t -> p q t", p=P)).then_inc(late_loaded, 16)
                act.wait_ge(cleared, 1)
                for n in range(NC_ + 1):
                    if n < NC_:
                        act.wait_ge(centred, n + 1)
                        if n >= 2:
                            act.wait_ge(var_done, n - 1)
                        act.activation(sq[:, n % 2], of(y, n), ACT.Square).then_inc(squared, 1)
                    if n:
                        v = n - 1
                        act.wait_ge(var_done, v + 1)
                        if v >= 2:
                            act.wait_ge(factor_ready, v - 1)
                        act.activation(dev[:, v % 2], vp[:, v % 2], ACT.Sqrt, bias=eps[:]).then_inc(var_copied, 1)

            @block.gpsimd
            def _(pool):
                pool.wait_ge(late_loaded, 48)
                n = 0

                def columns(j):
                    return cols[:, j, :].unsqueeze(2).to_broadcast([P, KD, RC])

                def factors(e):
                    nonlocal n
                    pool.tensor_tensor(of(bonus, e), of(bonus, e), columns(1), ALU.add).then_inc(pre_steps, 1)
                    pool.wait_ge(pre_steps, n + 1)
                    pool.tensor_tensor(of(bonus, e), of(bonus, e), of(gate, e), ALU.mult).then_inc(pre_steps, 1)
                    pool.wait_ge(pre_steps, n + 2)
                    pool.tensor_tensor(of(gate, e), of(gate, e), columns(0), ALU.mult).then_inc(pre_steps, 1)
                    pool.wait_ge(pre_steps, n + 3)
                    n += 3

                factors(0)
                for e in range(NC_):
                    if e + 1 < NC_:
                        factors(e + 1)
                    pool.wait_ge(inverted, e + 1)
                    pool.tensor_tensor(of(gate, e), of(gate, e), dev[:, e % 2], ALU.mult).then_inc(factor_ready, 1)

            @block.vector
            def _(dve):
                dve.memset(eps[:], 64e-5).then_inc(cleared, 1)
                dve.wait_ge(loaded, 16)
                for half in range(2):
                    own = slice(half * HQ, (half + 1) * HQ)
                    dve.tensor_copy(s[:, own], hs[:, own, 0, :]).then_inc(s_ready, 1)
                for e in range(1, NC_ + 4):
                    if e < NC_ - 1:
                        for half in range(2):
                            if half == 0:
                                dve.wait_ge(y_done, e)
                            dve.wait_ge(s_done, 2 * (e - 1) + half + 1)
                            own = slice(half * HQ, (half + 1) * HQ)
                            dve.tensor_tensor(s[:, own], sp_[:, own], pc[:, own, at(e)].unsqueeze(2).to_broadcast([P, HQ, P]),
                                              ALU.mult).then_inc(s_scaled, 1)
                        for half in range(2):
                            dve.wait_ge(s_scaled, 2 * (e - 1) + half + 1)
                            own = slice(half * HQ, (half + 1) * HQ)
                            dve.tensor_tensor(s[:, own], s[:, own], hs[:, own, at(e), :], ALU.add).then_inc(s_ready, 1)
                    if e < NC_:
                        dve.wait_ge(y_done, e)
                        dve.tensor_tensor(of(y, e), of(y, e), yp[:], ALU.add).then_inc(y_added, 1)
                    m = e - 1
                    if m < NC_:
                        dve.wait_ge(mu_done, m + 1)
                        dve.tensor_tensor(of(y, m), of(y, m), mp[:, m % 2], ALU.subtract).then_inc(centred, 1)
                    v = e - 3
                    if 0 <= v < NC_:
                        dve.wait_ge(var_copied, v + 1)
                        dve.reciprocal(dev[:, v % 2], dev[:, v % 2]).then_inc(inverted, 1)
                    o = e - 4
                    if o >= 0:
                        dve.wait_ge(factor_ready, o + 1)
                        dve.wait_ge(squared, o + 1)
                        dve.tensor_tensor(of(y, o), of(y, o), of(gate, o), ALU.mult).then_inc(scaled, 1)
                        dve.wait_ge(scaled, o + 1)
                        dve.tensor_tensor(of(y, o), of(y, o), of(bonus, o), ALU.add).then_inc(out_ready, 1)


def rwkv_recurrence(nc, d):
    with ExitStack() as ctx:
        sb, _ = tensors(nc, ctx)
        gt = sb("rr_gt", [P, KD, NC_, P])
        hs = sb("rr_hs", [P, KD, NC_, P])
        pc = sb("rr_pc", [P, KD, NC_])
        rwkv_chunks(nc, d, gt, hs, pc)
        rwkv_scan(nc, d, gt, hs, pc)
AH = 16
IH = 8
QL, KL = 256, 128
DSA_IN = QL + KL + 64 + IH
CHOSEN = 128
MASKED = -1.0e30
TAKEN = -3.0e38


def sparse_projections(nc, d, o):
    M = 640
    with phase(nc, "bias_loaded", "bias_done", "bias_copied", "bias_stored", "x_loaded", "w_loaded", "vec_loaded", "h_done", "h_copied", "summed", "rooted", "rows_done",
               "turned", "turn_copied", "bank_done", "act_copied", "dve_copied", "dve_steps", "pool_steps") as (
            bias_loaded, bias_done, bias_copied, bias_stored, x_loaded, w_loaded, vec_loaded, h_done, h_copied, summed, rooted, rows_done, turned, turn_copied,
            bank_done, act_copied, dve_copied, dve_steps, pool_steps), ExitStack() as ctx:
        sb, ps = tensors(nc, ctx)
        x = sb("sp_x", [P, KD, T])
        win = sb("sp_win", [P, KD, DSA_IN])
        wuq = sb("sp_wuq", [P, 2, D])
        wqi = sb("sp_wqi", [P, 2, IH * 64])
        wuk = sb("sp_wuk", [P, D])
        wuv = sb("sp_wuv", [P, D])
        vec = sb("sp_vec", [P, QL + KL + 128])
        ident = sb("sp_ident", [P, P])
        h = sb("sp_h", [P, TT, DSA_IN])
        ki2 = sb("sp_ki2", [P, TT, 2, 64])
        junk = sb("sp_junk", [P, QL])
        bs = sb("sp_bs", [P, TT, 6])
        mv = sb("sp_mv", [P, TT, 2])
        st = sb("sp_st", [P, TT, 3])
        rt = sb("sp_rt", [P, TT, 3])
        mhalf = sb("sp_mhalf", [P, 2])
        lat = sb("sp_lat", [P, 3, T])
        rb = sb("sp_rb", [32, AH])
        hot = sb("sp_hot", [32, M])
        fb = sb("sp_fb", [AH, M])
        hp = ps("sp_hp", [P, TT, W])
        op = ps("sp_op", [P, 4, W])
        outs = []
        for m in range(KD):
            outs.append(([(wuq[:, k, m * P:(m + 1) * P], lat[:, k, :]) for k in range(2)], o["qT"][:, m, :]))
        for m in range(IH * 64 // P):
            outs.append(([(wqi[:, k, m * P:(m + 1) * P], lat[:, k, :]) for k in range(2)], o["qiT"][:, m, :]))
        for m in range(KD):
            outs.append(([(wuk[:, m * P:(m + 1) * P], lat[:, 2, :])], o["kT"][:, m, :]))
        for i in range(TT):
            for half in range(2):
                outs.append(([(lat[:, 2, i * P:(i + 1) * P], wuv[:, half * W:(half + 1) * W])],
                             o["v"][:, i, half * W:(half + 1) * W]))
        with nc.Block() as block:
            @block.sync
            def _(sp):
                sp.dma_start(rb[:], d["rel_bias"]).then_inc(bias_loaded, 16)
                sp.dma_start(hot[:], d["buckets"]).then_inc(bias_loaded, 16)
                sp.dma_start(x[:], d["x4T"].rearrange("(k p) t -> p k t", p=P)).then_inc(x_loaded, 16)
                sp.dma_start(win[:], d["dsa_w_in"].rearrange("(k p) n -> p k n", p=P)).then_inc(x_loaded, 16)
                sp.dma_start(vec[:], over_partitions(d["dsa_vecs"])).then_inc(vec_loaded, 16)
                sp.dma_start(ident[:], d["ident"]).then_inc(vec_loaded, 16)
                sp.dma_start(wuq[:], d["dsa_w_uq"].rearrange("(k p) n -> p k n", p=P)).then_inc(w_loaded, 16)
                sp.dma_start(wqi[:], d["dsa_w_qidx"].rearrange("(k p) n -> p k n", p=P)).then_inc(w_loaded, 16)
                sp.dma_start(wuk[:], d["dsa_w_uk"]).then_inc(w_loaded, 16)
                sp.dma_start(wuv[:], d["dsa_w_uv"]).then_inc(w_loaded, 16)
                sp.wait_ge(bias_copied, 2)
                sp.dma_start(d["fb"], fb[:].unsqueeze(1).to_broadcast([AH, P, M])).then_inc(bias_stored, 16)
                sp.wait_ge(bias_stored, 16)

            @block.tensor
            def _(pe):
                pe.wait_ge(bias_loaded, 32)
                pe.matmul(op[0:AH, 0, :], rb[:], hot[:, 0:W], start=True, stop=True).then_inc(bias_done, 1)
                pe.matmul(op[0:AH, 1, 0:M - W], rb[:], hot[:, W:M], start=True, stop=True).then_inc(bias_done, 1)
                pe.wait_ge(x_loaded, 32)
                for i in range(TT):
                    for k in range(KD):
                        mm = pe.matmul(hp[:, i, 0:DSA_IN], x[:, k, i * P:(i + 1) * P], win[:, k, :], start=(k == 0),
                                       stop=(k == KD - 1))
                    mm.then_inc(h_done, 1)
                pe.wait_ge(vec_loaded, 32)
                for i in range(TT):
                    pe.wait_ge(rows_done, i + 1)
                    for c, rows in enumerate((h[:, i, 0:P], h[:, i, P:QL], h[:, i, QL:QL + KL],
                                              ki2[:, i].rearrange("p a b -> p (a b)"))):
                        mm = pe.transpose(hp[:, i, c * P:(c + 1) * P], rows, ident[:])
                    mm.then_inc(turned, 1)
                pe.wait_ge(turn_copied, TT)
                pe.wait_ge(w_loaded, 64)
                pe.wait_ge(bias_copied, 2)
                for n, (parts, _) in enumerate(outs):
                    if n >= 4:
                        pe.wait_ge((act_copied, dve_copied)[n % 2], n // 2 - 1)
                    for j, (lhs, rhs) in enumerate(parts):
                        mm = pe.matmul(op[:, n % 4, :], lhs, rhs, start=(j == 0), stop=(j == len(parts) - 1))
                    mm.then_inc(bank_done, 1)

            @block.scalar
            def _(act):
                for i in range(TT):
                    act.wait_ge(h_done, i + 1)
                    act.activation(h[:, i, :], hp[:, i, 0:DSA_IN], ACT.Copy).then_inc(h_copied, 1)
                for i in range(TT):
                    act.wait_ge(turned, i + 1)
                    act.activation(lat[:, :, i * P:(i + 1) * P], hp[:, i, 0:3 * P].rearrange("p (c t) -> p c t", c=3),
                                   ACT.Copy)
                    act.activation(o["kiT"][:, i * P:(i + 1) * P], hp[:, i, 3 * P:4 * P], ACT.Copy).then_inc(turn_copied, 1)
                for n in range(0, len(outs), 2):
                    act.wait_ge(bank_done, n + 1)
                    act.activation(outs[n][1], op[:, n % 4, :], ACT.Copy).then_inc(act_copied, 1)

            @block.gpsimd
            def _(pool):
                steps = Steps(pool, pool_steps)
                steps(pool.memset(mhalf[:], -0.5))
                for i in range(TT):
                    pool.wait_ge(summed, i + 1)
                    steps(root_reciprocal(pool, steps, rt[:, i, 0:2], st[:, i, 0:2], 1e-6, mhalf[:]), wait=False)
                    root_reciprocal(pool, steps, rt[:, i, 2:3], st[:, i, 2:3], 1e-5, mhalf[:, 0:1]).then_inc(rooted, 1)

            @block.vector
            def _(dve):
                step = Steps(dve, dve_steps)
                dve.wait_ge(bias_done, 2)
                dve.tensor_copy(fb[:, 0:W], op[0:AH, 0, :]).then_inc(bias_copied, 1)
                dve.tensor_copy(fb[:, W:M], op[0:AH, 1, 0:M - W]).then_inc(bias_copied, 1)
                dve.wait_ge(vec_loaded, 32)
                for i in range(TT):
                    dve.wait_ge(h_copied, i + 1)
                    cq, ckv, ki = h[:, i, 0:QL], h[:, i, QL:QL + KL], h[:, i, QL + KL:QL + KL + 64]
                    step(dve.tensor_tensor_reduce(junk[:], cq, cq, 1.0 / QL, 0.0, ALU.mult, ALU.add, st[:, i, 0:1]))
                    step(dve.tensor_tensor_reduce(junk[:, 0:KL], ckv, ckv, 1.0 / KL, 0.0, ALU.mult, ALU.add,
                                                  st[:, i, 1:2]), wait=False)
                    step(dve.bn_stats(bs[:, i, :], ki))
                    step(dve.bn_aggr(mv[:, i, :], bs[:, i, :]))
                    dve.tensor_copy(st[:, i, 2:3], mv[:, i, 1:2]).then_inc(summed, 1)
                    step(dve.tensor_scalar(o["wi"][:, i, :], h[:, i, QL + KL + 64:DSA_IN],
                                           IH ** -0.5 * 64 ** -0.5, None, ALU.mult), wait=False)
                    dve.wait_ge(rooted, i + 1)
                    step(dve.scalar_tensor_tensor(cq, cq, rt[:, i, 0:1], vec[:, 0:QL], ALU.mult, ALU.mult), wait=False)
                    step(dve.scalar_tensor_tensor(ckv, ckv, rt[:, i, 1:2], vec[:, QL:QL + KL], ALU.mult, ALU.mult), wait=False)
                    step(dve.tensor_scalar(ki, ki, mv[:, i, 0:1], rt[:, i, 2:3], ALU.subtract, ALU.mult))
                    step(dve.tensor_tensor(ki, ki, vec[:, QL + KL:QL + KL + 64], ALU.mult))
                    for half in range(2):
                        step(dve.tensor_tensor(ki2[:, i, half, :], ki, vec[:, QL + KL + 64:QL + KL + 128], ALU.add), wait=False)
                    step.wait()
                    dve.sem_inc(rows_done, 1)
                for n in range(1, len(outs), 2):
                    dve.wait_ge(bank_done, n + 1)
                    dve.tensor_copy(outs[n][1], op[:, n % 4, :]).then_inc(dve_copied, 1)


def choose_keys(nc, d, o):
    tiles = range(1, TT)
    with phase(nc, "s_done", "relu_done", "scored", "causal", "chain", "masked", "cleared", "all_done") as (
            s_done, relu_done, scored, causal, chain, masked, cleared, all_done), ExitStack() as ctx:
        sb, ps = tensors(nc, ctx)
        r = sb("ck_r", [P, 2, T])
        sc = sb("ck_sc", [P, TT, T])
        top = sb("ck_top", [P, TT, 8])
        sp_ = ps("ck_sp", [P, 4, T])
        order = [(i, h) for i in tiles for h in range(IH)]
        with nc.Block() as block:
            @block.tensor
            def _(pe):
                for n, (i, h) in enumerate(order):
                    if n >= 4:
                        pe.wait_ge(relu_done, n - 3)
                    rows, keys = slice(64 * (h % 2), 64 * (h % 2) + 64), (i + 1) * P
                    pe.matmul(sp_[:, n % 4, 0:keys], o["qiT"][rows, h // 2, i * P:(i + 1) * P], o["kiT"][rows, 0:keys],
                              start=True, stop=True).then_inc(s_done, 1)

            @block.scalar
            def _(act):
                for n, (i, h) in enumerate(order):
                    keys = (i + 1) * P
                    act.wait_ge(s_done, n + 1)
                    if n >= 2:
                        act.wait_ge(scored, n - 1)
                    act.activation(r[:, n % 2, 0:keys], sp_[:, n % 4, 0:keys], ACT.Relu).then_inc(relu_done, 1)

            @block.gpsimd
            def _(pool):
                pool.memset(o["am"][:, 0, :], 0.0).then_inc(cleared, 1)
                pool.wait_ge(cleared, 1)
                first = o["am"][:, 0, 0:P]
                pool.affine_select(out=first, in_=first, compare_op=ALU.is_ge, fill=MASKED, base=0, pattern=[[-1, P]],
                                   channel_multiplier=1).then_inc(cleared, 1)
                for i in tiles:
                    pool.wait_ge(scored, IH * i)
                    last = sc[:, i, i * P:(i + 1) * P]
                    pool.affine_select(out=last, in_=last, compare_op=ALU.is_ge, fill=MASKED, base=0, pattern=[[-1, P]],
                                       channel_multiplier=1).then_inc(causal, 1)

            @block.vector
            def _(dve):
                for n, (i, h) in enumerate(order):
                    keys = (i + 1) * P
                    dve.wait_ge(relu_done, n + 1)
                    if h == 0:
                        ins = dve.tensor_scalar(sc[:, i, 0:keys], r[:, n % 2, 0:keys], o["wi"][:, i, h:h + 1], None, ALU.mult)
                    else:
                        dve.wait_ge(scored, n)
                        ins = dve.scalar_tensor_tensor(sc[:, i, 0:keys], r[:, n % 2, 0:keys], o["wi"][:, i, h:h + 1],
                                                       sc[:, i, 0:keys], ALU.mult, ALU.add)
                    ins.then_inc(scored, 1)
                dve.wait_ge(causal, TT - 1)
                step = Steps(dve, chain)
                for _ in range(CHOSEN // 8):
                    for i in tiles:
                        step(dve.max(top[:, i, :], sc[:, i, 0:(i + 1) * P]), wait=False)
                    step.wait()
                    for i in tiles:
                        rows = sc[:, i, 0:(i + 1) * P]
                        step(dve.match_replace(rows, top[:, i, :], rows, TAKEN), wait=False)
                    step.wait()
                for i in tiles:
                    dve.tensor_scalar(o["am"][:, i, 0:(i + 1) * P], sc[:, i, 0:(i + 1) * P], -2.0e38, MASKED, ALU.is_gt,
                                      ALU.mult).then_inc(masked, 1)


def sparse_attention(nc, d, o, split):
    SCALE = 64 ** -0.5
    N = AH * TT
    SL = 4
    TURN, PV = 3, 4

    def job(n):
        return n // (2 * TT) * 2 + n % 2, n % (2 * TT) // 2

    with phase(nc, "bias_loaded", "ident_loaded", "bias_ready", "s_done", "logits_done", "max_done", "exp_done",
               "p_turned", "p_copied", "o_done", "o_scaled", "o_turned", "hi_done", "o_out",
               "dve_steps") as (
            bias_loaded, ident_loaded, bias_ready, s_done, logits_done, max_done, exp_done, p_turned, p_copied,
            o_done, o_scaled, o_turned, hi_done, o_out, dve_steps), ExitStack() as ctx:
        sb, ps = tensors(nc, ctx)
        tb = sb("sa_tb", [P, AH, T])
        ident = sb("sa_ident", [P, P])
        bm = sb("sa_bm", [P, 2, T])
        lg = sb("sa_lg", [P, SL, T])
        e = sb("sa_e", [P, SL, T])
        eT = sb("sa_eT", [P, SL, T])
        st = sb("sa_st", [P, N, 2])
        rs = sb("sa_rs", [P, N])
        rows = sb("sa_rows", [P, TT, D])
        sp_ = ps("sa_sp", [P, 4, T])
        tp = ps("sa_tp", [P, 2, T])
        op = ps("sa_op", [P, 2, T])
        rp = sp_[:].rearrange("p u t -> p (u t)").rearrange("p (u k t) -> p u k t", u=2, k=KD)
        with nc.Block() as block:
            @block.sync
            def _(sp):
                sp.dma_start(ident[:], d["ident"]).then_inc(ident_loaded, 16)
                fb = d["fb"]
                diagonals = bass.AP(fb.tensor, P - 1, [[640 - 1, P], [P * 640, AH], [1, T]])
                sp.dma_start(tb[:], diagonals).then_inc(bias_loaded, 16)

            @block.gpsimd
            def _(pool):
                pool.wait_ge(bias_loaded, 16)
                for n in range(N):
                    h, i = job(n)
                    if n >= 2:
                        pool.wait_ge(logits_done, n - 1)
                    pool.tensor_tensor(bm[:, n % 2, 0:(i + 1) * P], tb[:, h, 384 - i * P:T], o["am"][:, i, 0:(i + 1) * P],
                                       ALU.add).then_inc(bias_ready, 1)

            @block.tensor
            def _(pe):
                pe.wait_ge(ident_loaded, 16)
                for n in range(N + PV):
                    for j in ((n, n + 1) if n < N and n % 2 == 0 else ()):
                        h, i = job(j)
                        if j >= 4:
                            pe.wait_ge(logits_done, j - 3)
                        r = slice(64 * (h % 2), 64 * (h % 2) + 64)
                        pe.matmul(sp_[:, j % 4, 0:(i + 1) * P], o["qT"][r, h // 2, i * P:(i + 1) * P],
                                  o["kT"][r, h // 2, 0:(i + 1) * P], start=True, stop=True).then_inc(s_done, 1)
                    if TURN <= n < N + TURN:
                        m = n - TURN
                        i = job(m)[1]
                        pe.wait_ge(exp_done, m + 1)
                        if m >= 2:
                            pe.wait_ge(p_copied, m - 1)
                        for c in range(i + 1):
                            mm = pe.transpose(tp[:, m % 2, c * P:(c + 1) * P], e[:, m % SL, c * P:(c + 1) * P], ident[:])
                        mm.then_inc(p_turned, 1)
                    if n >= PV:
                        m = n - PV
                        h, i = job(m)
                        pe.wait_ge(p_copied, m + 1)
                        if m >= 2:
                            pe.wait_ge(o_scaled, m - 1)
                        for c in range(i + 1):
                            mm = pe.matmul(op[:, m % 2, 0:64], eT[:, m % SL, c * P:(c + 1) * P],
                                           o["v"][:, c, h * 64:(h + 1) * 64], start=(c == 0), stop=(c == i))
                        mm.then_inc(o_done, 1)
                pe.wait_ge(o_scaled, N)
                for i in range(TT):
                    if i >= 2:
                        pe.wait_ge(o_out, i - 1)
                    for c in range(KD):
                        mm = pe.transpose(rp[:, i % 2, c, :], rows[:, i, c * P:(c + 1) * P], ident[:])
                    mm.then_inc(o_turned, 1)

            @block.vector
            def _(dve):
                step = Steps(dve, dve_steps)

                def scale_o(m):
                    h, i = job(m)
                    step(dve.reciprocal(rs[:, m:m + 1], st[:, m, 1:2]))
                    dve.wait_ge(o_done, m + 1)
                    dve.tensor_scalar(rows[:, i, h * 64:(h + 1) * 64], op[:, m % 2, 0:64], rs[:, m:m + 1], None,
                                      ALU.mult).then_inc(o_scaled, 1)

                for n in range(N + PV + 1):
                    if n < N:
                        keys = (job(n)[1] + 1) * P
                        dve.wait_ge(s_done, n + 1)
                        dve.wait_ge(bias_ready, n + 1)
                        if n >= SL:
                            dve.wait_ge(exp_done, n - SL + 1)
                        dve.scalar_tensor_tensor(lg[:, n % SL, 0:keys], sp_[:, n % 4, 0:keys], SCALE,
                                                 bm[:, n % 2, 0:keys], ALU.mult, ALU.add).then_inc(logits_done, 1)
                    if 1 <= n <= N:
                        m = n - 1
                        dve.wait_ge(logits_done, m + 1)
                        dve.tensor_reduce(st[:, m, 0:1], lg[:, m % SL, 0:(job(m)[1] + 1) * P], AX.X, ALU.max,
                                          negate=True).then_inc(max_done, 1)
                    if n > PV:
                        scale_o(n - PV - 1)
                for i in range(TT):
                    split_lo(dve, split, i, rp, hi_done, o_out)

            @block.scalar
            def _(act):
                for n in range(N + TURN):
                    if n >= TURN:
                        m = n - TURN
                        keys = (job(m)[1] + 1) * P
                        act.wait_ge(p_turned, m + 1)
                        if m >= SL:
                            act.wait_ge(o_done, m - SL + 1)
                        act.activation(eT[:, m % SL, 0:keys], tp[:, m % 2, 0:keys], ACT.Copy).then_inc(p_copied, 1)
                    if n < N:
                        keys = (job(n)[1] + 1) * P
                        act.wait_ge(max_done, n + 1)
                        if n >= SL:
                            act.wait_ge(p_turned, n - SL + 1)
                        act.activation(e[:, n % SL, 0:keys], lg[:, n % SL, 0:keys], ACT.Exp, bias=st[:, n, 0:1],
                                       accum_out=st[:, n, 1:2]).then_inc(exp_done, 1)
                for i in range(TT):
                    act.wait_ge(o_turned, i + 1)
                    act.activation(split[0][:, :, i * P:(i + 1) * P], rp[:, i % 2], ACT.Copy).then_inc(hi_done, 1)


def sparse_block(nc, d, split):
    with ExitStack() as ctx:
        sb, _ = tensors(nc, ctx)
        o = {"qT": sb("so_qT", [P, KD, T]), "kT": sb("so_kT", [P, KD, T]), "v": sb("so_v", [P, TT, D]),
             "qiT": sb("so_qiT", [P, IH // 2, T]), "kiT": sb("so_kiT", [P, T]), "wi": sb("so_wi", [P, TT, IH]),
             "am": sb("so_am", [P, TT, T])}
        sparse_projections(nc, d, o)
        choose_keys(nc, d, o)
        sparse_attention(nc, d, o, split)


def whole_block(nc, d):
    with ExitStack() as ctx:
        h = split_pair(nc, ctx, "wb_h", LK)
        with ExitStack() as inner:
            sb, _ = tensors(nc, inner)
            rows, rstd = sb("wb_rows", [P, LK // P, D]), sb("wb_rstd", [P, LK // P])
            modulation(nc, d, rows, rstd)
            premix(nc, d, rows, rstd, h)
        project(nc, None, [t[:, :, CTX:LK] for t in h], (d["w_in"][:, 0:D], d["q"]), (d["w_in"][:, 3 * D:7 * D], d["zg"]))
        project(nc, None, h, (d["w_in"][:, D:3 * D], d["kv"]))
    diff_attention(nc, d)
    with ExitStack() as ctx:
        x = split_pair(nc, ctx, "wb_x")
        with ExitStack() as inner:
            ya, a_rows = product_rows(nc, inner, "wb_ya")
            ys, s_rows = product_rows(nc, inner, "wb_ys")
            spatial_gating(nc, d, x)
            project(nc, None, x, (d["w_branch_sgu"], None), keep=ys)
            project(nc, d["oT"], x, (d["w_branch_attn"], None), keep=ya)
            combine_branches(nc, d, a_rows, s_rows, x)
        with ExitStack() as inner:
            y, rows = product_rows(nc, inner, "wb_yo")
            project(nc, None, x, (d["w_out"], None), keep=y)
            join_rms(nc, d, "x", rows, "g_post_mix", 2, "x1", split=x, g_pre="g_pre_ffn", shift_at=3)
        project(nc, None, x, (d["peer_w_query"], d["qp"]))
        sb, _ = tensors(nc, ctx)
        sel = sb("wb_sel", [P, 3, T])
        expert_choice(nc, d, sel)
        expert_gates(nc, d, sel)
        total = sb("wb_po", [P, TT, D])
        experts(nc, d, x, total)
        join_rms(nc, d, "x1", total[:].rearrange("p t (u w) -> p t u w", u=2), "g_post_ffn", 5, "x2", hT_out="x2T")
    rwkv_inputs(nc, d)
    rwkv_recurrence(nc, d)
    with ExitStack() as ctx:
        projected_ffn(nc, d, d["tmT"], split_pair(nc, ctx, "wb_x3"), d["w_o"], 0, "x2", "x3", "x4", "x4T")
    with ExitStack() as ctx:
        x = split_pair(nc, ctx, "wb_x5")
        sparse_block(nc, d, x)
        projected_ffn(nc, d, None, x, d["dsa_w_o"], 1, "x4", "x5", "out", None)


def product_rows(nc, ctx, name):
    sb, _ = tensors(nc, ctx)
    y = sb(name, [P, 2, TT, W])
    return y, y[:].rearrange("p u t w -> p t u w")


def projected_ffn(nc, d, aT, x, w, n, x_in, x_mid, x_out, xT_out):
    def join(x_from, rows, at, x_to, **turned):
        join_ln(nc, d, x_from, rows, d["ln_g"][at:at + 1], d["ln_b"][at:at + 1], x_to, **turned)

    with ExitStack() as ctx:
        with ExitStack() as inner:
            y, rows = product_rows(nc, inner, f"pf_y{n}")
            project(nc, aT, x, (w, None), keep=y)
            join(x_in, rows, 2 * n, x_mid, split=x)
        sb, _ = tensors(nc, ctx)
        raw = sb(f"pf_raw{n}", [P, 2, 2, D])
        conv_ffn(nc, d, x, d["w_up"][n], d["conv_w"][n], d["conv_b"][n], d["w_down"][n], raw)
        join(x_mid, raw[:].rearrange("p a b (u w) -> p (a b) u w", u=2), 2 * n + 1, x_out, xT_out=xT_out)


SCRATCH = {
    "mod": (1, 8 * D), "q": (T, D), "kv": (LK, 2 * D), "zg": (T, 4 * D), "oT": (D, T), "x1": (T, D),
    "qp": (T, SEG * NK), "G": (T // RB, NK, NK, RB), "x2": (T, D),
    "x2T": (D, T), "vg": (2, D, T), "arbk": (KD, P, 4, T), "bonus": (D, T), "pc": (P, KD, NC_), "ry": (2, D, T),
    "tmT": (D, T), "x3": (T, D), "x4": (T, D), "x4T": (D, T), "fb": (AH, P, 640), "x5": (T, D),
}


def constants():
    f = np.float32
    c = {"ident": np.eye(P, dtype=f), "iota": np.tile(np.arange(P, dtype=f), (P, 1))}
    t = np.arange(T)
    inv = f(10000.0) ** (-np.arange(16, dtype=f) / f(16))
    ang = np.concatenate([(t // 64).astype(f)[:, None] * inv, (t % 64).astype(f)[:, None] * inv], 1)
    c["rope"] = np.stack([np.cos(ang), np.sin(ang)]).astype(f).reshape(2, TT, P, 32).transpose(2, 0, 1, 3)
    start = (np.arange(T) % RC == 0).astype(f)
    c["starts"] = np.tile(np.stack([1 - start, start])[None], (P, 1, 1)).astype(f)
    c["ones64"] = np.kron(np.eye(2, dtype=f), np.ones((64, 64), f))
    c["mean64"] = c["ones64"] / f(64)
    s, t = np.arange(P)[:, None], np.arange(P)[None]
    same = s // RC == t // RC
    c["mask2"] = np.stack([(s < t) & same, (s <= t) & same], 1).astype(f)

    def join(m):
        return ((s // (2 * m) == t // (2 * m)) & (s // m < t // m)).astype(f)

    c["lmask"] = np.stack([join(1).T, join(1)], 1)
    c["emask"] = np.stack([join(m) for m in (2, 4, 8, 16, 32)], 1)
    dist = np.maximum(T - 1 - np.arange(640), 0)
    far = 16 + (np.log(np.maximum(dist, 1).astype(f) / f(16)) / f(np.log(8.0)) * f(16)).astype(np.int32)
    c["buckets"] = (np.arange(32)[:, None] == np.where(dist < 16, dist, np.minimum(far, 31))[None]).astype(f)
    return c


def lay_out(a):
    def cols(v):
        return v.reshape(KD, P).T

    out = {
        "x": a["x"][0], "ctx": a["ctx"][0], "w_ada": a["w_ada"][0], "b_ada": a["b_ada"],
        "c_cols": np.stack([cols(a["c"][0]), cols(a["c_ctx"])], 2), "w_in": a["w_in"][0],
        "lambda4": np.concatenate([a["lambda_q1"], a["lambda_k1"], a["lambda_q2"], a["lambda_k2"]], 1),
        "sgu_wT": a["sgu_w"][0].transpose(2, 0, 1), "sgu_bT": a["sgu_b"][0].T,
        "w_branch_attn": a["w_branch_attn"][0], "w_branch_sgu": a["w_branch_sgu"][0], "w_out": a["w_out"][0],
        "peer_w_query": a["peer_w_query"][0], "keysT": a["peer_sub_keys"][0].transpose(2, 0, 1),
        "uT": a["peer_u"][0].reshape(NK, NK, KD, P).transpose(0, 3, 2, 1), "peer_v": a["peer_v"][0],
        "mix_cols": a["rwkv_mix_2"][0].reshape(6, KD, P).transpose(2, 0, 1), "w_rkv": a["rwkv_w_rkv_2"][0],
        "w0a0_cols": np.stack([cols(a["rwkv_w0_2"][0]), cols(a["rwkv_a0_2"][0])], 1),
        "k_cols": np.stack([cols(a["rwkv_k_k_2"][0]), cols(a["rwkv_k_a_2"][0]), cols(a["rwkv_r_k_2"][0].reshape(-1))], 1),
        "lnx_cols": np.stack([cols(a["rwkv_lnx_g_2"][0]), cols(a["rwkv_lnx_b_2"][0])], 1), "w_o": a["rwkv_w_o_2"][0],
        "ln_g": a["ln_g_2"].reshape(4, D), "ln_b": a["ln_b_2"].reshape(4, D),
        "w_up": a["ffn_w_up_2"], "w_down": a["ffn_w_down_2"],
        "conv_w": a["ffn_conv_w_2"].reshape(2, 3, -1, P).transpose(0, 3, 2, 1),
        "conv_b": a["ffn_conv_b_2"].reshape(2, -1, P).transpose(0, 2, 1),
        "dsa_w_in": a["dsa_w_in_2"][0], "dsa_w_uq": a["dsa_w_uq_2"][0], "dsa_w_qidx": a["dsa_w_qidx_2"][0],
        "dsa_vecs": np.concatenate([a["dsa_q_norm_g_2"], a["dsa_kv_norm_g_2"], a["dsa_kidx_g_2"], a["dsa_kidx_b_2"]], 1),
        "dsa_w_uk": a["dsa_w_uk_2"][0].transpose(2, 0, 1).reshape(P, D),
        "dsa_w_uv": a["dsa_w_uv_2"][0].transpose(1, 0, 2).reshape(P, D),
        "dsa_w_o": a["dsa_w_o_2"][0], "rel_bias": a["rel_bias_2"],
    }
    for n in ("w1", "a1", "g1", "w2", "a2", "g2"):
        out[n] = a[f"rwkv_{n}_2"][0]
    for n in ("g_pre_mix", "g_post_mix", "g_pre_ffn", "g_post_ffn", "b_gate", "subln_g", "sgu_ln_g", "sgu_ln_b"):
        out[n] = a[n]
    return out


def kernel(**inputs):
    import concourse.bacc as bacc
    from concourse.bass_utils import run_bass_kernel_spmd as run

    nc = bacc.Bacc("TRN2", target_bir_lowering=False, num_devices=1)
    arrays, d = {}, {}
    sent = {**lay_out({n: np.asarray(v) for n, v in inputs.items()}), **constants()}
    for n, v in sent.items():
        arrays["in_" + n] = np.ascontiguousarray(v)
        d[n] = nc.dram_tensor("in_" + n, v.shape, F32, kind="ExternalInput").ap()
    for n, shape in SCRATCH.items():
        d[n] = nc.dram_tensor("scratch_" + n, list(shape), F32).ap()
    d["out"] = nc.dram_tensor("out_0_dram", (T, D), F32, kind="ExternalOutput").ap()
    whole_block(nc, d)
    r = run(nc, [arrays], core_ids=[0])
    return r.results[0]["out_0_dram"].reshape(1, T, D)
```
